# Optimizing a Trainium2 kernel written in Bass

```python
import math
import jax
import jax.numpy as jnp
from jax import lax
import numpy as np
import jax, jax.numpy as jnp

D_MODEL = 1024
BATCH = 1
SEQ = 1024
DEPTH = 1

N_MEM = 256
D_MIX = D_MODEL
D_HYENA = D_MIX // 2
HYENA_GROUPS = 8
HYENA_ORDER = 2
D_MLSTM = D_MIX - D_HYENA
MLSTM_HEADS = 4
MLSTM_HEAD_DIM = D_MLSTM // MLSTM_HEADS
MLSTM_CHUNK = 64
FILTER_BANDS = 16
FILTER_EMB = 1 + 2 * FILTER_BANDS
FILTER_HIDDEN = 64
FILTER_DIRS = 2
FILTER_CH = HYENA_ORDER * FILTER_DIRS * D_HYENA
FILTER_OUT_SCALE = 0.05
DECAY_TARGET = 1e-2
SHORT_DECAY_PCT = 0.3
LONG_DECAY_PCT = 1.5
XATTN_HEADS = 4
XATTN_HEAD_DIM = D_MODEL // XATTN_HEADS
D_FF = 4 * D_MODEL
EPS = 1e-6
HY_COLS = (HYENA_ORDER + 1) * D_HYENA
ML_QK_COLS = 2 * D_MLSTM
ML_GATE_COLS = 4 * MLSTM_HEADS
D_IN_PROJ = HY_COLS + ML_QK_COLS + 2 * D_MLSTM + ML_GATE_COLS


def _rms_norm(x, g):
    xf = x.astype(jnp.float32)
    y = xf * lax.rsqrt(jnp.mean(xf * xf, axis=-1, keepdims=True) + EPS)
    return (y * g.astype(jnp.float32)).astype(x.dtype)

def _group_rms_norm(x, g, n_groups):
    lead = x.shape[:-1]
    c = x.shape[-1]
    xg = x.astype(jnp.float32).reshape(*lead, n_groups, c // n_groups)
    xg = xg * lax.rsqrt(jnp.mean(xg * xg, axis=-1, keepdims=True) + EPS)
    return (xg.reshape(*lead, c) * g.astype(jnp.float32)).astype(x.dtype)

def _short_conv_centred(u, w, b):
    L = u.shape[1]
    up = jnp.pad(u, ((0, 0), (1, 1), (0, 0)))
    return up[:, :L] * w[0] + up[:, 1:L + 1] * w[1] + up[:, 2:] * w[2] + b

def _hyena_filter_spectrum(L, w1, b1, fr1, w2, b2, fr2, w3):
    f32 = jnp.float32
    t = jnp.linspace(0.0, 1.0, L, dtype=f32)[:, None]
    ang = (2.0 * math.pi / L) * jnp.arange(L, dtype=f32)[:, None]
    bands = jnp.linspace(1e-4, FILTER_BANDS - 1, FILTER_BANDS, dtype=f32)[None, :]
    z = jnp.concatenate([t, jnp.cos(bands * ang), -jnp.sin(bands * ang)], axis=-1)
    hid = jnp.sin(fr1.astype(f32) * (z @ w1.astype(f32) + b1.astype(f32)))
    hid = jnp.sin(fr2.astype(f32) * (hid @ w2.astype(f32) + b2.astype(f32)))
    filt = (hid @ w3.astype(f32)).reshape(L, HYENA_ORDER, FILTER_DIRS, D_HYENA)
    max_decay = math.log(DECAY_TARGET) / SHORT_DECAY_PCT
    min_decay = math.log(DECAY_TARGET) / LONG_DECAY_PCT
    deltas = jnp.linspace(min_decay, max_decay, D_HYENA, dtype=f32)
    filt = filt * jnp.exp(-t * jnp.abs(deltas))[:, None, None, :]
    fwd = filt[:, :, 0]
    bwd = jnp.flip(filt[1:, :, 1], axis=0)
    two_sided = jnp.concatenate([fwd, jnp.zeros((1, HYENA_ORDER, D_HYENA), f32), bwd], axis=0)
    return jnp.fft.rfft(two_sided, axis=0)

def _hyena(hy, spec, skip):
    L = hy.shape[1]
    u = hy.astype(jnp.float32)
    z, g1, g2 = u[..., :D_HYENA], u[..., D_HYENA:2 * D_HYENA], u[..., 2 * D_HYENA:]
    for o, gate in enumerate((g1, g2)):
        conv = jnp.fft.irfft(jnp.fft.rfft(z, n=2 * L, axis=1) * spec[:, o], n=2 * L, axis=1)[:, :L]
        z = gate * (conv + z * skip[o].astype(jnp.float32))
    return z

def _mlstm_chunkwise(q, k, v, i_pre, log_f):
    B, H, L, Dh = q.shape
    nc = L // MLSTM_CHUNK

    def chunks(a):
        a = a.reshape(B, H, nc, MLSTM_CHUNK, *a.shape[3:])
        return jnp.moveaxis(a, 2, 0)

    lower = jnp.tril(jnp.ones((MLSTM_CHUNK, MLSTM_CHUNK), dtype=bool))

    def step(carry, inp):
        C, n, m = carry
        qc, kc, vc, ic, fc = inp
        F = jnp.cumsum(fc, axis=-1)
        logw = F[..., :, None] - F[..., None, :] + ic[..., None, :]
        logw = jnp.where(lower, logw, -jnp.inf)
        log_inter = F + m[..., None]
        m_t = jnp.maximum(log_inter, jnp.max(logw, axis=-1))
        w = jnp.exp(logw - m_t[..., None])
        inter = jnp.exp(log_inter - m_t)
        s = jnp.einsum('bhtd,bhsd->bhts', qc, kc) * w
        num = jnp.einsum('bhts,bhse->bhte', s, vc) + inter[..., None] * jnp.einsum('bhtd,bhde->bhte', qc, C)
        den = jnp.sum(s, axis=-1) + inter * jnp.einsum('bhtd,bhd->bht', qc, n)
        h = num / jnp.maximum(jnp.abs(den), jnp.exp(-m_t))[..., None]
        F_end = F[..., -1]
        log_end = F_end[..., None] - F + ic
        m_new = jnp.maximum(F_end + m, jnp.max(log_end, axis=-1))
        we = jnp.exp(log_end - m_new[..., None])
        carry_decay = jnp.exp(F_end + m - m_new)
        C_new = carry_decay[..., None, None] * C + jnp.einsum('bhs,bhsd,bhse->bhde', we, kc, vc)
        n_new = carry_decay[..., None] * n + jnp.einsum('bhs,bhsd->bhd', we, kc)
        return (C_new, n_new, m_new), h

    init = (jnp.zeros((B, H, Dh, Dh), jnp.float32),
            jnp.zeros((B, H, Dh), jnp.float32),
            jnp.zeros((B, H), jnp.float32))
    _, hs = lax.scan(step, init, tuple(chunks(a) for a in (q, k, v, i_pre, log_f)))
    return jnp.moveaxis(hs, 0, 2).reshape(B, H, L, Dh)

def _mlstm_bidirectional(q, k, v, o_pre, gates, gate_b):
    B, L, _ = q.shape
    f32 = jnp.float32

    def heads(a):
        return a.astype(f32).reshape(B, L, MLSTM_HEADS, MLSTM_HEAD_DIM).transpose(0, 2, 1, 3)

    qh = heads(q)
    kh = heads(k) * (MLSTM_HEAD_DIM ** -0.5)
    vh = heads(v)
    g = (gates.astype(f32) + gate_b.astype(f32)).reshape(B, L, 4, MLSTM_HEADS).transpose(2, 0, 3, 1)
    i_f, f_f, i_b, f_b = g[0], g[1], g[2], g[3]
    h_f = _mlstm_chunkwise(qh, kh, vh, i_f, jax.nn.log_sigmoid(f_f))

    def flip(a):
        return jnp.flip(a, axis=2)

    h_b = flip(_mlstm_chunkwise(flip(qh), flip(kh), flip(vh), flip(i_b), flip(jax.nn.log_sigmoid(f_b))))
    h_sum = (h_f + h_b).transpose(0, 2, 1, 3).reshape(B, L, D_MLSTM)
    return jax.nn.sigmoid(o_pre.astype(f32)) * h_sum

def _cross_attention(xn, memn, wq, wk, wv, wo):
    B, L, _ = xn.shape
    M = memn.shape[1]
    q = (xn @ wq).reshape(B, L, XATTN_HEADS, XATTN_HEAD_DIM)
    k = (memn @ wk).reshape(B, M, XATTN_HEADS, XATTN_HEAD_DIM)
    v = (memn @ wv).reshape(B, M, XATTN_HEADS, XATTN_HEAD_DIM)
    s = jnp.einsum('blhd,bmhd->bhlm', q, k).astype(jnp.float32) * (XATTN_HEAD_DIM ** -0.5)
    p = jax.nn.softmax(s, axis=-1).astype(v.dtype)
    o = jnp.einsum('bhlm,bmhd->blhd', p, v).reshape(B, L, D_MODEL)
    return o @ wo

def first_inputs(seed: int = 0) -> dict:
    key = jax.random.key(seed)
    keys = iter(jax.random.split(key, 32))

    def nrm(shape, scale):
        return jax.random.normal(next(keys), shape, jnp.float32) * scale

    def gain(shape):
        return 1.0 + nrm(shape, 0.02)

    D = D_MODEL
    x = nrm((BATCH, SEQ, D), 1.0)
    mem = nrm((BATCH, N_MEM, D), 1.0)
    f_bias = jnp.linspace(3.0, 6.0, MLSTM_HEADS, dtype=jnp.float32)
    zero_b = jnp.zeros_like(f_bias)
    gate_noise = nrm((DEPTH, 4, MLSTM_HEADS), 0.1)
    ml_gate_b = (gate_noise + jnp.stack([zero_b, f_bias, zero_b, f_bias])).reshape(DEPTH, ML_GATE_COLS)
    return {
        'x': x,
        'mem': mem,
        'norm_mix_g': gain((DEPTH, D)),
        'w_in': nrm((DEPTH, D, D_IN_PROJ), D ** -0.5),
        'hy_conv_w': nrm((DEPTH, 3, HY_COLS), 3 ** -0.5),
        'hy_conv_b': nrm((DEPTH, HY_COLS), 0.02),
        'hy_filt_w1': nrm((DEPTH, FILTER_EMB, FILTER_HIDDEN), FILTER_EMB ** -0.5),
        'hy_filt_b1': nrm((DEPTH, FILTER_HIDDEN), 0.1),
        'hy_filt_freq1': gain((DEPTH, FILTER_HIDDEN)),
        'hy_filt_w2': nrm((DEPTH, FILTER_HIDDEN, FILTER_HIDDEN), FILTER_HIDDEN ** -0.5),
        'hy_filt_b2': nrm((DEPTH, FILTER_HIDDEN), 0.1),
        'hy_filt_freq2': gain((DEPTH, FILTER_HIDDEN)),
        'hy_filt_w3': nrm((DEPTH, FILTER_HIDDEN, FILTER_CH), FILTER_OUT_SCALE * FILTER_HIDDEN ** -0.5),
        'hy_skip': nrm((DEPTH, HYENA_ORDER, D_HYENA), 1.0),
        'hy_norm_g': gain((DEPTH, D_HYENA)),
        'ml_conv_w': nrm((DEPTH, 3, ML_QK_COLS), 3 ** -0.5),
        'ml_conv_b': nrm((DEPTH, ML_QK_COLS), 0.02),
        'ml_gate_b': ml_gate_b,
        'ml_norm_g': gain((DEPTH, D_MLSTM)),
        'w_out': nrm((DEPTH, D_MIX, D), D_MIX ** -0.5),
        'norm_x_g': gain((DEPTH, D)),
        'norm_mem_g': gain((DEPTH, D)),
        'xa_wq': nrm((DEPTH, D, D), D ** -0.5),
        'xa_wk': nrm((DEPTH, D, D), D ** -0.5),
        'xa_wv': nrm((DEPTH, D, D), D ** -0.5),
        'xa_wo': nrm((DEPTH, D, D), D ** -0.5),
        'norm_ff_g': gain((DEPTH, D)),
        'ff_w1': nrm((DEPTH, D, D_FF), D ** -0.5),
        'ff_w2': nrm((DEPTH, D_FF, D), D_FF ** -0.5),
        'final_norm_g': gain((D,)),
    }

def first_block(x, mem, norm_mix_g, w_in, hy_conv_w, hy_conv_b, hy_filt_w1, hy_filt_b1, hy_filt_freq1,
              hy_filt_w2, hy_filt_b2, hy_filt_freq2, hy_filt_w3, hy_skip, hy_norm_g, ml_conv_w, ml_conv_b,
              ml_gate_b, ml_norm_g, w_out, norm_x_g, norm_mem_g, xa_wq, xa_wk, xa_wv, xa_wo, norm_ff_g,
              ff_w1, ff_w2, final_norm_g):
    L = x.shape[1]
    off = HY_COLS + ML_QK_COLS
    h = x
    for l in range(DEPTH):
        u = _rms_norm(h, norm_mix_g[l])
        proj = u @ w_in[l]
        hy = _short_conv_centred(proj[..., :HY_COLS], hy_conv_w[l], hy_conv_b[l])
        spec = _hyena_filter_spectrum(L, hy_filt_w1[l], hy_filt_b1[l], hy_filt_freq1[l],
                                      hy_filt_w2[l], hy_filt_b2[l], hy_filt_freq2[l], hy_filt_w3[l])
        y_hy = _group_rms_norm(_hyena(hy, spec, hy_skip[l]), hy_norm_g[l], HYENA_GROUPS)
        qk = jax.nn.silu(_short_conv_centred(proj[..., HY_COLS:off], ml_conv_w[l], ml_conv_b[l]))
        y_ml = _mlstm_bidirectional(qk[..., :D_MLSTM], qk[..., D_MLSTM:],
                                    proj[..., off:off + D_MLSTM],
                                    proj[..., off + D_MLSTM:off + 2 * D_MLSTM],
                                    proj[..., off + 2 * D_MLSTM:], ml_gate_b[l])
        y_ml = _group_rms_norm(y_ml, ml_norm_g[l], MLSTM_HEADS)
        mixed = jnp.concatenate([y_hy.astype(h.dtype), y_ml.astype(h.dtype)], axis=-1)
        h = h + mixed @ w_out[l]
        h = h + _cross_attention(_rms_norm(h, norm_x_g[l]), _rms_norm(mem, norm_mem_g[l]),
                                 xa_wq[l], xa_wk[l], xa_wv[l], xa_wo[l])
        h = h + jnp.square(jax.nn.relu(_rms_norm(h, norm_ff_g[l]) @ ff_w1[l])) @ ff_w2[l]
    return _rms_norm(h, final_norm_g)


HEAD_DIM = 64
N_HEADS = D_MODEL // HEAD_DIM
N_HEADS_A = N_HEADS // 2
N_HEADS_B = N_HEADS - N_HEADS_A
DILATED_CONFIGS = ((128, 1), (512, 4), (2048, 16))
BLOCK = 128
KV_RANK = D_MODEL // 8
IDX_HEADS = 8
IDX_DIM = 64
IDX_SCALE = (IDX_HEADS * IDX_DIM) ** -0.5
TOPK_MAX = 256
D_FF_2 = -(-8 * D_MODEL // (3 * 256)) * 256
SPLITS = (N_HEADS_A * HEAD_DIM, N_HEADS_A * HEAD_DIM, N_HEADS_A * HEAD_DIM,
          N_HEADS_B * HEAD_DIM, KV_RANK,
          IDX_HEADS * IDX_DIM, IDX_DIM, IDX_HEADS)
D_IN = sum(SPLITS)


def rmsnorm(x, g):
    xf = x.astype(jnp.float32)
    y = xf * lax.rsqrt(jnp.mean(xf * xf, axis=-1, keepdims=True) + EPS)
    return (y * g.astype(jnp.float32)).astype(x.dtype)

def alibi_slopes():
    s = 2.0 ** (-8.0 * (np.arange(N_HEADS, dtype=np.float32) + 1.0) / N_HEADS)
    return jnp.asarray(s[0::2], jnp.float32), jnp.asarray(s[1::2], jnp.float32)

def dilated_branch(q, k, v, window, dilation, slopes):
    bsz, seq, nh, hd = q.shape
    n = seq // dilation
    nb = -(-n // BLOCK)
    n_pad = nb * BLOCK
    w_res = window // dilation
    assert w_res <= BLOCK
    g = bsz * dilation

    def to_res(a):
        a = a.reshape(bsz, n, dilation, nh, hd).transpose(0, 2, 3, 1, 4).reshape(g, nh, n, hd)
        return jnp.pad(a, ((0, 0), (0, 0), (0, n_pad - n), (0, 0)))

    qr, kr, vr = to_res(q), to_res(k), to_res(v)

    def band(a):
        cur = a.reshape(g, nh, nb, BLOCK, hd)
        prev = jnp.pad(a, ((0, 0), (0, 0), (BLOCK, 0), (0, 0)))[:, :, :n_pad].reshape(g, nh, nb, BLOCK, hd)
        return jnp.concatenate([prev, cur], axis=3)

    kb, vb = band(kr), band(vr)
    qb = qr.reshape(g, nh, nb, BLOCK, hd)
    s = jnp.einsum('ghnqd,ghnkd->ghnqk', qb, kb).astype(jnp.float32) * (hd ** -0.5)
    dist = np.arange(BLOCK)[:, None] - np.arange(2 * BLOCK)[None, :] + BLOCK
    key_pos = np.arange(nb)[:, None] * BLOCK - BLOCK + np.arange(2 * BLOCK)[None, :]
    mask = ((dist >= 0) & (dist <= w_res))[None] & (key_pos >= 0)[:, None, :]
    bias = -slopes[:, None, None] * jnp.asarray(dist * dilation, jnp.float32)[None]
    s = jnp.where(mask[None, None], s + bias[None, :, None], -jnp.inf)
    m = jnp.max(s, axis=-1, keepdims=True)
    p = jnp.exp(s - m)
    l = jnp.sum(p, axis=-1, keepdims=True)
    o = jnp.einsum('ghnqk,ghnkd->ghnqd', (p / l).astype(v.dtype), vb)
    lse = (m + jnp.log(l))[..., 0]
    o = o.reshape(g, nh, n_pad, hd)[:, :, :n].reshape(bsz, dilation, nh, n, hd)
    o = o.transpose(0, 3, 1, 2, 4).reshape(bsz, seq, nh, hd)
    lse = lse.reshape(g, nh, n_pad)[:, :, :n].reshape(bsz, dilation, nh, n)
    lse = lse.transpose(0, 3, 1, 2).reshape(bsz, seq, nh)
    return o, lse

def dilated_mixture(q, k, v, slopes):
    outs, lses = [], []
    for window, dilation in DILATED_CONFIGS:
        o, lse = dilated_branch(q, k, v, window, dilation, slopes)
        outs.append(o.astype(jnp.float32))
        lses.append(lse)
    alpha = jax.nn.softmax(jnp.stack(lses, 0), axis=0)
    out = jnp.sum(alpha[..., None] * jnp.stack(outs, 0), axis=0)
    return out.astype(q.dtype)

def sparse_attention(q_idx, k_idx, w_idx, q_lat, c_kv, slopes):
    bsz, seq = c_kv.shape[0], c_kv.shape[1]
    nb = seq // BLOCK
    topk = min(TOPK_MAX, seq // 4)
    s_pos = jnp.arange(seq)
    k_idx_f = k_idx.astype(jnp.float32)

    def block_fn(i):
        start = i * BLOCK
        qi = lax.dynamic_slice_in_dim(q_idx, start, BLOCK, axis=1).astype(jnp.float32)
        wi = lax.dynamic_slice_in_dim(w_idx, start, BLOCK, axis=1).astype(jnp.float32)
        ql = lax.dynamic_slice_in_dim(q_lat, start, BLOCK, axis=1)
        t_pos = start + jnp.arange(BLOCK)
        logits = jnp.einsum('bqhd,bkd->bqhk', qi, k_idx_f)
        score = jnp.einsum('bqh,bqhk->bqk', wi, jax.nn.relu(logits))
        score = jnp.where(s_pos[None, None, :] <= t_pos[None, :, None], score, -jnp.inf)
        _, idx = lax.top_k(score, topk)
        c_sel = jax.vmap(lambda cb, ib: cb[ib])(c_kv, idx)
        s = jnp.einsum('bqhr,bqkr->bhqk', ql, c_sel).astype(jnp.float32) * (HEAD_DIM ** -0.5)
        dist = (t_pos[None, :, None] - idx).astype(jnp.float32)
        s = s - slopes[None, :, None, None] * dist[:, None]
        s = jnp.where((idx <= t_pos[None, :, None])[:, None], s, -jnp.inf)
        p = jax.nn.softmax(s, axis=-1)
        return jnp.einsum('bhqk,bqkr->bqhr', p.astype(c_sel.dtype), c_sel)

    o = lax.map(block_fn, jnp.arange(nb))
    return o.transpose(1, 0, 2, 3, 4).reshape(bsz, seq, o.shape[3], o.shape[4])

def second_inputs(seed: int = 0) -> dict:
    key = jax.random.key(seed)
    ks = jax.random.split(key, 16)
    f32 = jnp.float32
    nrm = lambda k, shape, scale: jax.random.normal(k, shape, f32) * scale
    return {
        "x": nrm(ks[0], (BATCH, SEQ, D_MODEL), 1.0),
        "c": nrm(ks[1], (BATCH, D_MODEL), 1.0),
        "w_ada": nrm(ks[2], (DEPTH, D_MODEL, 6 * D_MODEL), 0.5 * D_MODEL ** -0.5),
        "b_ada": nrm(ks[3], (DEPTH, 6 * D_MODEL), 0.01),
        "g_attn": 1.0 + nrm(ks[4], (DEPTH, D_MODEL), 0.02),
        "w_in": nrm(ks[5], (DEPTH, D_MODEL, D_IN), D_MODEL ** -0.5),
        "kv_norm_g": 1.0 + nrm(ks[6], (DEPTH, KV_RANK), 0.02),
        "w_uk": nrm(ks[7], (DEPTH, N_HEADS_B, HEAD_DIM, KV_RANK), HEAD_DIM ** -0.5),
        "w_uv": nrm(ks[8], (DEPTH, N_HEADS_B, KV_RANK, HEAD_DIM), KV_RANK ** -0.5),
        "w_out": nrm(ks[9], (DEPTH, D_MODEL, D_MODEL), D_MODEL ** -0.5),
        "g_ffn": 1.0 + nrm(ks[10], (DEPTH, D_MODEL), 0.02),
        "w_gu": nrm(ks[11], (DEPTH, D_MODEL, 2 * D_FF_2), D_MODEL ** -0.5),
        "w_down": nrm(ks[12], (DEPTH, D_FF_2, D_MODEL), D_FF_2 ** -0.5),
        "g_final": 1.0 + nrm(ks[13], (D_MODEL,), 0.02),
    }

def second_block(x, c, w_ada, b_ada, g_attn, w_in, kv_norm_g, w_uk, w_uv, w_out, g_ffn, w_gu, w_down, g_final):
    bsz, seq, _ = x.shape
    slopes_a, slopes_b = alibi_slopes()
    offsets = [int(o) for o in np.cumsum(SPLITS)[:-1]]
    c_act = jax.nn.silu(c)
    for l in range(DEPTH):
        mod = c_act @ w_ada[l] + b_ada[l]
        sh1, sc1, ga1, sh2, sc2, ga2 = [m[:, None, :] for m in jnp.split(mod, 6, axis=-1)]

        h = rmsnorm(x, g_attn[l]) * (1.0 + sc1) + sh1
        proj = h @ w_in[l]
        qa, ka, va, qb, ckv, qi, ki, wi = jnp.split(proj, offsets, axis=-1)
        shp_a = (bsz, seq, N_HEADS_A, HEAD_DIM)
        out_a = dilated_mixture(qa.reshape(shp_a), ka.reshape(shp_a), va.reshape(shp_a), slopes_a)
        ckv = rmsnorm(ckv, kv_norm_g[l])
        q_lat = jnp.einsum('bthd,hdr->bthr', qb.reshape(bsz, seq, N_HEADS_B, HEAD_DIM), w_uk[l])
        o_lat = sparse_attention(qi.reshape(bsz, seq, IDX_HEADS, IDX_DIM), ki, wi * IDX_SCALE,
                                 q_lat, ckv, slopes_b)
        out_b = jnp.einsum('bthr,hrd->bthd', o_lat, w_uv[l])
        mixed = jnp.concatenate([out_a.reshape(bsz, seq, -1), out_b.reshape(bsz, seq, -1)], axis=-1)
        x = x + ga1 * (mixed @ w_out[l])

        h2 = rmsnorm(x, g_ffn[l]) * (1.0 + sc2) + sh2
        gate, up = jnp.split(h2 @ w_gu[l], 2, axis=-1)
        x = x + ga2 * ((jax.nn.silu(gate) * up) @ w_down[l])
    return rmsnorm(x, g_final)


def setup_inputs(seed=0):
    out = dict(first_inputs(seed))
    for name, value in second_inputs(seed + 1).items():
        if name != "x":
            out[name + "_2"] = value
    return out


def reference(
    x, mem, norm_mix_g, w_in, hy_conv_w, hy_conv_b, hy_filt_w1, hy_filt_b1, hy_filt_freq1,
    hy_filt_w2, hy_filt_b2, hy_filt_freq2, hy_filt_w3, hy_skip, hy_norm_g, ml_conv_w, ml_conv_b,
    ml_gate_b, ml_norm_g, w_out, norm_x_g, norm_mem_g, xa_wq, xa_wk, xa_wv, xa_wo, norm_ff_g,
    ff_w1, ff_w2, final_norm_g, c_2, w_ada_2, b_ada_2, g_attn_2, w_in_2, kv_norm_g_2, w_uk_2,
    w_uv_2, w_out_2, g_ffn_2, w_gu_2, w_down_2, g_final_2,
):
    x = first_block(
        x, mem, norm_mix_g, w_in, hy_conv_w, hy_conv_b, hy_filt_w1, hy_filt_b1, hy_filt_freq1,
        hy_filt_w2, hy_filt_b2, hy_filt_freq2, hy_filt_w3, hy_skip, hy_norm_g, ml_conv_w,
        ml_conv_b, ml_gate_b, ml_norm_g, w_out, norm_x_g, norm_mem_g, xa_wq, xa_wk, xa_wv,
        xa_wo, norm_ff_g, ff_w1, ff_w2, final_norm_g,
    )
    return second_block(
        x, c_2, w_ada_2, b_ada_2, g_attn_2, w_in_2, kv_norm_g_2, w_uk_2, w_uv_2, w_out_2,
        g_ffn_2, w_gu_2, w_down_2, g_final_2,
    )


_drawn_inputs = setup_inputs


def setup_inputs(seed=0):
    import zlib

    import numpy as np

    out = dict(_drawn_inputs(seed))
    spreads = {}
    factors = {'hy_filt_freq1': 6.483,
     'hy_filt_freq2': 6.867,
     'hy_norm_g': 3.684,
     'ml_conv_b': 4.301,
     'ml_norm_g': 3.655,
     'norm_x_g': 8.0,
     'norm_mem_g': 8.0,
     'norm_ff_g': 2.906,
     'b_ada_2': 3.61,
     'g_attn_2': 4.231,
     'kv_norm_g_2': 8.0,
     'g_ffn_2': 8.0,
     'g_final_2': 2.788}
    for name, (base, spread) in spreads.items():
        noise = np.random.default_rng([zlib.crc32(name.encode()), seed]).standard_normal(out[name].shape)
        drawn = base * np.exp(spread * noise) if base else spread * noise
        out[name] = jnp.asarray(drawn.astype(out[name].dtype))
    for name, factor in factors.items():
        out[name] = (out[name] * factor).astype(out[name].dtype)
    return out
```

```python
import math

import numpy as np

import concourse.bass as bass
from concourse import mybir
from concourse.alu_op_type import AluOpType as ALU

F32 = mybir.dt.float32
ACT = mybir.ActivationFunctionType
AX = mybir.AxisListType

P = 128
BANK = 512
L = 1024
D = 1024
TT = L // P
KT = D // P
EPS = 1e-6
NMEM = 256
DH = 512
NH_ML = 4
HY_COLS = 3 * DH
FF = 4 * D
FF2 = -(-8 * D // (3 * 256)) * 256
NA = 8
HD = 64
RANK = 128
TOPK = 256
NEG = -1.0e30
QA0, KA0, VA0, QB0, CK0, QI0, KI0, WI0 = (int(v) for v in np.cumsum([0, 512, 512, 512, 512, 128, 512, 64]))
ARENA = 207 * 256 + 192


class Signal:

    def __init__(self, nc, name):
        self.sem = nc.alloc_semaphore(name)
        self.base = 0

    def at(self, n):
        return self.base + n

    def close(self, n):
        self.base += n


def constants():
    n = np.arange(L)
    ang = 2 * np.pi * ((n[:, None] * n[None, :]) % (2 * L)) / (2 * L)
    cos, sin = np.cos(ang).astype(np.float32), np.sin(ang).astype(np.float32)
    p = np.arange(P)
    alt = np.where(p % 2 == 0, 1.0, -1.0).astype(np.float32)
    small = np.zeros((P, 7, P), np.float32)
    small[:, 0] = np.eye(P)
    small[:, 1, 0] = alt
    small[0, 2, :] = alt
    small[:, 3] = np.where(p[None, :] >= p[:, None], 0.0, NEG)
    small[:, 4] = np.where(p[None, :] <= p[:, None], 0.0, NEG)
    small[:, 5, 0:TT] = -(np.arange(TT)[None, :] * P + p[:, None]) / (L - 1.0)
    small[:, 5, 8] = 2.0 / (2 * L)
    small[:, 5, 9] = 2.0 / (2 * L)
    small[0, 5, 9] = 1.0 / (2 * L)
    small[:, 5, 10] = 1.0
    small[:, 5, 11] = EPS
    small[:, 6] = 1.0
    sel = np.zeros((64, 8, P), np.float32)
    for h in range(8):
        sel[(h // 4) * 32 + h % 4, h, :] = 1.0
    f32 = np.float32
    t = np.linspace(0.0, 1.0, L, dtype=f32)[:, None]
    w = (f32(2.0 * math.pi / L) * np.arange(L, dtype=f32))[:, None]
    bands = np.linspace(1e-4, 15, 16, dtype=f32)[None, :]
    z = np.concatenate([t, np.cos(bands * w), -np.sin(bands * w)], axis=-1)
    deltas = np.abs(np.linspace(math.log(1e-2) / 1.5, math.log(1e-2) / 0.3, DH, dtype=f32))
    slopes = (2.0 ** (-8.0 * (np.arange(16, dtype=f32) + 1.0) / 16)).astype(f32)
    dist = p[:, None] - (np.arange(L) - (L - P))[None, :]
    mult = ((dist >= 0) & (dist <= 128)) * 1.0 + ((dist >= 0) & (dist % 4 == 0) & (dist <= 512)) + ((dist >= 0) & (dist % 16 == 0))
    lnm = np.where(mult > 0, np.log(np.maximum(mult, 1)), NEG)
    bias_a = np.stack([np.where(mult > 0, 8.0 * (lnm - float(slopes[2 * h]) * dist), NEG) for h in range(8)]).astype(f32)
    mdist = (-dist).astype(f32)
    return {
        "c_cos": cos, "c_sin": sin, "c_small": small, "c_sel": sel,
        "c_z": np.ascontiguousarray(z.T), "c_delta": deltas[None, :].copy(),
        "c_bias_a": bias_a, "c_mdist": mdist,
    }


SLOPES_B = [float(np.float32(2.0 ** (-8.0 * (2 * h + 2) / 16))) for h in range(8)]


class Core:

    def __init__(self, nc, ap):
        self.nc = nc
        self.ap = ap
        self.arena = nc.alloc_sbuf_tensor("arena", [P, ARENA], F32)
        self.psum = nc.alloc_psum_tensor("psum", [P, 8, BANK], F32)
        names = (
            "loaded", "loaded0", "loaded1", "loaded2", "loaded3", "stored",
            "mm_done", "tr_done", "act_done", "act_free", "act_chain", "dve_done", "dve_free", "dve_chain",
            "pool_done", "pool_chain", "aux_done", "aux_free", "aux2_done", "x_ready",
            "stat_ready", "row_ready", "col_ready",
        )
        self.sig = {n: Signal(nc, n) for n in names}
        self.small = self.view(0, 7 * P).rearrange("p (a b) -> p a b", a=7)
        self.ident = self.small[:, 0, :]
        self.colsA = self.view(3.5, 128)
        self.colsB = self.view(4.0, 64)
        self.tiny = self.view(4.25, 64)
        self.eps = self.small[:, 5, 11:12]
        self.tiny2 = self.view(4.5, 384)

    def view(self, kb, words, parts=P):
        start = int(round(kb * 256))
        assert start + words <= ARENA, (kb, words)
        return self.arena[0:parts, start:start + words]

    def view3(self, kb, a, b, parts=P):
        return self.view(kb, a * b, parts).rearrange("p (a b) -> p a b", a=a)


class Chain:

    def __init__(self, eng, signal):
        self.eng, self.count, self.n = eng, signal, 0

    def __call__(self, ins):
        self.n += 1
        ins.then_inc(self.count.sem, 1)
        self.eng.wait_ge(self.count.sem, self.count.at(self.n))


G_MIX, CW_HY, CB_HY, CW_ML, CB_ML, G_X, G_MEM, G_FF = 0, 8, 44, 56, 80, 88, 96, 104
G_ATT2, G_FFN2 = 112, 120
C_ACT, G_HY, G_ML, G_KV = 0, 8, 12, 16


def phase_load(core):
    nc, ap, S = core.nc, core.ap, core.sig
    x = core.view3(38, TT, D)
    rowsA = core.view(102, P)
    rowsB = core.view(103, P)
    loads = [
        (x, ap["x"].rearrange("a (t p) d -> p (a t) d", p=P)),
        (core.small, ap["c_small"]),
    ]
    at = 0
    for name, rows in (("norm_mix_g", 8), ("hy_conv_w", 36), ("hy_conv_b", 12), ("ml_conv_w", 24), ("ml_conv_b", 8),
                       ("norm_x_g", 8), ("norm_mem_g", 8), ("norm_ff_g", 8), ("g_attn_2", 8), ("g_ffn_2", 8)):
        src = ap[name]
        src = src.rearrange("a b (r c) -> (a b r) c", c=P) if len(src.shape) == 3 else src.rearrange("a (r c) -> (a r) c", c=P)
        loads.append((rowsA[at:at + rows, :], src))
        at += rows
    at = 0
    for name, rows in (("c_2", 8), ("hy_norm_g", 4), ("ml_norm_g", 4), ("kv_norm_g_2", 1)):
        loads.append((rowsB[at:at + rows, :], ap[name].rearrange("a (r c) -> (a r) c", c=P)))
        at += rows
    nB = at
    with nc.Block() as block:
        @block.sync
        def _(sp):
            for dst, src in loads:
                sp.dma_start(dst, src).then_inc(S["loaded"].sem, 16)

        @block.tensor
        def _(pe):
            pe.wait_ge(S["loaded"].sem, S["loaded"].at(16 * len(loads)))
            nc.tensor.transpose(core.psum[:, 0, 0:P], rowsA, core.ident)
            nc.tensor.transpose(core.psum[:, 0, P:P + nB], rowsB[0:nB, :], core.ident[0:nB, 0:nB]).then_inc(S["tr_done"].sem, 1)

        @block.vector
        def _(dve):
            dve.wait_ge(S["tr_done"].sem, S["tr_done"].at(1))
            nc.vector.tensor_copy(core.colsA, core.psum[:, 0, 0:P])
            nc.vector.tensor_copy(core.colsB[:, 0:nB], core.psum[:, 0, P:P + nB])
    S["loaded"].close(16 * len(loads))
    S["tr_done"].close(1)


def phase_norm(core, src, dst, gain, shift=None, scratch=150, rows=None, extra=None):
    nc, S = core.nc, core.sig
    tiles = src.shape[1]
    junk = dst.rearrange("p k t -> p (k t)").rearrange("p (i d) -> p i d", d=D)
    tmp = core.view3(scratch, 2, D)
    ss, rstd = core.tiny[:, 0:tiles], core.tiny[:, 8:8 + tiles]
    ps = core.psum
    with nc.Block() as block:
        if extra:
            extra(block)

        @block.scalar
        def _(act):
            chain = Chain(act, S["act_chain"])
            for i in range(tiles):
                last = nc.scalar.activation(junk[:, i, :], src[:, i, :], ACT.Square, accum_out=ss[:, i:i + 1])
            chain(last)
            nc.scalar.activation(rstd, ss, ACT.Sqrt, scale=1.0 / D, bias=core.eps).then_inc(S["stat_ready"].sem, 1)
            act.wait_ge(S["col_ready"].sem, S["col_ready"].at(1))
            for i in range(tiles):
                if i >= 2:
                    act.wait_ge(S["tr_done"].sem, S["tr_done"].at(2 * (i - 1)))
                nc.scalar.activation(tmp[:, i % 2, :], src[:, i, :], ACT.Copy, scale=rstd[:, i:i + 1]).then_inc(S["row_ready"].sem, 1)

        @block.tensor
        def _(pe):
            for i in range(tiles):
                pe.wait_ge(S["row_ready"].sem, S["row_ready"].at(i + 1))
                for q in range(2):
                    u = 2 * i + q
                    if u >= 8:
                        pe.wait_ge(S["dve_free"].sem, S["dve_free"].at(u - 7))
                    for j in range(4):
                        last = nc.tensor.transpose(ps[:, u % 8, j * P:(j + 1) * P], tmp[:, i % 2, (4 * q + j) * P:(4 * q + j + 1) * P], core.ident)
                    last.then_inc(S["tr_done"].sem, 1)

        @block.vector
        def _(dve):
            chain = Chain(dve, S["dve_chain"])
            dve.wait_ge(S["stat_ready"].sem, S["stat_ready"].at(1))
            nc.vector.reciprocal(rstd, rstd).then_inc(S["col_ready"].sem, 1)
            for u in range(2 * tiles):
                i, q = u // 2, u % 2
                dve.wait_ge(S["tr_done"].sem, S["tr_done"].at(u + 1))
                out = dst[:, 4 * q:4 * q + 4, i * P:(i + 1) * P]
                g = gain[:, 4 * q:4 * q + 4].unsqueeze(2).to_broadcast([P, 4, P])
                ins = nc.vector.tensor_tensor(out, ps[:, u % 8, :].rearrange("p (a b) -> p a b", a=4), g, ALU.mult)
                ins.then_inc(S["dve_free"].sem, 1)
                if shift is not None:
                    dve.wait_ge(S["dve_free"].sem, S["dve_free"].at(u + 1))
                    sh = shift[:, 4 * q:4 * q + 4].unsqueeze(2).to_broadcast([P, 4, P])
                    nc.vector.tensor_tensor(out, out, sh, ALU.add)
    S["act_chain"].close(1)
    S["stat_ready"].close(1)
    S["col_ready"].close(1)
    S["row_ready"].close(tiles)
    S["tr_done"].close(2 * tiles)
    S["dve_free"].close(2 * tiles)


def phase_conv_proj(core, xt, w, hy):
    nc, S, ps = core.nc, core.sig, core.psum
    ring = [core.view3(118 + 4 * s, KT, P) for s in range(4)]
    tmp = [core.view(134 + 4 * s, L) for s in range(2)]
    n_tiles = HY_COLS // P
    wv = w.rearrange("a (k p) n -> p (a k) n", p=P)
    ld = [S["loaded%d" % s] for s in range(4)]
    with nc.Block() as block:
        @block.sync
        def _(sp):
            for n in range(n_tiles):
                if n >= 4:
                    sp.wait_ge(S["mm_done"].sem, S["mm_done"].at(n - 3))
                sp.dma_start(ring[n % 4], wv[:, :, n * P:(n + 1) * P]).then_inc(ld[n % 4].sem, 16)

        @block.tensor
        def _(pe):
            for n in range(n_tiles + 1):
                if n < n_tiles:
                    pe.wait_ge(ld[n % 4].sem, ld[n % 4].at(16 * (n // 4 + 1)))
                    if n >= 2:
                        pe.wait_ge(S["dve_done"].sem, S["dve_done"].at(n - 1))
                    for half in range(2):
                        for k in range(KT):
                            last = nc.tensor.matmul(ps[:, 2 * (n % 2) + half, :], ring[n % 4][:, k, :], xt[:, k, half * BANK:(half + 1) * BANK],
                                                    start=k == 0, stop=k == KT - 1)
                    last.then_inc(S["mm_done"].sem, 1)
                if n >= 1:
                    m = n - 1
                    pe.wait_ge(S["dve_done"].sem, S["dve_done"].at(m + 1))
                    if m >= 2:
                        pe.wait_ge(S["act_free"].sem, S["act_free"].at(m - 1))
                    for t in range(TT):
                        last = nc.tensor.transpose(ps[:, 4 + 2 * (m % 2) + t // 4, (t % 4) * P:(t % 4 + 1) * P], tmp[m % 2][:, t * P:(t + 1) * P], core.ident)
                    last.then_inc(S["tr_done"].sem, 1)

        @block.scalar
        def _(act):
            def back(m):
                act.wait_ge(S["tr_done"].sem, S["tr_done"].at(m + 1))
                src = ps[:, 4 + 2 * (m % 2):6 + 2 * (m % 2), :].rearrange("p a (b c) -> p (a b) c", c=P)
                nc.scalar.activation(hy[:, :, m * P:(m + 1) * P], src, ACT.Copy).then_inc(S["act_free"].sem, 1)
            for n in range(n_tiles):
                act.wait_ge(S["mm_done"].sem, S["mm_done"].at(n + 1))
                if n >= 2:
                    act.wait_ge(S["tr_done"].sem, S["tr_done"].at(n - 1))
                nc.scalar.activation(tmp[n % 2], ps[:, 2 * (n % 2):2 * (n % 2) + 2, :].rearrange("p a b -> p (a b)"), ACT.Identity,
                                     scale=core.colsA[:, CW_HY + 12 + n:CW_HY + 13 + n],
                                     bias=core.colsA[:, CB_HY + n:CB_HY + n + 1]).then_inc(S["act_done"].sem, 1)
                if n >= 1:
                    back(n - 1)
            back(n_tiles - 1)

        @block.vector
        def _(dve):
            chain = Chain(dve, S["dve_chain"])
            for n in range(n_tiles):
                dve.wait_ge(S["act_done"].sem, S["act_done"].at(n + 1))
                pr = ps[:, 2 * (n % 2):2 * (n % 2) + 2, :].rearrange("p a b -> p (a b)")
                t = tmp[n % 2]
                chain(nc.vector.scalar_tensor_tensor(out=t[:, 1:L], in0=pr[:, 0:L - 1], scalar=core.colsA[:, CW_HY + n:CW_HY + n + 1],
                                                     in1=t[:, 1:L], op0=ALU.mult, op1=ALU.add))
                nc.vector.scalar_tensor_tensor(out=t[:, 0:L - 1], in0=pr[:, 1:L], scalar=core.colsA[:, CW_HY + 24 + n:CW_HY + 25 + n],
                                               in1=t[:, 0:L - 1], op0=ALU.mult, op1=ALU.add).then_inc(S["dve_done"].sem, 1)
    S["mm_done"].close(n_tiles)
    S["dve_done"].close(n_tiles)
    S["act_free"].close(n_tiles)
    S["tr_done"].close(n_tiles)
    S["act_done"].close(n_tiles)
    S["dve_chain"].close(n_tiles)
    for s in range(4):
        ld[s].close(16 * len(range(s, n_tiles, 4)))
XT_KB, MIXT_KB, HY_KB, HR_KB, HS_KB, XR_KB, XS_KB, DFT_RING_KB = 6, 38, 70, 118, 134, 150, 166, 182
TWO_PI_HI = 6.28125
TWO_PI_LO = 2 * math.pi - TWO_PI_HI
MAGIC = 1.5 * 2.0 ** 23


def phase_filter_hidden(core):
    nc, ap, S, ps = core.nc, core.ap, core.sig, core.psum
    hid = core.view(38, L, 64)
    z = core.view(42, L, 33)
    w1, w2 = core.view(46, 64, 33), core.view(46.5, 64, 64)
    vec = core.view(47, 8, 64)
    y, n = core.view(48, L, 64), core.view(52, L, 64)
    h1 = core.view(56, L, 64)
    loads = [(z, ap["c_z"]), (w1, ap["hy_filt_w1"][0]), (w2, ap["hy_filt_w2"][0])]
    for i, name in enumerate(("hy_filt_b1", "hy_filt_freq1", "hy_filt_b2", "hy_filt_freq2")):
        loads.append((vec[:, i:i + 1], ap[name].rearrange("a c -> c a")))
    with nc.Block() as block:
        @block.sync
        def _(sp):
            with nc.allow_non_contiguous_dma("64 biases and frequencies, one per partition"):
                for dst, src in loads:
                    sp.dma_start(dst, src).then_inc(S["loaded"].sem, 16)

        @block.tensor
        def _(pe):
            pe.wait_ge(S["loaded"].sem, S["loaded"].at(16 * len(loads)))
            for half in range(2):
                last = nc.tensor.matmul(ps[0:64, half, :], w1, z[:, half * BANK:(half + 1) * BANK], start=True, stop=True)
            last.then_inc(S["mm_done"].sem, 1)
            pe.wait_ge(S["act_done"].sem, S["act_done"].at(1))
            for half in range(2):
                last = nc.tensor.matmul(ps[0:64, 2 + half, :], w2, h1[:, half * BANK:(half + 1) * BANK], start=True, stop=True)
            last.then_inc(S["mm_done"].sem, 1)

        @block.vector
        def _(dve):
            chain = Chain(dve, S["dve_chain"])
            dve.wait_ge(S["loaded"].sem, S["loaded"].at(16 * len(loads)))
            for layer in range(2):
                fr, fb = vec[:, 2 * layer + 1:2 * layer + 2], vec[:, 4 + layer:5 + layer]
                chain(nc.vector.tensor_tensor(fb, vec[:, 2 * layer:2 * layer + 1], fr, ALU.mult))
                dve.wait_ge(S["mm_done"].sem, S["mm_done"].at(layer + 1))
                src = ps[0:64, 2 * layer:2 * layer + 2, :].rearrange("p a b -> p (a b)")
                chain(nc.vector.tensor_scalar(y, src, fr, fb, ALU.mult, ALU.add))
                chain(nc.vector.tensor_scalar(n, y, 1.0 / (2 * math.pi), MAGIC, ALU.mult, ALU.add))
                chain(nc.vector.tensor_scalar(n, n, MAGIC, None, ALU.subtract))
                chain(nc.vector.scalar_tensor_tensor(out=y, in0=n, scalar=-TWO_PI_HI, in1=y, op0=ALU.mult, op1=ALU.add))
                chain(nc.vector.scalar_tensor_tensor(out=y, in0=n, scalar=-TWO_PI_LO, in1=y, op0=ALU.mult, op1=ALU.add))
                nc.vector.tensor_scalar(y, y, 3.1415925, -3.1415925, ALU.min, ALU.max).then_inc(S["dve_done"].sem, 1)
                dve.wait_ge(S["act_done"].sem, S["act_done"].at(layer + 1))

        @block.scalar
        def _(act):
            for layer, out in enumerate((h1, hid)):
                act.wait_ge(S["dve_done"].sem, S["dve_done"].at(layer + 1))
                nc.scalar.activation(out, y, ACT.Sin).then_inc(S["act_done"].sem, 1)
    S["loaded"].close(16 * len(loads))
    S["mm_done"].close(2)
    S["dve_chain"].close(12)
    S["dve_done"].close(2)
    S["act_done"].close(2)


def phase_filter_time(core, o):
    nc, ap, S, ps = core.nc, core.ap, core.sig, core.psum
    hid = core.view(38, L, 64)
    w3 = core.view(42, L, 64)
    delta = core.view(46, DH)
    decay = core.view3(48, 2, DH)
    fd, bd = core.view3(52, 2, DH), core.view3(56, 2, DH)
    add, sub = core.view3(XR_KB, TT, DH), core.view3(XS_KB, TT, DH)
    mt = core.small[:, 5, 0:TT]
    with nc.Block() as block:
        @block.sync
        def _(sp):
            sp.dma_start(w3, ap["hy_filt_w3"][0][:, o * L:(o + 1) * L]).then_inc(S["loaded"].sem, 16)
            sp.dma_start(delta, ap["c_delta"][0].partition_broadcast(P)).then_inc(S["loaded0"].sem, 16)

        @block.tensor
        def _(pe):
            pe.wait_ge(S["loaded"].sem, S["loaded"].at(16))
            for t in range(TT):
                if t >= 4:
                    pe.wait_ge(S["dve_done"].sem, S["dve_done"].at(t - 3))
                for half in range(2):
                    last = nc.tensor.matmul(ps[:, 2 * (t % 4) + half, :], hid[:, t * P:(t + 1) * P], w3[:, half * DH:(half + 1) * DH], start=True, stop=True)
                last.then_inc(S["mm_done"].sem, 1)

        @block.scalar
        def _(act):
            act.wait_ge(S["loaded0"].sem, S["loaded0"].at(16))
            for t in range(TT):
                if t >= 2:
                    act.wait_ge(S["dve_done"].sem, S["dve_done"].at(t - 1))
                nc.scalar.activation(decay[:, t % 2, :], delta, ACT.Exp, scale=mt[:, t:t + 1]).then_inc(S["act_done"].sem, 1)

        @block.vector
        def _(dve):
            for t in range(TT):
                dve.wait_ge(S["act_done"].sem, S["act_done"].at(t + 1))
                dve.wait_ge(S["mm_done"].sem, S["mm_done"].at(t + 1))
                if t >= 2:
                    dve.wait_ge(S["pool_done"].sem, S["pool_done"].at(t - 1))
                nc.vector.tensor_tensor(fd[:, t % 2, :], ps[:, 2 * (t % 4), :], decay[:, t % 2, :], ALU.mult)
                nc.vector.tensor_tensor(bd[:, t % 2, :], ps[:, 2 * (t % 4) + 1, :], decay[:, t % 2, :], ALU.mult).then_inc(S["dve_done"].sem, 1)

        @block.gpsimd
        def _(pool):
            for t in range(TT):
                pool.wait_ge(S["dve_done"].sem, S["dve_done"].at(t + 1))
                if t == 0:
                    nc.gpsimd.memset(bd[0:1, 0, :], 0.0).then_inc(S["pool_chain"].sem, 1)
                    pool.wait_ge(S["pool_chain"].sem, S["pool_chain"].at(1))
                nc.gpsimd.tensor_tensor(add[:, t, :], fd[:, t % 2, :], bd[:, t % 2, :], ALU.add)
                nc.gpsimd.tensor_tensor(sub[:, t, :], fd[:, t % 2, :], bd[:, t % 2, :], ALU.subtract).then_inc(S["pool_done"].sem, 1)
    S["loaded"].close(16)
    S["loaded0"].close(16)
    for n in ("mm_done", "dve_done", "act_done", "pool_done"):
        S[n].close(TT)
    S["pool_chain"].close(1)


def dft_loads(core, sp):
    S = core.sig
    ring = [core.view3(DFT_RING_KB + 4 * s, TT, P) for s in range(4)]
    for u in range(2 * TT):
        if u >= 4:
            sp.wait_ge(S["aux_done"].sem, S["aux_done"].at(u - 3))
        table = core.ap["c_sin" if u % 2 else "c_cos"]
        sp.dma_start(ring[u % 4], table.rearrange("(a p) k -> p a k", p=P)[:, :, (u // 2) * P:(u // 2 + 1) * P]).then_inc(S["loaded%d" % (u % 4)].sem, 16)


def dft_forward_pe(core, pe, src_c, src_s, free_name):
    nc, S, ps = core.nc, core.sig, core.psum
    ring = [core.view3(DFT_RING_KB + 4 * s, TT, P) for s in range(4)]
    for u in range(2 * TT):
        pe.wait_ge(S["loaded%d" % (u % 4)].sem, S["loaded%d" % (u % 4)].at(16 * (u // 4 + 1)))
        if u >= 8 and u % 2 == 0:
            pe.wait_ge(S[free_name].sem, S[free_name].at(u // 2 - 3))
        src = src_s if u % 2 else src_c
        for k in range(TT):
            last = nc.tensor.matmul(ps[:, u % 8, :], ring[u % 4][:, k, :], src[:, k, :], start=k == 0, stop=k == TT - 1 and u != 1)
        if u == 1:
            for k in range(TT):
                last = nc.tensor.matmul(ps[:, 1, :], core.small[:, 1, :], src_c[:, k, :], start=False, stop=k == TT - 1)
        last.then_inc(S["aux_done"].sem, 1)


def close_dft(core):
    S = core.sig
    for s in range(4):
        S["loaded%d" % s].close(16 * TT * 2 // 4)
    S["aux_done"].close(2 * TT)


def phase_filter_spectrum(core):
    nc, S, ps = core.nc, core.sig, core.psum
    add, sub = core.view3(XR_KB, TT, DH), core.view3(XS_KB, TT, DH)
    hr, hs = core.view3(HR_KB, TT, DH), core.view3(HS_KB, TT, DH)
    hn = core.view(62, DH)
    with nc.Block() as block:
        @block.sync
        def _(sp):
            dft_loads(core, sp)

        @block.tensor
        def _(pe):
            dft_forward_pe(core, pe, add, sub, "act_free")

        @block.scalar
        def _(act):
            for j in range(TT):
                act.wait_ge(S["aux_done"].sem, S["aux_done"].at(2 * j + 2))
                w = core.small[:, 5, 9:10] if j == 0 else core.small[:, 5, 8:9]
                nc.scalar.activation(hr[:, j, :], ps[:, (2 * j) % 8, :], ACT.Copy, scale=w)
                nc.scalar.activation(hs[:, j, :], ps[:, (2 * j + 1) % 8, :], ACT.Copy, scale=w).then_inc(S["act_free"].sem, 1)

        @block.vector
        def _(dve):
            chain = Chain(dve, S["dve_chain"])
            dve.wait_ge(S["act_free"].sem, S["act_free"].at(1))
            chain(nc.vector.tensor_copy(hn, hr[:, 0, :]))
            chain(nc.vector.tensor_copy(hn[0:1, :], hs[0:1, 0, :]))
            nc.vector.memset(hs[0:1, 0, :], 0.0)
    close_dft(core)
    S["act_free"].close(TT)
    S["dve_chain"].close(2)


def phase_signal_spectrum(core, hy):
    nc, S, ps = core.nc, core.sig, core.psum
    z = hy[:, :, 0:DH]
    hr, hs = core.view3(HR_KB, TT, DH), core.view3(HS_KB, TT, DH)
    yr, ys = core.view3(XR_KB, TT, DH), core.view3(XS_KB, TT, DH)
    hn = core.view(62, DH)
    cross = core.view3(52, 4, DH)
    with nc.Block() as block:
        @block.sync
        def _(sp):
            dft_loads(core, sp)

        @block.tensor
        def _(pe):
            dft_forward_pe(core, pe, z, z, "dve_done")

        @block.vector
        def _(dve):
            for j in range(TT):
                dve.wait_ge(S["aux_done"].sem, S["aux_done"].at(2 * j + 2))
                if j >= 2:
                    dve.wait_ge(S["pool_done"].sem, S["pool_done"].at(j - 1))
                xr, xs = ps[:, (2 * j) % 8, :], ps[:, (2 * j + 1) % 8, :]
                nc.vector.tensor_tensor(yr[:, j, :], xr, hr[:, j, :], ALU.mult)
                nc.vector.tensor_tensor(cross[:, 2 * (j % 2), :], xs, hs[:, j, :], ALU.mult)
                nc.vector.tensor_tensor(ys[:, j, :], xr, hs[:, j, :], ALU.mult)
                nc.vector.tensor_tensor(cross[:, 2 * (j % 2) + 1, :], xs, hn if j == 0 else hr[:, j, :], ALU.mult).then_inc(S["dve_done"].sem, 1)

        @block.gpsimd
        def _(pool):
            for j in range(TT):
                pool.wait_ge(S["dve_done"].sem, S["dve_done"].at(j + 1))
                nc.gpsimd.tensor_tensor(yr[:, j, :], yr[:, j, :], cross[:, 2 * (j % 2), :], ALU.subtract)
                nc.gpsimd.tensor_tensor(ys[:, j, :], ys[:, j, :], cross[:, 2 * (j % 2) + 1, :], ALU.add).then_inc(S["pool_done"].sem, 1)
    close_dft(core)
    S["dve_done"].close(TT)
    S["pool_done"].close(TT)


def phase_inverse_gate(core, hy, o):
    nc, ap, S, ps = core.nc, core.ap, core.sig, core.psum
    yr, ys = core.view3(XR_KB, TT, DH), core.view3(XS_KB, TT, DH)
    ring = [core.view3(DFT_RING_KB + 4 * s, TT, P) for s in range(4)]
    skip = core.view(46, DH)
    zs = core.view3(52, 4, DH)
    with nc.Block() as block:
        @block.sync
        def _(sp):
            sp.dma_start(skip, ap["hy_skip"][0, o].partition_broadcast(P)).then_inc(S["loaded"].sem, 16)
            dft_loads(core, sp)

        @block.tensor
        def _(pe):
            for j in range(TT):
                for part, src in ((0, yr), (1, ys)):
                    u = 2 * j + part
                    pe.wait_ge(S["loaded%d" % (u % 4)].sem, S["loaded%d" % (u % 4)].at(16 * (u // 4 + 1)))
                    for k in range(TT):
                        last = nc.tensor.matmul(ps[:, j, :], ring[u % 4][:, k, :], src[:, k, :], start=part == 0 and k == 0, stop=False)
                    last.then_inc(S["aux_done"].sem, 1)
                nc.tensor.matmul(ps[:, j, :], core.small[:, 2, :], ys[:, 0, :], start=False, stop=True).then_inc(S["mm_done"].sem, 1)

        @block.gpsimd
        def _(pool):
            pool.wait_ge(S["loaded"].sem, S["loaded"].at(16))
            for j in range(TT):
                if j >= 4:
                    pool.wait_ge(S["dve_done"].sem, S["dve_done"].at(j - 3))
                nc.gpsimd.tensor_tensor(zs[:, j % 4, :], hy[:, j, 0:DH], skip, ALU.mult).then_inc(S["pool_done"].sem, 1)

        @block.vector
        def _(dve):
            chain = Chain(dve, S["dve_chain"])
            for j in range(TT):
                dve.wait_ge(S["mm_done"].sem, S["mm_done"].at(j + 1))
                dve.wait_ge(S["pool_done"].sem, S["pool_done"].at(j + 1))
                chain(nc.vector.tensor_tensor(zs[:, j % 4, :], ps[:, j, :], zs[:, j % 4, :], ALU.add))
                nc.vector.tensor_tensor(hy[:, j, 0:DH], zs[:, j % 4, :], hy[:, j, (o + 1) * DH:(o + 2) * DH], ALU.mult).then_inc(S["dve_done"].sem, 1)
    close_dft(core)
    S["mm_done"].close(TT)
    S["loaded"].close(16)
    S["dve_done"].close(TT)
    S["pool_done"].close(TT)
    S["dve_chain"].close(TT)


def phase_group_norm(core, src, groups, dst, gain, scratch):
    nc, S, ps = core.nc, core.sig, core.psum
    width = DH // groups
    sq = core.view3(scratch, 2, DH)
    ss = core.tiny2[:, 0:TT * groups]
    rstd = core.tiny2[:, 64:64 + TT * groups]
    with nc.Block() as block:
        @block.gpsimd
        def _(pool):
            for t in range(TT):
                if t >= 2:
                    pool.wait_ge(S["dve_done"].sem, S["dve_done"].at(t - 1))
                nc.gpsimd.tensor_tensor(sq[:, t % 2, :], src[:, t, :], src[:, t, :], ALU.mult).then_inc(S["pool_done"].sem, 1)

        @block.vector
        def _(dve):
            for t in range(TT):
                dve.wait_ge(S["pool_done"].sem, S["pool_done"].at(t + 1))
                nc.vector.reduce_sum(ss[:, t * groups:(t + 1) * groups], sq[:, t % 2, :].rearrange("p (g w) -> p g w", g=groups), AX.X).then_inc(S["dve_done"].sem, 1)
            dve.wait_ge(S["stat_ready"].sem, S["stat_ready"].at(1))
            nc.vector.reciprocal(rstd, rstd).then_inc(S["dve_chain"].sem, 1)
            dve.wait_ge(S["dve_chain"].sem, S["dve_chain"].at(1))
            for t in range(TT):
                v = src[:, t, :].rearrange("p (g w) -> p g w", g=groups)
                r = rstd[:, t * groups:(t + 1) * groups].unsqueeze(2).to_broadcast([P, groups, width])
                nc.vector.tensor_tensor(v, v, r, ALU.mult).then_inc(S["row_ready"].sem, 1)
            for t in range(TT):
                dve.wait_ge(S["tr_done"].sem, S["tr_done"].at(t + 1))
                g = gain.unsqueeze(2).to_broadcast([P, 4, P])
                nc.vector.tensor_tensor(dst[:, :, t * P:(t + 1) * P], ps[:, t, :].rearrange("p (a b) -> p a b", a=4), g, ALU.mult)

        @block.scalar
        def _(act):
            act.wait_ge(S["dve_done"].sem, S["dve_done"].at(TT))
            nc.scalar.activation(rstd, ss, ACT.Sqrt, scale=1.0 / width, bias=core.eps).then_inc(S["stat_ready"].sem, 1)

        @block.tensor
        def _(pe):
            for t in range(TT):
                pe.wait_ge(S["row_ready"].sem, S["row_ready"].at(t + 1))
                for j in range(4):
                    last = nc.tensor.transpose(ps[:, t, j * P:(j + 1) * P], src[:, t, j * P:(j + 1) * P], core.ident)
                last.then_inc(S["tr_done"].sem, 1)
    for n in ("pool_done", "dve_done", "row_ready", "tr_done"):
        S[n].close(TT)
    S["stat_ready"].close(1)
    S["dve_chain"].close(1)
QKT_KB, V_KB, O_KB, IG_KB, FG_KB = 70, 102, 119, 135, 139
MT_KB, ACOL_KB, EM_KB = 32, 203, 205
VW = 132


def phase_qk_proj(core, xt, w):
    nc, S, ps = core.nc, core.sig, core.psum
    qkt = core.view3(QKT_KB, 8, L)
    ring = [core.view3(159 + 4 * s, KT, P) for s in range(4)]
    sg = [core.view(143 + 4 * s, L) for s in range(2)]
    wv = w.rearrange("a (k p) n -> p (a k) n", p=P)
    ld = [S["loaded%d" % s] for s in range(4)]
    pair = lambda n: ps[:, 2 * (n % 4):2 * (n % 4) + 2, :].rearrange("p a b -> p (a b)")
    with nc.Block() as block:
        @block.sync
        def _(sp):
            for n in range(8):
                if n >= 4:
                    sp.wait_ge(S["mm_done"].sem, S["mm_done"].at(n - 3))
                sp.dma_start(ring[n % 4], wv[:, :, HY_COLS + n * P:HY_COLS + (n + 1) * P]).then_inc(ld[n % 4].sem, 16)

        @block.tensor
        def _(pe):
            for n in range(8):
                pe.wait_ge(ld[n % 4].sem, ld[n % 4].at(16 * (n // 4 + 1)))
                if n >= 4:
                    pe.wait_ge(S["dve_done"].sem, S["dve_done"].at(n - 3))
                for half in range(2):
                    for k in range(KT):
                        last = nc.tensor.matmul(ps[:, 2 * (n % 4) + half, :], ring[n % 4][:, k, :], xt[:, k, half * BANK:(half + 1) * BANK],
                                                start=k == 0, stop=k == KT - 1)
                last.then_inc(S["mm_done"].sem, 1)

        @block.scalar
        def _(act):
            for n in range(8):
                act.wait_ge(S["mm_done"].sem, S["mm_done"].at(n + 1))
                nc.scalar.activation(qkt[:, n, :], pair(n), ACT.Identity, scale=core.colsA[:, CW_ML + 8 + n:CW_ML + 9 + n],
                                     bias=core.colsA[:, CB_ML + n:CB_ML + n + 1]).then_inc(S["act_done"].sem, 1)
                act.wait_ge(S["dve_done"].sem, S["dve_done"].at(n + 1))
                nc.scalar.activation(qkt[:, n, :], qkt[:, n, :], ACT.Silu)

        @block.vector
        def _(dve):
            chain = Chain(dve, S["dve_chain"])
            for n in range(8):
                dve.wait_ge(S["act_done"].sem, S["act_done"].at(n + 1))
                pr, t = pair(n), qkt[:, n, :]
                chain(nc.vector.scalar_tensor_tensor(out=t[:, 1:L], in0=pr[:, 0:L - 1], scalar=core.colsA[:, CW_ML + n:CW_ML + n + 1],
                                                     in1=t[:, 1:L], op0=ALU.mult, op1=ALU.add))
                nc.vector.scalar_tensor_tensor(out=t[:, 0:L - 1], in0=pr[:, 1:L], scalar=core.colsA[:, CW_ML + 16 + n:CW_ML + 17 + n],
                                               in1=t[:, 0:L - 1], op0=ALU.mult, op1=ALU.add).then_inc(S["dve_done"].sem, 1)
    for n in ("mm_done", "dve_done", "act_done", "dve_chain"):
        S[n].close(8)
    for s in range(4):
        ld[s].close(32)


def phase_vo_gates(core, xt, w):
    nc, ap, S, ps = core.nc, core.ap, core.sig, core.psum
    v = core.view(V_KB, TT * 4 * VW).rearrange("p (t h c) -> p t h c", t=TT, h=4)
    og = core.view3(O_KB, TT, DH)
    wo, wv_ = core.view3(143, KT, DH), core.view3(159, KT, DH)
    gw = core.view3(175, 2, KT * 64).rearrange("p g (k c) -> p g k c", k=KT)
    gb = core.tiny[0:64, 16:18]
    gates = [core.view(IG_KB, L, 64), core.view(FG_KB, L, 64)]
    wv = w.rearrange("a (k p) n -> p (a k) n", p=P)
    base = HY_COLS + 1024
    with nc.Block() as block:
        @block.gpsimd
        def _(pool):
            nc.gpsimd.memset(gw, 0.0)
            nc.gpsimd.memset(gb, 0.0).then_inc(S["pool_done"].sem, 1)
            nc.gpsimd.memset(v[:, :, :, P:P + 1], 1.0)

        @block.sync
        def _(sp):
            sp.dma_start(wv_, wv[:, :, base:base + DH]).then_inc(S["loaded0"].sem, 16)
            sp.dma_start(wo, wv[:, :, base + DH:base + 2 * DH]).then_inc(S["loaded1"].sem, 16)
            sp.wait_ge(S["pool_done"].sem, S["pool_done"].at(1))
            with nc.allow_non_contiguous_dma("sixteen gate columns"):
                for kind in range(2):
                    for way in range(2):
                        c = 8 * way + 4 * kind
                        for k in range(KT):
                            sp.dma_start(gw[:, kind, k, 32 * way:32 * way + 4], wv[:, k, base + 2 * DH + c:base + 2 * DH + c + 4]).then_inc(S["loaded2"].sem, 16)
                        sp.dma_start(gb[32 * way:32 * way + 4, kind:kind + 1], ap["ml_gate_b"].rearrange("a c -> c a")[c:c + 4, :]).then_inc(S["loaded2"].sem, 16)

        @block.tensor
        def _(pe):
            for n, wt in ((0, wv_), (1, wo)):
                pe.wait_ge(S["loaded%d" % n].sem, S["loaded%d" % n].at(16))
                for t in range(TT):
                    if n == 1:
                        pe.wait_ge(S["act_free"].sem, S["act_free"].at(t + 1))
                    for k in range(KT):
                        last = nc.tensor.matmul(ps[:, t, :], xt[:, k, t * P:(t + 1) * P], wt[:, k, :], start=k == 0, stop=k == KT - 1)
                    last.then_inc(S["mm_done"].sem, 1)
            pe.wait_ge(S["loaded2"].sem, S["loaded2"].at(16 * 4 * (KT + 1)))
            for kind in range(2):
                for half in range(2):
                    u = 2 * kind + half
                    pe.wait_ge(S["act_free"].sem, S["act_free"].at(TT + u + 1))
                    for k in range(KT):
                        last = nc.tensor.matmul(ps[0:64, u, :], gw[:, kind, k, :], xt[:, k, half * BANK:(half + 1) * BANK], start=k == 0, stop=k == KT - 1)
                last.then_inc(S["mm_done"].sem, 1)

        @block.scalar
        def _(act):
            for t in range(TT):
                act.wait_ge(S["mm_done"].sem, S["mm_done"].at(t + 1))
                nc.scalar.activation(v[:, t, :, 0:P], ps[:, t, :].rearrange("p (h c) -> p h c", h=4), ACT.Copy).then_inc(S["act_free"].sem, 1)
            for t in range(TT):
                act.wait_ge(S["mm_done"].sem, S["mm_done"].at(TT + t + 1))
                nc.scalar.activation(og[:, t, :], ps[:, t, :], ACT.Sigmoid).then_inc(S["act_free"].sem, 1)

        @block.vector
        def _(dve):
            for kind in range(2):
                dve.wait_ge(S["mm_done"].sem, S["mm_done"].at(2 * TT + kind + 1))
                nc.vector.tensor_scalar(gates[kind], ps[0:64, 2 * kind:2 * kind + 2, :].rearrange("p a b -> p (a b)"), gb[:, kind:kind + 1], None, ALU.add)
    S["pool_done"].close(1)
    S["loaded0"].close(16)
    S["loaded1"].close(16)
    S["loaded2"].close(16 * 4 * (KT + 1))
    S["mm_done"].close(2 * TT + 2)
    S["act_free"].close(2 * TT)


def phase_gate_scans(core):
    nc, S, ps = core.nc, core.sig, core.psum
    ig, fg = core.view(IG_KB, L, 64), core.view(FG_KB, L, 64)
    t1, cum = core.view(143, L, 64), core.view(147, L, 64)
    mx, m = core.view(MT_KB, L, 64), core.view(155, L, 64)
    acol, em = core.view3(ACOL_KB, TT, 64), core.view3(EM_KB, TT, 64)
    one = core.small[:, 5, 10:11]
    with nc.Block() as block:
        @block.scalar
        def _(act):
            chain = Chain(act, S["act_chain"])
            chain(nc.scalar.activation(t1, fg, ACT.Abs))
            chain(nc.scalar.activation(t1, t1, ACT.Exp, scale=-1.0))
            nc.scalar.activation(t1, t1, ACT.Ln, bias=one[0:64, :]).then_inc(S["act_done"].sem, 1)
            act.wait_ge(S["tr_done"].sem, S["tr_done"].at(1))
            nc.scalar.activation(em, ps[:, 1, :].rearrange("p (a b) -> p a b", a=TT), ACT.Exp, scale=-1.0)

        @block.vector
        def _(dve):
            chain = Chain(dve, S["dve_chain"])
            dve.wait_ge(S["act_done"].sem, S["act_done"].at(1))
            chain(nc.vector.scalar_tensor_tensor(out=fg, in0=fg, scalar=0.0, in1=t1, op0=ALU.min, op1=ALU.subtract))
            for way in range(2):
                rows = slice(32 * way, 32 * way + 32)
                step = slice(None, None, -1) if way else slice(None)
                ones = one[rows, :].to_broadcast([32, L])
                chain(nc.vector.tensor_tensor_scan(cum[rows, step], ones, fg[rows, step], 0.0, ALU.mult, ALU.add))
            chain(nc.vector.tensor_tensor(ig, ig, cum, ALU.subtract))
            for way in range(2):
                rows = slice(32 * way, 32 * way + 32)
                step = slice(None, None, -1) if way else slice(None)
                chain(nc.vector.tensor_tensor_scan(mx[rows, step], ig[rows, step], ig[rows, step], 0.0, ALU.max, ALU.max))
            nc.vector.tensor_tensor(m, cum, mx, ALU.add).then_inc(S["dve_done"].sem, 1)
            dve.wait_ge(S["tr_done"].sem, S["tr_done"].at(1))
            nc.vector.tensor_copy(acol, ps[:, 0, :].rearrange("p (a b) -> p a b", a=TT))

        @block.tensor
        def _(pe):
            pe.wait_ge(S["dve_done"].sem, S["dve_done"].at(1))
            for n, src in ((0, ig), (1, m)):
                for t in range(TT):
                    last = nc.tensor.transpose(ps[:, n, t * 64:(t + 1) * 64], src[:, t * P:(t + 1) * P], core.ident[0:64, 0:64])
            last.then_inc(S["tr_done"].sem, 1)
    S["act_chain"].close(2)
    S["act_done"].close(1)
    S["dve_chain"].close(6)
    S["dve_done"].close(1)
    S["tr_done"].close(1)


def phase_mlstm(core):
    nc, ap, S, ps = core.nc, core.ap, core.sig, core.psum
    qkt = core.view3(QKT_KB, 8, L)
    v = core.view(V_KB, TT * 4 * VW).rearrange("p (t h c) -> p t h c", t=TT, h=4)
    og = core.view3(O_KB, TT, DH)
    mx = core.view(MT_KB, L, 64)
    acol, em = core.view3(ACOL_KB, TT, 64), core.view3(EM_KB, TT, 64)
    pt = [[core.view3(159, 36, P), core.view3(177, 36, P)], [core.view3(6, 36, P), core.view3(135, 36, P)]]
    nmb = [core.view3(195, 2, L), core.view3(24, 2, L)]
    dg = core.view3(36, 4, P)
    sel = core.view3(153, 8, P, 64)
    hsum = core.view3(157, 2, P)
    r2 = core.tiny2[:, 128:144].rearrange("p (a b) -> p a b", b=2)
    first = [[sum(TT - i for i in range(j)) for j in range(TT)], [sum(i + 1 for i in range(j)) for j in range(TT)]]
    scale = float(P) ** -0.5
    NH = NH_ML
    with nc.Block() as block:
        @block.sync
        def _(sp):
            sp.dma_start(sel, ap["c_sel"]).then_inc(S["loaded"].sem, 16)

        @block.tensor
        def _(pe):
            pe.wait_ge(S["loaded"].sem, S["loaded"].at(16))

            def spread(h):
                for way in range(2):
                    if 2 * h + way >= 1:
                        pe.wait_ge(S["act_free"].sem, S["act_free"].at(2 * h + way))
                    for half in range(2):
                        last = nc.tensor.matmul(ps[:, half, :], sel[:, 4 * way + h, :], mx[:, half * BANK:(half + 1) * BANK], start=True, stop=True)
                    last.then_inc(S["aux_done"].sem, 1)

            def scores(h, j):
                n = TT * h + j
                if n >= 2:
                    pe.wait_ge(S["dve_done"].sem, S["dve_done"].at(n - 1))
                for half in range(2):
                    last = nc.tensor.matmul(ps[:, 2 + 2 * (n % 2) + half, :], qkt[:, 4 + h, j * P:(j + 1) * P], qkt[:, h, half * BANK:(half + 1) * BANK],
                                            start=True, stop=True)
                last.then_inc(S["mm_done"].sem, 1)

            def values(h, t):
                n = TT * h + t
                pe.wait_ge(S["dve_done"].sem, S["dve_done"].at(TT * (h + 1)))
                if n >= 2:
                    pe.wait_ge(S["dve_free"].sem, S["dve_free"].at(n - 1))
                for way in range(2):
                    js = range(t + 1) if way == 0 else range(t, TT)
                    for j in js:
                        at = first[way][j] + (t - j if way == 0 else t)
                        last = nc.tensor.matmul(ps[:, 6 + n % 2, way * VW:way * VW + P + 1], pt[h % 2][way][:, at, :], v[:, j, h, 0:P + 1],
                                                start=j == js[0], stop=j == js[-1])
                last.then_inc(S["aux2_done"].sem, 1)

            spread(0)
            for h in range(NH + 1):
                for j in range(TT):
                    if h < NH:
                        scores(h, j)
                    if h >= 1:
                        values(h - 1, j)
                if h + 1 < NH:
                    spread(h + 1)

        @block.scalar
        def _(act):
            for h in range(NH):
                for way in range(2):
                    act.wait_ge(S["aux_done"].sem, S["aux_done"].at(2 * h + way + 1))
                    nc.scalar.activation(nmb[h % 2][:, way, :], ps[:, 0:2, :].rearrange("p a b -> p (a b)"), ACT.Copy, scale=-1.0).then_inc(S["act_free"].sem, 1)
                if h >= 2:
                    act.wait_ge(S["aux2_done"].sem, S["aux2_done"].at(TT * (h - 1)))
                act.wait_ge(S["act_free"].sem, S["act_free"].at(2 * h + 2))
                for j in range(TT):
                    n = TT * h + j
                    for way in range(2):
                        a = acol[:, j, 32 * way + h:32 * way + h + 1]
                        p = pt[h % 2][way]
                        f = first[way][j]
                        off = (f + 1, f + TT - j, (j + 1) * P, L) if way == 0 else (f, f + j, 0, j * P)
                        if off[1] > off[0]:
                            nc.scalar.activation(p[:, off[0]:off[1], :].rearrange("p a b -> p (a b)"), nmb[h % 2][:, way, off[2]:off[3]], ACT.Exp, bias=a)
                    act.wait_ge(S["row_ready"].sem, S["row_ready"].at(n + 1))
                    for way in range(2):
                        at = first[way][j] + (0 if way == 0 else j)
                        last = nc.scalar.activation(pt[h % 2][way][:, at, :], dg[:, 2 * (n % 2) + way, :], ACT.Exp)
                    last.then_inc(S["act_done"].sem, 1)

        @block.vector
        def _(dve):
            chain = Chain(dve, S["dve_chain"])

            def diagonal(h, j):
                n = TT * h + j
                if n >= 2:
                    dve.wait_ge(S["act_done"].sem, S["act_done"].at(n - 1))
                dve.wait_ge(S["act_free"].sem, S["act_free"].at(2 * h + 2))
                for way in range(2):
                    last = nc.vector.scalar_tensor_tensor(out=dg[:, 2 * (n % 2) + way, :], in0=nmb[h % 2][:, way, j * P:(j + 1) * P],
                                                          scalar=acol[:, j, 32 * way + h:32 * way + h + 1], in1=core.small[:, 3 + way, :],
                                                          op0=ALU.add, op1=ALU.add)
                last.then_inc(S["row_ready"].sem, 1)

            def weigh(h, j):
                n = TT * h + j
                dve.wait_ge(S["act_done"].sem, S["act_done"].at(n + 1))
                dve.wait_ge(S["mm_done"].sem, S["mm_done"].at(n + 1))
                sc = ps[:, 2 + 2 * (n % 2):4 + 2 * (n % 2), :].rearrange("p a b -> p (a b)")
                for way in range(2):
                    f = first[way][j]
                    lo, hi, a, b = (f, f + TT - j, j * P, L) if way == 0 else (f, f + j + 1, 0, (j + 1) * P)
                    w = pt[h % 2][way][:, lo:hi, :].rearrange("p a b -> p (a b)")
                    last = nc.vector.scalar_tensor_tensor(out=w, in0=sc[:, a:b], scalar=scale, in1=w, op0=ALU.mult, op1=ALU.mult)
                last.then_inc(S["dve_done"].sem, 1)

            def finish(h, t):
                n = TT * h + t
                dve.wait_ge(S["aux2_done"].sem, S["aux2_done"].at(n + 1))
                out = ps[:, 6 + n % 2, 0:2 * VW].rearrange("p (a b) -> p a b", a=2)
                r = r2[:, n % 8, :]
                den = out[:, :, P]
                chain(nc.vector.scalar_tensor_tensor(out=r, in0=den, scalar=-1.0, in1=em[:, t, h:h + 33:32], op0=ALU.mult, op1=ALU.max))
                chain(nc.vector.tensor_tensor(r, den, r, ALU.max))
                chain(nc.vector.reciprocal(r, r))
                hs = hsum[:, n % 2, :]
                chain(nc.vector.tensor_scalar(hs, out[:, 0, 0:P], r[:, 0:1], None, ALU.mult))
                ins = nc.vector.scalar_tensor_tensor(out=hs, in0=out[:, 1, 0:P], scalar=r[:, 1:2], in1=hs, op0=ALU.mult, op1=ALU.add)
                ins.then_inc(S["dve_free"].sem, 1)
                dve.wait_ge(S["dve_free"].sem, S["dve_free"].at(n + 1))
                o = og[:, t, h * P:(h + 1) * P]
                nc.vector.tensor_tensor(o, hs, o, ALU.mult)

            diagonal(0, 0)
            for h in range(NH + 1):
                for j in range(TT):
                    if h < NH:
                        n = TT * h + j + 1
                        if n < TT * NH:
                            diagonal(n // TT, n % TT)
                        weigh(h, j)
                    if h >= 1:
                        finish(h - 1, j)
    S["loaded"].close(16)
    S["aux_done"].close(2 * NH)
    S["act_free"].close(2 * NH)
    for n in ("mm_done", "act_done", "row_ready", "dve_done", "dve_free", "aux2_done"):
        S[n].close(TT * NH)
    S["dve_chain"].close(4 * TT * NH)
H_KB, WROWS_KB = 70, 102


def phase_rows_gemm(core, lhs, w, h, gate=None, residual=None, ring_kb=(102, 118), tmp_kb=None):
    nc, S, ps = core.nc, core.sig, core.psum
    nk = lhs.shape[1]
    ring = [core.view3(kb, nk, BANK) for kb in ring_kb]
    wv = w.rearrange("a (k p) n -> p (a k) n", p=P)
    with nc.Block() as block:
        @block.sync
        def _(sp):
            for c in range(2):
                sp.dma_start(ring[c], wv[:, :, c * BANK:(c + 1) * BANK]).then_inc(S["loaded%d" % c].sem, 16)
            if residual is not None:
                sp.dma_start(h, residual.rearrange("a (t p) d -> p (a t) d", p=P)).then_inc(S["loaded2"].sem, 16)

        @block.tensor
        def _(pe):
            for c in range(2):
                pe.wait_ge(S["loaded%d" % c].sem, S["loaded%d" % c].at(16))
                for t in range(TT):
                    if c == 1:
                        pe.wait_ge(S["dve_free"].sem, S["dve_free"].at(t + 1))
                    for k in range(nk):
                        last = nc.tensor.matmul(ps[:, t, :], lhs[:, k, t * P:(t + 1) * P], ring[c][:, k, :], start=k == 0, stop=k == nk - 1)
                    last.then_inc(S["mm_done"].sem, 1)

        @block.vector
        def _(dve):
            if residual is not None:
                dve.wait_ge(S["loaded2"].sem, S["loaded2"].at(16))
            for u in range(2 * TT):
                c, t = u // TT, u % TT
                dve.wait_ge(S["mm_done"].sem, S["mm_done"].at(u + 1))
                hv = h[:, t, c * BANK:(c + 1) * BANK]
                if gate is None:
                    nc.vector.tensor_tensor(hv, ps[:, t, :], hv, ALU.add).then_inc(S["dve_free"].sem, 1)
                else:
                    tmp = core.view3(tmp_kb, 2, BANK)[:, u % 2, :]
                    if u >= 2:
                        dve.wait_ge(S["pool_done"].sem, S["pool_done"].at(u - 1))
                    nc.vector.tensor_tensor(tmp, ps[:, t, :], gate[:, c * BANK:(c + 1) * BANK], ALU.mult).then_inc(S["dve_free"].sem, 1)

        @block.gpsimd
        def _(pool):
            if gate is not None:
                for u in range(2 * TT):
                    c, t = u // TT, u % TT
                    pool.wait_ge(S["dve_free"].sem, S["dve_free"].at(u + 1))
                    hv = h[:, t, c * BANK:(c + 1) * BANK]
                    nc.gpsimd.tensor_tensor(hv, core.view3(tmp_kb, 2, BANK)[:, u % 2, :], hv, ALU.add).then_inc(S["pool_done"].sem, 1)
    S["loaded0"].close(16)
    S["loaded1"].close(16)
    if residual is not None:
        S["loaded2"].close(16)
    S["mm_done"].close(2 * TT)
    S["dve_free"].close(2 * TT)
    if gate is not None:
        S["pool_done"].close(2 * TT)


def phase_cols_gemm(core, tiles, ring_kb=102):
    nc, S, ps = core.nc, core.sig, core.psum
    ring = [core.view3(ring_kb + 4 * s, KT, P) for s in range(4)]
    n_tiles = len(tiles)
    ld = [S["loaded%d" % s] for s in range(4)]
    with nc.Block() as block:
        @block.sync
        def _(sp):
            for n, (parts, xt, out) in enumerate(tiles):
                if n >= 4:
                    sp.wait_ge(S["mm_done"].sem, S["mm_done"].at(n - 3))
                at = 0
                for w in parts:
                    sp.dma_start(ring[n % 4][:, :, at:at + w.shape[2]], w).then_inc(ld[n % 4].sem, 16)
                    at += w.shape[2]

        @block.tensor
        def _(pe):
            arrived = [0] * 4
            for n, (parts, xt, out) in enumerate(tiles):
                arrived[n % 4] += 16 * len(parts)
                pe.wait_ge(ld[n % 4].sem, ld[n % 4].at(arrived[n % 4]))
                if n >= 4:
                    pe.wait_ge(S["act_free"].sem, S["act_free"].at(n - 3))
                cols, width = sum(w.shape[2] for w in parts), xt.shape[2]
                for a in range(0, width, BANK):
                    b = min(a + BANK, width)
                    for k in range(KT):
                        last = nc.tensor.matmul(ps[0:cols, 2 * (n % 4) + a // BANK, 0:b - a], ring[n % 4][:, k, 0:cols], xt[:, k, a:b],
                                                start=k == 0, stop=k == KT - 1)
                last.then_inc(S["mm_done"].sem, 1)

        @block.scalar
        def _(act):
            for n, (parts, xt, out) in enumerate(tiles):
                act.wait_ge(S["mm_done"].sem, S["mm_done"].at(n + 1))
                cols, width = out.shape[0], out.shape[1]
                src = ps[0:cols, 2 * (n % 4):2 * (n % 4) + 2, :].rearrange("p a b -> p (a b)")[:, 0:width]
                nc.scalar.activation(out, src, ACT.Copy).then_inc(S["act_free"].sem, 1)
    S["mm_done"].close(n_tiles)
    S["act_free"].close(n_tiles)
    for s in range(4):
        ld[s].close(16 * sum(len(t[0]) for t in tiles[s::4]))


def phase_rows_proj(core, chunks, slots):
    nc, S, ps = core.nc, core.sig, core.psum
    units = [(c, t) for c, (w, lhs, out) in enumerate(chunks) for t in range(lhs.shape[2] // P)]
    ring = [core.view3(kb, KT, w.shape[2]) for kb, (w, _, _) in zip(slots, chunks)]
    with nc.Block() as block:
        @block.sync
        def _(sp):
            for c, (w, lhs, out) in enumerate(chunks):
                sp.dma_start(ring[c], w).then_inc(S["loaded%d" % c].sem, 16)

        @block.tensor
        def _(pe):
            for u, (c, t) in enumerate(units):
                w, lhs, out = chunks[c]
                if t == 0:
                    pe.wait_ge(S["loaded%d" % c].sem, S["loaded%d" % c].at(16))
                if u >= 8:
                    pe.wait_ge(S["act_free"].sem, S["act_free"].at(u - 7))
                for k in range(KT):
                    last = nc.tensor.matmul(ps[:, u % 8, 0:w.shape[2]], lhs[:, k, t * P:(t + 1) * P], ring[c][:, k, :], start=k == 0, stop=k == KT - 1)
                last.then_inc(S["mm_done"].sem, 1)

        @block.scalar
        def _(act):
            for u, (c, t) in enumerate(units):
                w, lhs, out = chunks[c]
                act.wait_ge(S["mm_done"].sem, S["mm_done"].at(u + 1))
                nc.scalar.activation(out(t), ps[:, u % 8, 0:w.shape[2]], ACT.Copy).then_inc(S["act_free"].sem, 1)
    for c in range(len(chunks)):
        S["loaded%d" % c].close(16)
    S["mm_done"].close(len(units))
    S["act_free"].close(len(units))


def phase_cross_attention(core, qt, kt, v, ot, scratch):
    nc, S, ps = core.nc, core.sig, core.psum
    scale = float(NMEM) ** -0.5
    prob = [core.view3(scratch + 4 * s, 4, NMEM) for s in range(2)]
    probt = [core.view3(scratch + 8 + 4 * s, 2, BANK) for s in range(2)]
    mx, rs = core.tiny2[:, 0:64].rearrange("p (a b) -> p a b", b=8), core.tiny2[:, 64:128].rearrange("p (a b) -> p a b", b=8)
    groups = [(h, half) for h in range(4) for half in range(2)]
    G = len(groups)
    sbank = lambda g: ps[:, 2 * (g % 2):2 * (g % 2) + 2, :].rearrange("p a (b c) -> p (a b) c", c=NMEM)
    with nc.Block() as block:
        @block.tensor
        def _(pe):
            def scores(g):
                h, half = groups[g]
                if g >= 2:
                    pe.wait_ge(S["act_done"].sem, S["act_done"].at(g - 1))
                for i in range(4):
                    t = 4 * half + i
                    for c in range(2):
                        last = nc.tensor.matmul(sbank(g)[:, i, :], qt[:, 2 * h + c, t * P:(t + 1) * P], kt[:, 2 * h + c, :], start=c == 0, stop=c == 1)
                last.then_inc(S["mm_done"].sem, 1)

            scores(0)
            for g, (h, half) in enumerate(groups):
                if g + 1 < G:
                    scores(g + 1)
                pe.wait_ge(S["dve_done"].sem, S["dve_done"].at(g + 1))
                if g >= 1:
                    pe.wait_ge(S["dve_free"].sem, S["dve_free"].at(g))
                for m in range(2):
                    for i in range(4):
                        last = nc.tensor.transpose(ps[:, 4 + m, i * P:(i + 1) * P], prob[g % 2][:, i, m * P:(m + 1) * P], core.ident)
                last.then_inc(S["tr_done"].sem, 1)
                pe.wait_ge(S["dve_free"].sem, S["dve_free"].at(g + 1))
                if g >= 1:
                    pe.wait_ge(S["act_free"].sem, S["act_free"].at(g))
                for e in range(2):
                    for m in range(2):
                        last = nc.tensor.matmul(ps[:, 6 + e, :], v[:, m, h * 256 + e * P:h * 256 + (e + 1) * P], probt[g % 2][:, m, :], start=m == 0, stop=m == 1)
                last.then_inc(S["aux_done"].sem, 1)

        @block.vector
        def _(dve):
            chain = Chain(dve, S["dve_chain"])

            def maxima(g):
                dve.wait_ge(S["mm_done"].sem, S["mm_done"].at(g + 1))
                chain(nc.vector.reduce_max(mx[:, g, 0:4], sbank(g), AX.X))
                nc.vector.tensor_scalar(mx[:, g, 4:8], mx[:, g, 0:4], -scale, None, ALU.mult).then_inc(S["stat_ready"].sem, 1)

            maxima(0)
            for g in range(G):
                if g + 1 < G:
                    maxima(g + 1)
                dve.wait_ge(S["act_done"].sem, S["act_done"].at(g + 1))
                chain(nc.vector.reciprocal(rs[:, g, 4:8], rs[:, g, 0:4]))
                nc.vector.tensor_tensor(prob[g % 2], prob[g % 2], rs[:, g, 4:8].unsqueeze(2).to_broadcast([P, 4, NMEM]), ALU.mult).then_inc(S["dve_done"].sem, 1)
                dve.wait_ge(S["tr_done"].sem, S["tr_done"].at(g + 1))
                if g >= 2:
                    dve.wait_ge(S["aux_done"].sem, S["aux_done"].at(g - 1))
                nc.vector.tensor_copy(probt[g % 2], ps[:, 4:6, :]).then_inc(S["dve_free"].sem, 1)

        @block.scalar
        def _(act):
            def outputs(g):
                h, half = groups[g]
                act.wait_ge(S["aux_done"].sem, S["aux_done"].at(g + 1))
                nc.scalar.activation(ot[:, 2 * h:2 * h + 2, half * BANK:(half + 1) * BANK], ps[:, 6:8, :], ACT.Copy).then_inc(S["act_free"].sem, 1)

            for g, (h, half) in enumerate(groups):
                act.wait_ge(S["stat_ready"].sem, S["stat_ready"].at(g + 1))
                if g >= 2:
                    act.wait_ge(S["tr_done"].sem, S["tr_done"].at(g - 1))
                for i in range(4):
                    last = nc.scalar.activation(prob[g % 2][:, i, :], sbank(g)[:, i, :], ACT.Exp, scale=scale, bias=mx[:, g, 4 + i:5 + i], accum_out=rs[:, g, i:i + 1])
                last.then_inc(S["act_done"].sem, 1)
                if g >= 1:
                    outputs(g - 1)
            outputs(G - 1)

    for n in ("mm_done", "tr_done", "aux_done", "stat_ready", "act_done", "act_free", "dve_done", "dve_free", "dve_chain"):
        S[n].close(G * (2 if n == "dve_chain" else 1))


def phase_ffn1(core, xt, h):
    nc, ap, S, ps = core.nc, core.ap, core.sig, core.psum
    ft = core.view3(6, 8, L)
    r1 = [core.view3(102 + 4 * s, KT, P) for s in range(8)]
    r2 = [core.view3(134 + 16 * s, 8, BANK) for s in range(2)]
    w1 = ap["ff_w1"].rearrange("a (k p) n -> p (a k) n", p=P)
    w2 = ap["ff_w2"].rearrange("a (k p) n -> p (a k) n", p=P)
    Q = FF // L
    s1 = [S[n] for n in ("loaded", "x_ready", "stored", "stat_ready", "row_ready", "col_ready", "pool_chain", "act_chain")]
    s2 = [S["loaded0"], S["loaded1"]]

    def each_quarter(eng, body):
        body(0, True)
        with eng.Fori(1, Q) as q:
            body(q, False)

    with nc.Block() as block:
        @block.sync
        def _(sp):
            def loads(q, first):
                for f in range(8):
                    if not first:
                        sp.wait_ge(S["mm_done"].sem, S["mm_done"].at(8 * (q - 1) + f + 1))
                    sp.dma_start(r1[f], w1[:, :, bass.ds(q * L + f * P, P)]).then_inc(s1[f].sem, 16)
                for c in range(2):
                    if not first:
                        sp.wait_ge(S["aux_done"].sem, S["aux_done"].at(16 * (q - 1) + 8 * (c + 1)))
                    sp.dma_start(r2[c], w2[:, bass.ds(8 * q, 8), c * BANK:(c + 1) * BANK]).then_inc(s2[c].sem, 16)
            each_quarter(sp, loads)

        @block.tensor
        def _(pe):
            def products(q, first):
                for f in range(8):
                    pe.wait_ge(s1[f].sem, s1[f].at(16 * (q + 1)))
                    if f >= 4:
                        pe.wait_ge(S["act_free"].sem, S["act_free"].at(8 * q + f - 3))
                    elif not first:
                        pe.wait_ge(S["dve_free"].sem, S["dve_free"].at(16 * q - 6 + 2 * f))
                    for half in range(2):
                        for k in range(KT):
                            last = nc.tensor.matmul(ps[:, 2 * (f % 4) + half, :], r1[f][:, k, :], xt[:, k, half * BANK:(half + 1) * BANK],
                                                    start=k == 0, stop=k == KT - 1)
                    last.then_inc(S["mm_done"].sem, 1)
                pe.wait_ge(S["pool_done"].sem, S["pool_done"].at(8 * q + 8))
                for c in range(2):
                    pe.wait_ge(s2[c].sem, s2[c].at(16 * (q + 1)))
                    for t in range(TT):
                        if c == 1:
                            pe.wait_ge(S["dve_free"].sem, S["dve_free"].at(16 * q + t + 1))
                        for k in range(8):
                            last = nc.tensor.matmul(ps[:, t, :], ft[:, k, t * P:(t + 1) * P], r2[c][:, k, :], start=k == 0, stop=k == 7)
                        last.then_inc(S["aux_done"].sem, 1)
            each_quarter(pe, products)

        @block.scalar
        def _(act):
            def relus(q, first):
                for f in range(8):
                    act.wait_ge(S["mm_done"].sem, S["mm_done"].at(8 * q + f + 1))
                    nc.scalar.activation(ft[:, f, :], ps[:, 2 * (f % 4):2 * (f % 4) + 2, :].rearrange("p a b -> p (a b)"), ACT.Relu).then_inc(S["act_free"].sem, 1)
            each_quarter(act, relus)

        @block.gpsimd
        def _(pool):
            def squares(q, first):
                for f in range(8):
                    pool.wait_ge(S["act_free"].sem, S["act_free"].at(8 * q + f + 1))
                    nc.gpsimd.tensor_tensor(ft[:, f, :], ft[:, f, :], ft[:, f, :], ALU.mult).then_inc(S["pool_done"].sem, 1)
            each_quarter(pool, squares)

        @block.vector
        def _(dve):
            def sums(q, first):
                for c in range(2):
                    for t in range(TT):
                        dve.wait_ge(S["aux_done"].sem, S["aux_done"].at(16 * q + 8 * c + t + 1))
                        hv = h[:, t, c * BANK:(c + 1) * BANK]
                        nc.vector.tensor_tensor(hv, ps[:, t, :], hv, ALU.add).then_inc(S["dve_free"].sem, 1)
            each_quarter(dve, sums)
    for s in s1 + s2:
        s.close(16 * Q)
    for n, k in (("mm_done", 8), ("act_free", 8), ("pool_done", 8), ("aux_done", 16), ("dve_free", 16)):
        S[n].close(k * Q)


def phase_final_norm(core, h, gain, gain_kb, out_dram=None):
    nc, S = core.nc, core.sig
    g = core.view(gain_kb, D)
    junk = core.view3(gain_kb + 4, 2, D)
    ss, rstd = core.tiny[:, 0:TT], core.tiny[:, 8:8 + TT]
    with nc.Block() as block:
        @block.sync
        def _(sp):
            sp.dma_start(g, gain.partition_broadcast(P)).then_inc(S["loaded"].sem, 16)
            if out_dram is not None:
                rows = out_dram.rearrange("a (t p) d -> p (a t) d", p=P)
                for t in range(TT):
                    sp.wait_ge(S["dve_done"].sem, S["dve_done"].at(t + 1))
                    sp.dma_start(rows[:, t, :], h[:, t, :]).then_inc(S["stored"].sem, 16)
                sp.wait_ge(S["stored"].sem, S["stored"].at(16 * TT))

        @block.scalar
        def _(act):
            chain = Chain(act, S["act_chain"])
            for i in range(TT):
                chain(nc.scalar.activation(junk[:, i % 2, :], h[:, i, :], ACT.Square, accum_out=ss[:, i:i + 1]))
            nc.scalar.activation(rstd, ss, ACT.Sqrt, scale=1.0 / D, bias=core.eps).then_inc(S["stat_ready"].sem, 1)

        @block.vector
        def _(dve):
            dve.wait_ge(S["loaded"].sem, S["loaded"].at(16))
            dve.wait_ge(S["stat_ready"].sem, S["stat_ready"].at(1))
            nc.vector.reciprocal(rstd, rstd).then_inc(S["dve_chain"].sem, 1)
            dve.wait_ge(S["dve_chain"].sem, S["dve_chain"].at(1))
            for t in range(TT):
                nc.vector.scalar_tensor_tensor(out=h[:, t, :], in0=h[:, t, :], scalar=rstd[:, t:t + 1], in1=g, op0=ALU.mult, op1=ALU.mult).then_inc(S["dve_done"].sem, 1)
    S["loaded"].close(16)
    S["act_chain"].close(TT)
    S["stat_ready"].close(1)
    S["dve_chain"].close(1)
    S["dve_done"].close(TT)
    if out_dram is not None:
        S["stored"].close(16 * TT)


def phase_load_memory(core, mem):
    nc, S = core.nc, core.sig
    with nc.Block() as block:
        @block.sync
        def _(sp):
            sp.dma_start(mem, core.ap["mem"].rearrange("a (t p) d -> p (a t) d", p=P)).then_inc(S["loaded"].sem, 16)
            sp.wait_ge(S["loaded"].sem, S["loaded"].at(16))
    S["loaded"].close(16)


def first_block(core):
    ap = core.ap
    x, xt = core.view3(38, TT, D), core.view3(6, KT, L)
    w_in = ap["w_in"]
    phase_load(core)
    phase_norm(core, x, xt, core.colsA[:, G_MIX:G_MIX + 8])
    hy = core.view3(70, TT, HY_COLS)
    phase_conv_proj(core, xt, w_in, hy)
    phase_filter_hidden(core)
    for o in range(2):
        phase_filter_time(core, o)
        phase_filter_spectrum(core)
        phase_signal_spectrum(core, hy)
        phase_inverse_gate(core, hy, o)
    mixt = core.view3(38, 8, L)
    phase_group_norm(core, hy[:, :, 0:DH], 8, mixt[:, 0:4, :], core.colsB[:, G_HY:G_HY + 4], 182)
    phase_qk_proj(core, xt, w_in)
    phase_vo_gates(core, xt, w_in)
    phase_gate_scans(core)
    phase_mlstm(core)
    phase_group_norm(core, core.view3(O_KB, TT, DH), 4, mixt[:, 4:8, :], core.colsB[:, G_ML:G_ML + 4], 182)
    second_half(core, mixt)


def second_half(core, mixt):
    ap = core.ap
    h = core.view3(H_KB, TT, D)
    phase_rows_gemm(core, mixt, ap["w_out"], h, residual=ap["x"])
    xt = core.view3(6, KT, L)
    phase_norm(core, h, xt, core.colsA[:, G_X:G_X + 8])
    mem, memt = core.view3(134, 2, D), core.view3(142, KT, NMEM)
    phase_load_memory(core, mem)
    phase_norm(core, mem, memt, core.colsA[:, G_MEM:G_MEM + 8])
    qt, kt, v = core.view3(38, 8, L), core.view3(166, 8, NMEM), core.view3(174, 2, D)
    wt = {n: ap[n].rearrange("a (k p) n -> p (a k) n", p=P) for n in ("xa_wq", "xa_wk", "xa_wv")}
    phase_cols_gemm(core, [([wt["xa_wk"][:, :, n * P:(n + 1) * P]], memt, kt[:, n, :]) for n in range(8)]
                    + [([wt["xa_wq"][:, :, n * P:(n + 1) * P]], xt, qt[:, n, :]) for n in range(8)])
    phase_rows_proj(core, [(wt["xa_wv"][:, :, c * BANK:(c + 1) * BANK], memt, lambda t, c=c: v[:, t, c * BANK:(c + 1) * BANK]) for c in range(2)], (102, 118))
    ot = core.view3(6, 8, L)
    phase_cross_attention(core, qt, kt, v, ot, 182)
    phase_rows_gemm(core, ot, ap["xa_wo"], h)
    xt = core.view3(38, KT, L)
    phase_norm(core, h, xt, core.colsA[:, G_FF:G_FF + 8], scratch=182)
    phase_ffn1(core, xt, h)
    phase_final_norm(core, h, ap["final_norm_g"], 182)
QAT_KB, KAT_KB, RING2_KB, QBT_KB, QIT_KB, KIT_KB, VA_KB, CKV_KB, CKVT_KB = 38, 54, 102, 134, 150, 166, 170, 186, 190.5
GA1_KB, GA2_KB, QLT_KB, SEL_KB, MIX_KB = 199.75, 203.75, 6, 102, 134
IDX_SCALE = (8 * 64) ** -0.5
TAKEN = -3.0e38
FIRST_SEL = TOPK // P
SCALE = HD ** -0.5


def phase_ada(core):
    nc, ap, S, ps = core.nc, core.ap, core.sig, core.psum
    ring = [core.view3(102 + 16 * s, KT, BANK) for s in range(2)]
    brow = [core.view(134 + 2 * s, BANK) for s in range(2)]
    crep = core.view3(138, KT, P)
    rows = [core.view(142 + 2 * s, BANK) for s in range(2)]
    ga = {4: core.view(GA1_KB, BANK), 5: core.view(GA1_KB + 2, BANK), 10: core.view(GA2_KB, BANK), 11: core.view(GA2_KB + 2, BANK)}
    cact = core.tiny[:, 24:32]
    cols = core.tiny2[:, 200:248]
    core.mod_scale = [core.tiny2[:, 256:264], core.tiny2[:, 264:272]]
    core.mod_shift = [cols[:, 0:8], cols[:, 24:32]]
    w = ap["w_ada_2"].rearrange("a (k p) n -> p (a k) n", p=P)
    N = 12
    with nc.Block() as block:
        @block.sync
        def _(sp):
            for n in range(N):
                if n >= 2:
                    sp.wait_ge(S["mm_done"].sem, S["mm_done"].at(n - 1))
                sp.dma_start(ring[n % 2], w[:, :, n * BANK:(n + 1) * BANK]).then_inc(S["loaded%d" % (n % 2)].sem, 16)
                if n >= 2:
                    sp.wait_ge(S["dve_free"].sem, S["dve_free"].at(n - 1))
                sp.dma_start(brow[n % 2], ap["b_ada_2"][0, n * BANK:(n + 1) * BANK].partition_broadcast(P)).then_inc(S["loaded%d" % (2 + n % 2)].sem, 16)

        @block.scalar
        def _(act):
            nc.scalar.activation(cact, core.colsB[:, C_ACT:C_ACT + 8], ACT.Silu).then_inc(S["act_done"].sem, 1)

        @block.tensor
        def _(pe):
            def columns(n):
                pe.wait_ge(S["dve_free"].sem, S["dve_free"].at(n + 1))
                for j in range(4):
                    last = nc.tensor.matmul(ps[:, 7, 4 * n + j:4 * n + j + 1], rows[n % 2][0:1, j * P:(j + 1) * P], core.small[0:1, 5, 10:11], start=True, stop=True)
                last.then_inc(S["tr_done"].sem, 1)
            pe.wait_ge(S["dve_done"].sem, S["dve_done"].at(1))
            for n in range(N):
                pe.wait_ge(S["loaded%d" % (n % 2)].sem, S["loaded%d" % (n % 2)].at(16 * (n // 2 + 1)))
                if n >= 4:
                    pe.wait_ge(S["dve_free"].sem, S["dve_free"].at(n - 3))
                for k in range(KT):
                    last = nc.tensor.matmul(ps[:, n % 4, :], crep[:, k, :], ring[n % 2][:, k, :], start=k == 0, stop=k == KT - 1)
                last.then_inc(S["mm_done"].sem, 1)
                if n >= 1 and n - 1 not in ga:
                    columns(n - 1)

        @block.vector
        def _(dve):
            dve.wait_ge(S["act_done"].sem, S["act_done"].at(1))
            nc.vector.tensor_copy(crep, cact.unsqueeze(2).to_broadcast([P, KT, P])).then_inc(S["dve_done"].sem, 1)
            made = 0
            for n in range(N):
                dve.wait_ge(S["mm_done"].sem, S["mm_done"].at(n + 1))
                dve.wait_ge(S["loaded%d" % (2 + n % 2)].sem, S["loaded%d" % (2 + n % 2)].at(16 * (n // 2 + 1)))
                if n >= 2 and n - 2 not in ga:
                    made += 1
                    dve.wait_ge(S["tr_done"].sem, S["tr_done"].at(made))
                nc.vector.tensor_tensor(ga[n] if n in ga else rows[n % 2], ps[:, n % 4, :], brow[n % 2], ALU.add).then_inc(S["dve_free"].sem, 1)
            dve.wait_ge(S["tr_done"].sem, S["tr_done"].at(8))
            chain = Chain(dve, S["dve_chain"])
            chain(nc.vector.tensor_copy(cols[:, 0:16], ps[:, 7, 0:16]))
            chain(nc.vector.tensor_copy(cols[:, 24:40], ps[:, 7, 24:40]))
            for n, (scale, gain) in enumerate(((cols[:, 8:16], G_ATT2), (cols[:, 32:40], G_FFN2))):
                nc.vector.scalar_tensor_tensor(out=core.mod_scale[n], in0=scale, scalar=1.0, in1=core.colsA[:, gain:gain + 8], op0=ALU.add, op1=ALU.mult)
    for s in range(4):
        S["loaded%d" % s].close(16 * N // 2)
    S["mm_done"].close(N)
    S["dve_free"].close(N)
    S["act_done"].close(1)
    S["dve_done"].close(1)
    S["tr_done"].close(8)
    S["dve_chain"].close(2)


def phase_latent(core):
    nc, ap, S, ps = core.nc, core.ap, core.sig, core.psum
    ckv, ckvt = core.view3(CKV_KB, TT, RANK), core.view(CKVT_KB, L)
    qbt = core.view3(QBT_KB, 4, L)
    qlt = core.view3(QLT_KB, 8, L)
    wuk, grow, junk = core.view3(102, 4, RANK), core.view(104, RANK), core.view3(106, TT, RANK)
    ss, rstd = core.tiny[:, 0:TT], core.tiny[:, 8:8 + TT]
    with nc.Block() as block:
        @block.sync
        def _(sp):
            sp.dma_start(wuk, ap["w_uk_2"][0].rearrange("(a b) d r -> (b d) a r", b=2)).then_inc(S["loaded0"].sem, 16)
            sp.dma_start(grow, ap["kv_norm_g_2"][0].partition_broadcast(P)).then_inc(S["loaded1"].sem, 16)

        @block.scalar
        def _(act):
            for t in range(TT):
                last = nc.scalar.activation(junk[:, t, :], ckv[:, t, :], ACT.Square, accum_out=ss[:, t:t + 1])
            last.then_inc(S["act_chain"].sem, 1)
            act.wait_ge(S["act_chain"].sem, S["act_chain"].at(1))
            nc.scalar.activation(rstd, ss, ACT.Sqrt, scale=1.0 / RANK, bias=core.eps).then_inc(S["stat_ready"].sem, 1)
            for n in range(16):
                act.wait_ge(S["mm_done"].sem, S["mm_done"].at(n + 1))
                nc.scalar.activation(qlt[:, n // 2, (n % 2) * BANK:(n % 2 + 1) * BANK], ps[:, n % 4, :], ACT.Copy).then_inc(S["act_free"].sem, 1)

        @block.vector
        def _(dve):
            nc.vector.tensor_scalar(core.wi, core.wi, IDX_SCALE, None, ALU.mult)
            dve.wait_ge(S["stat_ready"].sem, S["stat_ready"].at(1))
            nc.vector.reciprocal(rstd, rstd).then_inc(S["dve_chain"].sem, 1)
            dve.wait_ge(S["dve_chain"].sem, S["dve_chain"].at(1))
            dve.wait_ge(S["loaded1"].sem, S["loaded1"].at(16))
            for t in range(TT):
                last = nc.vector.scalar_tensor_tensor(out=ckv[:, t, :], in0=ckv[:, t, :], scalar=rstd[:, t:t + 1], in1=grow, op0=ALU.mult, op1=ALU.mult)
            last.then_inc(S["dve_done"].sem, 1)
            dve.wait_ge(S["tr_done"].sem, S["tr_done"].at(1))
            nc.vector.tensor_copy(ckvt, ps[:, 4:6, :].rearrange("p a b -> p (a b)"))

        @block.tensor
        def _(pe):
            pe.wait_ge(S["loaded0"].sem, S["loaded0"].at(16))
            for n in range(16):
                h, half = n // 2, n % 2
                if n >= 4:
                    pe.wait_ge(S["act_free"].sem, S["act_free"].at(n - 3))
                rows = slice(64 * (h % 2), 64 * (h % 2) + 64)
                nc.tensor.matmul(ps[:, n % 4, :], wuk[rows, h // 2, :], qbt[rows, h // 2, half * BANK:(half + 1) * BANK], start=True, stop=True).then_inc(S["mm_done"].sem, 1)
            pe.wait_ge(S["dve_done"].sem, S["dve_done"].at(1))
            for t in range(TT):
                last = nc.tensor.transpose(ps[:, 4 + t // 4, (t % 4) * P:(t % 4 + 1) * P], ckv[:, t, :], core.ident)
            last.then_inc(S["tr_done"].sem, 1)
    S["loaded0"].close(16)
    S["loaded1"].close(16)
    for n in ("act_chain", "stat_ready", "dve_chain", "dve_done", "tr_done"):
        S[n].close(1)
    S["mm_done"].close(16)
    S["act_free"].close(16)


def sel_tile(core, i):
    start = i * (i + 1) // 2 * P
    return core.view(SEL_KB, 36 * P)[:, start:start + (i + 1) * P]


def phase_index_scores(core):
    nc, ap, S, ps = core.nc, core.ap, core.sig, core.psum
    qit, kit = core.view3(QIT_KB, 4, L), core.view(KIT_KB, L)
    rel = [core.view(120 + 4 * s, L) for s in range(3)]
    steps = [(i, h) for i in range(FIRST_SEL, TT) for h in range(8)]
    pair = lambda n, w: ps[:, 2 * (n % 4):2 * (n % 4) + 2, :].rearrange("p a b -> p (a b)")[:, 0:w]
    with nc.Block() as block:
        @block.tensor
        def _(pe):
            for n, (i, h) in enumerate(steps):
                if n >= 4:
                    pe.wait_ge(S["act_done"].sem, S["act_done"].at(n - 3))
                rows = slice(64 * (h % 2), 64 * (h % 2) + 64)
                w = (i + 1) * P
                for a in range(0, w, BANK):
                    b = min(a + BANK, w)
                    last = nc.tensor.matmul(ps[:, 2 * (n % 4) + a // BANK, 0:b - a], qit[rows, h // 2, i * P:(i + 1) * P], kit[rows, a:b], start=True, stop=True)
                last.then_inc(S["mm_done"].sem, 1)

        @block.scalar
        def _(act):
            for n, (i, h) in enumerate(steps):
                act.wait_ge(S["mm_done"].sem, S["mm_done"].at(n + 1))
                if n >= 3:
                    act.wait_ge(S["dve_done"].sem, S["dve_done"].at(n - 2))
                w = (i + 1) * P
                nc.scalar.activation(rel[n % 3][:, 0:w], pair(n, w), ACT.Relu).then_inc(S["act_done"].sem, 1)

        @block.vector
        def _(dve):
            for n, (i, h) in enumerate(steps):
                dve.wait_ge(S["act_done"].sem, S["act_done"].at(n + 1))
                w = (i + 1) * P
                sc, wc = sel_tile(core, i), core.wi[:, i, h:h + 1]
                if h == 0:
                    ins = nc.vector.tensor_scalar(sc, rel[n % 3][:, 0:w], wc, None, ALU.mult)
                else:
                    dve.wait_ge(S["dve_done"].sem, S["dve_done"].at(n))
                    ins = nc.vector.scalar_tensor_tensor(out=sc, in0=rel[n % 3][:, 0:w], scalar=wc, in1=sc, op0=ALU.mult, op1=ALU.add)
                ins.then_inc(S["dve_done"].sem, 1)
            dve.wait_ge(S["dve_done"].sem, S["dve_done"].at(len(steps)))
            for i in range(TT):
                sc = sel_tile(core, i)
                if i < FIRST_SEL:
                    if i:
                        nc.vector.memset(sc[:, 0:i * P], 0.0)
                    nc.vector.tensor_copy(sc[:, i * P:], core.small[:, 4, :])
                else:
                    nc.vector.tensor_tensor(sc[:, i * P:], sc[:, i * P:], core.small[:, 4, :], ALU.add)
    for n in ("mm_done", "act_done", "dve_done"):
        S[n].close(len(steps))


def phase_select(core):
    nc, S = core.nc, core.sig
    top = core.tiny[:, 32:48].rearrange("p (a b) -> p a b", a=2)
    with nc.Block() as block:
        @block.vector
        def _(dve):
            chain = Chain(dve, S["dve_chain"])
            for i in range(FIRST_SEL, TT):
                sc = sel_tile(core, i)
                for r in range(TOPK // 8):
                    chain(nc.vector.max(top[:, r % 2, :], sc))
                    chain(nc.vector.match_replace(out=sc, in_to_replace=top[:, r % 2, :], in_values=sc, imm_value=TAKEN))
                nc.vector.tensor_scalar(sc, sc, TAKEN, NEG, ALU.not_equal, ALU.mult)
    S["dve_chain"].close(2 * (TT - FIRST_SEL) * (TOPK // 8))


def phase_attention(core, sparse):
    nc, ap, S, ps = core.nc, core.ap, core.sig, core.psum
    qat, kat = core.view3(QAT_KB, 4, L), core.view3(KAT_KB, 4, L)
    qlt, ckvt = core.view3(QLT_KB, 8, L), core.view(CKVT_KB, L)
    va, ckv = core.view3(VA_KB, TT, 512), core.view3(CKV_KB, TT, RANK)
    mix = core.view3(MIX_KB, TT, D)
    sc = [core.view(120 + 4 * s, L) for s in range(2)]
    pt = [core.view3(166, TT, P), core.view3(194.5, TT, P)]
    bias = core.view(128, L)
    tb = [core.view(38 + 4 * s, L) for s in range(2)]
    mdist = core.view(50, L)
    olt = core.view3(54, 2, P)
    wuv = core.view3(55, 8, HD)
    stat = core.tiny2[:, 0:64].rearrange("p (a b) -> p a b", b=4)
    steps = [(h, i) for h in range(8) for i in range(TT)]
    N = len(steps)
    pair = lambda n, w: ps[:, 2 * (n % 2):2 * (n % 2) + 2, :].rearrange("p a b -> p (a b)")[:, 0:w]
    with nc.Block() as block:
        @block.sync
        def _(sp):
            if sparse:
                sp.dma_start(mdist, ap["c_mdist"]).then_inc(S["loaded0"].sem, 16)
                sp.dma_start(wuv, ap["w_uv_2"][0].rearrange("h r d -> r h d")).then_inc(S["loaded1"].sem, 16)
            else:
                for h in range(8):
                    if h >= 1:
                        sp.wait_ge(S["dve_done"].sem, S["dve_done"].at(TT * h))
                    sp.dma_start(bias, ap["c_bias_a"][h]).then_inc(S["loaded0"].sem, 16)

        @block.tensor
        def _(pe):
            def scores(n):
                h, i = steps[n]
                if n >= 2:
                    pe.wait_ge(S["dve_done"].sem, S["dve_done"].at(n - 1))
                w = (i + 1) * P
                if sparse:
                    q, k = qlt[:, h, i * P:(i + 1) * P], ckvt
                else:
                    rows = slice(64 * (h % 2), 64 * (h % 2) + 64)
                    q, k = qat[rows, h // 2, i * P:(i + 1) * P], kat[rows, h // 2, :]
                for a in range(0, w, BANK):
                    b = min(a + BANK, w)
                    last = nc.tensor.matmul(ps[:, 2 * (n % 2) + a // BANK, 0:b - a], q, k[:, a:b], start=True, stop=True)
                last.then_inc(S["mm_done"].sem, 1)

            def transposes(n):
                h, i = steps[n]
                pe.wait_ge(S["act_done"].sem, S["act_done"].at(n + 1))
                if n >= 1:
                    pe.wait_ge(S["dve_free"].sem, S["dve_free"].at(n))
                for j in range(i + 1):
                    last = nc.tensor.transpose(ps[:, 4 + j // 4, (j % 4) * P:(j % 4 + 1) * P], sc[n % 2][:, j * P:(j + 1) * P], core.ident)
                last.then_inc(S["tr_done"].sem, 1)

            def values(n):
                h, i = steps[n]
                pe.wait_ge(S["dve_free"].sem, S["dve_free"].at(n + 1))
                if n >= 2:
                    pe.wait_ge(S["act_free"].sem, S["act_free"].at(n - 1))
                for j in range(i + 1):
                    if sparse:
                        last = nc.tensor.matmul(ps[:, 6 + n % 2, 0:P], ckv[:, j, :], pt[n % 2][:, j, :], start=j == 0, stop=j == i)
                    else:
                        last = nc.tensor.matmul(ps[:, 6 + n % 2, 0:HD], pt[n % 2][:, j, :], va[:, j, h * HD:(h + 1) * HD], start=j == 0, stop=j == i)
                last.then_inc(S["aux_done"].sem, 1)

            def expand(n):
                h, i = steps[n]
                if n == 0:
                    pe.wait_ge(S["loaded1"].sem, S["loaded1"].at(16))
                pe.wait_ge(S["row_ready"].sem, S["row_ready"].at(n + 1))
                nc.tensor.matmul(ps[:, 6 + n % 2, P:P + HD], olt[:, n % 2, :], wuv[:, h, :], start=True, stop=True).then_inc(S["aux2_done"].sem, 1)

            scores(0)
            scores(1)
            for n in range(N + 2):
                if n < N:
                    transposes(n)
                if n + 2 < N:
                    scores(n + 2)
                if 1 <= n <= N:
                    values(n - 1)
                if sparse and n >= 2:
                    expand(n - 2)

        @block.gpsimd
        def _(pool):
            if sparse:
                for n, (h, i) in enumerate(steps):
                    pool.wait_ge(S["x_ready"].sem, S["x_ready"].at(h + 1))
                    if n >= 2:
                        pool.wait_ge(S["dve_done"].sem, S["dve_done"].at(n - 1))
                    w = (i + 1) * P
                    nc.gpsimd.tensor_tensor(tb[n % 2][:, 0:w], bias[:, L - w:L], sel_tile(core, i), ALU.add).then_inc(S["pool_done"].sem, 1)

        @block.vector
        def _(dve):
            chain = Chain(dve, S["dve_chain"])

            def biased(n):
                h, i = steps[n]
                w = (i + 1) * P
                if sparse:
                    dve.wait_ge(S["pool_done"].sem, S["pool_done"].at(n + 1))
                elif i == 0:
                    dve.wait_ge(S["loaded0"].sem, S["loaded0"].at(16 * (h + 1)))
                dve.wait_ge(S["mm_done"].sem, S["mm_done"].at(n + 1))
                if n >= 2:
                    dve.wait_ge(S["tr_done"].sem, S["tr_done"].at(n - 1))
                b = tb[n % 2][:, 0:w] if sparse else bias[:, L - w:L]
                st = stat[:, n % 16, :]
                nc.vector.tensor_tensor_reduce(out=sc[n % 2][:, 0:w], in0=pair(n, w), in1=b, scale=SCALE, scalar=-3.0e38,
                                               op0=ALU.add, op1=ALU.max, accum_out=st[:, 0:1]).then_inc(S["dve_done"].sem, 1)
                dve.wait_ge(S["dve_done"].sem, S["dve_done"].at(n + 1))
                nc.vector.tensor_scalar(st[:, 1:2], st[:, 0:1], -1.0, None, ALU.mult).then_inc(S["stat_ready"].sem, 1)

            def copied(n):
                h, i = steps[n]
                w = (i + 1) * P
                dve.wait_ge(S["act_done"].sem, S["act_done"].at(n + 1))
                nc.vector.reciprocal(stat[:, n % 16, 3:4], stat[:, n % 16, 2:3])
                dve.wait_ge(S["tr_done"].sem, S["tr_done"].at(n + 1))
                if n >= 2:
                    dve.wait_ge(S["aux_done"].sem, S["aux_done"].at(n - 1))
                nc.vector.tensor_copy(pt[n % 2][:, 0:i + 1, :].rearrange("p a b -> p (a b)"),
                                      ps[:, 4:6, :].rearrange("p a b -> p (a b)")[:, 0:w]).then_inc(S["dve_free"].sem, 1)

            biased(0)
            for n in range(N):
                if n + 1 < N:
                    biased(n + 1)
                copied(n)

        @block.scalar
        def _(act):
            if sparse:
                act.wait_ge(S["loaded0"].sem, S["loaded0"].at(16))

            def output(n):
                h, i = steps[n]
                if sparse:
                    act.wait_ge(S["aux2_done"].sem, S["aux2_done"].at(n + 1))
                    src, at = ps[:, 6 + n % 2, P:P + HD], 512 + h * HD
                else:
                    act.wait_ge(S["aux_done"].sem, S["aux_done"].at(n + 1))
                    src, at = ps[:, 6 + n % 2, 0:HD], h * HD
                act.wait_ge(S["dve_free"].sem, S["dve_free"].at(n + 1))
                nc.scalar.activation(mix[:, i, at:at + HD], src, ACT.Copy, scale=stat[:, n % 16, 3:4]).then_inc(S["act_free"].sem, 1)

            def latent(n):
                act.wait_ge(S["aux_done"].sem, S["aux_done"].at(n + 1))
                nc.scalar.activation(olt[:, n % 2, :], ps[:, 6 + n % 2, 0:P], ACT.Copy).then_inc(S["row_ready"].sem, 1)

            for n in range(N + 2):
                if n < N:
                    h, i = steps[n]
                    w = (i + 1) * P
                    if sparse and i == 0:
                        if h >= 1:
                            act.wait_ge(S["pool_done"].sem, S["pool_done"].at(n))
                        nc.scalar.activation(bias, mdist, ACT.Copy, scale=SLOPES_B[h] / SCALE).then_inc(S["x_ready"].sem, 1)
                    act.wait_ge(S["stat_ready"].sem, S["stat_ready"].at(n + 1))
                    nc.scalar.activation(sc[n % 2][:, 0:w], sc[n % 2][:, 0:w], ACT.Exp, bias=stat[:, n % 16, 1:2],
                                         accum_out=stat[:, n % 16, 2:3]).then_inc(S["act_done"].sem, 1)
                if sparse:
                    if 1 <= n <= N:
                        latent(n - 1)
                    if n >= 2:
                        output(n - 2)
                elif n >= 1 and n <= N:
                    output(n - 1)
    for n in ("mm_done", "tr_done", "aux_done", "dve_done", "stat_ready", "dve_free", "act_done", "act_free"):
        S[n].close(N)
    if sparse:
        for n in ("aux2_done", "row_ready", "pool_done"):
            S[n].close(N)
        S["x_ready"].close(8)
        S["loaded0"].close(16)
        S["loaded1"].close(16)
    else:
        S["loaded0"].close(16 * 8)


def phase_mix_transpose(core, mix, mixt):
    nc, S, ps = core.nc, core.sig, core.psum
    with nc.Block() as block:
        @block.tensor
        def _(pe):
            for u in range(2 * TT):
                i, q = u // 2, u % 2
                if u >= 8:
                    pe.wait_ge(S["act_free"].sem, S["act_free"].at((u - 8) // 2 + 1))
                    if u % 2:
                        pe.wait_ge(S["dve_free"].sem, S["dve_free"].at((u - 8) // 2 + 1))
                for j in range(4):
                    last = nc.tensor.transpose(ps[:, u % 8, j * P:(j + 1) * P], mix[:, i, (4 * q + j) * P:(4 * q + j + 1) * P], core.ident)
                last.then_inc(S["tr_done"].sem, 1)

        def copies(eng, odd, signal, copy):
            for u in range(odd, 2 * TT, 2):
                eng.wait_ge(S["tr_done"].sem, S["tr_done"].at(u + 1))
                i, q = u // 2, u % 2
                copy(mixt[:, 4 * q:4 * q + 4, i * P:(i + 1) * P], ps[:, u % 8, :].rearrange("p (a b) -> p a b", a=4)).then_inc(signal.sem, 1)

        @block.scalar
        def _(act):
            copies(act, 0, S["act_free"], lambda o, s: nc.scalar.activation(o, s, ACT.Copy))

        @block.vector
        def _(dve):
            copies(dve, 1, S["dve_free"], nc.vector.tensor_copy)
    S["tr_done"].close(2 * TT)
    S["act_free"].close(TT)
    S["dve_free"].close(TT)


def phase_ffn2(core, xt, h, ga):
    nc, ap, S, ps = core.nc, core.ap, core.sig, core.psum
    F = FF2 // P // 2
    ft = core.view3(134, F, L)
    ring = [core.view3(102 + 4 * s, KT, P) for s in range(8)]
    wd = [core.view3(38, F, BANK), core.view3(178, F, BANK)]
    tg = [core.view(60 + 4 * s, L) for s in range(2)]
    tmp = [core.view(68, BANK), core.view(200, BANK)]
    wgu = ap["w_gu_2"].rearrange("a (k p) n -> p (a k) n", p=P)
    wdv = ap["w_down_2"].rearrange("a (k p) n -> p (a k) n", p=P)
    s1 = [S[n] for n in ("loaded", "x_ready", "stored", "stat_ready", "row_ready", "col_ready", "pool_chain", "act_chain")]
    s2 = [S["loaded0"], S["loaded1"]]
    banks = lambda f, part: ps[:, 4 * (f % 2) + 2 * part:4 * (f % 2) + 2 * part + 2, :].rearrange("p a b -> p (a b)")
    N = 2 * F
    with nc.Block() as block:
        @block.sync
        def _(sp):
            for n in range(N):
                for part in range(2):
                    if n >= 4:
                        sp.wait_ge(S["mm_done"].sem, S["mm_done"].at(2 * (n - 4) + part + 1))
                    slot = 2 * (n % 4) + part
                    sp.dma_start(ring[slot], wgu[:, :, part * FF2 + n * P:part * FF2 + (n + 1) * P]).then_inc(s1[slot].sem, 16)
                if n % F in (4, 5):
                    c = n % F - 4
                    if n >= F:
                        sp.wait_ge(S["aux_done"].sem, S["aux_done"].at(TT * (c + 1)))
                    sp.dma_start(wd[c], wdv[:, (n // F) * F:(n // F + 1) * F, c * BANK:(c + 1) * BANK]).then_inc(s2[c].sem, 16)

        @block.tensor
        def _(pe):
            for q in range(2):
                for f in range(F):
                    n = q * F + f
                    for part in range(2):
                        slot = 2 * (n % 4) + part
                        pe.wait_ge(s1[slot].sem, s1[slot].at(16 * (n // 4 + 1)))
                        if f >= 2:
                            pe.wait_ge(S["dve_done"].sem, S["dve_done"].at(n - 1))
                        elif q:
                            pe.wait_ge(S["dve_free"].sem, S["dve_free"].at(2 * TT * q))
                        for half in range(2):
                            for k in range(KT):
                                last = nc.tensor.matmul(ps[:, 4 * (f % 2) + 2 * part + half, :], ring[slot][:, k, :], xt[:, k, half * BANK:(half + 1) * BANK],
                                                        start=k == 0, stop=k == KT - 1)
                        last.then_inc(S["mm_done"].sem, 1)
                pe.wait_ge(S["dve_done"].sem, S["dve_done"].at((q + 1) * F))
                for c in range(2):
                    pe.wait_ge(s2[c].sem, s2[c].at(16 * (q + 1)))
                    for t in range(TT):
                        if c == 1:
                            pe.wait_ge(S["dve_free"].sem, S["dve_free"].at(2 * TT * q + t + 1))
                        for k in range(F):
                            last = nc.tensor.matmul(ps[:, t, :], ft[:, k, t * P:(t + 1) * P], wd[c][:, k, :], start=k == 0, stop=k == F - 1)
                        last.then_inc(S["aux_done"].sem, 1)

        @block.scalar
        def _(act):
            for n in range(N):
                act.wait_ge(S["mm_done"].sem, S["mm_done"].at(2 * n + 1))
                if n >= 2:
                    act.wait_ge(S["dve_done"].sem, S["dve_done"].at(n - 1))
                nc.scalar.activation(tg[n % 2], banks(n % F, 0), ACT.Silu).then_inc(S["act_done"].sem, 1)

        @block.vector
        def _(dve):
            for q in range(2):
                for f in range(F):
                    n = q * F + f
                    dve.wait_ge(S["act_done"].sem, S["act_done"].at(n + 1))
                    dve.wait_ge(S["mm_done"].sem, S["mm_done"].at(2 * n + 2))
                    nc.vector.tensor_tensor(ft[:, f, :], banks(f, 1), tg[n % 2], ALU.mult).then_inc(S["dve_done"].sem, 1)
                for u in range(2 * TT):
                    c, t = u // TT, u % TT
                    m = 2 * TT * q + u
                    dve.wait_ge(S["aux_done"].sem, S["aux_done"].at(m + 1))
                    if m >= 2:
                        dve.wait_ge(S["pool_done"].sem, S["pool_done"].at(m - 1))
                    nc.vector.tensor_tensor(tmp[m % 2], ps[:, t, :], ga[:, c * BANK:(c + 1) * BANK], ALU.mult).then_inc(S["dve_free"].sem, 1)

        @block.gpsimd
        def _(pool):
            for m in range(4 * TT):
                c, t = m % (2 * TT) // TT, m % TT
                pool.wait_ge(S["dve_free"].sem, S["dve_free"].at(m + 1))
                hv = h[:, t, c * BANK:(c + 1) * BANK]
                nc.gpsimd.tensor_tensor(hv, tmp[m % 2], hv, ALU.add).then_inc(S["pool_done"].sem, 1)
    for slot in range(8):
        s1[slot].close(16 * len(range(slot // 2, N, 4)))
    for s in s2:
        s.close(32)
    S["mm_done"].close(2 * N)
    S["act_done"].close(N)
    S["dve_done"].close(N)
    for n in ("aux_done", "dve_free", "pool_done"):
        S[n].close(4 * TT)


def second_block(core):
    ap = core.ap
    h, xt = core.view3(H_KB, TT, D), core.view3(6, KT, L)
    phase_ada(core)
    phase_norm(core, h, xt, core.mod_scale[0], shift=core.mod_shift[0], scratch=142)
    w = ap["w_in_2"].rearrange("a (k p) n -> p (a k) n", p=P)
    tiles = []
    for kb, start in ((QAT_KB, QA0), (KAT_KB, KA0), (QBT_KB, QB0), (QIT_KB, QI0)):
        dst = core.view3(kb, 4, L)
        tiles += [([w[:, :, start + n * P:start + (n + 1) * P]], xt, dst[:, n, :]) for n in range(4)]
    tiles.append(([w[:, :, KI0:KI0 + 64]] * 2, xt, core.view(KIT_KB, L)))
    phase_cols_gemm(core, tiles)
    va, ckv = core.view3(VA_KB, TT, 512), core.view3(CKV_KB, TT, RANK)
    core.wi = core.tiny2[:, 300:364].rearrange("p (t h) -> p t h", t=TT)
    phase_rows_proj(core, [(w[:, :, VA0:VA0 + 512], xt, lambda t: va[:, t, :]),
                           (w[:, :, CK0:CK0 + RANK], xt, lambda t: ckv[:, t, :]),
                           (w[:, :, WI0:WI0 + 8], xt, lambda t: core.wi[:, t, :])], (102, 118, 122))
    phase_latent(core)
    phase_index_scores(core)
    phase_select(core)
    phase_attention(core, sparse=False)
    phase_attention(core, sparse=True)
    mix, mixt = core.view3(MIX_KB, TT, D), core.view3(38, 8, L)
    phase_mix_transpose(core, mix, mixt)
    phase_rows_gemm(core, mixt, ap["w_out_2"], h, gate=core.view(GA1_KB, D), tmp_kb=166)
    phase_norm(core, h, xt, core.mod_scale[1], shift=core.mod_shift[1], scratch=142)
    phase_ffn2(core, xt, h, core.view(GA2_KB, D))
    phase_final_norm(core, h, ap["g_final_2"][:], 134, out_dram=ap["out"])


def build_program(nc, ap):
    core = Core(nc, ap)
    first_block(core)
    second_block(core)


def kernel(**inputs):
    import concourse.bacc as bacc
    from concourse.bass_utils import run_bass_kernel_spmd

    nc = bacc.Bacc("TRN2", target_bir_lowering=False, num_devices=1)
    arrays, ap = {}, {}
    for name, value in [*inputs.items(), *constants().items()]:
        a = np.ascontiguousarray(value)
        arrays[f"in_{name}_dram"] = a
        ap[name] = nc.dram_tensor(f"in_{name}_dram", a.shape, mybir.dt.from_np(a.dtype), kind="ExternalInput").ap()
    ap["out"] = nc.dram_tensor("out_0_dram", (1, L, D), F32, kind="ExternalOutput").ap()
    build_program(nc, ap)
    r = run_bass_kernel_spmd(nc, [arrays], core_ids=[0])
    return r.results[0]["out_0_dram"]
```

```python
import math

import numpy as np

import concourse.bass as bass
from concourse import mybir
from concourse.alu_op_type import AluOpType as ALU

F32 = mybir.dt.float32
F32R = mybir.dt.float32r
ACT = mybir.ActivationFunctionType
AX = mybir.AxisListType

P = 128
BANK = 512
L = 1024
D = 1024
TT = L // P
KT = D // P
EPS = 1e-6
NMEM = 256
DH = 512
NH_ML = 4
HY_COLS = 3 * DH
FF = 4 * D
FF2 = -(-8 * D // (3 * 256)) * 256
NA = 8
HD = 64
RANK = 128
TOPK = 256
NEG = -1.0e30
QA0, KA0, VA0, QB0, CK0, QI0, KI0, WI0 = (int(v) for v in np.cumsum([0, 512, 512, 512, 512, 128, 512, 64]))
ARENA = 207 * 256 + 192


class Signal:

    def __init__(self, nc, name):
        self.sem = nc.alloc_semaphore(name)
        self.base = 0

    def at(self, n):
        return self.base + n

    def close(self, n):
        self.base += n


def constants():
    half = L // 2
    n, even = np.arange(half)[:, None], 2 * np.arange(half)[None, :]
    tables = []
    for part, k in ((np.cos, even), (np.sin, even), (np.cos, even + 1), (np.sin, even + 1)):
        t = part(np.pi * ((n * k) % (2 * L)) / L)
        if (part is np.cos) == (k[0, 0] == 0):
            t[0] = (-1.0) ** np.arange(half)
        tables.append(t.astype(np.float32))
    block = lambda t, j: t.reshape(4, P, half)[:, :, j * P:(j + 1) * P].transpose(1, 0, 2)
    fwd = np.stack([block(tables[2 * (j // 4) + part], j % 4) for j in range(TT) for part in range(2)])
    inv = np.stack([block(np.ascontiguousarray(tables[m].T), j) for j in range(4) for m in (0, 3, 2, 1)])
    p = np.arange(P)
    alt = np.where(p % 2 == 0, 1.0, -1.0).astype(np.float32)
    small = np.zeros((P, 7, P), np.float32)
    small[:, 0] = np.eye(P)
    mats = np.zeros((P, 6, P), np.float32)
    mats[:, 0] = np.eye(P)[::-1]
    mats[:, 1, 0] = alt
    mats[0, 2, :] = alt
    mats[0, 3, :] = 1.0
    mats[:, 4, 0] = 1.0
    mats[0, 5, 0] = 1.0
    order = np.concatenate([np.arange(half), [half], L - np.arange(1, half)])
    small[:, 3] = np.where(p[None, :] >= p[:, None], 0.0, NEG)
    small[:, 4] = np.where(p[None, :] <= p[:, None], 0.0, NEG)
    small[:, 5, 0:TT] = -order.reshape(TT, P).T / (L - 1.0)
    small[:, 5, 8] = 2.0 / (2 * L)
    small[:, 5, 9] = 2.0 / (2 * L)
    small[0, 5, 9] = 1.0 / (2 * L)
    small[:, 5, 10] = 1.0
    small[:, 5, 11] = EPS
    small[:, 6] = 1.0
    sel = np.zeros((64, 8, P), np.float32)
    for h in range(8):
        sel[(h // 4) * 32 + h % 4, h, :] = 1.0
    f32 = np.float32
    t = np.linspace(0.0, 1.0, L, dtype=f32)[:, None]
    w = (f32(2.0 * math.pi / L) * np.arange(L, dtype=f32))[:, None]
    bands = np.linspace(1e-4, 15, 16, dtype=f32)[None, :]
    z = np.concatenate([t, np.cos(bands * w), -np.sin(bands * w)], axis=-1)
    deltas = np.abs(np.linspace(math.log(1e-2) / 1.5, math.log(1e-2) / 0.3, DH, dtype=f32))
    slopes = (2.0 ** (-8.0 * (np.arange(16, dtype=f32) + 1.0) / 16)).astype(f32)
    dist = p[:, None] - (np.arange(L) - (L - P))[None, :]
    mult = ((dist >= 0) & (dist <= 128)) * 1.0 + ((dist >= 0) & (dist % 4 == 0) & (dist <= 512)) + ((dist >= 0) & (dist % 16 == 0))
    lnm = np.where(mult > 0, np.log(np.maximum(mult, 1)), NEG)
    bias_a = np.stack([np.where(mult > 0, 8.0 * (lnm - float(slopes[2 * h]) * dist), NEG) for h in range(8)]).astype(f32)
    mdist = (-dist).astype(f32)
    return {
        "c_fwd": fwd, "c_inv": inv, "c_mats": mats, "c_small": small, "c_sel": sel,
        "c_z": np.ascontiguousarray(z.T[:, order]), "c_delta": deltas[None, :].copy(),
        "c_bias_a": bias_a, "c_mdist": mdist,
    }


SLOPES_B = [float(np.float32(2.0 ** (-8.0 * (2 * h + 2) / 16))) for h in range(8)]


class Core:

    def __init__(self, nc, ap):
        self.nc = nc
        self.ap = ap
        self.base = (nc.sbuf_base + 63) // 64 * 64
        self.placed = {}
        self.psum = nc.alloc_psum_tensor("psum", [P, 8, BANK], F32)
        names = (
            "loaded", "loaded0", "loaded1", "loaded2", "loaded3", "stored",
            "mm_done", "tr_done", "act_done", "act_free", "act_chain", "dve_done", "dve_free", "dve_chain",
            "pool_done", "pool_chain", "aux_done", "aux_free", "aux2_done", "x_ready",
            "stat_ready", "row_ready", "col_ready", "w_hi", "w_lo", "v_hi", "v_lo", "square_done",
            "bank_free", "ft_hi", "ft_lo", "table0", "table1", "table2", "table3", "mirrored", "selected",
        )
        self.sig = {n: Signal(nc, n) for n in names}
        self.small = self.view(0, 7 * P).rearrange("p (a b) -> p a b", a=7)
        self.ident = self.small[:, 0, :]
        self.colsA = self.view(3.5, 128)
        self.colsB = self.view(4.0, 64)
        self.tiny = self.view(4.25, 64)
        self.eps = self.small[:, 5, 11:12]
        self.tiny2 = self.view(4.5, 384)

    def place(self, kb, shape, dtype):
        start, words = int(round(kb * 256)), int(np.prod(shape[1:]))
        assert start + words <= ARENA, (kb, shape)
        key = (start, words, dtype)
        if key not in self.placed:
            name = "%s_%d_%d" % ("rounded" if dtype == F32R else "plain", start, words)
            self.placed[key] = self.nc.alloc_sbuf_tensor_at(name, [P, words], dtype, offset=self.base + 4 * start)
        return self.placed[key]

    def view(self, kb, words, parts=P):
        return self.place(kb, [P, words], F32)[0:parts, :]

    def view3(self, kb, a, b, parts=P):
        return self.view(kb, a * b, parts).rearrange("p (a b) -> p a b", a=a)


    def view_r(self, kb, a, b):
        return self.place(kb, [P, a * b], F32R)[:, :].rearrange("p (a b) -> p a b", a=a)


class Split:

    def __init__(self, core, kb, a, b):
        self.hi, self.lo = core.view_r(kb, a, b), core.view_r(kb + a * b / 256, a, b)
        self.raw = core.view3(kb + a * b / 256, a, b)
        self.hi_raw = self.hi.bitcast(F32)
        self.before = core.view3(kb, a, b)


def mm3(nc, out, wh, wl, xh, xl, first, last):
    nc.tensor.matmul(out, wh, xh, start=first, stop=False)
    nc.tensor.matmul(out, wh, xl, start=False, stop=False)
    return nc.tensor.matmul(out, wl, xh, start=False, stop=last)


class Chain:

    def __init__(self, eng, signal):
        self.eng, self.count, self.n = eng, signal, 0

    def __call__(self, ins):
        self.n += 1
        ins.then_inc(self.count.sem, 1)
        self.eng.wait_ge(self.count.sem, self.count.at(self.n))


G_MIX, CW_HY, CB_HY, CW_ML, CB_ML, G_X, G_MEM, G_FF = 0, 8, 44, 56, 80, 88, 96, 104
G_ATT2, G_FFN2 = 112, 120
C_ACT, G_HY, G_ML, G_KV = 0, 8, 12, 16


def phase_load(core):
    nc, ap, S = core.nc, core.ap, core.sig
    x = core.view3(118, TT, D)
    rowsA = core.view(102, P)
    rowsB = core.view(103, P)
    loads = [
        (x, ap["x"].rearrange("a (t p) d -> p (a t) d", p=P)),
        (core.small, ap["c_small"]),
    ]
    at = 0
    for name, rows in (("norm_mix_g", 8), ("hy_conv_w", 36), ("hy_conv_b", 12), ("ml_conv_w", 24), ("ml_conv_b", 8),
                       ("norm_x_g", 8), ("norm_mem_g", 8), ("norm_ff_g", 8), ("g_attn_2", 8), ("g_ffn_2", 8)):
        src = ap[name]
        src = src.rearrange("a b (r c) -> (a b r) c", c=P) if len(src.shape) == 3 else src.rearrange("a (r c) -> (a r) c", c=P)
        loads.append((rowsA[at:at + rows, :], src))
        at += rows
    at = 0
    for name, rows in (("c_2", 8), ("hy_norm_g", 4), ("ml_norm_g", 4), ("kv_norm_g_2", 1)):
        loads.append((rowsB[at:at + rows, :], ap[name].rearrange("a (r c) -> (a r) c", c=P)))
        at += rows
    nB = at
    with nc.Block() as block:
        @block.sync
        def _(sp):
            for dst, src in loads:
                sp.dma_start(dst, src).then_inc(S["loaded"].sem, 16)

        @block.tensor
        def _(pe):
            pe.wait_ge(S["loaded"].sem, S["loaded"].at(16 * len(loads)))
            nc.tensor.transpose(core.psum[:, 0, 0:P], rowsA, core.ident)
            nc.tensor.transpose(core.psum[:, 0, P:P + nB], rowsB[0:nB, :], core.ident[0:nB, 0:nB]).then_inc(S["tr_done"].sem, 1)

        @block.vector
        def _(dve):
            dve.wait_ge(S["tr_done"].sem, S["tr_done"].at(1))
            nc.vector.tensor_copy(core.colsA, core.psum[:, 0, 0:P])
            nc.vector.tensor_copy(core.colsB[:, 0:nB], core.psum[:, 0, P:P + nB])
    S["loaded"].close(16 * len(loads))
    S["tr_done"].close(1)


def phase_norm(core, src, dst, gain, shift=None, scratch=150):
    nc, S = core.nc, core.sig
    tiles = src.shape[1]
    junk = dst.before.rearrange("p k t -> p (k t)").rearrange("p (i d) -> p i d", d=D)
    tmp = core.view3(scratch, 2, D)
    full = [core.view3(scratch + 8 + 2 * s, 4, P) for s in range(2)]
    ss, rstd = core.tiny[:, 0:tiles], core.tiny[:, 8:8 + tiles]
    ps = core.psum
    U = 2 * tiles
    part = lambda x, u: x[:, 4 * (u % 2):4 * (u % 2) + 4, (u // 2) * P:(u // 2 + 1) * P]
    with nc.Block() as block:
        @block.scalar
        def _(act):
            for i in range(tiles):
                last = nc.scalar.activation(junk[:, i, :], src[:, i, :], ACT.Square, accum_out=ss[:, i:i + 1])
            Chain(act, S["act_chain"])(last)
            nc.scalar.activation(rstd, ss, ACT.Sqrt, scale=1.0 / D, bias=core.eps).then_inc(S["stat_ready"].sem, 1)

            def scaled(i):
                if i >= 2:
                    act.wait_ge(S["tr_done"].sem, S["tr_done"].at(2 * (i - 1)))
                nc.scalar.activation(tmp[:, i % 2, :], src[:, i, :], ACT.Copy, scale=rstd[:, i:i + 1]).then_inc(S["row_ready"].sem, 1)

            act.wait_ge(S["col_ready"].sem, S["col_ready"].at(1))
            scaled(0)
            for i in range(tiles):
                if i + 1 < tiles:
                    scaled(i + 1)
                for u in (2 * i, 2 * i + 1):
                    act.wait_ge(S["dve_done"].sem, S["dve_done"].at(u + 1))
                    nc.scalar.activation(part(dst.hi, u), full[u % 2], ACT.Copy).then_inc(S["act_done"].sem, 1)

        @block.tensor
        def _(pe):
            for i in range(tiles):
                pe.wait_ge(S["row_ready"].sem, S["row_ready"].at(i + 1))
                for q in range(2):
                    u = 2 * i + q
                    if u >= 8:
                        pe.wait_ge(S["dve_done"].sem, S["dve_done"].at(u - 7))
                    for j in range(4):
                        last = nc.tensor.transpose(ps[:, u % 8, j * P:(j + 1) * P], tmp[:, i % 2, (4 * q + j) * P:(4 * q + j + 1) * P], core.ident)
                    last.then_inc(S["tr_done"].sem, 1)

        @block.vector
        def _(dve):
            chain = Chain(dve, S["dve_chain"])
            dve.wait_ge(S["stat_ready"].sem, S["stat_ready"].at(1))
            nc.vector.reciprocal(rstd, rstd).then_inc(S["col_ready"].sem, 1)
            for u in range(U):
                q = u % 2
                dve.wait_ge(S["tr_done"].sem, S["tr_done"].at(u + 1))
                if u >= 2:
                    dve.wait_ge(S["pool_done"].sem, S["pool_done"].at(u - 1))
                g = gain[:, 4 * q:4 * q + 4].unsqueeze(2).to_broadcast([P, 4, P])
                ins = nc.vector.tensor_tensor(full[q], ps[:, u % 8, :].rearrange("p (a b) -> p a b", a=4), g, ALU.mult)
                if shift is not None:
                    chain(ins)
                    sh = shift[:, 4 * q:4 * q + 4].unsqueeze(2).to_broadcast([P, 4, P])
                    ins = nc.vector.tensor_tensor(full[q], full[q], sh, ALU.add)
                ins.then_inc(S["dve_done"].sem, 1)

        @block.gpsimd
        def _(pool):
            for u in range(U):
                pool.wait_ge(S["act_done"].sem, S["act_done"].at(u + 1))
                nc.gpsimd.tensor_tensor(part(dst.lo, u), full[u % 2], part(dst.hi_raw, u), ALU.subtract).then_inc(S["pool_done"].sem, 1)
    S["act_chain"].close(1)
    S["stat_ready"].close(1)
    S["col_ready"].close(1)
    S["row_ready"].close(tiles)
    for n in ("tr_done", "dve_done", "act_done", "pool_done"):
        S[n].close(U)
    if shift is not None:
        S["dve_chain"].close(U)


def phase_split(core, pairs):
    nc, S = core.nc, core.sig
    with nc.Block() as block:
        @block.scalar
        def _(act):
            for src, hi, lo, hi_raw in pairs:
                nc.scalar.activation(hi, src, ACT.Copy).then_inc(S["act_done"].sem, 1)

        @block.vector
        def _(dve):
            for n, (src, hi, lo, hi_raw) in enumerate(pairs):
                dve.wait_ge(S["act_done"].sem, S["act_done"].at(n + 1))
                nc.vector.tensor_tensor(lo, src, hi_raw, ALU.subtract)
    S["act_done"].close(len(pairs))


def split_pairs(src, dst, at=0):
    return [(src[:, n, :], dst.hi[:, at + n, :], dst.lo[:, at + n, :], dst.hi_raw[:, at + n, :]) for n in range(src.shape[1])]


def weight_tiles(core, kb, slots=4):
    return [Split(core, kb + 8 * s, KT, P) for s in range(slots)]


def mm3_cols(nc, out, w, cols, xt, a, b):
    for k in range(KT):
        last = mm3(nc, out, w.hi[:, k, cols], w.lo[:, k, cols], xt.hi[:, k, a:b], xt.lo[:, k, a:b], k == 0, k == KT - 1)
    return last


def phase_conv_proj(core, xt, w, hy):
    nc, S, ps = core.nc, core.sig, core.psum
    ring = weight_tiles(core, 118)
    tmp = [core.view(150 + 4.25 * s, L + 1) for s in range(2)]
    cuts = [t * P for t in range(4)] + [L + 1 - (j + 1) * P for j in range(4)]
    n_tiles = HY_COLS // P
    wv = w.rearrange("a (k p) n -> p (a k) n", p=P)
    ld = [S["loaded%d" % s] for s in range(4)]
    with nc.Block() as block:
        @block.sync
        def _(sp):
            for n in range(n_tiles):
                if n >= 4:
                    sp.wait_ge(S["mm_done"].sem, S["mm_done"].at(n - 3))
                sp.dma_start(ring[n % 4].raw, wv[:, :, n * P:(n + 1) * P]).then_inc(ld[n % 4].sem, 16)

        @block.tensor
        def _(pe):
            for n in range(n_tiles + 1):
                if n < n_tiles:
                    pe.wait_ge(S["w_lo"].sem, S["w_lo"].at(n + 1))
                    if n >= 2:
                        pe.wait_ge(S["dve_done"].sem, S["dve_done"].at(n - 1))
                    for half in range(2):
                        last = mm3_cols(nc, ps[:, 2 * (n % 2) + half, :], ring[n % 4], slice(0, P), xt, half * BANK, (half + 1) * BANK)
                    last.then_inc(S["mm_done"].sem, 1)
                if n >= 1:
                    m = n - 1
                    pe.wait_ge(S["dve_done"].sem, S["dve_done"].at(m + 1))
                    if m >= 2:
                        pe.wait_ge(S["act_free"].sem, S["act_free"].at(m - 1))
                    for t in range(TT):
                        last = nc.tensor.transpose(ps[:, 4 + 2 * (m % 2) + t // 4, (t % 4) * P:(t % 4 + 1) * P], tmp[m % 2][:, cuts[t]:cuts[t] + P], core.ident)
                    last.then_inc(S["tr_done"].sem, 1)

        @block.scalar
        def _(act):
            def back(m):
                act.wait_ge(S["tr_done"].sem, S["tr_done"].at(m + 1))
                src = ps[:, 4 + 2 * (m % 2):6 + 2 * (m % 2), :].rearrange("p a (b c) -> p (a b) c", c=P)
                nc.scalar.activation(hy[:, :, m * P:(m + 1) * P], src, ACT.Copy).then_inc(S["act_free"].sem, 1)

            def weights(n):
                act.wait_ge(ld[n % 4].sem, ld[n % 4].at(16 * (n // 4 + 1)))
                nc.scalar.activation(ring[n % 4].hi, ring[n % 4].raw, ACT.Copy).then_inc(S["w_hi"].sem, 1)

            weights(0)
            weights(1)
            for n in range(n_tiles):
                if n + 2 < n_tiles:
                    weights(n + 2)
                act.wait_ge(S["mm_done"].sem, S["mm_done"].at(n + 1))
                if n >= 2:
                    act.wait_ge(S["tr_done"].sem, S["tr_done"].at(n - 1))
                nc.scalar.activation(tmp[n % 2][:, 0:L], ps[:, 2 * (n % 2):2 * (n % 2) + 2, :].rearrange("p a b -> p (a b)"), ACT.Identity,
                                     scale=core.colsA[:, CW_HY + 12 + n:CW_HY + 13 + n],
                                     bias=core.colsA[:, CB_HY + n:CB_HY + n + 1]).then_inc(S["act_done"].sem, 1)
                if n >= 1:
                    back(n - 1)
            back(n_tiles - 1)

        @block.vector
        def _(dve):
            chain = Chain(dve, S["dve_chain"])

            def weights(n):
                dve.wait_ge(S["w_hi"].sem, S["w_hi"].at(n + 1))
                nc.vector.tensor_tensor(ring[n % 4].lo, ring[n % 4].raw, ring[n % 4].hi_raw, ALU.subtract).then_inc(S["w_lo"].sem, 1)

            weights(0)
            weights(1)
            for n in range(n_tiles):
                if n + 2 < n_tiles:
                    weights(n + 2)
                dve.wait_ge(S["act_done"].sem, S["act_done"].at(n + 1))
                pr = ps[:, 2 * (n % 2):2 * (n % 2) + 2, :].rearrange("p a b -> p (a b)")
                t = tmp[n % 2]
                chain(nc.vector.scalar_tensor_tensor(out=t[:, 1:L], in0=pr[:, 0:L - 1], scalar=core.colsA[:, CW_HY + n:CW_HY + n + 1],
                                                     in1=t[:, 1:L], op0=ALU.mult, op1=ALU.add))
                chain(nc.vector.scalar_tensor_tensor(out=t[:, 0:L - 1], in0=pr[:, 1:L], scalar=core.colsA[:, CW_HY + 24 + n:CW_HY + 25 + n],
                                                     in1=t[:, 0:L - 1], op0=ALU.mult, op1=ALU.add))
                nc.vector.tensor_copy(t[:, L:L + 1], t[:, L // 2:L // 2 + 1]).then_inc(S["dve_done"].sem, 1)
    for n in ("mm_done", "dve_done", "act_free", "tr_done", "act_done", "w_hi", "w_lo"):
        S[n].close(n_tiles)
    S["dve_chain"].close(2 * n_tiles)
    for s in range(4):
        ld[s].close(16 * len(range(s, n_tiles, 4)))
FOLD_KB, HY_KB, HR_KB, HS_KB, ZFOLD_KB, DFT_RING_KB, MATS_KB, NYQ_KB, HID_KB = 6, 70, 118, 134, 150, 182, 198, 200.75, 203
TWO_PI_HI = 6.28125
TWO_PI_LO = 2 * math.pi - TWO_PI_HI
MAGIC = 1.5 * 2.0 ** 23
UNITS = 16
ALT_COL, ALT_ROW, ONE_ROW, ONE_COL, CORNER = 0, 1, 2, 3, 4


def phase_filter_hidden(core, hy):
    nc, ap, S, ps = core.nc, core.ap, core.sig, core.psum
    hid = core.view(HID_KB, L, 64)
    z = core.view(42, L, 33)
    w1, w2 = core.view(46, 64, 33), core.view(46.5, 64, 64)
    vec = core.view(47, 8, 64)
    y, n = core.view(48, L, 64), core.view(52, L, 64)
    h1 = core.view(56, L, 64)
    mats, rounded = core.view3(60, 6, P), core.view_r(MATS_KB, 5, P)
    loads = [(z, ap["c_z"]), (w1, ap["hy_filt_w1"][0]), (w2, ap["hy_filt_w2"][0])]
    for i, name in enumerate(("hy_filt_b1", "hy_filt_freq1", "hy_filt_b2", "hy_filt_freq2")):
        loads.append((vec[:, i:i + 1], ap[name].rearrange("a c -> c a")))
    blocks = [(4 + j, c) for j in range(4) for c in range(3)]
    with nc.Block() as block:
        @block.sync
        def _(sp):
            sp.dma_start(mats, ap["c_mats"]).then_inc(S["loaded0"].sem, 16)
            with nc.allow_non_contiguous_dma("64 biases and frequencies, one per partition"):
                for dst, src in loads:
                    sp.dma_start(dst, src).then_inc(S["loaded"].sem, 16)

        @block.tensor
        def _(pe):
            def mirror(m):
                t, c = blocks[m]
                if m >= 4:
                    pe.wait_ge(S["mirrored"].sem, S["mirrored"].at(m - 3))
                nc.tensor.matmul(ps[:, 4 + m % 4, :], mats[:, 0, :], hy[:, t, c * BANK:(c + 1) * BANK], start=True, stop=True).then_inc(S["tr_done"].sem, 1)

            pe.wait_ge(S["loaded"].sem, S["loaded"].at(16 * len(loads)))
            pe.wait_ge(S["loaded0"].sem, S["loaded0"].at(16))
            for half in range(2):
                last = nc.tensor.matmul(ps[0:64, half, :], w1, z[:, half * BANK:(half + 1) * BANK], start=True, stop=True)
            last.then_inc(S["mm_done"].sem, 1)
            for m in range(8):
                mirror(m)
            pe.wait_ge(S["act_done"].sem, S["act_done"].at(1))
            for half in range(2):
                last = nc.tensor.matmul(ps[0:64, 2 + half, :], w2, h1[:, half * BANK:(half + 1) * BANK], start=True, stop=True)
            last.then_inc(S["mm_done"].sem, 1)
            for m in range(8, 12):
                mirror(m)

        @block.vector
        def _(dve):
            chain = Chain(dve, S["dve_chain"])
            dve.wait_ge(S["loaded"].sem, S["loaded"].at(16 * len(loads)))
            for layer in range(2):
                fr, fb = vec[:, 2 * layer + 1:2 * layer + 2], vec[:, 4 + layer:5 + layer]
                chain(nc.vector.tensor_tensor(fb, vec[:, 2 * layer:2 * layer + 1], fr, ALU.mult))
                dve.wait_ge(S["mm_done"].sem, S["mm_done"].at(layer + 1))
                src = ps[0:64, 2 * layer:2 * layer + 2, :].rearrange("p a b -> p (a b)")
                chain(nc.vector.tensor_scalar(y, src, fr, fb, ALU.mult, ALU.add))
                chain(nc.vector.tensor_scalar(n, y, 1.0 / (2 * math.pi), MAGIC, ALU.mult, ALU.add))
                chain(nc.vector.tensor_scalar(n, n, MAGIC, None, ALU.subtract))
                chain(nc.vector.scalar_tensor_tensor(out=y, in0=n, scalar=-TWO_PI_HI, in1=y, op0=ALU.mult, op1=ALU.add))
                chain(nc.vector.scalar_tensor_tensor(out=y, in0=n, scalar=-TWO_PI_LO, in1=y, op0=ALU.mult, op1=ALU.add))
                nc.vector.tensor_scalar(y, y, 3.1415925, -3.1415925, ALU.min, ALU.max).then_inc(S["dve_done"].sem, 1)
                dve.wait_ge(S["act_done"].sem, S["act_done"].at(layer + 1))

        @block.scalar
        def _(act):
            def back(m):
                t, c = blocks[m]
                act.wait_ge(S["tr_done"].sem, S["tr_done"].at(m + 1))
                nc.scalar.activation(hy[:, t, c * BANK:(c + 1) * BANK], ps[:, 4 + m % 4, :], ACT.Copy).then_inc(S["mirrored"].sem, 1)

            act.wait_ge(S["loaded0"].sem, S["loaded0"].at(16))
            nc.scalar.activation(rounded, mats[:, 1:6, :], ACT.Copy)
            for m in range(4):
                back(m)
            act.wait_ge(S["dve_done"].sem, S["dve_done"].at(1))
            nc.scalar.activation(h1, y, ACT.Sin).then_inc(S["act_done"].sem, 1)
            for m in range(4, 10):
                back(m)
            act.wait_ge(S["dve_done"].sem, S["dve_done"].at(2))
            nc.scalar.activation(hid, y, ACT.Sin).then_inc(S["act_done"].sem, 1)
            for m in range(10, 12):
                back(m)
    S["loaded"].close(16 * len(loads))
    S["loaded0"].close(16)
    S["mm_done"].close(2)
    S["dve_chain"].close(12)
    S["dve_done"].close(2)
    S["act_done"].close(2)
    S["tr_done"].close(12)
    S["mirrored"].close(12)


def phase_filter_time(core, o):
    nc, ap, S, ps = core.nc, core.ap, core.sig, core.psum
    hid = core.view(HID_KB, L, 64)
    w3, delta = core.view(150, L, 64), core.view(154, DH)
    decay = core.view3(156, 2, DH)
    both = core.view3(160, 4, DH)
    windowed = core.view3(182, 4, DH)
    fold = Split(core, FOLD_KB, 16, DH)
    mt = core.small[:, 5, 0:TT]
    steps = [(j, m) for j in range(4) for m in range(2)]
    with nc.Block() as block:
        @block.sync
        def _(sp):
            sp.dma_start(w3, ap["hy_filt_w3"][0][:, o * L:(o + 1) * L]).then_inc(S["loaded"].sem, 16)
            sp.dma_start(delta, ap["c_delta"][0].partition_broadcast(P)).then_inc(S["loaded0"].sem, 16)

        @block.tensor
        def _(pe):
            pe.wait_ge(S["loaded"].sem, S["loaded"].at(16))
            for n, (j, m) in enumerate(steps):
                t = j + 4 * m
                if n >= 4:
                    pe.wait_ge(S["dve_done"].sem, S["dve_done"].at(n - 3))
                for half in range(2):
                    last = nc.tensor.matmul(ps[:, 2 * (n % 4) + half, :], hid[:, t * P:(t + 1) * P], w3[:, half * DH:(half + 1) * DH], start=True, stop=True)
                last.then_inc(S["mm_done"].sem, 1)

        @block.scalar
        def _(act):
            def rounded(j):
                for q in range(4):
                    act.wait_ge(S["v_hi"].sem, S["v_hi"].at(4 * j + q + 1))
                    nc.scalar.activation(fold.hi[:, 4 * q + j, :], fold.raw[:, 4 * q + j, :], ACT.Copy).then_inc(S["w_hi"].sem, 1)

            act.wait_ge(S["loaded0"].sem, S["loaded0"].at(16))
            for n, (j, m) in enumerate(steps):
                t = j + 4 * m
                if n >= 2:
                    act.wait_ge(S["dve_done"].sem, S["dve_done"].at(n - 1))
                nc.scalar.activation(decay[:, n % 2, :], delta, ACT.Exp, scale=mt[:, t:t + 1]).then_inc(S["act_done"].sem, 1)
                if m == 1 and j >= 1:
                    rounded(j - 1)
            rounded(3)

        @block.vector
        def _(dve):
            chain = Chain(dve, S["dve_chain"])

            def folded(j):
                dve.wait_ge(S["pool_done"].sem, S["pool_done"].at(2 * j + 2))
                for q in range(4):
                    a, b = both[:, q // 2, :], both[:, 2 + q // 2, :]
                    out = fold.raw[:, 4 * q + j, :]
                    ins = nc.vector.tensor_tensor(out, a, b, ALU.subtract if q % 2 else ALU.add)
                    if j == 0:
                        chain(ins)
                        ins = nc.vector.tensor_copy(out[0:1, :], (a if q % 2 else b)[0:1, :])
                    ins.then_inc(S["v_hi"].sem, 1)

            for n, (j, m) in enumerate(steps):
                dve.wait_ge(S["act_done"].sem, S["act_done"].at(n + 1))
                dve.wait_ge(S["mm_done"].sem, S["mm_done"].at(n + 1))
                if n >= 2:
                    dve.wait_ge(S["pool_done"].sem, S["pool_done"].at(n - 1))
                nc.vector.tensor_tensor(windowed[:, 2 * m, :], ps[:, 2 * (n % 4), :], decay[:, n % 2, :], ALU.mult)
                nc.vector.tensor_tensor(windowed[:, 2 * m + 1, :], ps[:, 2 * (n % 4) + 1, :], decay[:, n % 2, :], ALU.mult).then_inc(S["dve_done"].sem, 1)
                if m == 1:
                    folded(j)

        @block.gpsimd
        def _(pool):
            def low(j):
                for q in range(4):
                    pool.wait_ge(S["w_hi"].sem, S["w_hi"].at(4 * j + q + 1))
                    nc.gpsimd.tensor_tensor(fold.lo[:, 4 * q + j, :], fold.raw[:, 4 * q + j, :], fold.hi_raw[:, 4 * q + j, :], ALU.subtract)

            for n, (j, m) in enumerate(steps):
                pool.wait_ge(S["dve_done"].sem, S["dve_done"].at(n + 1))
                if j >= 1:
                    pool.wait_ge(S["v_hi"].sem, S["v_hi"].at(4 * j))
                f, b = windowed[:, 2 * m, :], windowed[:, 2 * m + 1, :]
                if n == 0:
                    nc.gpsimd.memset(b[0:1, :], 0.0).then_inc(S["pool_chain"].sem, 1)
                    pool.wait_ge(S["pool_chain"].sem, S["pool_chain"].at(1))
                nc.gpsimd.tensor_tensor(both[:, 2 * m, :], f, b, ALU.add)
                nc.gpsimd.tensor_tensor(both[:, 2 * m + 1, :], f, b, ALU.subtract).then_inc(S["pool_done"].sem, 1)
                if m == 1 and j >= 1:
                    low(j - 1)
            low(3)
    S["loaded"].close(16)
    S["loaded0"].close(16)
    for n in ("mm_done", "dve_done", "act_done", "pool_done"):
        S[n].close(TT)
    S["pool_chain"].close(1)
    S["dve_chain"].close(4)
    S["v_hi"].close(16)
    S["w_hi"].close(16)


class Tables:

    def __init__(self, core):
        self.core, self.begun = core, 0
        self.ring = [Split(core, DFT_RING_KB + 4 * s, 4, P) for s in range(4)]
        self.loaded = [core.sig["table%d" % s].sem for s in range(4)]

    def load(self, sp, current, following, ahead):
        S = self.core.sig
        for u in range(4 if ahead else 0, UNITS + (4 if following is not None else 0)):
            if u >= 4:
                sp.wait_ge(S["aux_done"].sem, S["aux_done"].at(u - 3))
            src = current[u] if u < UNITS else following[u - UNITS]
            sp.dma_start(self.ring[u % 4].raw, src).then_inc(self.loaded[u % 4], 16)

    def high(self, act, u):
        S = self.core.sig
        act.wait_ge(self.loaded[u % 4], 16 * ((self.begun + u) // 4 + 1))
        self.core.nc.scalar.activation(self.ring[u % 4].hi, self.ring[u % 4].raw, ACT.Copy).then_inc(S["ft_hi"].sem, 1)

    def low(self, pool, u):
        S, w = self.core.sig, self.ring[u % 4]
        pool.wait_ge(S["ft_hi"].sem, S["ft_hi"].at(u + 1))
        self.core.nc.gpsimd.tensor_tensor(w.lo, w.raw, w.hi_raw, ALU.subtract).then_inc(S["ft_lo"].sem, 1)

    def products(self, pe, out, u, src, at, first, last):
        nc, S, w = self.core.nc, self.core.sig, self.ring[u % 4]
        pe.wait_ge(S["ft_lo"].sem, S["ft_lo"].at(u + 1))
        for k in range(4):
            ins = mm3(nc, out, w.hi[:, k, :], w.lo[:, k, :], src.hi[:, at + k, :], src.lo[:, at + k, :], first and k == 0, last and k == 3)
        return ins

    def close(self):
        for n in ("ft_hi", "ft_lo", "aux_done"):
            self.core.sig[n].close(UNITS)
        self.begun += UNITS


def exact(nc, out, mat, src, at, last=False):
    nc.tensor.matmul(out, mat, src.hi[:, at, :], start=False, stop=False)
    return nc.tensor.matmul(out, mat, src.lo[:, at, :], start=False, stop=last)


def forward_pe(core, pe, tables, src, at_c, at_s, free_name):
    nc, S, ps = core.nc, core.sig, core.psum
    mats = core.view_r(MATS_KB, 5, P)
    for u in range(UNITS):
        j, part = u // 2, u % 2
        bank = ps[:, u % 8, :]
        if u >= 8 and part == 0:
            pe.wait_ge(S[free_name].sem, S[free_name].at(j - 3))
        at = (at_s if part else at_c) + 4 * ((j >= 4) != (part == 1))
        more = (j < 4 and part == 0) or u == 1
        ins = tables.products(pe, bank, u, src, at, True, not more)
        if j < 4 and part == 0:
            ins = exact(nc, bank, mats[:, ONE_ROW, :], src, at_c + 4, last=True)
        if u == 1:
            for k in range(4):
                exact(nc, bank, mats[:, ALT_COL, :], src, at_c + k)
            ins = exact(nc, bank, mats[:, CORNER, :], src, at_c + 4, last=True)
        ins.then_inc(S["aux_done"].sem, 1)


def phase_filter_spectrum(core, tables, hy):
    nc, ap, S, ps = core.nc, core.ap, core.sig, core.psum
    fold, zfold = Split(core, FOLD_KB, 16, DH), Split(core, ZFOLD_KB, 8, DH)
    hr, hs = core.view3(HR_KB, TT, DH), core.view3(HS_KB, TT, DH)
    hn = core.view(NYQ_KB, DH)
    with nc.Block() as block:
        @block.sync
        def _(sp):
            tables.load(sp, ap["c_fwd"], ap["c_fwd"], False)

        @block.tensor
        def _(pe):
            forward_pe(core, pe, tables, fold, 0, 8, "act_free")

        @block.scalar
        def _(act):
            for u in range(3):
                tables.high(act, u)
            for j in range(TT):
                for u in (2 * j + 3, 2 * j + 4):
                    if u < UNITS:
                        tables.high(act, u)
                act.wait_ge(S["aux_done"].sem, S["aux_done"].at(2 * j + 2))
                w = core.small[:, 5, 9:10] if j == 0 else core.small[:, 5, 8:9]
                nc.scalar.activation(hr[:, j, :], ps[:, (2 * j) % 8, :], ACT.Copy, scale=w)
                nc.scalar.activation(hs[:, j, :], ps[:, (2 * j + 1) % 8, :], ACT.Copy, scale=w).then_inc(S["act_free"].sem, 1)
                act.wait_ge(S["v_hi"].sem, S["v_hi"].at(j + 1))
                nc.scalar.activation(zfold.hi[:, j, :], zfold.raw[:, j, :], ACT.Copy).then_inc(S["w_hi"].sem, 1)

        @block.vector
        def _(dve):
            chain = Chain(dve, S["dve_chain"])
            for n in range(8):
                q, j = n // 4, n % 4
                a, b, out = hy[:, j, 0:DH], hy[:, 4 + j, 0:DH], zfold.raw[:, n, :]
                ins = nc.vector.tensor_tensor(out, a, b, ALU.subtract if q else ALU.add)
                if j == 0:
                    chain(ins)
                    ins = nc.vector.tensor_copy(out[0:1, :], (a if q else b)[0:1, :])
                ins.then_inc(S["v_hi"].sem, 1)
            dve.wait_ge(S["act_free"].sem, S["act_free"].at(1))
            chain(nc.vector.tensor_copy(hn, hr[:, 0, :]))
            chain(nc.vector.tensor_copy(hn[0:1, :], hs[0:1, 0, :]))
            nc.vector.memset(hs[0:1, 0, :], 0.0)
            for n in range(8):
                dve.wait_ge(S["w_hi"].sem, S["w_hi"].at(n + 1))
                nc.vector.tensor_tensor(zfold.lo[:, n, :], zfold.raw[:, n, :], zfold.hi_raw[:, n, :], ALU.subtract)

        @block.gpsimd
        def _(pool):
            for u in range(UNITS):
                tables.low(pool, u)
    tables.close()
    S["act_free"].close(TT)
    S["v_hi"].close(8)
    S["w_hi"].close(8)
    S["dve_chain"].close(4)


def phase_signal_spectrum(core, tables):
    nc, ap, S, ps = core.nc, core.ap, core.sig, core.psum
    zfold, y = Split(core, ZFOLD_KB, 8, DH), Split(core, FOLD_KB, 16, DH)
    hr, hs = core.view3(HR_KB, TT, DH), core.view3(HS_KB, TT, DH)
    hn = core.view(NYQ_KB, DH)
    yr, ys, cross = y.raw[:, 0:8, :], y.raw[:, 8:16, :], y.before
    with nc.Block() as block:
        @block.sync
        def _(sp):
            tables.load(sp, ap["c_fwd"], ap["c_inv"], True)

        @block.tensor
        def _(pe):
            forward_pe(core, pe, tables, zfold, 0, 0, "dve_done")

        @block.scalar
        def _(act):
            def rounded(j):
                act.wait_ge(S["pool_done"].sem, S["pool_done"].at(j + 1))
                nc.scalar.activation(y.hi[:, j, :], yr[:, j, :], ACT.Copy)
                nc.scalar.activation(y.hi[:, 8 + j, :], ys[:, j, :], ACT.Copy).then_inc(S["w_hi"].sem, 1)

            for u in range(4):
                tables.high(act, u)
            for j in range(TT):
                for u in (2 * j + 4, 2 * j + 5):
                    if u < UNITS:
                        tables.high(act, u)
                if j >= 1:
                    rounded(j - 1)
            rounded(TT - 1)

        @block.vector
        def _(dve):
            def low(j):
                dve.wait_ge(S["w_hi"].sem, S["w_hi"].at(j + 1))
                for n in (j, 8 + j):
                    nc.vector.tensor_tensor(y.lo[:, n, :], y.raw[:, n, :], y.hi_raw[:, n, :], ALU.subtract)

            for j in range(TT):
                dve.wait_ge(S["aux_done"].sem, S["aux_done"].at(2 * j + 2))
                xr, xs = ps[:, (2 * j) % 8, :], ps[:, (2 * j + 1) % 8, :]
                nc.vector.tensor_tensor(yr[:, j, :], xr, hr[:, j, :], ALU.mult)
                nc.vector.tensor_tensor(cross[:, j, :], xs, hs[:, j, :], ALU.mult)
                nc.vector.tensor_tensor(ys[:, j, :], xr, hs[:, j, :], ALU.mult)
                nc.vector.tensor_tensor(cross[:, 8 + j, :], xs, hn if j == 0 else hr[:, j, :], ALU.mult).then_inc(S["dve_done"].sem, 1)
                if j >= 1:
                    low(j - 1)
            low(TT - 1)

        @block.gpsimd
        def _(pool):
            for u in range(4):
                tables.low(pool, u)
            for j in range(TT):
                for u in (2 * j + 4, 2 * j + 5):
                    if u < UNITS:
                        tables.low(pool, u)
                pool.wait_ge(S["dve_done"].sem, S["dve_done"].at(j + 1))
                nc.gpsimd.tensor_tensor(yr[:, j, :], yr[:, j, :], cross[:, j, :], ALU.subtract)
                nc.gpsimd.tensor_tensor(ys[:, j, :], ys[:, j, :], cross[:, 8 + j, :], ALU.add).then_inc(S["pool_done"].sem, 1)
    tables.close()
    for n in ("dve_done", "pool_done", "w_hi"):
        S[n].close(TT)


def phase_inverse_gate(core, tables, hy, o):
    nc, ap, S, ps = core.nc, core.ap, core.sig, core.psum
    y = Split(core, FOLD_KB, 16, DH)
    mats = core.view_r(MATS_KB, 5, P)
    zs = core.view3(150, 4, DH)
    even = core.view3(158, 2, DH)
    both = core.view3(162, 4, DH)
    skip = core.view(170, DH)
    with nc.Block() as block:
        @block.sync
        def _(sp):
            sp.dma_start(skip, ap["hy_skip"][0, o].partition_broadcast(P)).then_inc(S["loaded"].sem, 16)
            tables.load(sp, ap["c_inv"], None, True)

        @block.tensor
        def _(pe):
            for j in range(4):
                even_bank, odd_bank, u = ps[:, 2 * j, :], ps[:, 2 * j + 1, :], 4 * j
                tables.products(pe, even_bank, u, y, 0, True, False).then_inc(S["aux_done"].sem, 1)
                exact(nc, even_bank, mats[:, ALT_ROW, :], y, 8)
                tables.products(pe, even_bank, u + 1, y, 12, False, True).then_inc(S["aux_done"].sem, 1)
                tables.products(pe, odd_bank, u + 2, y, 4, True, False).then_inc(S["aux_done"].sem, 1)
                if j == 0:
                    for k in range(4):
                        exact(nc, odd_bank, mats[:, ONE_COL, :], y, k)
                    exact(nc, odd_bank, mats[:, CORNER, :], y, 8)
                tables.products(pe, odd_bank, u + 3, y, 8, False, True).then_inc(S["aux_done"].sem, 1)

        @block.scalar
        def _(act):
            for u in range(4):
                tables.high(act, u)
            for j in range(4):
                for u in range(4 * j + 4, 4 * j + 6):
                    if u < UNITS:
                        tables.high(act, u)
                act.wait_ge(S["aux_done"].sem, S["aux_done"].at(4 * j + 2))
                if j >= 2:
                    act.wait_ge(S["dve_free"].sem, S["dve_free"].at(j - 1))
                nc.scalar.activation(even[:, j % 2, :], ps[:, 2 * j, :], ACT.Copy).then_inc(S["act_done"].sem, 1)
                for u in range(4 * j + 6, 4 * j + 8):
                    if u < UNITS:
                        tables.high(act, u)

        @block.gpsimd
        def _(pool):
            for u in range(4):
                tables.low(pool, u)
            pool.wait_ge(S["loaded"].sem, S["loaded"].at(16))
            for j in range(4):
                if j >= 2:
                    pool.wait_ge(S["dve_done"].sem, S["dve_done"].at(j - 1))
                for m in range(2):
                    nc.gpsimd.tensor_tensor(zs[:, 2 * (j % 2) + m, :], hy[:, j + 4 * m, 0:DH], skip, ALU.mult).then_inc(S["pool_done"].sem, 1)
                for u in range(4 * j + 4, 4 * j + 8):
                    if u < UNITS:
                        tables.low(pool, u)

        @block.vector
        def _(dve):
            chain = Chain(dve, S["dve_chain"])
            for j in range(4):
                dve.wait_ge(S["act_done"].sem, S["act_done"].at(j + 1))
                dve.wait_ge(S["aux_done"].sem, S["aux_done"].at(4 * j + 4))
                a, b = even[:, j % 2, :], ps[:, 2 * j + 1, :]
                out = both[:, 2 * (j % 2):2 * (j % 2) + 2, :]
                nc.vector.tensor_tensor(out[:, 0, :], a, b, ALU.add)
                ins = nc.vector.tensor_tensor(out[:, 1, :], a, b, ALU.subtract)
                if j == 0:
                    chain(ins)
                    nc.vector.tensor_copy(out[0:1, 0, :], b[0:1, :])
                    ins = nc.vector.tensor_copy(out[0:1, 1, :], a[0:1, :])
                ins.then_inc(S["dve_free"].sem, 1)
                dve.wait_ge(S["dve_free"].sem, S["dve_free"].at(j + 1))
                dve.wait_ge(S["pool_done"].sem, S["pool_done"].at(2 * j + 2))
                chain(nc.vector.tensor_tensor(out, out, zs[:, 2 * (j % 2):2 * (j % 2) + 2, :], ALU.add))
                for m in range(2):
                    t = j + 4 * m
                    ins = nc.vector.tensor_tensor(hy[:, t, 0:DH], out[:, m, :], hy[:, t, (o + 1) * DH:(o + 2) * DH], ALU.mult)
                ins.then_inc(S["dve_done"].sem, 1)
    tables.close()
    S["loaded"].close(16)
    for n in ("act_done", "dve_done", "dve_free"):
        S[n].close(4)
    S["pool_done"].close(8)
    S["dve_chain"].close(5)


def phase_group_norm(core, src, groups, dst, gain, scratch, mirrored=False):
    nc, S, ps = core.nc, core.sig, core.psum
    width = DH // groups
    sq = core.view3(scratch, 2, DH)
    ss = core.tiny2[:, 0:TT * groups]
    rstd = core.tiny2[:, 64:64 + TT * groups]
    reverse = core.view(scratch + 4, P)
    with nc.Block() as block:
        @block.sync
        def _(sp):
            if mirrored:
                sp.dma_start(reverse, core.ap["c_mats"][:, 0, :]).then_inc(S["loaded"].sem, 16)

        @block.gpsimd
        def _(pool):
            for t in range(TT):
                if t >= 2:
                    pool.wait_ge(S["dve_done"].sem, S["dve_done"].at(t - 1))
                nc.gpsimd.tensor_tensor(sq[:, t % 2, :], src[:, t, :], src[:, t, :], ALU.mult).then_inc(S["pool_done"].sem, 1)

        @block.vector
        def _(dve):
            for t in range(TT):
                dve.wait_ge(S["pool_done"].sem, S["pool_done"].at(t + 1))
                nc.vector.reduce_sum(ss[:, t * groups:(t + 1) * groups], sq[:, t % 2, :].rearrange("p (g w) -> p g w", g=groups), AX.X).then_inc(S["dve_done"].sem, 1)
            dve.wait_ge(S["stat_ready"].sem, S["stat_ready"].at(1))
            nc.vector.reciprocal(rstd, rstd).then_inc(S["dve_chain"].sem, 1)
            dve.wait_ge(S["dve_chain"].sem, S["dve_chain"].at(1))
            for t in range(TT):
                v = src[:, t, :].rearrange("p (g w) -> p g w", g=groups)
                r = rstd[:, t * groups:(t + 1) * groups].unsqueeze(2).to_broadcast([P, groups, width])
                nc.vector.tensor_tensor(v, v, r, ALU.mult).then_inc(S["row_ready"].sem, 1)
            for t in range(TT):
                dve.wait_ge(S["tr_done"].sem, S["tr_done"].at(t + 1))
                g = gain.unsqueeze(2).to_broadcast([P, 4, P])
                ranges = [(0, t * P, P)]
                if mirrored and t == 4:
                    ranges = [(0, L - P + 1, P - 1), (P - 1, L // 2, 1)]
                elif mirrored and t > 4:
                    ranges = [(0, L - (t - 3) * P + 1, P)]
                for c, at, w in ranges:
                    nc.vector.tensor_tensor(dst[:, :, at:at + w], ps[:, t, :].rearrange("p (a b) -> p a b", a=4)[:, :, c:c + w], g[:, :, 0:w], ALU.mult)

        @block.scalar
        def _(act):
            act.wait_ge(S["dve_done"].sem, S["dve_done"].at(TT))
            nc.scalar.activation(rstd, ss, ACT.Sqrt, scale=1.0 / width, bias=core.eps).then_inc(S["stat_ready"].sem, 1)

        @block.tensor
        def _(pe):
            for t in range(TT):
                pe.wait_ge(S["row_ready"].sem, S["row_ready"].at(t + 1))
                flip = mirrored and t >= 4
                if flip and t == 4:
                    pe.wait_ge(S["loaded"].sem, S["loaded"].at(16))
                for j in range(4):
                    out, tile = ps[:, t, j * P:(j + 1) * P], src[:, t, j * P:(j + 1) * P]
                    last = nc.tensor.matmul(out, tile, reverse, start=True, stop=True) if flip else nc.tensor.transpose(out, tile, core.ident)
                last.then_inc(S["tr_done"].sem, 1)
    for n in ("pool_done", "dve_done", "row_ready", "tr_done"):
        S[n].close(TT)
    S["stat_ready"].close(1)
    S["dve_chain"].close(1)
    if mirrored:
        S["loaded"].close(16)
QKT_KB, V_KB, O_KB, IG_KB, FG_KB = 70, 102, 119, 135, 139
MT_KB, ACOL_KB, EM_KB = 169, 178, 180
VW = 132


def phase_qk_proj(core, xt, w):
    nc, S, ps = core.nc, core.sig, core.psum
    qkt = core.view3(QKT_KB, 8, L)
    ring = weight_tiles(core, 143)
    wv = w.rearrange("a (k p) n -> p (a k) n", p=P)
    ld = [S["loaded%d" % s] for s in range(4)]
    pair = lambda n: ps[:, 2 * (n % 4):2 * (n % 4) + 2, :].rearrange("p a b -> p (a b)")
    with nc.Block() as block:
        @block.sync
        def _(sp):
            for n in range(8):
                if n >= 4:
                    sp.wait_ge(S["mm_done"].sem, S["mm_done"].at(n - 3))
                sp.dma_start(ring[n % 4].raw, wv[:, :, HY_COLS + n * P:HY_COLS + (n + 1) * P]).then_inc(ld[n % 4].sem, 16)

        @block.tensor
        def _(pe):
            for n in range(8):
                pe.wait_ge(S["w_lo"].sem, S["w_lo"].at(n + 1))
                if n >= 4:
                    pe.wait_ge(S["dve_done"].sem, S["dve_done"].at(n - 3))
                for half in range(2):
                    last = mm3_cols(nc, ps[:, 2 * (n % 4) + half, :], ring[n % 4], slice(0, P), xt, half * BANK, (half + 1) * BANK)
                last.then_inc(S["mm_done"].sem, 1)

        @block.scalar
        def _(act):
            def weights(n):
                act.wait_ge(ld[n % 4].sem, ld[n % 4].at(16 * (n // 4 + 1)))
                nc.scalar.activation(ring[n % 4].hi, ring[n % 4].raw, ACT.Copy).then_inc(S["w_hi"].sem, 1)

            weights(0)
            weights(1)
            for n in range(8):
                if n + 2 < 8:
                    weights(n + 2)
                act.wait_ge(S["mm_done"].sem, S["mm_done"].at(n + 1))
                nc.scalar.activation(qkt[:, n, :], pair(n), ACT.Identity, scale=core.colsA[:, CW_ML + 8 + n:CW_ML + 9 + n],
                                     bias=core.colsA[:, CB_ML + n:CB_ML + n + 1]).then_inc(S["act_done"].sem, 1)
                act.wait_ge(S["dve_done"].sem, S["dve_done"].at(n + 1))
                nc.scalar.activation(qkt[:, n, :], qkt[:, n, :], ACT.Silu)

        @block.vector
        def _(dve):
            chain = Chain(dve, S["dve_chain"])

            def weights(n):
                dve.wait_ge(S["w_hi"].sem, S["w_hi"].at(n + 1))
                nc.vector.tensor_tensor(ring[n % 4].lo, ring[n % 4].raw, ring[n % 4].hi_raw, ALU.subtract).then_inc(S["w_lo"].sem, 1)

            weights(0)
            weights(1)
            for n in range(8):
                if n + 2 < 8:
                    weights(n + 2)
                dve.wait_ge(S["act_done"].sem, S["act_done"].at(n + 1))
                pr, t = pair(n), qkt[:, n, :]
                chain(nc.vector.scalar_tensor_tensor(out=t[:, 1:L], in0=pr[:, 0:L - 1], scalar=core.colsA[:, CW_ML + n:CW_ML + n + 1],
                                                     in1=t[:, 1:L], op0=ALU.mult, op1=ALU.add))
                nc.vector.scalar_tensor_tensor(out=t[:, 0:L - 1], in0=pr[:, 1:L], scalar=core.colsA[:, CW_ML + 16 + n:CW_ML + 17 + n],
                                               in1=t[:, 0:L - 1], op0=ALU.mult, op1=ALU.add).then_inc(S["dve_done"].sem, 1)
    for n in ("mm_done", "dve_done", "act_done", "dve_chain", "w_hi", "w_lo"):
        S[n].close(8)
    for s in range(4):
        ld[s].close(32)


def phase_gates(core, xt, w):
    nc, ap, S, ps = core.nc, core.ap, core.sig, core.psum
    gw = Split(core, 175, KT, P)
    gb = core.tiny[0:64, 16:18]
    gates = [core.view(IG_KB, L, 64), core.view(FG_KB, L, 64)]
    wv = w.rearrange("a (k p) n -> p (a k) n", p=P)
    base = HY_COLS + 2048
    with nc.Block() as block:
        @block.gpsimd
        def _(pool):
            nc.gpsimd.memset(gw.raw, 0.0)
            nc.gpsimd.memset(gb, 0.0).then_inc(S["pool_done"].sem, 1)

        @block.sync
        def _(sp):
            sp.wait_ge(S["pool_done"].sem, S["pool_done"].at(1))
            with nc.allow_non_contiguous_dma("sixteen gate columns"):
                for kind in range(2):
                    for way in range(2):
                        c = 8 * way + 4 * kind
                        at = 64 * kind + 32 * way
                        sp.dma_start(gw.raw[:, :, at:at + 4], wv[:, :, base + c:base + c + 4]).then_inc(S["loaded2"].sem, 16)
                        sp.dma_start(gb[32 * way:32 * way + 4, kind:kind + 1], ap["ml_gate_b"].rearrange("a c -> c a")[c:c + 4, :]).then_inc(S["loaded2"].sem, 16)

        @block.scalar
        def _(act):
            act.wait_ge(S["loaded2"].sem, S["loaded2"].at(16 * 8))
            nc.scalar.activation(gw.hi, gw.raw, ACT.Copy).then_inc(S["w_hi"].sem, 1)

        @block.tensor
        def _(pe):
            pe.wait_ge(S["w_lo"].sem, S["w_lo"].at(1))
            for half in range(2):
                last = mm3_cols(nc, ps[:, half, :], gw, slice(0, P), xt, half * BANK, (half + 1) * BANK)
            last.then_inc(S["mm_done"].sem, 1)

        @block.vector
        def _(dve):
            dve.wait_ge(S["w_hi"].sem, S["w_hi"].at(1))
            nc.vector.tensor_tensor(gw.lo, gw.raw, gw.hi_raw, ALU.subtract).then_inc(S["w_lo"].sem, 1)
            dve.wait_ge(S["mm_done"].sem, S["mm_done"].at(1))
            for kind in range(2):
                nc.vector.tensor_scalar(gates[kind], ps[64 * kind:64 * kind + 64, 0:2, :].rearrange("p a b -> p (a b)"), gb[:, kind:kind + 1], None, ALU.add)
    S["pool_done"].close(1)
    S["loaded2"].close(16 * 8)
    for n in ("w_hi", "w_lo", "mm_done"):
        S[n].close(1)


def phase_rows_proj(core, chunks, slots, before=None, beside=None):
    nc, S, ps = core.nc, core.sig, core.psum
    KH = KT // 2
    pieces = [(c, kh) for c in range(len(chunks)) for kh in range(2)]
    ring = [Split(core, kb, KH, BANK) for kb in slots]
    R = len(ring)
    n_rows = [lhs.hi.shape[2] // P for _, lhs, _, _ in chunks]
    done = [sum(2 * r for r in n_rows[:c]) for c in range(len(chunks) + 1)]
    units = [sum(n_rows[:c]) for c in range(len(chunks) + 1)]
    ld = [S["loaded%d" % s] for s in range(R)]
    after = [done[c] + (kh + 1) * n_rows[c] for c, kh in pieces]
    with nc.Block() as block:
        if before is not None:
            before(block)

        @block.sync
        def _(sp):
            for p, (c, kh) in enumerate(pieces):
                if p >= R:
                    sp.wait_ge(S["mm_done"].sem, S["mm_done"].at(after[p - R]))
                w = chunks[c][0]
                sp.dma_start(ring[p % R].raw[:, :, 0:w.shape[2]], w[:, kh * KH:(kh + 1) * KH, :]).then_inc(ld[p % R].sem, 16)

        @block.tensor
        def _(pe):
            for p, (c, kh) in enumerate(pieces):
                w, lhs, out, func = chunks[c]
                cols = w.shape[2]
                pe.wait_ge(S["w_lo"].sem, S["w_lo"].at(p + 1))
                for t in range(n_rows[c]):
                    u = units[c] + t
                    if kh == 0 and u >= 8:
                        pe.wait_ge(S["act_free"].sem, S["act_free"].at(u - 7))
                    for k in range(KH):
                        kk = kh * KH + k
                        lt = slice(t * P, (t + 1) * P)
                        last = mm3(nc, ps[:, u % 8, 0:cols], lhs.hi[:, kk, lt], lhs.lo[:, kk, lt], ring[p % R].hi[:, k, 0:cols], ring[p % R].lo[:, k, 0:cols],
                                   kk == 0, kk == KT - 1)
                    last.then_inc(S["mm_done"].sem, 1)

        @block.scalar
        def _(act):
            def weights(p):
                act.wait_ge(ld[p % R].sem, ld[p % R].at(16 * (p // R + 1)))
                cols = chunks[pieces[p][0]][0].shape[2]
                nc.scalar.activation(ring[p % R].hi[:, :, 0:cols], ring[p % R].raw[:, :, 0:cols], ACT.Copy).then_inc(S["w_hi"].sem, 1)

            made = 0
            while made < min(R, len(pieces)):
                weights(made)
                made += 1
            for p, (c, kh) in enumerate(pieces):
                if made < len(pieces) and p >= 1:
                    weights(made)
                    made += 1
                if kh == 1:
                    w, lhs, out, func = chunks[c]
                    for t in range(n_rows[c]):
                        act.wait_ge(S["mm_done"].sem, S["mm_done"].at(done[c] + n_rows[c] + t + 1))
                        dst = out(t)
                        src = ps[:, (units[c] + t) % 8, w.shape[2] - int(np.prod(dst.shape[1:])):w.shape[2]]
                        if len(dst.shape) == 3:
                            src = src.rearrange("p (h c) -> p h c", h=dst.shape[1])
                        nc.scalar.activation(dst, src, func).then_inc(S["act_free"].sem, 1)

        @block.vector
        def _(dve):
            for p, (c, kh) in enumerate(pieces):
                cols = chunks[c][0].shape[2]
                dve.wait_ge(S["w_hi"].sem, S["w_hi"].at(p + 1))
                r = ring[p % R]
                nc.vector.tensor_tensor(r.lo[:, :, 0:cols], r.raw[:, :, 0:cols], r.hi_raw[:, :, 0:cols], ALU.subtract).then_inc(S["w_lo"].sem, 1)
                if beside is not None:
                    beside(dve)
    for s in range(R):
        ld[s].close(16 * len(range(s, len(pieces), R)))
    S["mm_done"].close(done[-1])
    S["act_free"].close(units[-1])
    S["w_hi"].close(len(pieces))
    S["w_lo"].close(len(pieces))


def phase_vo(core, xt, w):
    nc = core.nc
    v = core.view(V_KB, TT * 4 * VW).rearrange("p (t h c) -> p t h c", t=TT, h=4)
    og = core.view3(O_KB, TT, DH)
    wv = w.rearrange("a (k p) n -> p (a k) n", p=P)
    base = HY_COLS + 1024

    def ones(block):
        @block.gpsimd
        def _(pool):
            nc.gpsimd.memset(v[:, :, :, P:P + 1], 1.0)

    phase_rows_proj(core, [(wv[:, :, base:base + DH], xt, lambda t: v[:, t, :, 0:P], ACT.Copy),
                           (wv[:, :, base + DH:base + 2 * DH], xt, lambda t: og[:, t, :], ACT.Sigmoid)], (143, 159, 175), before=ones)


def phase_gate_scans(core):
    nc, S, ps = core.nc, core.sig, core.psum
    ig, fg = core.view(IG_KB, L, 64), core.view(FG_KB, L, 64)
    t1, cum = core.view(143, L, 64), core.view(147, L, 64)
    mx, m = core.view(MT_KB, L, 64), core.view(155, L, 64)
    acol, em = core.view3(ACOL_KB, TT, 64), core.view3(EM_KB, TT, 64)
    one = core.small[:, 5, 10:11]
    with nc.Block() as block:
        @block.scalar
        def _(act):
            chain = Chain(act, S["act_chain"])
            chain(nc.scalar.activation(t1, fg, ACT.Abs))
            chain(nc.scalar.activation(t1, t1, ACT.Exp, scale=-1.0))
            nc.scalar.activation(t1, t1, ACT.Ln, bias=one[0:64, :]).then_inc(S["act_done"].sem, 1)
            act.wait_ge(S["tr_done"].sem, S["tr_done"].at(1))
            nc.scalar.activation(em, ps[:, 1, :].rearrange("p (a b) -> p a b", a=TT), ACT.Exp, scale=-1.0)

        @block.vector
        def _(dve):
            chain = Chain(dve, S["dve_chain"])
            dve.wait_ge(S["act_done"].sem, S["act_done"].at(1))
            chain(nc.vector.scalar_tensor_tensor(out=fg, in0=fg, scalar=0.0, in1=t1, op0=ALU.min, op1=ALU.subtract))
            for way in range(2):
                rows = slice(32 * way, 32 * way + 32)
                step = slice(None, None, -1) if way else slice(None)
                ones = one[rows, :].to_broadcast([32, L])
                chain(nc.vector.tensor_tensor_scan(cum[rows, step], ones, fg[rows, step], 0.0, ALU.mult, ALU.add))
            chain(nc.vector.tensor_tensor(ig, ig, cum, ALU.subtract))
            for way in range(2):
                rows = slice(32 * way, 32 * way + 32)
                step = slice(None, None, -1) if way else slice(None)
                chain(nc.vector.tensor_tensor_scan(mx[rows, step], ig[rows, step], ig[rows, step], 0.0, ALU.max, ALU.max))
            nc.vector.tensor_tensor(m, cum, mx, ALU.add).then_inc(S["dve_done"].sem, 1)
            dve.wait_ge(S["tr_done"].sem, S["tr_done"].at(1))
            nc.vector.tensor_copy(acol, ps[:, 0, :].rearrange("p (a b) -> p a b", a=TT))

        @block.tensor
        def _(pe):
            pe.wait_ge(S["dve_done"].sem, S["dve_done"].at(1))
            for n, src in ((0, ig), (1, m)):
                for t in range(TT):
                    last = nc.tensor.transpose(ps[:, n, t * 64:(t + 1) * 64], src[:, t * P:(t + 1) * P], core.ident[0:64, 0:64])
            last.then_inc(S["tr_done"].sem, 1)
    S["act_chain"].close(2)
    S["act_done"].close(1)
    S["dve_chain"].close(6)
    S["dve_done"].close(1)
    S["tr_done"].close(1)


def phase_mlstm(core):
    nc, ap, S, ps = core.nc, core.ap, core.sig, core.psum
    qkt = core.view3(QKT_KB, 8, L)
    v = core.view(V_KB, TT * 4 * VW).rearrange("p (t h c) -> p t h c", t=TT, h=4)
    og = core.view3(O_KB, TT, DH)
    mx = core.view(MT_KB, L, 64)
    acol, em = core.view3(ACOL_KB, TT, 64), core.view3(EM_KB, TT, 64)
    pt = [[core.view3(42, 36, P), core.view3(143, 36, P)], [core.view3(6, 36, P), core.view3(24, 36, P)]]
    nmb = [core.view3(60, 2, L), core.view3(161, 2, L)]
    dg = core.view3(68, 4, P)
    sel = core.view3(173, 8, P, 64)
    hsum = core.view3(177, 2, P)
    r2 = core.tiny2[:, 128:144].rearrange("p (a b) -> p a b", b=2)
    first = [[sum(TT - i for i in range(j)) for j in range(TT)], [sum(i + 1 for i in range(j)) for j in range(TT)]]
    scale = float(P) ** -0.5
    NH = NH_ML
    with nc.Block() as block:
        @block.sync
        def _(sp):
            sp.dma_start(sel, ap["c_sel"]).then_inc(S["loaded"].sem, 16)

        @block.tensor
        def _(pe):
            pe.wait_ge(S["loaded"].sem, S["loaded"].at(16))

            def spread(h):
                for way in range(2):
                    if 2 * h + way >= 1:
                        pe.wait_ge(S["act_free"].sem, S["act_free"].at(2 * h + way))
                    for half in range(2):
                        last = nc.tensor.matmul(ps[:, half, :], sel[:, 4 * way + h, :], mx[:, half * BANK:(half + 1) * BANK], start=True, stop=True)
                    last.then_inc(S["aux_done"].sem, 1)

            def scores(h, j):
                n = TT * h + j
                if n >= 2:
                    pe.wait_ge(S["dve_done"].sem, S["dve_done"].at(n - 1))
                for half in range(2):
                    last = nc.tensor.matmul(ps[:, 2 + 2 * (n % 2) + half, :], qkt[:, 4 + h, j * P:(j + 1) * P], qkt[:, h, half * BANK:(half + 1) * BANK],
                                            start=True, stop=True)
                last.then_inc(S["mm_done"].sem, 1)

            def values(h, t):
                n = TT * h + t
                pe.wait_ge(S["dve_done"].sem, S["dve_done"].at(TT * (h + 1)))
                if n >= 2:
                    pe.wait_ge(S["dve_free"].sem, S["dve_free"].at(n - 1))
                for way in range(2):
                    js = range(t + 1) if way == 0 else range(t, TT)
                    for j in js:
                        at = first[way][j] + (t - j if way == 0 else t)
                        last = nc.tensor.matmul(ps[:, 6 + n % 2, way * VW:way * VW + P + 1], pt[h % 2][way][:, at, :], v[:, j, h, 0:P + 1],
                                                start=j == js[0], stop=j == js[-1])
                last.then_inc(S["aux2_done"].sem, 1)

            spread(0)
            for h in range(NH + 1):
                for j in range(TT):
                    if h < NH:
                        scores(h, j)
                    if h >= 1:
                        values(h - 1, j)
                if h + 1 < NH:
                    spread(h + 1)

        @block.scalar
        def _(act):
            for h in range(NH):
                for way in range(2):
                    act.wait_ge(S["aux_done"].sem, S["aux_done"].at(2 * h + way + 1))
                    nc.scalar.activation(nmb[h % 2][:, way, :], ps[:, 0:2, :].rearrange("p a b -> p (a b)"), ACT.Copy, scale=-1.0).then_inc(S["act_free"].sem, 1)
                if h >= 2:
                    act.wait_ge(S["aux2_done"].sem, S["aux2_done"].at(TT * (h - 1)))
                act.wait_ge(S["act_free"].sem, S["act_free"].at(2 * h + 2))
                for j in range(TT):
                    n = TT * h + j
                    for way in range(2):
                        a = acol[:, j, 32 * way + h:32 * way + h + 1]
                        p = pt[h % 2][way]
                        f = first[way][j]
                        off = (f + 1, f + TT - j, (j + 1) * P, L) if way == 0 else (f, f + j, 0, j * P)
                        if off[1] > off[0]:
                            nc.scalar.activation(p[:, off[0]:off[1], :].rearrange("p a b -> p (a b)"), nmb[h % 2][:, way, off[2]:off[3]], ACT.Exp, bias=a)
                    act.wait_ge(S["row_ready"].sem, S["row_ready"].at(n + 1))
                    for way in range(2):
                        at = first[way][j] + (0 if way == 0 else j)
                        last = nc.scalar.activation(pt[h % 2][way][:, at, :], dg[:, 2 * (n % 2) + way, :], ACT.Exp)
                    last.then_inc(S["act_done"].sem, 1)

        @block.vector
        def _(dve):
            chain = Chain(dve, S["dve_chain"])

            def diagonal(h, j):
                n = TT * h + j
                if n >= 2:
                    dve.wait_ge(S["act_done"].sem, S["act_done"].at(n - 1))
                dve.wait_ge(S["act_free"].sem, S["act_free"].at(2 * h + 2))
                for way in range(2):
                    last = nc.vector.scalar_tensor_tensor(out=dg[:, 2 * (n % 2) + way, :], in0=nmb[h % 2][:, way, j * P:(j + 1) * P],
                                                          scalar=acol[:, j, 32 * way + h:32 * way + h + 1], in1=core.small[:, 3 + way, :],
                                                          op0=ALU.add, op1=ALU.add)
                last.then_inc(S["row_ready"].sem, 1)

            def weigh(h, j):
                n = TT * h + j
                dve.wait_ge(S["act_done"].sem, S["act_done"].at(n + 1))
                dve.wait_ge(S["mm_done"].sem, S["mm_done"].at(n + 1))
                sc = ps[:, 2 + 2 * (n % 2):4 + 2 * (n % 2), :].rearrange("p a b -> p (a b)")
                for way in range(2):
                    f = first[way][j]
                    lo, hi, a, b = (f, f + TT - j, j * P, L) if way == 0 else (f, f + j + 1, 0, (j + 1) * P)
                    w = pt[h % 2][way][:, lo:hi, :].rearrange("p a b -> p (a b)")
                    last = nc.vector.scalar_tensor_tensor(out=w, in0=sc[:, a:b], scalar=scale, in1=w, op0=ALU.mult, op1=ALU.mult)
                last.then_inc(S["dve_done"].sem, 1)

            def finish(h, t):
                n = TT * h + t
                dve.wait_ge(S["aux2_done"].sem, S["aux2_done"].at(n + 1))
                out = ps[:, 6 + n % 2, 0:2 * VW].rearrange("p (a b) -> p a b", a=2)
                r = r2[:, n % 8, :]
                den = out[:, :, P]
                chain(nc.vector.scalar_tensor_tensor(out=r, in0=den, scalar=-1.0, in1=em[:, t, h:h + 33:32], op0=ALU.mult, op1=ALU.max))
                chain(nc.vector.tensor_tensor(r, den, r, ALU.max))
                chain(nc.vector.reciprocal(r, r))
                hs = hsum[:, n % 2, :]
                chain(nc.vector.tensor_scalar(hs, out[:, 0, 0:P], r[:, 0:1], None, ALU.mult))
                ins = nc.vector.scalar_tensor_tensor(out=hs, in0=out[:, 1, 0:P], scalar=r[:, 1:2], in1=hs, op0=ALU.mult, op1=ALU.add)
                ins.then_inc(S["dve_free"].sem, 1)
                dve.wait_ge(S["dve_free"].sem, S["dve_free"].at(n + 1))
                o = og[:, t, h * P:(h + 1) * P]
                nc.vector.tensor_tensor(o, hs, o, ALU.mult)

            diagonal(0, 0)
            for h in range(NH + 1):
                for j in range(TT):
                    if h < NH:
                        n = TT * h + j + 1
                        if n < TT * NH:
                            diagonal(n // TT, n % TT)
                        weigh(h, j)
                    if h >= 1:
                        finish(h - 1, j)
    S["loaded"].close(16)
    S["aux_done"].close(2 * NH)
    S["act_free"].close(2 * NH)
    for n in ("mm_done", "act_done", "row_ready", "dve_done", "dve_free", "aux2_done"):
        S[n].close(TT * NH)
    S["dve_chain"].close(4 * TT * NH)
H_KB, WROWS_KB = 70, 102


def phase_rows_gemm(core, lhs, w, h, gate=None, residual=None, ring_kb=(102, 118, 134), tmp_kb=None):
    nc, S, ps = core.nc, core.sig, core.psum
    KH = KT // 2
    ring = [Split(core, kb, KH, BANK) for kb in ring_kb]
    R = len(ring)
    wv = w.rearrange("a (k p) n -> p (a k) n", p=P)
    ld = [S["loaded%d" % s] for s in range(R)]
    with nc.Block() as block:
        @block.sync
        def _(sp):
            for p in range(4):
                c, kh = p // 2, p % 2
                if p >= R:
                    sp.wait_ge(S["mm_done"].sem, S["mm_done"].at(TT * (p - R + 1)))
                sp.dma_start(ring[p % R].raw, wv[:, kh * KH:(kh + 1) * KH, c * BANK:(c + 1) * BANK]).then_inc(ld[p % R].sem, 16)
                if p == R - 1 and residual is not None:
                    sp.dma_start(h, residual.rearrange("a (t p) d -> p (a t) d", p=P)).then_inc(S["x_ready"].sem, 16)

        @block.tensor
        def _(pe):
            for p in range(4):
                c, kh = p // 2, p % 2
                pe.wait_ge(S["w_lo"].sem, S["w_lo"].at(p + 1))
                for t in range(TT):
                    if c == 1 and kh == 0:
                        pe.wait_ge(S["dve_free"].sem, S["dve_free"].at(t + 1))
                    lt = slice(t * P, (t + 1) * P)
                    for k in range(KH):
                        kk = kh * KH + k
                        last = mm3(nc, ps[:, t, :], lhs.hi[:, kk, lt], lhs.lo[:, kk, lt], ring[p % R].hi[:, k, :], ring[p % R].lo[:, k, :], kk == 0, kk == KT - 1)
                    last.then_inc(S["mm_done"].sem, 1)

        @block.scalar
        def _(act):
            for p in range(4):
                act.wait_ge(ld[p % R].sem, ld[p % R].at(16 * (p // R + 1)))
                nc.scalar.activation(ring[p % R].hi, ring[p % R].raw, ACT.Copy).then_inc(S["w_hi"].sem, 1)

        @block.vector
        def _(dve):
            for p in range(4):
                dve.wait_ge(S["w_hi"].sem, S["w_hi"].at(p + 1))
                nc.vector.tensor_tensor(ring[p % R].lo, ring[p % R].raw, ring[p % R].hi_raw, ALU.subtract).then_inc(S["w_lo"].sem, 1)
            if residual is not None:
                dve.wait_ge(S["x_ready"].sem, S["x_ready"].at(16))
            for u in range(2 * TT):
                c, t = u // TT, u % TT
                dve.wait_ge(S["mm_done"].sem, S["mm_done"].at(TT * (2 * c + 1) + t + 1))
                hv = h[:, t, c * BANK:(c + 1) * BANK]
                if gate is None:
                    nc.vector.tensor_tensor(hv, ps[:, t, :], hv, ALU.add).then_inc(S["dve_free"].sem, 1)
                else:
                    tmp = core.view3(tmp_kb, 2, BANK)[:, u % 2, :]
                    if u >= 2:
                        dve.wait_ge(S["pool_done"].sem, S["pool_done"].at(u - 1))
                    nc.vector.tensor_tensor(tmp, ps[:, t, :], gate[:, c * BANK:(c + 1) * BANK], ALU.mult).then_inc(S["dve_free"].sem, 1)

        @block.gpsimd
        def _(pool):
            if gate is not None:
                if residual is not None:
                    pool.wait_ge(S["x_ready"].sem, S["x_ready"].at(16))
                for u in range(2 * TT):
                    c, t = u // TT, u % TT
                    pool.wait_ge(S["dve_free"].sem, S["dve_free"].at(u + 1))
                    hv = h[:, t, c * BANK:(c + 1) * BANK]
                    nc.gpsimd.tensor_tensor(hv, core.view3(tmp_kb, 2, BANK)[:, u % 2, :], hv, ALU.add).then_inc(S["pool_done"].sem, 1)
    for s in range(R):
        ld[s].close(16 * len(range(s, 4, R)))
    if residual is not None:
        S["x_ready"].close(16)
    S["w_hi"].close(4)
    S["w_lo"].close(4)
    S["mm_done"].close(4 * TT)
    S["dve_free"].close(2 * TT)
    if gate is not None:
        S["pool_done"].close(2 * TT)


def phase_cols_gemm(core, tiles, ring_kb, beside=None):
    nc, S, ps = core.nc, core.sig, core.psum
    ring = [Split(core, kb, KT, P) for kb in ring_kb] if isinstance(ring_kb, tuple) else weight_tiles(core, ring_kb)
    n_tiles = len(tiles)
    ld = [S["loaded%d" % s] for s in range(4)]
    arrived, count = [], [0] * 4
    for n, (parts, _, _) in enumerate(tiles):
        count[n % 4] += 16 * len(parts)
        arrived.append(count[n % 4])
    with nc.Block() as block:
        @block.sync
        def _(sp):
            for n, (parts, xt, out) in enumerate(tiles):
                if n >= 4:
                    sp.wait_ge(S["mm_done"].sem, S["mm_done"].at(n - 3))
                at = 0
                for w in parts:
                    sp.dma_start(ring[n % 4].raw[:, :, at:at + w.shape[2]], w).then_inc(ld[n % 4].sem, 16)
                    at += w.shape[2]

        @block.tensor
        def _(pe):
            for n, (parts, xt, out) in enumerate(tiles):
                pe.wait_ge(S["w_lo"].sem, S["w_lo"].at(n + 1))
                if n >= 4:
                    pe.wait_ge(S["act_free"].sem, S["act_free"].at(n - 3))
                width = xt.hi.shape[2]
                for a in range(0, width, BANK):
                    b = min(a + BANK, width)
                    last = mm3_cols(nc, ps[:, 2 * (n % 4) + a // BANK, 0:b - a], ring[n % 4], slice(0, P), xt, a, b)
                last.then_inc(S["mm_done"].sem, 1)

        @block.scalar
        def _(act):
            def weights(n):
                act.wait_ge(ld[n % 4].sem, ld[n % 4].at(arrived[n]))
                nc.scalar.activation(ring[n % 4].hi, ring[n % 4].raw, ACT.Copy).then_inc(S["w_hi"].sem, 1)

            weights(0)
            weights(1)
            for n, (parts, xt, out) in enumerate(tiles):
                if n + 2 < n_tiles:
                    weights(n + 2)
                act.wait_ge(S["mm_done"].sem, S["mm_done"].at(n + 1))
                src = ps[:, 2 * (n % 4):2 * (n % 4) + 2, :].rearrange("p a b -> p (a b)")[:, 0:out.shape[1]]
                nc.scalar.activation(out, src, ACT.Copy).then_inc(S["act_free"].sem, 1)

        @block.vector
        def _(dve):
            for n in range(n_tiles):
                dve.wait_ge(S["w_hi"].sem, S["w_hi"].at(n + 1))
                nc.vector.tensor_tensor(ring[n % 4].lo, ring[n % 4].raw, ring[n % 4].hi_raw, ALU.subtract).then_inc(S["w_lo"].sem, 1)
                if beside is not None:
                    beside(dve)
    for n in ("mm_done", "act_free", "w_hi", "w_lo"):
        S[n].close(n_tiles)
    for s in range(4):
        ld[s].close(count[s])


def phase_cross_attention(core, qt, kt, v, ot, scratch):
    nc, S, ps = core.nc, core.sig, core.psum
    scale = float(NMEM) ** -0.5
    prob = [core.view3(scratch + 4 * s, 4, NMEM) for s in range(2)]
    probt = [core.view3(scratch + 8 + 4 * s, 2, BANK) for s in range(2)]
    mx, rs = core.tiny2[:, 0:64].rearrange("p (a b) -> p a b", b=8), core.tiny2[:, 64:128].rearrange("p (a b) -> p a b", b=8)
    groups = [(h, half) for h in range(4) for half in range(2)]
    G = len(groups)
    sbank = lambda g: ps[:, 2 * (g % 2):2 * (g % 2) + 2, :].rearrange("p a (b c) -> p (a b) c", c=NMEM)
    with nc.Block() as block:
        @block.tensor
        def _(pe):
            def scores(g):
                h, half = groups[g]
                if g >= 2:
                    pe.wait_ge(S["act_done"].sem, S["act_done"].at(g - 1))
                for i in range(4):
                    t = 4 * half + i
                    for c in range(2):
                        last = nc.tensor.matmul(sbank(g)[:, i, :], qt[:, 2 * h + c, t * P:(t + 1) * P], kt[:, 2 * h + c, :], start=c == 0, stop=c == 1)
                last.then_inc(S["mm_done"].sem, 1)

            scores(0)
            for g, (h, half) in enumerate(groups):
                if g + 1 < G:
                    scores(g + 1)
                pe.wait_ge(S["dve_done"].sem, S["dve_done"].at(g + 1))
                if g >= 1:
                    pe.wait_ge(S["dve_free"].sem, S["dve_free"].at(g))
                for m in range(2):
                    for i in range(4):
                        last = nc.tensor.transpose(ps[:, 4 + m, i * P:(i + 1) * P], prob[g % 2][:, i, m * P:(m + 1) * P], core.ident)
                last.then_inc(S["tr_done"].sem, 1)
                pe.wait_ge(S["dve_free"].sem, S["dve_free"].at(g + 1))
                if g >= 1:
                    pe.wait_ge(S["act_free"].sem, S["act_free"].at(g))
                for e in range(2):
                    for m in range(2):
                        last = nc.tensor.matmul(ps[:, 6 + e, :], v[:, m, h * 256 + e * P:h * 256 + (e + 1) * P], probt[g % 2][:, m, :], start=m == 0, stop=m == 1)
                last.then_inc(S["aux_done"].sem, 1)

        @block.vector
        def _(dve):
            chain = Chain(dve, S["dve_chain"])

            def maxima(g):
                dve.wait_ge(S["mm_done"].sem, S["mm_done"].at(g + 1))
                chain(nc.vector.reduce_max(mx[:, g, 0:4], sbank(g), AX.X))
                nc.vector.tensor_scalar(mx[:, g, 4:8], mx[:, g, 0:4], -scale, None, ALU.mult).then_inc(S["stat_ready"].sem, 1)

            maxima(0)
            for g in range(G):
                if g + 1 < G:
                    maxima(g + 1)
                dve.wait_ge(S["act_done"].sem, S["act_done"].at(g + 1))
                chain(nc.vector.reciprocal(rs[:, g, 4:8], rs[:, g, 0:4]))
                nc.vector.tensor_tensor(prob[g % 2], prob[g % 2], rs[:, g, 4:8].unsqueeze(2).to_broadcast([P, 4, NMEM]), ALU.mult).then_inc(S["dve_done"].sem, 1)
                dve.wait_ge(S["tr_done"].sem, S["tr_done"].at(g + 1))
                if g >= 2:
                    dve.wait_ge(S["aux_done"].sem, S["aux_done"].at(g - 1))
                nc.vector.tensor_copy(probt[g % 2], ps[:, 4:6, :]).then_inc(S["dve_free"].sem, 1)

        @block.scalar
        def _(act):
            def outputs(g):
                h, half = groups[g]
                act.wait_ge(S["aux_done"].sem, S["aux_done"].at(g + 1))
                nc.scalar.activation(ot[:, 2 * h:2 * h + 2, half * BANK:(half + 1) * BANK], ps[:, 6:8, :], ACT.Copy).then_inc(S["act_free"].sem, 1)

            for g, (h, half) in enumerate(groups):
                act.wait_ge(S["stat_ready"].sem, S["stat_ready"].at(g + 1))
                if g >= 2:
                    act.wait_ge(S["tr_done"].sem, S["tr_done"].at(g - 1))
                for i in range(4):
                    last = nc.scalar.activation(prob[g % 2][:, i, :], sbank(g)[:, i, :], ACT.Exp, scale=scale, bias=mx[:, g, 4 + i:5 + i], accum_out=rs[:, g, i:i + 1])
                last.then_inc(S["act_done"].sem, 1)
                if g >= 1:
                    outputs(g - 1)
            outputs(G - 1)

    for n in ("mm_done", "tr_done", "aux_done", "stat_ready", "act_done", "act_free", "dve_done", "dve_free", "dve_chain"):
        S[n].close(G * (2 if n == "dve_chain" else 1))


def phase_ffn(core, xt, h, gated, places):
    nc, ap, S, ps = core.nc, core.ap, core.sig, core.psum
    ft = [Split(core, places["ft"] + 16 * s, 2, L) for s in range(2)]
    ring = weight_tiles(core, places["ring"])
    w2s = [Split(core, places["w2"] + 8 * s, 2, BANK) for s in range(2)]
    first = [core.view(places["act"] + 2 * s, BANK) for s in range(2)]
    full = [core.view(places["full"] + 2 * s, BANK) for s in range(2)]
    tmp = [core.view(places["tmp"] + 2 * s, BANK) for s in range(2)]
    G = (FF2 if gated is not None else FF) // (2 * P)
    per = 4 if gated is not None else 2
    w1 = ap["w_gu_2" if gated is not None else "ff_w1"].rearrange("a (k p) n -> p (a k) n", p=P)
    w2 = ap["w_down_2" if gated is not None else "ff_w2"].rearrange("a (k p) n -> p (a k) n", p=P)
    ld = [S["loaded%d" % s] for s in range(4)]
    ld2 = [S["loaded"], S["stored"]]
    unit = lambda g, f, half: 4 * g + 2 * f + half

    def slots(b, f):
        return (2 * f, 2 * f + 1) if gated is not None else (2 * b + f,)

    def over_groups(eng, body):
        body(0, 0, 0)
        body(1, 1, 0)
        with eng.Fori(1, (G - 1) // 2) as i:
            body(2 * i, 0, i)
            body(2 * i + 1, 1, i)
        for g in range((G - 1) // 2 * 2, G):
            body(g, g % 2, g // 2)

    known = lambda v: isinstance(v, int)
    last_group = lambda g: known(g) and g == G - 1

    with nc.Block() as block:
        @block.sync
        def _(sp):
            def up_weights(g, b):
                back = 1 if gated is not None else 2
                for f in range(2):
                    for part, slot in enumerate(slots(b, f)):
                        if not (known(g) and g < back):
                            sp.wait_ge(S["mm_done"].sem, S["mm_done"].at(unit(g - back, f, 1) + 1))
                        sp.dma_start(ring[slot].raw, w1[:, :, bass.ds(part * FF2 + (2 * g + f) * P, P)]).then_inc(ld[slot].sem, 16)

            def group(g, b, n):
                if not last_group(g):
                    up_weights(g + 1, 1 - b)
                for c in range(2):
                    if not (known(g) and g < 1):
                        sp.wait_ge(S["aux_done"].sem, S["aux_done"].at(2 * TT * (g - 1) + TT * (c + 1)))
                    sp.dma_start(w2s[c].raw, w2[:, bass.ds(2 * g, 2), c * BANK:(c + 1) * BANK]).then_inc(ld2[c].sem, 16)

            up_weights(0, 0)
            over_groups(sp, group)

        @block.tensor
        def _(pe):
            def up(g, b):
                for f in range(2):
                    pe.wait_ge(S["w_lo"].sem, S["w_lo"].at(per * g + per // 2 * (f + 1)))
                    for half in range(2):
                        banks = (2 * half, 2 * half + 1) if gated is not None else (2 * f + half,)
                        u = unit(g, f, half)
                        if gated is not None and not (known(u) and u < 2):
                            pe.wait_ge(S["square_done"].sem, S["square_done"].at(u - 1))
                        if gated is None and not (known(u) and u < 4):
                            pe.wait_ge(S["bank_free"].sem, S["bank_free"].at(u - 3))
                        for bank, slot in zip(banks, slots(b, f)):
                            last = mm3_cols(nc, ps[:, bank, :], ring[slot], slice(0, P), xt, half * BANK, (half + 1) * BANK)
                        last.then_inc(S["mm_done"].sem, 1)

            def down(g, b):
                pe.wait_ge(S["ft_lo"].sem, S["ft_lo"].at(4 * g + 4))
                for c in range(2):
                    pe.wait_ge(S["v_lo"].sem, S["v_lo"].at(2 * g + c + 1))
                    for t in range(TT):
                        u = 2 * TT * g + TT * c + t
                        if not (known(u) and u < 4):
                            pe.wait_ge(S["dve_free"].sem, S["dve_free"].at(u - 3))
                        lt = slice(t * P, (t + 1) * P)
                        for k in range(2):
                            last = mm3(nc, ps[:, 4 + t % 4, :], ft[b].hi[:, k, lt], ft[b].lo[:, k, lt], w2s[c].hi[:, k, :], w2s[c].lo[:, k, :], k == 0, k == 1)
                        last.then_inc(S["aux_done"].sem, 1)

            def group(g, b, n):
                up(g, b)
                if not (known(g) and g == 0):
                    down(g - 1, 1 - b)
            over_groups(pe, group)
            down(G - 1, (G - 1) % 2)

        @block.scalar
        def _(act):
            def weights(g, b, f, n):
                for part, slot in enumerate(slots(b, f)):
                    act.wait_ge(ld[slot].sem, ld[slot].at(16 * (g + 1 if gated is not None else n + 1)))
                    nc.scalar.activation(ring[slot].hi, ring[slot].raw, ACT.Copy).then_inc(S["w_hi"].sem, 1)

            def split(g, b, f, half):
                u = unit(g, f, half)
                act.wait_ge(S["square_done"].sem, S["square_done"].at(u + 1))
                nc.scalar.activation(ft[b].hi[:, f, half * BANK:(half + 1) * BANK], full[half], ACT.Copy).then_inc(S["ft_hi"].sem, 1)

            def group(g, b, n):
                for f in range(2):
                    for half in range(2):
                        u = unit(g, f, half)
                        act.wait_ge(S["mm_done"].sem, S["mm_done"].at(u + 1))
                        if not (known(u) and u < 2):
                            act.wait_ge(S["square_done"].sem, S["square_done"].at(u - 1))
                        if gated is not None:
                            nc.scalar.activation(first[half], ps[:, 2 * half, :], ACT.Silu).then_inc(S["act_done"].sem, 1)
                        else:
                            nc.scalar.activation(first[half], ps[:, 2 * f + half, :], ACT.Relu).then_inc(S["bank_free"].sem, 1)
                        if (f, half) != (0, 0):
                            if (f, half) == (0, 1) and not (known(g) and g < 2):
                                act.wait_ge(S["aux_done"].sem, S["aux_done"].at(2 * TT * (g - 1)))
                            split(g, b, *((0, 0) if (f, half) == (0, 1) else (0, 1) if (f, half) == (1, 0) else (1, 0)))
                split(g, b, 1, 1)
                if not last_group(g):
                    for f in range(2):
                        weights(g + 1, 1 - b, f, n + b)
                for c in range(2):
                    act.wait_ge(ld2[c].sem, ld2[c].at(16 * (g + 1)))
                    nc.scalar.activation(w2s[c].hi, w2s[c].raw, ACT.Copy).then_inc(S["v_hi"].sem, 1)

            for f in range(2):
                weights(0, 0, f, 0)
            over_groups(act, group)

        if gated is None:
            @block.gpsimd
            def _(pool):
                def squares(g, b, n):
                    for f in range(2):
                        for half in range(2):
                            u = unit(g, f, half)
                            pool.wait_ge(S["bank_free"].sem, S["bank_free"].at(u + 1))
                            if not (known(u) and u < 2):
                                pool.wait_ge(S["ft_lo"].sem, S["ft_lo"].at(u - 1))
                            nc.gpsimd.tensor_tensor(full[half], first[half], first[half], ALU.mult).then_inc(S["square_done"].sem, 1)
                over_groups(pool, squares)
        else:
            @block.gpsimd
            def _(pool):
                def sums(g):
                    for c in range(2):
                        for t in range(TT):
                            u = 2 * TT * g + TT * c + t
                            pool.wait_ge(S["dve_free"].sem, S["dve_free"].at(u + 1))
                            hv = h[:, t, c * BANK:(c + 1) * BANK]
                            nc.gpsimd.tensor_tensor(hv, tmp[t % 2], hv, ALU.add).then_inc(S["pool_done"].sem, 1)

                def group(g, b, n):
                    if not (known(g) and g == 0):
                        sums(g - 1)
                over_groups(pool, group)
                sums(G - 1)

        @block.vector
        def _(dve):
            def weights(g, b, f):
                for part, slot in enumerate(slots(b, f)):
                    dve.wait_ge(S["w_hi"].sem, S["w_hi"].at(per * g + per // 2 * f + part + 1))
                    nc.vector.tensor_tensor(ring[slot].lo, ring[slot].raw, ring[slot].hi_raw, ALU.subtract).then_inc(S["w_lo"].sem, 1)

            def split(g, b, f, half):
                dve.wait_ge(S["ft_hi"].sem, S["ft_hi"].at(unit(g, f, half) + 1))
                cols = slice(half * BANK, (half + 1) * BANK)
                nc.vector.tensor_tensor(ft[b].lo[:, f, cols], full[half], ft[b].hi_raw[:, f, cols], ALU.subtract).then_inc(S["ft_lo"].sem, 1)

            def sums(g, which):
                for v in which:
                    c, t = v // TT, v % TT
                    u = 2 * TT * g + v
                    dve.wait_ge(S["aux_done"].sem, S["aux_done"].at(u + 1))
                    hv = h[:, t, c * BANK:(c + 1) * BANK]
                    if gated is None:
                        nc.vector.tensor_tensor(hv, ps[:, 4 + t % 4, :], hv, ALU.add).then_inc(S["dve_free"].sem, 1)
                    else:
                        if not (known(u) and u < 2):
                            dve.wait_ge(S["pool_done"].sem, S["pool_done"].at(u - 1))
                        nc.vector.tensor_tensor(tmp[t % 2], ps[:, 4 + t % 4, :], gated[:, c * BANK:(c + 1) * BANK], ALU.mult).then_inc(S["dve_free"].sem, 1)

            def group(g, b, n):
                order = [(0, 0), (0, 1), (1, 0), (1, 1)]
                for m, (f, half) in enumerate(order):
                    u = unit(g, f, half)
                    if gated is not None:
                        dve.wait_ge(S["act_done"].sem, S["act_done"].at(u + 1))
                        if not (known(u) and u < 2):
                            dve.wait_ge(S["ft_lo"].sem, S["ft_lo"].at(u - 1))
                        nc.vector.tensor_tensor(full[half], ps[:, 2 * half + 1, :], first[half], ALU.mult).then_inc(S["square_done"].sem, 1)
                    if m:
                        split(g, b, *order[m - 1])
                split(g, b, 1, 1)
                if not last_group(g):
                    for f in range(2):
                        weights(g + 1, 1 - b, f)
                for c in range(2):
                    if not (known(g) and g == 0):
                        sums(g - 1, range(TT * c, TT * (c + 1)))
                    dve.wait_ge(S["v_hi"].sem, S["v_hi"].at(2 * g + c + 1))
                    nc.vector.tensor_tensor(w2s[c].lo, w2s[c].raw, w2s[c].hi_raw, ALU.subtract).then_inc(S["v_lo"].sem, 1)

            for f in range(2):
                weights(0, 0, f)
            over_groups(dve, group)
            sums(G - 1, range(2 * TT))
    for s in range(4):
        ld[s].close(16 * (G if gated is not None else G // 2))
    for s in ld2:
        s.close(16 * G)
    for n, k in (("mm_done", 4), ("ft_hi", 4), ("ft_lo", 4), ("square_done", 4), ("aux_done", 2 * TT), ("dve_free", 2 * TT),
                 ("w_hi", per), ("w_lo", per), ("v_hi", 2), ("v_lo", 2)):
        S[n].close(k * G)
    if gated is None:
        S["bank_free"].close(4 * G)
    else:
        S["act_done"].close(4 * G)
        S["pool_done"].close(2 * TT * G)


def phase_final_norm(core, h, gain, gain_kb, out_dram=None):
    nc, S = core.nc, core.sig
    g = core.view(gain_kb, D)
    junk = core.view3(gain_kb + 4, 2, D)
    ss, rstd = core.tiny[:, 0:TT], core.tiny[:, 8:8 + TT]
    with nc.Block() as block:
        @block.sync
        def _(sp):
            sp.dma_start(g, gain.partition_broadcast(P)).then_inc(S["loaded"].sem, 16)
            if out_dram is not None:
                rows = out_dram.rearrange("a (t p) d -> p (a t) d", p=P)
                for t in range(TT):
                    sp.wait_ge(S["dve_done"].sem, S["dve_done"].at(t + 1))
                    sp.dma_start(rows[:, t, :], h[:, t, :]).then_inc(S["stored"].sem, 16)
                sp.wait_ge(S["stored"].sem, S["stored"].at(16 * TT))

        @block.scalar
        def _(act):
            chain = Chain(act, S["act_chain"])
            for i in range(TT):
                chain(nc.scalar.activation(junk[:, i % 2, :], h[:, i, :], ACT.Square, accum_out=ss[:, i:i + 1]))
            nc.scalar.activation(rstd, ss, ACT.Sqrt, scale=1.0 / D, bias=core.eps).then_inc(S["stat_ready"].sem, 1)

        @block.vector
        def _(dve):
            dve.wait_ge(S["loaded"].sem, S["loaded"].at(16))
            dve.wait_ge(S["stat_ready"].sem, S["stat_ready"].at(1))
            nc.vector.reciprocal(rstd, rstd).then_inc(S["dve_chain"].sem, 1)
            dve.wait_ge(S["dve_chain"].sem, S["dve_chain"].at(1))
            for t in range(TT):
                nc.vector.scalar_tensor_tensor(out=h[:, t, :], in0=h[:, t, :], scalar=rstd[:, t:t + 1], in1=g, op0=ALU.mult, op1=ALU.mult).then_inc(S["dve_done"].sem, 1)
    S["loaded"].close(16)
    S["act_chain"].close(TT)
    S["stat_ready"].close(1)
    S["dve_chain"].close(1)
    S["dve_done"].close(TT)
    if out_dram is not None:
        S["stored"].close(16 * TT)


def phase_reload(core, dst, src):
    nc, S = core.nc, core.sig
    with nc.Block() as block:
        @block.sync
        def _(sp):
            sp.dma_start(dst, src.rearrange("a (t p) d -> p (a t) d", p=P)).then_inc(S["loaded"].sem, 16)
            sp.wait_ge(S["loaded"].sem, S["loaded"].at(16))
    S["loaded"].close(16)


def first_block(core):
    ap = core.ap
    x, xt = core.view3(118, TT, D), Split(core, 6, KT, L)
    w_in = ap["w_in"]
    phase_load(core)
    phase_norm(core, x, xt, core.colsA[:, G_MIX:G_MIX + 8])
    hy = core.view3(HY_KB, TT, HY_COLS)
    phase_conv_proj(core, xt, w_in, hy)
    phase_filter_hidden(core, hy)
    tables = Tables(core)
    for o in range(2):
        phase_filter_time(core, o)
        phase_filter_spectrum(core, tables, hy)
        phase_signal_spectrum(core, tables)
        phase_inverse_gate(core, tables, hy, o)
    yht, ymt = core.view3(191.5, 4, L), core.view3(70, 4, L)
    phase_group_norm(core, hy[:, :, 0:DH], 8, yht, core.colsB[:, G_HY:G_HY + 4], 182, mirrored=True)
    phase_reload(core, x, ap["x"])
    phase_norm(core, x, xt, core.colsA[:, G_MIX:G_MIX + 8])
    phase_qk_proj(core, xt, w_in)
    phase_vo(core, xt, w_in)
    phase_gates(core, xt, w_in)
    phase_gate_scans(core)
    phase_mlstm(core)
    phase_group_norm(core, core.view3(O_KB, TT, DH), 4, ymt, core.colsB[:, G_ML:G_ML + 4], 182)
    mixed = Split(core, 6, 8, L)
    phase_split(core, split_pairs(yht, mixed) + split_pairs(ymt, mixed, at=4))
    second_half(core, mixed)


def second_half(core, mixed):
    ap = core.ap
    h = core.view3(H_KB, TT, D)
    phase_rows_gemm(core, mixed, ap["w_out"], h, residual=ap["x"])
    xt = Split(core, 6, KT, L)
    phase_norm(core, h, xt, core.colsA[:, G_X:G_X + 8])
    mem, memt = core.view3(134, 2, D), Split(core, 142, KT, NMEM)
    phase_reload(core, mem, ap["mem"])
    phase_norm(core, mem, memt, core.colsA[:, G_MEM:G_MEM + 8], scratch=162)
    qt, kt, v = core.view3(102, 8, L), core.view3(158, 8, NMEM), core.view3(166, 2, D)
    wt = {n: ap[n].rearrange("a (k p) n -> p (a k) n", p=P) for n in ("xa_wq", "xa_wk", "xa_wv")}
    phase_cols_gemm(core, [([wt["xa_wk"][:, :, n * P:(n + 1) * P]], memt, kt[:, n, :]) for n in range(8)]
                    + [([wt["xa_wq"][:, :, n * P:(n + 1) * P]], xt, qt[:, n, :]) for n in range(8)], 174)
    phase_rows_proj(core, [(wt["xa_wv"][:, :, c * BANK:(c + 1) * BANK], memt, lambda t, c=c: v[:, t, c * BANK:(c + 1) * BANK], ACT.Copy) for c in range(2)], (6, 22, 38))
    ot = core.view3(6, 8, L)
    phase_cross_attention(core, qt, kt, v, ot, 182)
    attended = Split(core, 102, 8, L)
    phase_split(core, split_pairs(ot, attended))
    phase_rows_gemm(core, attended, ap["xa_wo"], h, ring_kb=(6, 22, 38))
    phase_norm(core, h, xt, core.colsA[:, G_FF:G_FF + 8], scratch=182)
    phase_ffn(core, xt, h, None, {"ft": 102, "ring": 134, "w2": 166, "act": 182, "full": 186, "tmp": 190})
    phase_final_norm(core, h, ap["final_norm_g"], 182)
QAT_KB, KAT_KB, QBT_KB, QIT_KB, KIT_KB, VA_KB, CKV_KB, RING2_KB, CKVT_KB = 70, 86, 102, 118, 134, 138, 154, 160, 192
GA1_KB, GA2_KB, QLT_KB, SEL_KB, MIX_KB, H2_KB = 199.75, 203.75, 6, 160, 38, 38
IDX_SCALE = (8 * 64) ** -0.5
TAKEN = -3.0e38
FIRST_SEL = TOPK // P
SCALE = HD ** -0.5


def phase_ada(core, h, saved):
    nc, ap, S, ps = core.nc, core.ap, core.sig, core.psum
    ring = [core.view3(102 + 16 * s, KT, BANK) for s in range(2)]
    brow = [core.view(134 + 2 * s, BANK) for s in range(2)]
    crep = core.view3(138, KT, P)
    rows = [core.view(142 + 2 * s, BANK) for s in range(2)]
    ga1, ga2 = core.view3(GA1_KB, 2, BANK), core.view3(GA2_KB, 2, BANK)
    ga = {4: ga1[:, 0, :], 5: ga1[:, 1, :], 10: ga2[:, 0, :], 11: ga2[:, 1, :]}
    cact = core.tiny[:, 24:32]
    cols = core.tiny2[:, 200:248]
    core.mod_scale = [core.tiny2[:, 256:264], core.tiny2[:, 264:272]]
    core.mod_shift = [cols[:, 0:8], cols[:, 24:32]]
    w = ap["w_ada_2"].rearrange("a (k p) n -> p (a k) n", p=P)
    N = 12
    with nc.Block() as block:
        @block.sync
        def _(sp):
            sp.dma_start(saved.rearrange("a (t p) d -> p (a t) d", p=P), h).then_inc(S["stored"].sem, 16)
            for n in range(N):
                if n >= 2:
                    sp.wait_ge(S["mm_done"].sem, S["mm_done"].at(n - 1))
                sp.dma_start(ring[n % 2], w[:, :, n * BANK:(n + 1) * BANK]).then_inc(S["loaded%d" % (n % 2)].sem, 16)
                if n >= 2:
                    sp.wait_ge(S["dve_free"].sem, S["dve_free"].at(n - 1))
                sp.dma_start(brow[n % 2], ap["b_ada_2"][0, n * BANK:(n + 1) * BANK].partition_broadcast(P)).then_inc(S["loaded%d" % (2 + n % 2)].sem, 16)
            sp.wait_ge(S["stored"].sem, S["stored"].at(16))

        @block.scalar
        def _(act):
            nc.scalar.activation(cact, core.colsB[:, C_ACT:C_ACT + 8], ACT.Silu).then_inc(S["act_done"].sem, 1)

        @block.tensor
        def _(pe):
            def columns(n):
                pe.wait_ge(S["dve_free"].sem, S["dve_free"].at(n + 1))
                for j in range(4):
                    last = nc.tensor.matmul(ps[:, 7, 4 * n + j:4 * n + j + 1], rows[n % 2][0:1, j * P:(j + 1) * P], core.small[0:1, 5, 10:11], start=True, stop=True)
                last.then_inc(S["tr_done"].sem, 1)
            pe.wait_ge(S["dve_done"].sem, S["dve_done"].at(1))
            for n in range(N):
                pe.wait_ge(S["loaded%d" % (n % 2)].sem, S["loaded%d" % (n % 2)].at(16 * (n // 2 + 1)))
                if n >= 4:
                    pe.wait_ge(S["dve_free"].sem, S["dve_free"].at(n - 3))
                for k in range(KT):
                    last = nc.tensor.matmul(ps[:, n % 4, :], crep[:, k, :], ring[n % 2][:, k, :], start=k == 0, stop=k == KT - 1)
                last.then_inc(S["mm_done"].sem, 1)
                if n >= 1 and n - 1 not in ga:
                    columns(n - 1)

        @block.vector
        def _(dve):
            dve.wait_ge(S["act_done"].sem, S["act_done"].at(1))
            nc.vector.tensor_copy(crep, cact.unsqueeze(2).to_broadcast([P, KT, P])).then_inc(S["dve_done"].sem, 1)
            made = 0
            for n in range(N):
                dve.wait_ge(S["mm_done"].sem, S["mm_done"].at(n + 1))
                dve.wait_ge(S["loaded%d" % (2 + n % 2)].sem, S["loaded%d" % (2 + n % 2)].at(16 * (n // 2 + 1)))
                if n >= 2 and n - 2 not in ga:
                    made += 1
                    dve.wait_ge(S["tr_done"].sem, S["tr_done"].at(made))
                nc.vector.tensor_tensor(ga[n] if n in ga else rows[n % 2], ps[:, n % 4, :], brow[n % 2], ALU.add).then_inc(S["dve_free"].sem, 1)
            dve.wait_ge(S["tr_done"].sem, S["tr_done"].at(8))
            chain = Chain(dve, S["dve_chain"])
            chain(nc.vector.tensor_copy(cols[:, 0:16], ps[:, 7, 0:16]))
            chain(nc.vector.tensor_copy(cols[:, 24:40], ps[:, 7, 24:40]))
            for n, (scale, gain) in enumerate(((cols[:, 8:16], G_ATT2), (cols[:, 32:40], G_FFN2))):
                nc.vector.scalar_tensor_tensor(out=core.mod_scale[n], in0=scale, scalar=1.0, in1=core.colsA[:, gain:gain + 8], op0=ALU.add, op1=ALU.mult)
    S["stored"].close(16)
    for s in range(4):
        S["loaded%d" % s].close(16 * N // 2)
    S["mm_done"].close(N)
    S["dve_free"].close(N)
    S["act_done"].close(1)
    S["dve_done"].close(1)
    S["tr_done"].close(8)
    S["dve_chain"].close(2)


def phase_latent(core):
    nc, ap, S, ps = core.nc, core.ap, core.sig, core.psum
    ckv, ckvt = core.view3(CKV_KB, TT, RANK), core.view(CKVT_KB, L)
    qbt = core.view3(QBT_KB, 4, L)
    qlt = core.view3(QLT_KB, 8, L)
    wuk, grow, junk = core.view3(118, 4, RANK), core.view(120, RANK), core.view3(122, TT, RANK)
    ss, rstd = core.tiny[:, 0:TT], core.tiny[:, 8:8 + TT]
    with nc.Block() as block:
        @block.sync
        def _(sp):
            sp.dma_start(wuk, ap["w_uk_2"][0].rearrange("(a b) d r -> (b d) a r", b=2)).then_inc(S["loaded0"].sem, 16)
            sp.dma_start(grow, ap["kv_norm_g_2"][0].partition_broadcast(P)).then_inc(S["loaded1"].sem, 16)

        @block.scalar
        def _(act):
            for t in range(TT):
                last = nc.scalar.activation(junk[:, t, :], ckv[:, t, :], ACT.Square, accum_out=ss[:, t:t + 1])
            last.then_inc(S["act_chain"].sem, 1)
            act.wait_ge(S["act_chain"].sem, S["act_chain"].at(1))
            nc.scalar.activation(rstd, ss, ACT.Sqrt, scale=1.0 / RANK, bias=core.eps).then_inc(S["stat_ready"].sem, 1)
            for n in range(16):
                act.wait_ge(S["mm_done"].sem, S["mm_done"].at(n + 1))
                nc.scalar.activation(qlt[:, n // 2, (n % 2) * BANK:(n % 2 + 1) * BANK], ps[:, n % 4, :], ACT.Copy).then_inc(S["act_free"].sem, 1)

        @block.vector
        def _(dve):
            dve.wait_ge(S["stat_ready"].sem, S["stat_ready"].at(1))
            nc.vector.reciprocal(rstd, rstd).then_inc(S["dve_chain"].sem, 1)
            dve.wait_ge(S["dve_chain"].sem, S["dve_chain"].at(1))
            dve.wait_ge(S["loaded1"].sem, S["loaded1"].at(16))
            for t in range(TT):
                last = nc.vector.scalar_tensor_tensor(out=ckv[:, t, :], in0=ckv[:, t, :], scalar=rstd[:, t:t + 1], in1=grow, op0=ALU.mult, op1=ALU.mult)
            last.then_inc(S["dve_done"].sem, 1)
            dve.wait_ge(S["tr_done"].sem, S["tr_done"].at(1))
            nc.vector.tensor_copy(ckvt, ps[:, 4:6, :].rearrange("p a b -> p (a b)"))

        @block.tensor
        def _(pe):
            pe.wait_ge(S["loaded0"].sem, S["loaded0"].at(16))
            for n in range(16):
                h, half = n // 2, n % 2
                if n >= 4:
                    pe.wait_ge(S["act_free"].sem, S["act_free"].at(n - 3))
                rows = slice(64 * (h % 2), 64 * (h % 2) + 64)
                nc.tensor.matmul(ps[:, n % 4, :], wuk[rows, h // 2, :], qbt[rows, h // 2, half * BANK:(half + 1) * BANK], start=True, stop=True).then_inc(S["mm_done"].sem, 1)
            pe.wait_ge(S["dve_done"].sem, S["dve_done"].at(1))
            for t in range(TT):
                last = nc.tensor.transpose(ps[:, 4 + t // 4, (t % 4) * P:(t % 4 + 1) * P], ckv[:, t, :], core.ident)
            last.then_inc(S["tr_done"].sem, 1)
    S["loaded0"].close(16)
    S["loaded1"].close(16)
    for n in ("act_chain", "stat_ready", "dve_chain", "dve_done", "tr_done"):
        S[n].close(1)
    S["mm_done"].close(16)
    S["act_free"].close(16)


def sel_tile(core, i):
    start = i * (i + 1) // 2 * P
    return core.view(SEL_KB, 36 * P)[:, start:start + (i + 1) * P]


def phase_index_scores(core):
    nc, ap, S, ps = core.nc, core.ap, core.sig, core.psum
    qit, kit = core.view3(QIT_KB, 4, L), core.view(KIT_KB, L)
    rel = [core.view(178 + 4 * s, L) for s in range(3)]
    steps = [(i, h) for i in range(FIRST_SEL, TT) for h in range(8)]
    pair = lambda n, w: ps[:, 2 * (n % 4):2 * (n % 4) + 2, :].rearrange("p a b -> p (a b)")[:, 0:w]
    with nc.Block() as block:
        @block.tensor
        def _(pe):
            for n, (i, h) in enumerate(steps):
                if n >= 4:
                    pe.wait_ge(S["act_done"].sem, S["act_done"].at(n - 3))
                rows = slice(64 * (h % 2), 64 * (h % 2) + 64)
                w = (i + 1) * P
                for a in range(0, w, BANK):
                    b = min(a + BANK, w)
                    last = nc.tensor.matmul(ps[:, 2 * (n % 4) + a // BANK, 0:b - a], qit[rows, h // 2, i * P:(i + 1) * P], kit[rows, a:b], start=True, stop=True)
                last.then_inc(S["mm_done"].sem, 1)

        @block.scalar
        def _(act):
            for n, (i, h) in enumerate(steps):
                act.wait_ge(S["mm_done"].sem, S["mm_done"].at(n + 1))
                if n >= 3:
                    act.wait_ge(S["dve_done"].sem, S["dve_done"].at(n - 2))
                w = (i + 1) * P
                nc.scalar.activation(rel[n % 3][:, 0:w], pair(n, w), ACT.Relu).then_inc(S["act_done"].sem, 1)

        @block.vector
        def _(dve):
            Chain(dve, S["dve_chain"])(nc.vector.tensor_scalar(core.wi, core.wi, IDX_SCALE, None, ALU.mult))
            for n, (i, h) in enumerate(steps):
                dve.wait_ge(S["act_done"].sem, S["act_done"].at(n + 1))
                w = (i + 1) * P
                sc, wc = sel_tile(core, i), core.wi[:, i, h:h + 1]
                if h == 0:
                    ins = nc.vector.tensor_scalar(sc, rel[n % 3][:, 0:w], wc, None, ALU.mult)
                else:
                    dve.wait_ge(S["dve_done"].sem, S["dve_done"].at(n))
                    ins = nc.vector.scalar_tensor_tensor(out=sc, in0=rel[n % 3][:, 0:w], scalar=wc, in1=sc, op0=ALU.mult, op1=ALU.add)
                ins.then_inc(S["dve_done"].sem, 1)
            dve.wait_ge(S["dve_done"].sem, S["dve_done"].at(len(steps)))
            for i in range(TT):
                sc = sel_tile(core, i)
                if i < FIRST_SEL:
                    if i:
                        nc.vector.memset(sc[:, 0:i * P], 0.0)
                    nc.vector.tensor_copy(sc[:, i * P:], core.small[:, 4, :])
                else:
                    nc.vector.tensor_tensor(sc[:, i * P:], sc[:, i * P:], core.small[:, 4, :], ALU.add)
    for n in ("mm_done", "act_done", "dve_done"):
        S[n].close(len(steps))
    S["dve_chain"].close(1)


class Selection:

    def __init__(self, core):
        self.core, self.tile, self.round, self.steps = core, FIRST_SEL, 0, 0
        self.done = core.sig["selected"].sem
        self.top = core.tiny[:, 32:48].rearrange("p (a b) -> p a b", a=2)

    def rounds(self, dve, us=None):
        nc = self.core.nc
        while self.tile < TT and (us is None or us > 0):
            sc, best = sel_tile(self.core, self.tile), self.top[:, self.round % 2, :]
            if self.steps:
                dve.wait_ge(self.done, self.steps)
            nc.vector.max(best, sc).then_inc(self.done, 1)
            dve.wait_ge(self.done, self.steps + 1)
            nc.vector.match_replace(out=sc, in_to_replace=best, in_values=sc, imm_value=TAKEN).then_inc(self.done, 1)
            self.steps += 2
            self.round += 1
            if us is not None:
                us -= 2 * (0.06 + (self.tile + 1) * P / 960)
            if self.round == TOPK // 8:
                dve.wait_ge(self.done, self.steps)
                nc.vector.tensor_scalar(sc, sc, TAKEN, NEG, ALU.not_equal, ALU.mult)
                self.tile, self.round = self.tile + 1, 0


def phase_attention(core, sparse, selection=None):
    nc, ap, S, ps = core.nc, core.ap, core.sig, core.psum
    qat, kat = core.view3(QAT_KB, 4, L), core.view3(KAT_KB, 4, L)
    qlt, ckvt = core.view3(QLT_KB, 8, L), core.view(CKVT_KB, L)
    va, ckv = core.view3(VA_KB, TT, 512), core.view3(CKV_KB, TT, RANK)
    mix = core.view3(MIX_KB, TT, D)
    sc = [core.view(102 + 4 * s, L) for s in range(2)]
    pt = [core.view3(110 + 4 * s, TT, P) for s in range(2)]
    biases = [core.view(118 + 4 * s, L) for s in range(2)]
    tb = [core.view(126 + 4 * s, L) for s in range(2)]
    mdist = core.view(178, L)
    olt = core.view3(182, 2, P)
    wuv = core.view3(183, 8, HD)
    stat = core.tiny2[:, 0:64].rearrange("p (a b) -> p a b", b=4)
    steps = [(h, i) for h in range(8) for i in range(TT)]
    N = len(steps)
    pair = lambda n, w: ps[:, 2 * (n % 2):2 * (n % 2) + 2, :].rearrange("p a b -> p (a b)")[:, 0:w]
    with nc.Block() as block:
        @block.sync
        def _(sp):
            if sparse:
                sp.dma_start(mdist, ap["c_mdist"]).then_inc(S["loaded0"].sem, 16)
                sp.dma_start(wuv, ap["w_uv_2"][0].rearrange("h r d -> r h d")).then_inc(S["loaded1"].sem, 16)
            else:
                for h in range(8):
                    if h >= 2:
                        sp.wait_ge(S["dve_done"].sem, S["dve_done"].at(TT * (h - 1)))
                    sp.dma_start(biases[h % 2], ap["c_bias_a"][h]).then_inc(S["loaded%d" % (2 + h % 2)].sem, 16)

        @block.tensor
        def _(pe):
            def scores(n):
                h, i = steps[n]
                if n >= 2:
                    pe.wait_ge(S["dve_done"].sem, S["dve_done"].at(n - 1))
                w = (i + 1) * P
                if sparse:
                    q, k = qlt[:, h, i * P:(i + 1) * P], ckvt
                else:
                    rows = slice(64 * (h % 2), 64 * (h % 2) + 64)
                    q, k = qat[rows, h // 2, i * P:(i + 1) * P], kat[rows, h // 2, :]
                for a in range(0, w, BANK):
                    b = min(a + BANK, w)
                    last = nc.tensor.matmul(ps[:, 2 * (n % 2) + a // BANK, 0:b - a], q, k[:, a:b], start=True, stop=True)
                last.then_inc(S["mm_done"].sem, 1)

            def transposes(n):
                h, i = steps[n]
                pe.wait_ge(S["act_done"].sem, S["act_done"].at(n + 1))
                if n >= 1:
                    pe.wait_ge(S["dve_free"].sem, S["dve_free"].at(n))
                for j in range(i + 1):
                    last = nc.tensor.transpose(ps[:, 4 + j // 4, (j % 4) * P:(j % 4 + 1) * P], sc[n % 2][:, j * P:(j + 1) * P], core.ident)
                last.then_inc(S["tr_done"].sem, 1)

            def values(n):
                h, i = steps[n]
                pe.wait_ge(S["dve_free"].sem, S["dve_free"].at(n + 1))
                if sparse and n >= 1:
                    pe.wait_ge(S["row_ready"].sem, S["row_ready"].at(n))
                elif not sparse and n >= 2:
                    pe.wait_ge(S["act_free"].sem, S["act_free"].at(n - 1))
                for j in range(i + 1):
                    if sparse:
                        last = nc.tensor.matmul(ps[:, 6, 0:P], ckv[:, j, :], pt[n % 2][:, j, :], start=j == 0, stop=j == i)
                    else:
                        last = nc.tensor.matmul(ps[:, 6 + n % 2, 0:HD], pt[n % 2][:, j, :], va[:, j, h * HD:(h + 1) * HD], start=j == 0, stop=j == i)
                last.then_inc(S["aux_done"].sem, 1)

            def expand(n):
                h, i = steps[n]
                if n == 0:
                    pe.wait_ge(S["loaded1"].sem, S["loaded1"].at(16))
                pe.wait_ge(S["row_ready"].sem, S["row_ready"].at(n + 1))
                if n >= 1:
                    pe.wait_ge(S["act_free"].sem, S["act_free"].at(n))
                nc.tensor.matmul(ps[:, 7, 0:HD], olt[:, n % 2, :], wuv[:, h, :], start=True, stop=True).then_inc(S["aux2_done"].sem, 1)

            scores(0)
            scores(1)
            for n in range(N + 3):
                if n < N:
                    transposes(n)
                if n + 2 < N:
                    scores(n + 2)
                if 1 <= n <= N:
                    values(n - 1)
                if sparse and n >= 3:
                    expand(n - 3)

        @block.gpsimd
        def _(pool):
            if sparse:
                for n, (h, i) in enumerate(steps):
                    pool.wait_ge(S["x_ready"].sem, S["x_ready"].at(h + 1))
                    if n >= 2:
                        pool.wait_ge(S["dve_done"].sem, S["dve_done"].at(n - 1))
                    w = (i + 1) * P
                    nc.gpsimd.tensor_tensor(tb[n % 2][:, 0:w], biases[h % 2][:, L - w:L], sel_tile(core, i), ALU.add).then_inc(S["pool_done"].sem, 1)

        @block.vector
        def _(dve):
            chain = Chain(dve, S["dve_chain"])

            def biased(n):
                h, i = steps[n]
                w = (i + 1) * P
                if sparse:
                    dve.wait_ge(S["pool_done"].sem, S["pool_done"].at(n + 1))
                elif i == 0:
                    dve.wait_ge(S["loaded%d" % (2 + h % 2)].sem, S["loaded%d" % (2 + h % 2)].at(16 * (h // 2 + 1)))
                dve.wait_ge(S["mm_done"].sem, S["mm_done"].at(n + 1))
                if n >= 2:
                    dve.wait_ge(S["tr_done"].sem, S["tr_done"].at(n - 1))
                b = tb[n % 2][:, 0:w] if sparse else biases[h % 2][:, L - w:L]
                st = stat[:, n % 16, :]
                nc.vector.tensor_tensor_reduce(out=sc[n % 2][:, 0:w], in0=pair(n, w), in1=b, scale=SCALE, scalar=-3.0e38,
                                               op0=ALU.add, op1=ALU.max, accum_out=st[:, 0:1]).then_inc(S["dve_done"].sem, 1)
                dve.wait_ge(S["dve_done"].sem, S["dve_done"].at(n + 1))
                nc.vector.tensor_scalar(st[:, 1:2], st[:, 0:1], -1.0, None, ALU.mult).then_inc(S["stat_ready"].sem, 1)

            def copied(n):
                h, i = steps[n]
                w = (i + 1) * P
                dve.wait_ge(S["act_done"].sem, S["act_done"].at(n + 1))
                nc.vector.reciprocal(stat[:, n % 16, 3:4], stat[:, n % 16, 2:3])
                dve.wait_ge(S["tr_done"].sem, S["tr_done"].at(n + 1))
                if n >= 2:
                    dve.wait_ge(S["aux_done"].sem, S["aux_done"].at(n - 1))
                nc.vector.tensor_copy(pt[n % 2][:, 0:i + 1, :].rearrange("p a b -> p (a b)"),
                                      ps[:, 4:6, :].rearrange("p a b -> p (a b)")[:, 0:w]).then_inc(S["dve_free"].sem, 1)

            biased(0)
            for n in range(N):
                if n + 1 < N:
                    biased(n + 1)
                copied(n)
                if selection is not None:
                    selection.rounds(dve, 3.0 if n + 1 < N else None)

        @block.scalar
        def _(act):
            if sparse:
                act.wait_ge(S["loaded0"].sem, S["loaded0"].at(16))

            def output(n):
                h, i = steps[n]
                if sparse:
                    act.wait_ge(S["aux2_done"].sem, S["aux2_done"].at(n + 1))
                    src, at = ps[:, 7, 0:HD], 512 + h * HD
                else:
                    act.wait_ge(S["aux_done"].sem, S["aux_done"].at(n + 1))
                    src, at = ps[:, 6 + n % 2, 0:HD], h * HD
                act.wait_ge(S["dve_free"].sem, S["dve_free"].at(n + 1))
                nc.scalar.activation(mix[:, i, at:at + HD], src, ACT.Copy, scale=stat[:, n % 16, 3:4]).then_inc(S["act_free"].sem, 1)

            def latent(n):
                act.wait_ge(S["aux_done"].sem, S["aux_done"].at(n + 1))
                if n >= 2:
                    act.wait_ge(S["aux2_done"].sem, S["aux2_done"].at(n - 1))
                nc.scalar.activation(olt[:, n % 2, :], ps[:, 6, 0:P], ACT.Copy).then_inc(S["row_ready"].sem, 1)

            for n in range(N + 4):
                if n < N:
                    h, i = steps[n]
                    w = (i + 1) * P
                    if sparse and i == 0:
                        if h >= 2:
                            act.wait_ge(S["pool_done"].sem, S["pool_done"].at(n - TT))
                        nc.scalar.activation(biases[h % 2], mdist, ACT.Copy, scale=SLOPES_B[h] / SCALE).then_inc(S["x_ready"].sem, 1)
                    act.wait_ge(S["stat_ready"].sem, S["stat_ready"].at(n + 1))
                    nc.scalar.activation(sc[n % 2][:, 0:w], sc[n % 2][:, 0:w], ACT.Exp, bias=stat[:, n % 16, 1:2],
                                         accum_out=stat[:, n % 16, 2:3]).then_inc(S["act_done"].sem, 1)
                if sparse:
                    if 2 <= n <= N + 1:
                        latent(n - 2)
                    if n >= 4:
                        output(n - 4)
                elif 2 <= n <= N + 1:
                    output(n - 2)
    for n in ("mm_done", "tr_done", "aux_done", "dve_done", "stat_ready", "dve_free", "act_done", "act_free"):
        S[n].close(N)
    if sparse:
        for n in ("aux2_done", "row_ready", "pool_done"):
            S[n].close(N)
        S["x_ready"].close(8)
        S["loaded0"].close(16)
        S["loaded1"].close(16)
    else:
        S["loaded2"].close(16 * 4)
        S["loaded3"].close(16 * 4)


def phase_mix_transpose(core, mix, mixt):
    nc, S, ps = core.nc, core.sig, core.psum
    part = lambda x, u: x[:, 4 * (u % 2):4 * (u % 2) + 4, (u // 2) * P:(u // 2 + 1) * P]
    bank = lambda u: ps[:, u % 8, :].rearrange("p (a b) -> p a b", a=4)
    with nc.Block() as block:
        @block.tensor
        def _(pe):
            for u in range(2 * TT):
                i, q = u // 2, u % 2
                if u >= 8:
                    pe.wait_ge(S["dve_free"].sem, S["dve_free"].at(u - 7))
                for j in range(4):
                    last = nc.tensor.transpose(ps[:, u % 8, j * P:(j + 1) * P], mix[:, i, (4 * q + j) * P:(4 * q + j + 1) * P], core.ident)
                last.then_inc(S["tr_done"].sem, 1)

        @block.scalar
        def _(act):
            for u in range(2 * TT):
                act.wait_ge(S["tr_done"].sem, S["tr_done"].at(u + 1))
                nc.scalar.activation(part(mixt.hi, u), bank(u), ACT.Copy).then_inc(S["act_done"].sem, 1)

        @block.vector
        def _(dve):
            for u in range(2 * TT):
                dve.wait_ge(S["act_done"].sem, S["act_done"].at(u + 1))
                nc.vector.tensor_tensor(part(mixt.lo, u), bank(u), part(mixt.hi_raw, u), ALU.subtract).then_inc(S["dve_free"].sem, 1)
    for n in ("tr_done", "act_done", "dve_free"):
        S[n].close(2 * TT)


def second_block(core):
    ap = core.ap
    h, xt = core.view3(H_KB, TT, D), Split(core, 6, KT, L)
    saved = core.nc.dram_tensor("saved_x", (1, L, D), F32, kind="Internal").ap()
    phase_ada(core, h, saved)
    phase_norm(core, h, xt, core.mod_scale[0], shift=core.mod_shift[0], scratch=142)
    w = ap["w_in_2"].rearrange("a (k p) n -> p (a k) n", p=P)
    columns = lambda kb, start: [([w[:, :, start + n * P:start + (n + 1) * P]], xt, core.view3(kb, 4, L)[:, n, :]) for n in range(4)]
    core.wi = core.tiny2[:, 300:364].rearrange("p (t h) -> p t h", t=TT)
    phase_rows_proj(core, [(w[:, :, WI0 + 8 - P:WI0 + 8], xt, lambda t: core.wi[:, t, :], ACT.Copy)], (70, 86))
    phase_cols_gemm(core, columns(QIT_KB, QI0) + [([w[:, :, KI0:KI0 + 64]] * 2, xt, core.view(KIT_KB, L))], 70)
    phase_index_scores(core)
    selection = Selection(core)
    phase_cols_gemm(core, columns(QAT_KB, QA0) + columns(KAT_KB, KA0) + columns(QBT_KB, QB0), (118, 126, 178, 186),
                    beside=lambda dve: selection.rounds(dve, 8.0))
    va, ckv = core.view3(VA_KB, TT, 512), core.view3(CKV_KB, TT, RANK)
    phase_rows_proj(core, [(w[:, :, VA0:VA0 + 512], xt, lambda t: va[:, t, :], ACT.Copy),
                           (w[:, :, CK0:CK0 + RANK], xt, lambda t: ckv[:, t, :], ACT.Copy)], (118, 178),
                    beside=lambda dve: selection.rounds(dve, 10.0))
    phase_latent(core)
    phase_attention(core, sparse=False, selection=selection)
    phase_attention(core, sparse=True)
    mix, mixt = core.view3(MIX_KB, TT, D), Split(core, 70, 8, L)
    phase_mix_transpose(core, mix, mixt)
    h, xt = core.view3(H2_KB, TT, D), Split(core, 70, KT, L)
    phase_rows_gemm(core, mixt, ap["w_out_2"], h, gate=core.view(GA1_KB, D), residual=saved, ring_kb=(134, 150, 166), tmp_kb=182)
    phase_norm(core, h, xt, core.mod_scale[1], shift=core.mod_shift[1], scratch=142)
    phase_ffn(core, xt, h, core.view(GA2_KB, D), {"ft": 6, "ring": 134, "w2": 166, "act": 182, "full": 186, "tmp": 190})
    phase_final_norm(core, h, ap["g_final_2"][:], 134, out_dram=ap["out"])


def build_program(nc, ap):
    core = Core(nc, ap)
    first_block(core)
    second_block(core)


def kernel(**inputs):
    import concourse.bacc as bacc
    from concourse.bass_utils import run_bass_kernel_spmd

    nc = bacc.Bacc("TRN2", target_bir_lowering=False, num_devices=1)
    arrays, ap = {}, {}
    for name, value in [*inputs.items(), *constants().items()]:
        a = np.ascontiguousarray(value)
        arrays[f"in_{name}_dram"] = a
        ap[name] = nc.dram_tensor(f"in_{name}_dram", a.shape, mybir.dt.from_np(a.dtype), kind="ExternalInput").ap()
    ap["out"] = nc.dram_tensor("out_0_dram", (1, L, D), F32, kind="ExternalOutput").ap()
    build_program(nc, ap)
    r = run_bass_kernel_spmd(nc, [arrays], core_ids=[0])
    return r.results[0]["out_0_dram"]
```

```python
import math

import numpy as np

import concourse.bass as bass
from concourse import mybir
from concourse.alu_op_type import AluOpType as ALU

F32 = mybir.dt.float32
F32R = mybir.dt.float32r
ACT = mybir.ActivationFunctionType
AX = mybir.AxisListType

P = 128
BANK = 512
L = 1024
D = 1024
TT = L // P
KT = D // P
EPS = 1e-6
NMEM = 256
DH = 512
NH_ML = 4
HY_COLS = 3 * DH
FF = 4 * D
FF2 = -(-8 * D // (3 * 256)) * 256
HD = 64
RANK = 128
TOPK = 256
NEG = -1.0e30
QA0, KA0, VA0, QB0, CK0, QI0, KI0, WI0 = (int(v) for v in np.cumsum([0, 512, 512, 512, 512, 128, 512, 64]))
ARENA = 207 * 256 + 192


class Signal:

    def __init__(self, nc, name):
        self.sem = nc.alloc_semaphore(name)
        self.base = 0

    def at(self, n):
        return self.base + n

    def close(self, n):
        self.base += n


def constants():
    half = L // 2
    n, even = np.arange(half)[:, None], 2 * np.arange(half)[None, :]
    tables = []
    for part, k in ((np.cos, even), (np.sin, even), (np.cos, even + 1), (np.sin, even + 1)):
        t = part(np.pi * ((n * k) % (2 * L)) / L)
        if (part is np.cos) == (k[0, 0] == 0):
            t[0] = (-1.0) ** np.arange(half)
        tables.append(t.astype(np.float32))
    block = lambda t, j: t.reshape(4, P, half)[:, :, j * P:(j + 1) * P].transpose(1, 0, 2)
    fwd = np.stack([block(tables[2 * (j // 4) + part], j % 4) for j in range(TT) for part in range(2)])
    inv = np.stack([block(np.ascontiguousarray(tables[m].T), j) for j in range(4) for m in (0, 3, 2, 1)])
    p = np.arange(P)
    alt = np.where(p % 2 == 0, 1.0, -1.0).astype(np.float32)
    small = np.zeros((P, 7, P), np.float32)
    small[:, 0] = np.eye(P)
    mats = np.zeros((P, 6, P), np.float32)
    mats[:, 0] = np.eye(P)[::-1]
    mats[:, 1, 0] = alt
    mats[0, 2, :] = alt
    mats[0, 3, :] = 1.0
    mats[:, 4, 0] = 1.0
    mats[0, 5, 0] = 1.0
    order = np.concatenate([np.arange(half), [half], L - np.arange(1, half)])
    small[:, 3] = np.where(p[None, :] >= p[:, None], 0.0, NEG)
    small[:, 4] = np.where(p[None, :] <= p[:, None], 0.0, NEG)
    small[:, 5, 0:TT] = -order.reshape(TT, P).T / (L - 1.0)
    small[:, 5, 8] = 2.0 / (2 * L)
    small[:, 5, 9] = 2.0 / (2 * L)
    small[0, 5, 9] = 1.0 / (2 * L)
    small[:, 5, 10] = 1.0
    small[:, 5, 11] = EPS
    small[:, 6] = 1.0
    sel = np.zeros((64, 8, P), np.float32)
    for h in range(8):
        sel[(h // 4) * 32 + h % 4, h, :] = 1.0
    f32 = np.float32
    t = np.linspace(0.0, 1.0, L, dtype=f32)[:, None]
    w = (f32(2.0 * math.pi / L) * np.arange(L, dtype=f32))[:, None]
    bands = np.linspace(1e-4, 15, 16, dtype=f32)[None, :]
    z = np.concatenate([t, np.cos(bands * w), -np.sin(bands * w)], axis=-1)
    deltas = np.abs(np.linspace(math.log(1e-2) / 1.5, math.log(1e-2) / 0.3, DH, dtype=f32))
    slopes = (2.0 ** (-8.0 * (np.arange(16, dtype=f32) + 1.0) / 16)).astype(f32)
    dist = p[:, None] - (np.arange(L) - (L - P))[None, :]
    mult = ((dist >= 0) & (dist <= 128)) * 1.0 + ((dist >= 0) & (dist % 4 == 0) & (dist <= 512)) + ((dist >= 0) & (dist % 16 == 0))
    lnm = np.where(mult > 0, np.log(np.maximum(mult, 1)), NEG)
    bias_a = np.stack([np.where(mult > 0, 8.0 * (lnm - float(slopes[2 * h]) * dist), NEG) for h in range(8)]).astype(f32)
    mdist = (-dist).astype(f32)
    return {
        "c_fwd": fwd, "c_inv": inv, "c_mats": mats, "c_small": small, "c_sel": sel,
        "c_z": np.ascontiguousarray(z.T[:, order]), "c_delta": deltas[None, :].copy(),
        "c_bias_a": bias_a, "c_mdist": mdist,
    }


SLOPES_B = [float(np.float32(2.0 ** (-8.0 * (2 * h + 2) / 16))) for h in range(8)]


class Core:

    def __init__(self, nc, ap):
        self.nc = nc
        self.ap = ap
        self.base = (nc.sbuf_base + 63) // 64 * 64
        self.placed = {}
        self.psum = nc.alloc_psum_tensor("psum", [P, 8, BANK], F32)
        names = (
            "loaded", "loaded0", "loaded1", "loaded2", "loaded3", "stored",
            "mm_done", "tr_done", "act_done", "act_free", "act_chain", "dve_done", "dve_free", "dve_chain",
            "pool_done", "pool_chain", "aux_done", "aux2_done", "x_ready",
            "stat_ready", "row_ready", "col_ready", "w_hi", "w_lo", "v_hi", "v_lo", "square_done",
            "bank_free", "ft_hi", "ft_lo", "table0", "table1", "table2", "table3", "mirrored", "selected", "row_ready_dve", "probs_turned", "mod_ready", "mod_chain", "ada0", "ada1", "ada2", "ada3", "ada4", "ada5",
        )
        self.sig = {n: Signal(nc, n) for n in names}
        self.small = self.view(0, 7 * P).rearrange("p (a b) -> p a b", a=7)
        self.ident = self.small[:, 0, :]
        self.colsA = self.view(3.5, 128)
        self.colsB = self.view(4.0, 64)
        self.tiny = self.view(4.25, 64)
        self.eps = self.small[:, 5, 11:12]
        self.tiny2 = self.view(4.5, 384)

    def place(self, kb, shape, dtype):
        start, words = int(round(kb * 256)), int(np.prod(shape[1:]))
        assert start + words <= ARENA, (kb, shape)
        key = (start, words, dtype)
        if key not in self.placed:
            name = "%s_%d_%d" % ("rounded" if dtype == F32R else "plain", start, words)
            self.placed[key] = self.nc.alloc_sbuf_tensor_at(name, [P, words], dtype, offset=self.base + 4 * start)
        return self.placed[key]

    def view(self, kb, words, parts=P):
        return self.place(kb, [P, words], F32)[0:parts, :]

    def view3(self, kb, a, b, parts=P):
        return self.view(kb, a * b, parts).rearrange("p (a b) -> p a b", a=a)


    def view_r(self, kb, a, b):
        return self.place(kb, [P, a * b], F32R)[:, :].rearrange("p (a b) -> p a b", a=a)


class Split:

    def __init__(self, core, kb, a, b):
        self.hi, self.lo = core.view_r(kb, a, b), core.view_r(kb + a * b / 256, a, b)
        self.raw = core.view3(kb + a * b / 256, a, b)
        self.hi_raw = self.hi.bitcast(F32)
        self.before = core.view3(kb, a, b)


def mm3(nc, out, wh, wl, xh, xl, first, last):
    nc.tensor.matmul(out, wh, xh, start=first, stop=False)
    nc.tensor.matmul(out, wh, xl, start=False, stop=False)
    return nc.tensor.matmul(out, wl, xh, start=False, stop=last)


def keep_clock(core, count=3, bank=7):
    for _ in range(count):
        core.nc.tensor.matmul(core.psum[:, bank, :], core.ident, core.small[:, 0:4, :], start=True, stop=True)


class Chain:

    def __init__(self, eng, signal):
        self.eng, self.count, self.n = eng, signal, 0

    def __call__(self, ins):
        self.n += 1
        ins.then_inc(self.count.sem, 1)
        self.eng.wait_ge(self.count.sem, self.count.at(self.n))


G_MIX, CW_HY, CB_HY, CW_ML, CB_ML, G_X, G_MEM, G_FF = 0, 8, 44, 56, 80, 88, 96, 104
G_ATT2, G_FFN2 = 112, 120
C_ACT, G_HY, G_ML, G_KV = 0, 8, 12, 16


def phase_load(core):
    nc, ap, S = core.nc, core.ap, core.sig
    x = core.view3(118, TT, D)
    rowsA = core.view(102, P)
    rowsB = core.view(103, P)
    loads = [
        (x, ap["x"].rearrange("a (t p) d -> p (a t) d", p=P)),
        (core.small, ap["c_small"]),
    ]
    at = 0
    for name, rows in (("norm_mix_g", 8), ("hy_conv_w", 36), ("hy_conv_b", 12), ("ml_conv_w", 24), ("ml_conv_b", 8),
                       ("norm_x_g", 8), ("norm_mem_g", 8), ("norm_ff_g", 8), ("g_attn_2", 8), ("g_ffn_2", 8)):
        src = ap[name]
        src = src.rearrange("a b (r c) -> (a b r) c", c=P) if len(src.shape) == 3 else src.rearrange("a (r c) -> (a r) c", c=P)
        loads.append((rowsA[at:at + rows, :], src))
        at += rows
    at = 0
    for name, rows in (("c_2", 8), ("hy_norm_g", 4), ("ml_norm_g", 4), ("kv_norm_g_2", 1)):
        loads.append((rowsB[at:at + rows, :], ap[name].rearrange("a (r c) -> (a r) c", c=P)))
        at += rows
    nB = at
    with nc.Block() as block:
        @block.sync
        def _(sp):
            for dst, src in loads:
                sp.dma_start(dst, src).then_inc(S["loaded"].sem, 16)

        @block.tensor
        def _(pe):
            pe.wait_ge(S["loaded"].sem, S["loaded"].at(16 * len(loads)))
            nc.tensor.transpose(core.psum[:, 0, 0:P], rowsA, core.ident)
            nc.tensor.transpose(core.psum[:, 0, P:P + nB], rowsB[0:nB, :], core.ident[0:nB, 0:nB]).then_inc(S["tr_done"].sem, 1)

        @block.vector
        def _(dve):
            dve.wait_ge(S["tr_done"].sem, S["tr_done"].at(1))
            nc.vector.tensor_copy(core.colsA, core.psum[:, 0, 0:P])
            nc.vector.tensor_copy(core.colsB[:, 0:nB], core.psum[:, 0, P:P + nB])
    S["loaded"].close(16 * len(loads))
    S["tr_done"].close(1)


def load_ahead(sp, loads):
    for dst, src, signal in loads:
        sp.dma_start(dst, src).then_inc(signal.sem, 16)


def first_columns(core, ring, w, at, count=4):
    return [(ring[s].raw, w[:, :, at + s * P:at + (s + 1) * P], core.sig["loaded%d" % s]) for s in range(count)]


def phase_norm(core, src, dst, gain, shift=None, scratch=150, ahead=(), arrives=False):
    nc, S = core.nc, core.sig
    tiles = src.shape[1]
    junk = dst.before.rearrange("p k t -> p (k t)").rearrange("p (i d) -> p i d", d=D)
    tmp = core.view3(scratch, 2, D)
    full = [core.view3(scratch + 8 + 2 * s, 4, P) for s in range(2)]
    ss, rstd = core.tiny[:, 0:tiles], core.tiny[:, 8:8 + tiles]
    ps = core.psum
    U = 2 * tiles
    part = lambda x, u: x[:, 4 * (u % 2):4 * (u % 2) + 4, (u // 2) * P:(u // 2 + 1) * P]
    with nc.Block() as block:
        @block.sync
        def _(sp):
            load_ahead(sp, ahead)

        def scaled(eng, i):
            if i >= 2:
                eng.wait_ge(S["tr_done"].sem, S["tr_done"].at(2 * (i - 1)))
            if i % 2 == 0:
                nc.scalar.activation(tmp[:, 0, :], src[:, i, :], ACT.Copy, scale=rstd[:, i:i + 1]).then_inc(S["row_ready"].sem, 1)
            else:
                nc.vector.tensor_scalar(tmp[:, 1, :], src[:, i, :], rstd[:, i:i + 1], None, ALU.mult).then_inc(S["row_ready_dve"].sem, 1)

        @block.scalar
        def _(act):
            if arrives:
                act.wait_ge(S["x_ready"].sem, S["x_ready"].at(16))
            for i in range(0, tiles, 2):
                last = nc.scalar.activation(junk[:, i, :], src[:, i, :], ACT.Square, accum_out=ss[:, i:i + 1])
            Chain(act, S["act_chain"])(last)
            act.wait_ge(S["square_done"].sem, S["square_done"].at(1))
            nc.scalar.activation(rstd, ss, ACT.Sqrt, scale=1.0 / D, bias=core.eps).then_inc(S["stat_ready"].sem, 1)
            act.wait_ge(S["col_ready"].sem, S["col_ready"].at(1))
            scaled(act, 0)
            for i in range(tiles):
                if i % 2 == 1 and i + 1 < tiles:
                    scaled(act, i + 1)
                for u in (2 * i, 2 * i + 1):
                    act.wait_ge(S["dve_done"].sem, S["dve_done"].at(u + 1))
                    nc.scalar.activation(part(dst.hi, u), full[u % 2], ACT.Copy).then_inc(S["act_done"].sem, 1)

        @block.tensor
        def _(pe):
            for i in range(tiles):
                ready = S["row_ready_dve" if i % 2 else "row_ready"]
                pe.wait_ge(ready.sem, ready.at(i // 2 + 1))
                for q in range(2):
                    u = 2 * i + q
                    if u >= 8:
                        pe.wait_ge(S["dve_done"].sem, S["dve_done"].at(u - 7))
                    for j in range(4):
                        last = nc.tensor.transpose(ps[:, u % 8, j * P:(j + 1) * P], tmp[:, i % 2, (4 * q + j) * P:(4 * q + j + 1) * P], core.ident)
                    last.then_inc(S["tr_done"].sem, 1)

        @block.vector
        def _(dve):
            chain = Chain(dve, S["dve_chain"])
            if arrives:
                dve.wait_ge(S["x_ready"].sem, S["x_ready"].at(16))
            for i in range(1, tiles, 2):
                last = nc.vector.tensor_tensor_reduce(out=junk[:, i, :], in0=src[:, i, :], in1=src[:, i, :], scale=1.0, scalar=0.0,
                                                      op0=ALU.mult, op1=ALU.add, accum_out=ss[:, i:i + 1])
            last.then_inc(S["square_done"].sem, 1)
            dve.wait_ge(S["stat_ready"].sem, S["stat_ready"].at(1))
            nc.vector.reciprocal(rstd, rstd).then_inc(S["col_ready"].sem, 1)
            dve.wait_ge(S["col_ready"].sem, S["col_ready"].at(1))
            scaled(dve, 1)
            for u in range(U):
                q = u % 2
                dve.wait_ge(S["tr_done"].sem, S["tr_done"].at(u + 1))
                if u >= 2:
                    dve.wait_ge(S["pool_done"].sem, S["pool_done"].at(u - 1))
                g = gain[:, 4 * q:4 * q + 4].unsqueeze(2).to_broadcast([P, 4, P])
                ins = nc.vector.tensor_tensor(full[q], ps[:, u % 8, :].rearrange("p (a b) -> p a b", a=4), g, ALU.mult)
                if shift is not None:
                    chain(ins)
                    sh = shift[:, 4 * q:4 * q + 4].unsqueeze(2).to_broadcast([P, 4, P])
                    ins = nc.vector.tensor_tensor(full[q], full[q], sh, ALU.add)
                ins.then_inc(S["dve_done"].sem, 1)
                if u % 4 == 3 and u // 2 + 2 < tiles:
                    scaled(dve, u // 2 + 2)

        @block.gpsimd
        def _(pool):
            for u in range(U):
                pool.wait_ge(S["act_done"].sem, S["act_done"].at(u + 1))
                nc.gpsimd.tensor_tensor(part(dst.lo, u), full[u % 2], part(dst.hi_raw, u), ALU.subtract).then_inc(S["pool_done"].sem, 1)
    S["act_chain"].close(1)
    S["stat_ready"].close(1)
    S["col_ready"].close(1)
    S["square_done"].close(1)
    S["row_ready"].close(tiles // 2)
    S["row_ready_dve"].close(tiles // 2)
    if arrives:
        S["x_ready"].close(16)
    for n in ("tr_done", "dve_done", "act_done", "pool_done"):
        S[n].close(U)
    if shift is not None:
        S["dve_chain"].close(U)


def phase_split(core, pairs):
    nc, S = core.nc, core.sig
    with nc.Block() as block:
        @block.scalar
        def _(act):
            for src, hi, lo, hi_raw in pairs:
                nc.scalar.activation(hi, src, ACT.Copy).then_inc(S["act_done"].sem, 1)

        @block.vector
        def _(dve):
            for n, (src, hi, lo, hi_raw) in enumerate(pairs):
                dve.wait_ge(S["act_done"].sem, S["act_done"].at(n + 1))
                nc.vector.tensor_tensor(lo, src, hi_raw, ALU.subtract)
    S["act_done"].close(len(pairs))


def split_pairs(src, dst, at=0):
    return [(src[:, n, :], dst.hi[:, at + n, :], dst.lo[:, at + n, :], dst.hi_raw[:, at + n, :]) for n in range(src.shape[1])]


def weight_tiles(core, kb, slots=4):
    return [Split(core, kb + 8 * s, KT, P) for s in range(slots)]


def mm3_cols(nc, out, w, cols, xt, a, b):
    for k in range(KT):
        last = mm3(nc, out, w.hi[:, k, cols], w.lo[:, k, cols], xt.hi[:, k, a:b], xt.lo[:, k, a:b], k == 0, k == KT - 1)
    return last


CONV_RING_KB = 162


def phase_conv_proj(core, xt, w, hy):
    nc, S, ps = core.nc, core.sig, core.psum
    ring = weight_tiles(core, CONV_RING_KB)
    tmp = [core.view(150 + 4.25 * s, L + 1) for s in range(2)]
    cuts = [t * P for t in range(4)] + [L + 1 - (j + 1) * P for j in range(4)]
    n_tiles = HY_COLS // P
    wv = w.rearrange("a (k p) n -> p (a k) n", p=P)
    ld = [S["loaded%d" % s] for s in range(4)]
    with nc.Block() as block:
        @block.sync
        def _(sp):
            for n in range(4, n_tiles):
                sp.wait_ge(S["mm_done"].sem, S["mm_done"].at(n - 3))
                sp.dma_start(ring[n % 4].raw, wv[:, :, n * P:(n + 1) * P]).then_inc(ld[n % 4].sem, 16)

        @block.tensor
        def _(pe):
            for n in range(n_tiles + 1):
                if n < n_tiles:
                    pe.wait_ge(S["w_lo"].sem, S["w_lo"].at(n + 1))
                    if n >= 2:
                        pe.wait_ge(S["dve_done"].sem, S["dve_done"].at(n - 1))
                    for half in range(2):
                        last = mm3_cols(nc, ps[:, 2 * (n % 2) + half, :], ring[n % 4], slice(0, P), xt, half * BANK, (half + 1) * BANK)
                    last.then_inc(S["mm_done"].sem, 1)
                if n >= 1:
                    m = n - 1
                    pe.wait_ge(S["dve_done"].sem, S["dve_done"].at(m + 1))
                    if m >= 2:
                        pe.wait_ge(S["act_free"].sem, S["act_free"].at(m - 1))
                    for t in range(TT):
                        last = nc.tensor.transpose(ps[:, 4 + 2 * (m % 2) + t // 4, (t % 4) * P:(t % 4 + 1) * P], tmp[m % 2][:, cuts[t]:cuts[t] + P], core.ident)
                    last.then_inc(S["tr_done"].sem, 1)

        @block.scalar
        def _(act):
            def back(m):
                act.wait_ge(S["tr_done"].sem, S["tr_done"].at(m + 1))
                src = ps[:, 4 + 2 * (m % 2):6 + 2 * (m % 2), :].rearrange("p a (b c) -> p (a b) c", c=P)
                nc.scalar.activation(hy[:, :, m * P:(m + 1) * P], src, ACT.Copy).then_inc(S["act_free"].sem, 1)

            def weights(n):
                act.wait_ge(ld[n % 4].sem, ld[n % 4].at(16 * (n // 4 + 1)))
                nc.scalar.activation(ring[n % 4].hi, ring[n % 4].raw, ACT.Copy).then_inc(S["w_hi"].sem, 1)

            weights(0)
            weights(1)
            for n in range(n_tiles):
                if n + 2 < n_tiles:
                    weights(n + 2)
                act.wait_ge(S["mm_done"].sem, S["mm_done"].at(n + 1))
                if n >= 2:
                    act.wait_ge(S["tr_done"].sem, S["tr_done"].at(n - 1))
                nc.scalar.activation(tmp[n % 2][:, 0:L], ps[:, 2 * (n % 2):2 * (n % 2) + 2, :].rearrange("p a b -> p (a b)"), ACT.Identity,
                                     scale=core.colsA[:, CW_HY + 12 + n:CW_HY + 13 + n],
                                     bias=core.colsA[:, CB_HY + n:CB_HY + n + 1]).then_inc(S["act_done"].sem, 1)
                if n >= 1:
                    back(n - 1)
            back(n_tiles - 1)

        @block.vector
        def _(dve):
            chain = Chain(dve, S["dve_chain"])

            def weights(n):
                dve.wait_ge(S["w_hi"].sem, S["w_hi"].at(n + 1))
                nc.vector.tensor_tensor(ring[n % 4].lo, ring[n % 4].raw, ring[n % 4].hi_raw, ALU.subtract).then_inc(S["w_lo"].sem, 1)

            weights(0)
            weights(1)
            for n in range(n_tiles):
                if n + 2 < n_tiles:
                    weights(n + 2)
                dve.wait_ge(S["act_done"].sem, S["act_done"].at(n + 1))
                pr = ps[:, 2 * (n % 2):2 * (n % 2) + 2, :].rearrange("p a b -> p (a b)")
                t = tmp[n % 2]
                chain(nc.vector.scalar_tensor_tensor(out=t[:, 1:L], in0=pr[:, 0:L - 1], scalar=core.colsA[:, CW_HY + n:CW_HY + n + 1],
                                                     in1=t[:, 1:L], op0=ALU.mult, op1=ALU.add))
                chain(nc.vector.scalar_tensor_tensor(out=t[:, 0:L - 1], in0=pr[:, 1:L], scalar=core.colsA[:, CW_HY + 24 + n:CW_HY + 25 + n],
                                                     in1=t[:, 0:L - 1], op0=ALU.mult, op1=ALU.add))
                nc.vector.tensor_copy(t[:, L:L + 1], t[:, L // 2:L // 2 + 1]).then_inc(S["dve_done"].sem, 1)
    for n in ("mm_done", "dve_done", "act_free", "tr_done", "act_done", "w_hi", "w_lo"):
        S[n].close(n_tiles)
    S["dve_chain"].close(2 * n_tiles)
    for s in range(4):
        ld[s].close(16 * len(range(s, n_tiles, 4)))
FOLD_KB, HY_KB, HR_KB, HS_KB, ZFOLD_KB, DFT_RING_KB, MATS_KB, NYQ_KB, HID_KB = 6, 70, 118, 134, 150, 182, 198, 200.75, 203
TWO_PI_HI = 6.28125
TWO_PI_LO = 2 * math.pi - TWO_PI_HI
MAGIC = 1.5 * 2.0 ** 23
UNITS = 16
ALT_COL, ALT_ROW, ONE_ROW, ONE_COL, CORNER = 0, 1, 2, 3, 4


def phase_filter_hidden(core, hy):
    nc, ap, S, ps = core.nc, core.ap, core.sig, core.psum
    hid = core.view(HID_KB, L, 64)
    z = core.view(42, L, 33)
    w1, w2 = core.view(46, 64, 33), core.view(46.5, 64, 64)
    vec = core.view(47, 8, 64)
    y, n = core.view(48, L, 64), core.view(52, L, 64)
    h1 = core.view(56, L, 64)
    mats, rounded = core.view3(60, 6, P), core.view_r(MATS_KB, 5, P)
    loads = [(z, ap["c_z"]), (w1, ap["hy_filt_w1"][0]), (w2, ap["hy_filt_w2"][0])]
    for i, name in enumerate(("hy_filt_b1", "hy_filt_freq1", "hy_filt_b2", "hy_filt_freq2")):
        loads.append((vec[:, i:i + 1], ap[name].rearrange("a c -> c a")))
    blocks = [(4 + j, c) for j in range(4) for c in range(3)]
    with nc.Block() as block:
        @block.sync
        def _(sp):
            sp.dma_start(mats, ap["c_mats"]).then_inc(S["loaded0"].sem, 16)
            with nc.allow_non_contiguous_dma("64 biases and frequencies, one per partition"):
                for dst, src in loads:
                    sp.dma_start(dst, src).then_inc(S["loaded"].sem, 16)

        @block.tensor
        def _(pe):
            def mirror(m):
                t, c = blocks[m]
                if m >= 4:
                    pe.wait_ge(S["mirrored"].sem, S["mirrored"].at(m - 3))
                nc.tensor.matmul(ps[:, 4 + m % 4, :], mats[:, 0, :], hy[:, t, c * BANK:(c + 1) * BANK], start=True, stop=True).then_inc(S["tr_done"].sem, 1)

            pe.wait_ge(S["loaded"].sem, S["loaded"].at(16 * len(loads)))
            pe.wait_ge(S["loaded0"].sem, S["loaded0"].at(16))
            for half in range(2):
                last = nc.tensor.matmul(ps[0:64, half, :], w1, z[:, half * BANK:(half + 1) * BANK], start=True, stop=True)
            last.then_inc(S["mm_done"].sem, 1)
            for m in range(8):
                mirror(m)
            pe.wait_ge(S["act_done"].sem, S["act_done"].at(1))
            for half in range(2):
                last = nc.tensor.matmul(ps[0:64, 2 + half, :], w2, h1[:, half * BANK:(half + 1) * BANK], start=True, stop=True)
            last.then_inc(S["mm_done"].sem, 1)
            for m in range(8, 12):
                mirror(m)

        @block.vector
        def _(dve):
            chain = Chain(dve, S["dve_chain"])
            dve.wait_ge(S["loaded"].sem, S["loaded"].at(16 * len(loads)))
            for layer in range(2):
                fr, fb = vec[:, 2 * layer + 1:2 * layer + 2], vec[:, 4 + layer:5 + layer]
                chain(nc.vector.tensor_tensor(fb, vec[:, 2 * layer:2 * layer + 1], fr, ALU.mult))
                dve.wait_ge(S["mm_done"].sem, S["mm_done"].at(layer + 1))
                src = ps[0:64, 2 * layer:2 * layer + 2, :].rearrange("p a b -> p (a b)")
                chain(nc.vector.tensor_scalar(y, src, fr, fb, ALU.mult, ALU.add))
                chain(nc.vector.tensor_scalar(n, y, 1.0 / (2 * math.pi), MAGIC, ALU.mult, ALU.add))
                chain(nc.vector.tensor_scalar(n, n, MAGIC, None, ALU.subtract))
                chain(nc.vector.scalar_tensor_tensor(out=y, in0=n, scalar=-TWO_PI_HI, in1=y, op0=ALU.mult, op1=ALU.add))
                chain(nc.vector.scalar_tensor_tensor(out=y, in0=n, scalar=-TWO_PI_LO, in1=y, op0=ALU.mult, op1=ALU.add))
                nc.vector.tensor_scalar(y, y, 3.1415925, -3.1415925, ALU.min, ALU.max).then_inc(S["dve_done"].sem, 1)
                dve.wait_ge(S["act_done"].sem, S["act_done"].at(layer + 1))

        @block.scalar
        def _(act):
            def back(m):
                t, c = blocks[m]
                act.wait_ge(S["tr_done"].sem, S["tr_done"].at(m + 1))
                nc.scalar.activation(hy[:, t, c * BANK:(c + 1) * BANK], ps[:, 4 + m % 4, :], ACT.Copy).then_inc(S["mirrored"].sem, 1)

            act.wait_ge(S["loaded0"].sem, S["loaded0"].at(16))
            nc.scalar.activation(rounded, mats[:, 1:6, :], ACT.Copy)
            for m in range(4):
                back(m)
            act.wait_ge(S["dve_done"].sem, S["dve_done"].at(1))
            nc.scalar.activation(h1, y, ACT.Sin).then_inc(S["act_done"].sem, 1)
            for m in range(4, 10):
                back(m)
            act.wait_ge(S["dve_done"].sem, S["dve_done"].at(2))
            nc.scalar.activation(hid, y, ACT.Sin).then_inc(S["act_done"].sem, 1)
            for m in range(10, 12):
                back(m)
    S["loaded"].close(16 * len(loads))
    S["loaded0"].close(16)
    S["mm_done"].close(2)
    S["dve_chain"].close(12)
    S["dve_done"].close(2)
    S["act_done"].close(2)
    S["tr_done"].close(12)
    S["mirrored"].close(12)


def phase_filter_time(core, tables, o):
    nc, ap, S, ps = core.nc, core.ap, core.sig, core.psum
    hid = core.view(HID_KB, L, 64)
    w3, delta = core.view(150, L, 64), core.view(154, DH)
    decay = core.view3(156, 2, DH)
    both = core.view3(HR_KB, 8, DH)
    windowed = core.view3(168, 4, DH)
    fold = Split(core, FOLD_KB, 16, DH)
    mt = core.small[:, 5, 0:TT]
    steps = [(j, m) for j in range(4) for m in range(2)]
    with nc.Block() as block:
        @block.sync
        def _(sp):
            sp.dma_start(w3, ap["hy_filt_w3"][0][:, o * L:(o + 1) * L]).then_inc(S["loaded"].sem, 16)
            sp.dma_start(delta, ap["c_delta"][0].partition_broadcast(P)).then_inc(S["loaded0"].sem, 16)
            tables.begin(sp, ap["c_fwd"])

        @block.tensor
        def _(pe):
            pe.wait_ge(S["loaded"].sem, S["loaded"].at(16))
            for n, (j, m) in enumerate(steps):
                t = j + 4 * m
                if n >= 4:
                    pe.wait_ge(S["dve_done"].sem, S["dve_done"].at(n - 3))
                for half in range(2):
                    last = nc.tensor.matmul(ps[:, 2 * (n % 4) + half, :], hid[:, t * P:(t + 1) * P], w3[:, half * DH:(half + 1) * DH], start=True, stop=True)
                last.then_inc(S["mm_done"].sem, 1)

        @block.scalar
        def _(act):
            def rounded(j):
                for q in range(4):
                    act.wait_ge(S["v_hi"].sem, S["v_hi"].at(4 * j + q + 1))
                    nc.scalar.activation(fold.hi[:, 4 * q + j, :], fold.raw[:, 4 * q + j, :], ACT.Copy).then_inc(S["w_hi"].sem, 1)

            act.wait_ge(S["loaded0"].sem, S["loaded0"].at(16))
            for n, (j, m) in enumerate(steps):
                t = j + 4 * m
                if n >= 2:
                    act.wait_ge(S["dve_done"].sem, S["dve_done"].at(n - 1))
                nc.scalar.activation(decay[:, n % 2, :], delta, ACT.Exp, scale=mt[:, t:t + 1]).then_inc(S["act_done"].sem, 1)
                if m == 1 and j >= 1:
                    rounded(j - 1)
            rounded(3)

        @block.vector
        def _(dve):
            chain = Chain(dve, S["dve_chain"])

            def low(j):
                for q in range(4):
                    dve.wait_ge(S["w_hi"].sem, S["w_hi"].at(4 * j + q + 1))
                    nc.vector.tensor_tensor(fold.lo[:, 4 * q + j, :], fold.raw[:, 4 * q + j, :], fold.hi_raw[:, 4 * q + j, :], ALU.subtract)

            def folded(j):
                dve.wait_ge(S["pool_done"].sem, S["pool_done"].at(2 * j + 2))
                for q in range(4):
                    a, b = both[:, 4 * (j % 2) + q // 2, :], both[:, 4 * (j % 2) + 2 + q // 2, :]
                    out = fold.raw[:, 4 * q + j, :]
                    ins = nc.vector.tensor_tensor(out, a, b, ALU.subtract if q % 2 else ALU.add)
                    if j == 0:
                        chain(ins)
                        ins = nc.vector.tensor_copy(out[0:1, :], (a if q % 2 else b)[0:1, :])
                    ins.then_inc(S["v_hi"].sem, 1)

            for n, (j, m) in enumerate(steps):
                dve.wait_ge(S["act_done"].sem, S["act_done"].at(n + 1))
                dve.wait_ge(S["mm_done"].sem, S["mm_done"].at(n + 1))
                if n >= 2:
                    dve.wait_ge(S["pool_done"].sem, S["pool_done"].at(n - 1))
                nc.vector.tensor_tensor(windowed[:, 2 * m, :], ps[:, 2 * (n % 4), :], decay[:, n % 2, :], ALU.mult)
                nc.vector.tensor_tensor(windowed[:, 2 * m + 1, :], ps[:, 2 * (n % 4) + 1, :], decay[:, n % 2, :], ALU.mult).then_inc(S["dve_done"].sem, 1)
                if m == 0 and j >= 1:
                    folded(j - 1)
                elif m == 1 and j >= 1:
                    low(j - 1)
            folded(3)
            low(3)

        @block.gpsimd
        def _(pool):
            for n, (j, m) in enumerate(steps):
                pool.wait_ge(S["dve_done"].sem, S["dve_done"].at(n + 1))
                if j >= 2:
                    pool.wait_ge(S["v_hi"].sem, S["v_hi"].at(4 * (j - 1)))
                f, b = windowed[:, 2 * m, :], windowed[:, 2 * m + 1, :]
                if n == 0:
                    nc.gpsimd.memset(b[0:1, :], 0.0).then_inc(S["pool_chain"].sem, 1)
                    pool.wait_ge(S["pool_chain"].sem, S["pool_chain"].at(1))
                at = 4 * (j % 2) + 2 * m
                nc.gpsimd.tensor_tensor(both[:, at, :], f, b, ALU.add)
                nc.gpsimd.tensor_tensor(both[:, at + 1, :], f, b, ALU.subtract).then_inc(S["pool_done"].sem, 1)
    S["loaded"].close(16)
    S["loaded0"].close(16)
    for n in ("mm_done", "dve_done", "act_done", "pool_done"):
        S[n].close(TT)
    S["pool_chain"].close(1)
    S["dve_chain"].close(4)
    S["v_hi"].close(16)
    S["w_hi"].close(16)


class Tables:

    def __init__(self, core):
        self.core, self.begun = core, 0
        self.ring = [Split(core, DFT_RING_KB + 4 * s, 4, P) for s in range(4)]
        self.loaded = [core.sig["table%d" % s].sem for s in range(4)]

    def begin(self, sp, table):
        for u in range(4):
            sp.dma_start(self.ring[u].raw, table[u]).then_inc(self.loaded[u], 16)

    def load(self, sp, current, following):
        S = self.core.sig
        for u in range(4, UNITS + (4 if following is not None else 0)):
            sp.wait_ge(S["aux_done"].sem, S["aux_done"].at(u - 3))
            src = current[u] if u < UNITS else following[u - UNITS]
            sp.dma_start(self.ring[u % 4].raw, src).then_inc(self.loaded[u % 4], 16)

    def high(self, act, u):
        S = self.core.sig
        act.wait_ge(self.loaded[u % 4], 16 * ((self.begun + u) // 4 + 1))
        self.core.nc.scalar.activation(self.ring[u % 4].hi, self.ring[u % 4].raw, ACT.Copy).then_inc(S["ft_hi"].sem, 1)

    def low(self, pool, u):
        S, w = self.core.sig, self.ring[u % 4]
        pool.wait_ge(S["ft_hi"].sem, S["ft_hi"].at(u + 1))
        self.core.nc.gpsimd.tensor_tensor(w.lo, w.raw, w.hi_raw, ALU.subtract).then_inc(S["ft_lo"].sem, 1)

    def products(self, pe, out, u, src, at, first, last):
        nc, S, w = self.core.nc, self.core.sig, self.ring[u % 4]
        pe.wait_ge(S["ft_lo"].sem, S["ft_lo"].at(u + 1))
        for k in range(4):
            ins = mm3(nc, out, w.hi[:, k, :], w.lo[:, k, :], src.hi[:, at + k, :], src.lo[:, at + k, :], first and k == 0, last and k == 3)
        return ins

    def close(self):
        for n in ("ft_hi", "ft_lo", "aux_done"):
            self.core.sig[n].close(UNITS)
        self.begun += UNITS


def exact(nc, out, mat, src, at, last=False):
    nc.tensor.matmul(out, mat, src.hi[:, at, :], start=False, stop=False)
    return nc.tensor.matmul(out, mat, src.lo[:, at, :], start=False, stop=last)


def forward_pe(core, pe, tables, src, at_c, at_s, free_name):
    nc, S, ps = core.nc, core.sig, core.psum
    mats = core.view_r(MATS_KB, 5, P)
    for u in range(UNITS):
        j, part = u // 2, u % 2
        bank = ps[:, u % 8, :]
        if u >= 8 and part == 0:
            pe.wait_ge(S[free_name].sem, S[free_name].at(j - 3))
        at = (at_s if part else at_c) + 4 * ((j >= 4) != (part == 1))
        more = (j < 4 and part == 0) or u == 1
        ins = tables.products(pe, bank, u, src, at, True, not more)
        if j < 4 and part == 0:
            ins = exact(nc, bank, mats[:, ONE_ROW, :], src, at_c + 4, last=True)
        if u == 1:
            for k in range(4):
                exact(nc, bank, mats[:, ALT_COL, :], src, at_c + k)
            ins = exact(nc, bank, mats[:, CORNER, :], src, at_c + 4, last=True)
        ins.then_inc(S["aux_done"].sem, 1)


def phase_filter_spectrum(core, tables, hy):
    nc, ap, S, ps = core.nc, core.ap, core.sig, core.psum
    fold, zfold = Split(core, FOLD_KB, 16, DH), Split(core, ZFOLD_KB, 8, DH)
    hr, hs = core.view3(HR_KB, TT, DH), core.view3(HS_KB, TT, DH)
    hn = core.view(NYQ_KB, DH)
    with nc.Block() as block:
        @block.sync
        def _(sp):
            tables.load(sp, ap["c_fwd"], ap["c_fwd"])

        @block.tensor
        def _(pe):
            forward_pe(core, pe, tables, fold, 0, 8, "act_free")

        @block.scalar
        def _(act):
            for u in range(3):
                tables.high(act, u)
            for j in range(TT):
                for u in (2 * j + 3, 2 * j + 4):
                    if u < UNITS:
                        tables.high(act, u)
                act.wait_ge(S["aux_done"].sem, S["aux_done"].at(2 * j + 2))
                w = core.small[:, 5, 9:10] if j == 0 else core.small[:, 5, 8:9]
                nc.scalar.activation(hr[:, j, :], ps[:, (2 * j) % 8, :], ACT.Copy, scale=w)
                nc.scalar.activation(hs[:, j, :], ps[:, (2 * j + 1) % 8, :], ACT.Copy, scale=w).then_inc(S["act_free"].sem, 1)
                act.wait_ge(S["v_hi"].sem, S["v_hi"].at(j + 1))
                nc.scalar.activation(zfold.hi[:, j, :], zfold.raw[:, j, :], ACT.Copy).then_inc(S["w_hi"].sem, 1)

        @block.vector
        def _(dve):
            chain = Chain(dve, S["dve_chain"])
            for n in range(8):
                q, j = n // 4, n % 4
                a, b, out = hy[:, j, 0:DH], hy[:, 4 + j, 0:DH], zfold.raw[:, n, :]
                ins = nc.vector.tensor_tensor(out, a, b, ALU.subtract if q else ALU.add)
                if j == 0:
                    chain(ins)
                    ins = nc.vector.tensor_copy(out[0:1, :], (a if q else b)[0:1, :])
                ins.then_inc(S["v_hi"].sem, 1)
            dve.wait_ge(S["act_free"].sem, S["act_free"].at(1))
            chain(nc.vector.tensor_copy(hn, hr[:, 0, :]))
            chain(nc.vector.tensor_copy(hn[0:1, :], hs[0:1, 0, :]))
            nc.vector.memset(hs[0:1, 0, :], 0.0)
            for n in range(8):
                dve.wait_ge(S["w_hi"].sem, S["w_hi"].at(n + 1))
                nc.vector.tensor_tensor(zfold.lo[:, n, :], zfold.raw[:, n, :], zfold.hi_raw[:, n, :], ALU.subtract)

        @block.gpsimd
        def _(pool):
            for u in range(UNITS):
                tables.low(pool, u)
    tables.close()
    S["act_free"].close(TT)
    S["v_hi"].close(8)
    S["w_hi"].close(8)
    S["dve_chain"].close(4)


def phase_signal_spectrum(core, tables):
    nc, ap, S, ps = core.nc, core.ap, core.sig, core.psum
    zfold, y = Split(core, ZFOLD_KB, 8, DH), Split(core, FOLD_KB, 16, DH)
    hr, hs = core.view3(HR_KB, TT, DH), core.view3(HS_KB, TT, DH)
    hn = core.view(NYQ_KB, DH)
    yr, ys, cross = y.raw[:, 0:8, :], y.raw[:, 8:16, :], y.before
    with nc.Block() as block:
        @block.sync
        def _(sp):
            tables.load(sp, ap["c_fwd"], ap["c_inv"])

        @block.tensor
        def _(pe):
            forward_pe(core, pe, tables, zfold, 0, 0, "dve_done")

        @block.scalar
        def _(act):
            def rounded(j):
                act.wait_ge(S["pool_done"].sem, S["pool_done"].at(j + 1))
                nc.scalar.activation(y.hi[:, j, :], yr[:, j, :], ACT.Copy)
                nc.scalar.activation(y.hi[:, 8 + j, :], ys[:, j, :], ACT.Copy).then_inc(S["w_hi"].sem, 1)

            for u in range(4):
                tables.high(act, u)
            for j in range(TT):
                for u in (2 * j + 4, 2 * j + 5):
                    if u < UNITS:
                        tables.high(act, u)
                if j >= 1:
                    rounded(j - 1)
            rounded(TT - 1)

        @block.vector
        def _(dve):
            def low(j):
                dve.wait_ge(S["w_hi"].sem, S["w_hi"].at(j + 1))
                for n in (j, 8 + j):
                    nc.vector.tensor_tensor(y.lo[:, n, :], y.raw[:, n, :], y.hi_raw[:, n, :], ALU.subtract)

            for j in range(TT):
                dve.wait_ge(S["aux_done"].sem, S["aux_done"].at(2 * j + 2))
                xr, xs = ps[:, (2 * j) % 8, :], ps[:, (2 * j + 1) % 8, :]
                nc.vector.tensor_tensor(yr[:, j, :], xr, hr[:, j, :], ALU.mult)
                nc.vector.tensor_tensor(cross[:, j, :], xs, hs[:, j, :], ALU.mult)
                nc.vector.tensor_tensor(ys[:, j, :], xr, hs[:, j, :], ALU.mult)
                nc.vector.tensor_tensor(cross[:, 8 + j, :], xs, hn if j == 0 else hr[:, j, :], ALU.mult).then_inc(S["dve_done"].sem, 1)
                if j >= 1:
                    low(j - 1)
            low(TT - 1)

        @block.gpsimd
        def _(pool):
            for u in range(4):
                tables.low(pool, u)
            for j in range(TT):
                for u in (2 * j + 4, 2 * j + 5):
                    if u < UNITS:
                        tables.low(pool, u)
                pool.wait_ge(S["dve_done"].sem, S["dve_done"].at(j + 1))
                nc.gpsimd.tensor_tensor(yr[:, j, :], yr[:, j, :], cross[:, j, :], ALU.subtract)
                nc.gpsimd.tensor_tensor(ys[:, j, :], ys[:, j, :], cross[:, 8 + j, :], ALU.add).then_inc(S["pool_done"].sem, 1)
    tables.close()
    for n in ("dve_done", "pool_done", "w_hi"):
        S[n].close(TT)


def phase_inverse_gate(core, tables, hy, o):
    nc, ap, S, ps = core.nc, core.ap, core.sig, core.psum
    y = Split(core, FOLD_KB, 16, DH)
    mats = core.view_r(MATS_KB, 5, P)
    zs = core.view3(150, 4, DH)
    even = core.view3(158, 2, DH)
    both = core.view3(162, 4, DH)
    skip = core.view(170, DH)
    with nc.Block() as block:
        @block.sync
        def _(sp):
            sp.dma_start(skip, ap["hy_skip"][0, o].partition_broadcast(P)).then_inc(S["loaded"].sem, 16)
            tables.load(sp, ap["c_inv"], None)

        @block.tensor
        def _(pe):
            for j in range(4):
                even_bank, odd_bank, u = ps[:, 2 * j, :], ps[:, 2 * j + 1, :], 4 * j
                tables.products(pe, even_bank, u, y, 0, True, False).then_inc(S["aux_done"].sem, 1)
                exact(nc, even_bank, mats[:, ALT_ROW, :], y, 8)
                tables.products(pe, even_bank, u + 1, y, 12, False, True).then_inc(S["aux_done"].sem, 1)
                tables.products(pe, odd_bank, u + 2, y, 4, True, False).then_inc(S["aux_done"].sem, 1)
                if j == 0:
                    for k in range(4):
                        exact(nc, odd_bank, mats[:, ONE_COL, :], y, k)
                    exact(nc, odd_bank, mats[:, CORNER, :], y, 8)
                tables.products(pe, odd_bank, u + 3, y, 8, False, True).then_inc(S["aux_done"].sem, 1)

        @block.scalar
        def _(act):
            for u in range(4):
                tables.high(act, u)
            for j in range(4):
                for u in range(4 * j + 4, 4 * j + 6):
                    if u < UNITS:
                        tables.high(act, u)
                act.wait_ge(S["aux_done"].sem, S["aux_done"].at(4 * j + 2))
                if j >= 2:
                    act.wait_ge(S["dve_free"].sem, S["dve_free"].at(j - 1))
                nc.scalar.activation(even[:, j % 2, :], ps[:, 2 * j, :], ACT.Copy).then_inc(S["act_done"].sem, 1)
                for u in range(4 * j + 6, 4 * j + 8):
                    if u < UNITS:
                        tables.high(act, u)

        @block.gpsimd
        def _(pool):
            for u in range(4):
                tables.low(pool, u)
            pool.wait_ge(S["loaded"].sem, S["loaded"].at(16))
            for j in range(4):
                if j >= 2:
                    pool.wait_ge(S["dve_done"].sem, S["dve_done"].at(j - 1))
                for m in range(2):
                    nc.gpsimd.tensor_tensor(zs[:, 2 * (j % 2) + m, :], hy[:, j + 4 * m, 0:DH], skip, ALU.mult).then_inc(S["pool_done"].sem, 1)
                for u in range(4 * j + 4, 4 * j + 8):
                    if u < UNITS:
                        tables.low(pool, u)

        @block.vector
        def _(dve):
            chain = Chain(dve, S["dve_chain"])
            for j in range(4):
                dve.wait_ge(S["act_done"].sem, S["act_done"].at(j + 1))
                dve.wait_ge(S["aux_done"].sem, S["aux_done"].at(4 * j + 4))
                a, b = even[:, j % 2, :], ps[:, 2 * j + 1, :]
                out = both[:, 2 * (j % 2):2 * (j % 2) + 2, :]
                nc.vector.tensor_tensor(out[:, 0, :], a, b, ALU.add)
                ins = nc.vector.tensor_tensor(out[:, 1, :], a, b, ALU.subtract)
                if j == 0:
                    chain(ins)
                    nc.vector.tensor_copy(out[0:1, 0, :], b[0:1, :])
                    ins = nc.vector.tensor_copy(out[0:1, 1, :], a[0:1, :])
                ins.then_inc(S["dve_free"].sem, 1)
                dve.wait_ge(S["dve_free"].sem, S["dve_free"].at(j + 1))
                dve.wait_ge(S["pool_done"].sem, S["pool_done"].at(2 * j + 2))
                chain(nc.vector.tensor_tensor(out, out, zs[:, 2 * (j % 2):2 * (j % 2) + 2, :], ALU.add))
                for m in range(2):
                    t = j + 4 * m
                    ins = nc.vector.tensor_tensor(hy[:, t, 0:DH], out[:, m, :], hy[:, t, (o + 1) * DH:(o + 2) * DH], ALU.mult)
                ins.then_inc(S["dve_done"].sem, 1)
    tables.close()
    S["loaded"].close(16)
    for n in ("act_done", "dve_done", "dve_free"):
        S[n].close(4)
    S["pool_done"].close(8)
    S["dve_chain"].close(5)


def phase_group_norm(core, src, groups, dst, gain, scratch, mirrored=False, ahead=()):
    nc, S, ps = core.nc, core.sig, core.psum
    width = DH // groups
    sq = core.view3(scratch, 2, DH)
    ss = core.tiny2[:, 0:TT * groups]
    rstd = core.tiny2[:, 64:64 + TT * groups]
    reverse = core.view(scratch + 4, P)
    with nc.Block() as block:
        @block.sync
        def _(sp):
            if mirrored:
                sp.dma_start(reverse, core.ap["c_mats"][:, 0, :]).then_inc(S["loaded"].sem, 16)
            load_ahead(sp, ahead)

        @block.gpsimd
        def _(pool):
            for t in range(TT):
                if t >= 2:
                    pool.wait_ge(S["dve_done"].sem, S["dve_done"].at(t - 1))
                nc.gpsimd.tensor_tensor(sq[:, t % 2, :], src[:, t, :], src[:, t, :], ALU.mult).then_inc(S["pool_done"].sem, 1)

        @block.vector
        def _(dve):
            for t in range(TT):
                dve.wait_ge(S["pool_done"].sem, S["pool_done"].at(t + 1))
                nc.vector.reduce_sum(ss[:, t * groups:(t + 1) * groups], sq[:, t % 2, :].rearrange("p (g w) -> p g w", g=groups), AX.X).then_inc(S["dve_done"].sem, 1)
            dve.wait_ge(S["stat_ready"].sem, S["stat_ready"].at(1))
            nc.vector.reciprocal(rstd, rstd).then_inc(S["dve_chain"].sem, 1)
            dve.wait_ge(S["dve_chain"].sem, S["dve_chain"].at(1))
            for t in range(TT):
                v = src[:, t, :].rearrange("p (g w) -> p g w", g=groups)
                r = rstd[:, t * groups:(t + 1) * groups].unsqueeze(2).to_broadcast([P, groups, width])
                nc.vector.tensor_tensor(v, v, r, ALU.mult).then_inc(S["row_ready"].sem, 1)
            for t in range(TT):
                dve.wait_ge(S["tr_done"].sem, S["tr_done"].at(t + 1))
                g = gain.unsqueeze(2).to_broadcast([P, 4, P])
                ranges = [(0, t * P, P)]
                if mirrored and t == 4:
                    ranges = [(0, L - P + 1, P - 1), (P - 1, L // 2, 1)]
                elif mirrored and t > 4:
                    ranges = [(0, L - (t - 3) * P + 1, P)]
                for c, at, w in ranges:
                    nc.vector.tensor_tensor(dst[:, :, at:at + w], ps[:, t, :].rearrange("p (a b) -> p a b", a=4)[:, :, c:c + w], g[:, :, 0:w], ALU.mult)

        @block.scalar
        def _(act):
            act.wait_ge(S["dve_done"].sem, S["dve_done"].at(TT))
            nc.scalar.activation(rstd, ss, ACT.Sqrt, scale=1.0 / width, bias=core.eps).then_inc(S["stat_ready"].sem, 1)

        @block.tensor
        def _(pe):
            for t in range(TT):
                pe.wait_ge(S["row_ready"].sem, S["row_ready"].at(t + 1))
                flip = mirrored and t >= 4
                if flip and t == 4:
                    pe.wait_ge(S["loaded"].sem, S["loaded"].at(16))
                for j in range(4):
                    out, tile = ps[:, t, j * P:(j + 1) * P], src[:, t, j * P:(j + 1) * P]
                    last = nc.tensor.matmul(out, tile, reverse, start=True, stop=True) if flip else nc.tensor.transpose(out, tile, core.ident)
                last.then_inc(S["tr_done"].sem, 1)
    for n in ("pool_done", "dve_done", "row_ready", "tr_done"):
        S[n].close(TT)
    S["stat_ready"].close(1)
    S["dve_chain"].close(1)
    if mirrored:
        S["loaded"].close(16)
QKT_KB, V_KB, O_KB, IG_KB, FG_KB = 70, 102, 119, 135, 139
MT_KB, ACOL_KB, EM_KB = 169, 178, 180
QK_RING_KB, VO_KB = 159, (143, 159, 175)
VW = 132


def phase_qk_proj(core, xt, w, ahead):
    nc, S, ps = core.nc, core.sig, core.psum
    qkt = core.view3(QKT_KB, 8, L)
    ring = weight_tiles(core, QK_RING_KB)
    wv = w.rearrange("a (k p) n -> p (a k) n", p=P)
    ld = [S["loaded%d" % s] for s in range(4)]
    pair = lambda n: ps[:, 2 * (n % 4):2 * (n % 4) + 2, :].rearrange("p a b -> p (a b)")
    with nc.Block() as block:
        @block.sync
        def _(sp):
            for n in range(4, 8):
                sp.wait_ge(S["mm_done"].sem, S["mm_done"].at(n - 3))
                sp.dma_start(ring[n % 4].raw, wv[:, :, HY_COLS + n * P:HY_COLS + (n + 1) * P]).then_inc(ld[n % 4].sem, 16)
            sp.wait_ge(S["mm_done"].sem, S["mm_done"].at(5))
            load_ahead(sp, ahead)

        @block.tensor
        def _(pe):
            for n in range(8):
                pe.wait_ge(S["w_lo"].sem, S["w_lo"].at(n + 1))
                if n >= 4:
                    pe.wait_ge(S["dve_done"].sem, S["dve_done"].at(n - 3))
                for half in range(2):
                    last = mm3_cols(nc, ps[:, 2 * (n % 4) + half, :], ring[n % 4], slice(0, P), xt, half * BANK, (half + 1) * BANK)
                last.then_inc(S["mm_done"].sem, 1)

        @block.scalar
        def _(act):
            def weights(n):
                act.wait_ge(ld[n % 4].sem, ld[n % 4].at(16 * (n // 4 + 1)))
                nc.scalar.activation(ring[n % 4].hi, ring[n % 4].raw, ACT.Copy).then_inc(S["w_hi"].sem, 1)

            weights(0)
            weights(1)
            for n in range(8):
                if n + 2 < 8:
                    weights(n + 2)
                act.wait_ge(S["mm_done"].sem, S["mm_done"].at(n + 1))
                nc.scalar.activation(qkt[:, n, :], pair(n), ACT.Identity, scale=core.colsA[:, CW_ML + 8 + n:CW_ML + 9 + n],
                                     bias=core.colsA[:, CB_ML + n:CB_ML + n + 1]).then_inc(S["act_done"].sem, 1)
                act.wait_ge(S["dve_done"].sem, S["dve_done"].at(n + 1))
                nc.scalar.activation(qkt[:, n, :], qkt[:, n, :], ACT.Silu)

        @block.vector
        def _(dve):
            chain = Chain(dve, S["dve_chain"])

            def weights(n):
                dve.wait_ge(S["w_hi"].sem, S["w_hi"].at(n + 1))
                nc.vector.tensor_tensor(ring[n % 4].lo, ring[n % 4].raw, ring[n % 4].hi_raw, ALU.subtract).then_inc(S["w_lo"].sem, 1)

            weights(0)
            weights(1)
            for n in range(8):
                if n + 2 < 8:
                    weights(n + 2)
                dve.wait_ge(S["act_done"].sem, S["act_done"].at(n + 1))
                pr, t = pair(n), qkt[:, n, :]
                chain(nc.vector.scalar_tensor_tensor(out=t[:, 1:L], in0=pr[:, 0:L - 1], scalar=core.colsA[:, CW_ML + n:CW_ML + n + 1],
                                                     in1=t[:, 1:L], op0=ALU.mult, op1=ALU.add))
                nc.vector.scalar_tensor_tensor(out=t[:, 0:L - 1], in0=pr[:, 1:L], scalar=core.colsA[:, CW_ML + 16 + n:CW_ML + 17 + n],
                                               in1=t[:, 0:L - 1], op0=ALU.mult, op1=ALU.add).then_inc(S["dve_done"].sem, 1)
    for n in ("mm_done", "dve_done", "act_done", "dve_chain", "w_hi", "w_lo"):
        S[n].close(8)
    for s in range(4):
        ld[s].close(32)


def phase_gates(core, xt, w):
    nc, ap, S, ps = core.nc, core.ap, core.sig, core.psum
    gw = Split(core, 175, KT, P)
    gb = core.tiny[0:64, 16:18]
    gates = [core.view(IG_KB, L, 64), core.view(FG_KB, L, 64)]
    wv = w.rearrange("a (k p) n -> p (a k) n", p=P)
    base = HY_COLS + 2048
    with nc.Block() as block:
        @block.gpsimd
        def _(pool):
            nc.gpsimd.memset(gw.raw, 0.0)
            nc.gpsimd.memset(gb, 0.0).then_inc(S["pool_done"].sem, 1)

        @block.sync
        def _(sp):
            sp.wait_ge(S["pool_done"].sem, S["pool_done"].at(1))
            with nc.allow_non_contiguous_dma("sixteen gate columns"):
                for kind in range(2):
                    for way in range(2):
                        c = 8 * way + 4 * kind
                        at = 64 * kind + 32 * way
                        sp.dma_start(gw.raw[:, :, at:at + 4], wv[:, :, base + c:base + c + 4]).then_inc(S["loaded2"].sem, 16)
                        sp.dma_start(gb[32 * way:32 * way + 4, kind:kind + 1], ap["ml_gate_b"].rearrange("a c -> c a")[c:c + 4, :]).then_inc(S["loaded2"].sem, 16)

        @block.scalar
        def _(act):
            act.wait_ge(S["loaded2"].sem, S["loaded2"].at(16 * 8))
            nc.scalar.activation(gw.hi, gw.raw, ACT.Copy).then_inc(S["w_hi"].sem, 1)

        @block.tensor
        def _(pe):
            pe.wait_ge(S["w_lo"].sem, S["w_lo"].at(1))
            for half in range(2):
                last = mm3_cols(nc, ps[:, half, :], gw, slice(0, P), xt, half * BANK, (half + 1) * BANK)
            last.then_inc(S["mm_done"].sem, 1)

        @block.vector
        def _(dve):
            dve.wait_ge(S["w_hi"].sem, S["w_hi"].at(1))
            nc.vector.tensor_tensor(gw.lo, gw.raw, gw.hi_raw, ALU.subtract).then_inc(S["w_lo"].sem, 1)
            dve.wait_ge(S["mm_done"].sem, S["mm_done"].at(1))
            for kind in range(2):
                nc.vector.tensor_scalar(gates[kind], ps[64 * kind:64 * kind + 64, 0:2, :].rearrange("p a b -> p (a b)"), gb[:, kind:kind + 1], None, ALU.add)
    S["pool_done"].close(1)
    S["loaded2"].close(16 * 8)
    for n in ("w_hi", "w_lo", "mm_done"):
        S[n].close(1)


def phase_rows_proj(core, chunks, slots, before=None, beside=None, ahead=0):
    nc, S, ps = core.nc, core.sig, core.psum
    KH = KT // 2
    pieces = [(c, kh) for c in range(len(chunks)) for kh in range(2)]
    ring = [Split(core, kb, KH, BANK) for kb in slots]
    R = len(ring)
    n_rows = [lhs.hi.shape[2] // P for _, lhs, _, _ in chunks]
    done = [sum(2 * r for r in n_rows[:c]) for c in range(len(chunks) + 1)]
    units = [sum(n_rows[:c]) for c in range(len(chunks) + 1)]
    ld = [S["loaded%d" % s] for s in range(R)]
    after = [done[c] + (kh + 1) * n_rows[c] for c, kh in pieces]
    with nc.Block() as block:
        if before is not None:
            before(block)

        @block.sync
        def _(sp):
            for p, (c, kh) in enumerate(pieces):
                if p < ahead:
                    continue
                if p >= R:
                    sp.wait_ge(S["mm_done"].sem, S["mm_done"].at(after[p - R]))
                w = chunks[c][0]
                sp.dma_start(ring[p % R].raw[:, :, 0:w.shape[2]], w[:, kh * KH:(kh + 1) * KH, :]).then_inc(ld[p % R].sem, 16)

        @block.tensor
        def _(pe):
            for p, (c, kh) in enumerate(pieces):
                w, lhs, out, func = chunks[c]
                cols = w.shape[2]
                pe.wait_ge(S["w_lo"].sem, S["w_lo"].at(p + 1))
                for t in range(n_rows[c]):
                    u = units[c] + t
                    if kh == 0 and u >= 8:
                        pe.wait_ge(S["act_free"].sem, S["act_free"].at(u - 7))
                    for k in range(KH):
                        kk = kh * KH + k
                        lt = slice(t * P, (t + 1) * P)
                        last = mm3(nc, ps[:, u % 8, 0:cols], lhs.hi[:, kk, lt], lhs.lo[:, kk, lt], ring[p % R].hi[:, k, 0:cols], ring[p % R].lo[:, k, 0:cols],
                                   kk == 0, kk == KT - 1)
                    last.then_inc(S["mm_done"].sem, 1)

        @block.scalar
        def _(act):
            def weights(p):
                act.wait_ge(ld[p % R].sem, ld[p % R].at(16 * (p // R + 1)))
                cols = chunks[pieces[p][0]][0].shape[2]
                nc.scalar.activation(ring[p % R].hi[:, :, 0:cols], ring[p % R].raw[:, :, 0:cols], ACT.Copy).then_inc(S["w_hi"].sem, 1)

            made = 0
            while made < min(R, len(pieces)):
                weights(made)
                made += 1
            for p, (c, kh) in enumerate(pieces):
                if made < len(pieces) and p >= 1:
                    weights(made)
                    made += 1
                if kh == 1:
                    w, lhs, out, func = chunks[c]
                    for t in range(n_rows[c]):
                        act.wait_ge(S["mm_done"].sem, S["mm_done"].at(done[c] + n_rows[c] + t + 1))
                        dst = out(t)
                        src = ps[:, (units[c] + t) % 8, w.shape[2] - int(np.prod(dst.shape[1:])):w.shape[2]]
                        if len(dst.shape) == 3:
                            src = src.rearrange("p (h c) -> p h c", h=dst.shape[1])
                        nc.scalar.activation(dst, src, func).then_inc(S["act_free"].sem, 1)

        @block.vector
        def _(dve):
            for p, (c, kh) in enumerate(pieces):
                cols = chunks[c][0].shape[2]
                dve.wait_ge(S["w_hi"].sem, S["w_hi"].at(p + 1))
                r = ring[p % R]
                nc.vector.tensor_tensor(r.lo[:, :, 0:cols], r.raw[:, :, 0:cols], r.hi_raw[:, :, 0:cols], ALU.subtract).then_inc(S["w_lo"].sem, 1)
                if beside is not None:
                    beside(dve)
    for s in range(R):
        ld[s].close(16 * len(range(s, len(pieces), R)))
    S["mm_done"].close(done[-1])
    S["act_free"].close(units[-1])
    S["w_hi"].close(len(pieces))
    S["w_lo"].close(len(pieces))


def first_pieces(core, slots, w, count=2):
    KH = KT // 2
    return [(Split(core, slots[kh], KH, BANK).raw[:, :, 0:w.shape[2]], w[:, kh * KH:(kh + 1) * KH, :], core.sig["loaded%d" % kh]) for kh in range(count)]


def phase_vo(core, xt, w):
    nc = core.nc
    v = core.view(V_KB, TT * 4 * VW).rearrange("p (t h c) -> p t h c", t=TT, h=4)
    og = core.view3(O_KB, TT, DH)
    wv = w.rearrange("a (k p) n -> p (a k) n", p=P)
    base = HY_COLS + 1024

    def ones(block):
        @block.gpsimd
        def _(pool):
            nc.gpsimd.memset(v[:, :, :, P:P + 1], 1.0)

    phase_rows_proj(core, [(wv[:, :, base:base + DH], xt, lambda t: v[:, t, :, 0:P], ACT.Copy),
                           (wv[:, :, base + DH:base + 2 * DH], xt, lambda t: og[:, t, :], ACT.Sigmoid)], VO_KB, before=ones, ahead=1)


def phase_gate_scans(core):
    nc, S, ps = core.nc, core.sig, core.psum
    ig, fg = core.view(IG_KB, L, 64), core.view(FG_KB, L, 64)
    t1, cum = core.view(143, L, 64), core.view(147, L, 64)
    mx, m = core.view(MT_KB, L, 64), core.view(155, L, 64)
    acol, em = core.view3(ACOL_KB, TT, 64), core.view3(EM_KB, TT, 64)
    one = core.small[:, 5, 10:11]
    with nc.Block() as block:
        @block.scalar
        def _(act):
            chain = Chain(act, S["act_chain"])
            chain(nc.scalar.activation(t1, fg, ACT.Abs))
            chain(nc.scalar.activation(t1, t1, ACT.Exp, scale=-1.0))
            nc.scalar.activation(t1, t1, ACT.Ln, bias=one[0:64, :]).then_inc(S["act_done"].sem, 1)
            act.wait_ge(S["tr_done"].sem, S["tr_done"].at(1))
            nc.scalar.activation(em, ps[:, 1, :].rearrange("p (a b) -> p a b", a=TT), ACT.Exp, scale=-1.0)

        @block.vector
        def _(dve):
            chain = Chain(dve, S["dve_chain"])
            dve.wait_ge(S["act_done"].sem, S["act_done"].at(1))
            chain(nc.vector.scalar_tensor_tensor(out=fg, in0=fg, scalar=0.0, in1=t1, op0=ALU.min, op1=ALU.subtract))
            for way in range(2):
                rows = slice(32 * way, 32 * way + 32)
                step = slice(None, None, -1) if way else slice(None)
                ones = one[rows, :].to_broadcast([32, L])
                chain(nc.vector.tensor_tensor_scan(cum[rows, step], ones, fg[rows, step], 0.0, ALU.mult, ALU.add))
            chain(nc.vector.tensor_tensor(ig, ig, cum, ALU.subtract))
            for way in range(2):
                rows = slice(32 * way, 32 * way + 32)
                step = slice(None, None, -1) if way else slice(None)
                chain(nc.vector.tensor_tensor_scan(mx[rows, step], ig[rows, step], ig[rows, step], 0.0, ALU.max, ALU.max))
            nc.vector.tensor_tensor(m, cum, mx, ALU.add).then_inc(S["dve_done"].sem, 1)
            dve.wait_ge(S["tr_done"].sem, S["tr_done"].at(1))
            nc.vector.tensor_copy(acol, ps[:, 0, :].rearrange("p (a b) -> p a b", a=TT))

        @block.tensor
        def _(pe):
            pe.wait_ge(S["dve_done"].sem, S["dve_done"].at(1))
            for n, src in ((0, ig), (1, m)):
                for t in range(TT):
                    last = nc.tensor.transpose(ps[:, n, t * 64:(t + 1) * 64], src[:, t * P:(t + 1) * P], core.ident[0:64, 0:64])
            last.then_inc(S["tr_done"].sem, 1)
    S["act_chain"].close(2)
    S["act_done"].close(1)
    S["dve_chain"].close(6)
    S["dve_done"].close(1)
    S["tr_done"].close(1)


def phase_mlstm(core):
    nc, ap, S, ps = core.nc, core.ap, core.sig, core.psum
    qkt = core.view3(QKT_KB, 8, L)
    v = core.view(V_KB, TT * 4 * VW).rearrange("p (t h c) -> p t h c", t=TT, h=4)
    og = core.view3(O_KB, TT, DH)
    mx = core.view(MT_KB, L, 64)
    acol, em = core.view3(ACOL_KB, TT, 64), core.view3(EM_KB, TT, 64)
    pt = [[core.view3(42, 36, P), core.view3(143, 36, P)], [core.view3(6, 36, P), core.view3(24, 36, P)]]
    nmb = [core.view3(60, 2, L), core.view3(161, 2, L)]
    dg = core.view3(68, 4, P)
    sel = core.view3(173, 8, P, 64)
    hsum = core.view3(177, 2, P)
    r2 = core.tiny2[:, 128:144].rearrange("p (a b) -> p a b", b=2)
    first = [[sum(TT - i for i in range(j)) for j in range(TT)], [sum(i + 1 for i in range(j)) for j in range(TT)]]
    scale = float(P) ** -0.5
    NH = NH_ML
    with nc.Block() as block:
        @block.sync
        def _(sp):
            sp.dma_start(sel, ap["c_sel"]).then_inc(S["loaded"].sem, 16)

        @block.tensor
        def _(pe):
            pe.wait_ge(S["loaded"].sem, S["loaded"].at(16))

            def spread(h):
                for way in range(2):
                    if 2 * h + way >= 1:
                        pe.wait_ge(S["act_free"].sem, S["act_free"].at(2 * h + way))
                    for half in range(2):
                        last = nc.tensor.matmul(ps[:, half, :], sel[:, 4 * way + h, :], mx[:, half * BANK:(half + 1) * BANK], start=True, stop=True)
                    last.then_inc(S["aux_done"].sem, 1)

            def scores(h, j):
                n = TT * h + j
                if n >= 2:
                    pe.wait_ge(S["dve_done"].sem, S["dve_done"].at(n - 1))
                for half in range(2):
                    last = nc.tensor.matmul(ps[:, 2 + 2 * (n % 2) + half, :], qkt[:, 4 + h, j * P:(j + 1) * P], qkt[:, h, half * BANK:(half + 1) * BANK],
                                            start=True, stop=True)
                last.then_inc(S["mm_done"].sem, 1)

            def values(h, t):
                n = TT * h + t
                pe.wait_ge(S["dve_done"].sem, S["dve_done"].at(TT * (h + 1)))
                if n >= 2:
                    pe.wait_ge(S["dve_free"].sem, S["dve_free"].at(n - 1))
                for way in range(2):
                    js = range(t + 1) if way == 0 else range(t, TT)
                    for j in js:
                        at = first[way][j] + (t - j if way == 0 else t)
                        last = nc.tensor.matmul(ps[:, 6 + n % 2, way * VW:way * VW + P + 1], pt[h % 2][way][:, at, :], v[:, j, h, 0:P + 1],
                                                start=j == js[0], stop=j == js[-1])
                last.then_inc(S["aux2_done"].sem, 1)

            spread(0)
            for h in range(NH + 1):
                for j in range(TT):
                    if h < NH:
                        scores(h, j)
                    if h >= 1:
                        values(h - 1, j)
                if h + 1 < NH:
                    spread(h + 1)

        @block.scalar
        def _(act):
            for h in range(NH):
                for way in range(2):
                    act.wait_ge(S["aux_done"].sem, S["aux_done"].at(2 * h + way + 1))
                    nc.scalar.activation(nmb[h % 2][:, way, :], ps[:, 0:2, :].rearrange("p a b -> p (a b)"), ACT.Copy, scale=-1.0).then_inc(S["act_free"].sem, 1)
                if h >= 2:
                    act.wait_ge(S["aux2_done"].sem, S["aux2_done"].at(TT * (h - 1)))
                act.wait_ge(S["act_free"].sem, S["act_free"].at(2 * h + 2))
                for j in range(TT):
                    n = TT * h + j
                    for way in range(2):
                        a = acol[:, j, 32 * way + h:32 * way + h + 1]
                        p = pt[h % 2][way]
                        f = first[way][j]
                        off = (f + 1, f + TT - j, (j + 1) * P, L) if way == 0 else (f, f + j, 0, j * P)
                        if off[1] > off[0]:
                            nc.scalar.activation(p[:, off[0]:off[1], :].rearrange("p a b -> p (a b)"), nmb[h % 2][:, way, off[2]:off[3]], ACT.Exp, bias=a)
                    act.wait_ge(S["row_ready"].sem, S["row_ready"].at(n + 1))
                    for way in range(2):
                        at = first[way][j] + (0 if way == 0 else j)
                        last = nc.scalar.activation(pt[h % 2][way][:, at, :], dg[:, 2 * (n % 2) + way, :], ACT.Exp)
                    last.then_inc(S["act_done"].sem, 1)

        @block.vector
        def _(dve):
            chain = Chain(dve, S["dve_chain"])

            def diagonal(h, j):
                n = TT * h + j
                if n >= 2:
                    dve.wait_ge(S["act_done"].sem, S["act_done"].at(n - 1))
                dve.wait_ge(S["act_free"].sem, S["act_free"].at(2 * h + 2))
                for way in range(2):
                    last = nc.vector.scalar_tensor_tensor(out=dg[:, 2 * (n % 2) + way, :], in0=nmb[h % 2][:, way, j * P:(j + 1) * P],
                                                          scalar=acol[:, j, 32 * way + h:32 * way + h + 1], in1=core.small[:, 3 + way, :],
                                                          op0=ALU.add, op1=ALU.add)
                last.then_inc(S["row_ready"].sem, 1)

            def weigh(h, j):
                n = TT * h + j
                dve.wait_ge(S["act_done"].sem, S["act_done"].at(n + 1))
                dve.wait_ge(S["mm_done"].sem, S["mm_done"].at(n + 1))
                sc = ps[:, 2 + 2 * (n % 2):4 + 2 * (n % 2), :].rearrange("p a b -> p (a b)")
                for way in range(2):
                    f = first[way][j]
                    lo, hi, a, b = (f, f + TT - j, j * P, L) if way == 0 else (f, f + j + 1, 0, (j + 1) * P)
                    w = pt[h % 2][way][:, lo:hi, :].rearrange("p a b -> p (a b)")
                    last = nc.vector.scalar_tensor_tensor(out=w, in0=sc[:, a:b], scalar=scale, in1=w, op0=ALU.mult, op1=ALU.mult)
                last.then_inc(S["dve_done"].sem, 1)

            def finish(h, t):
                n = TT * h + t
                dve.wait_ge(S["aux2_done"].sem, S["aux2_done"].at(n + 1))
                out = ps[:, 6 + n % 2, 0:2 * VW].rearrange("p (a b) -> p a b", a=2)
                r = r2[:, n % 8, :]
                den = out[:, :, P]
                chain(nc.vector.scalar_tensor_tensor(out=r, in0=den, scalar=-1.0, in1=em[:, t, h:h + 33:32], op0=ALU.mult, op1=ALU.max))
                chain(nc.vector.tensor_tensor(r, den, r, ALU.max))
                chain(nc.vector.reciprocal(r, r))
                hs = hsum[:, n % 2, :]
                chain(nc.vector.tensor_scalar(hs, out[:, 0, 0:P], r[:, 0:1], None, ALU.mult))
                ins = nc.vector.scalar_tensor_tensor(out=hs, in0=out[:, 1, 0:P], scalar=r[:, 1:2], in1=hs, op0=ALU.mult, op1=ALU.add)
                ins.then_inc(S["dve_free"].sem, 1)
                dve.wait_ge(S["dve_free"].sem, S["dve_free"].at(n + 1))
                o = og[:, t, h * P:(h + 1) * P]
                nc.vector.tensor_tensor(o, hs, o, ALU.mult)

            diagonal(0, 0)
            for h in range(NH + 1):
                for j in range(TT):
                    if h < NH:
                        n = TT * h + j + 1
                        if n < TT * NH:
                            diagonal(n // TT, n % TT)
                        weigh(h, j)
                    if h >= 1:
                        finish(h - 1, j)
    S["loaded"].close(16)
    S["aux_done"].close(2 * NH)
    S["act_free"].close(2 * NH)
    for n in ("mm_done", "act_done", "row_ready", "dve_done", "dve_free", "aux2_done"):
        S[n].close(TT * NH)
    S["dve_chain"].close(4 * TT * NH)
H_KB = 70


def phase_rows_gemm(core, lhs, w, h, gate=None, residual=None, ring_kb=(102, 118, 134), tmp_kb=None, ahead=0):
    nc, S, ps = core.nc, core.sig, core.psum
    KH = KT // 2
    ring = [Split(core, kb, KH, BANK) for kb in ring_kb]
    R = len(ring)
    wv = w.rearrange("a (k p) n -> p (a k) n", p=P)
    ld = [S["loaded%d" % s] for s in range(R)]
    with nc.Block() as block:
        @block.sync
        def _(sp):
            for p in range(4):
                c, kh = p // 2, p % 2
                if p >= R:
                    sp.wait_ge(S["mm_done"].sem, S["mm_done"].at(TT * (p - R + 1)))
                if p >= ahead:
                    sp.dma_start(ring[p % R].raw, wv[:, kh * KH:(kh + 1) * KH, c * BANK:(c + 1) * BANK]).then_inc(ld[p % R].sem, 16)
                if p == R - 1 and residual is not None:
                    sp.dma_start(h, residual.rearrange("a (t p) d -> p (a t) d", p=P)).then_inc(S["x_ready"].sem, 16)

        @block.tensor
        def _(pe):
            for p in range(4):
                c, kh = p // 2, p % 2
                pe.wait_ge(S["w_lo"].sem, S["w_lo"].at(p + 1))
                for t in range(TT):
                    if c == 1 and kh == 0:
                        pe.wait_ge(S["dve_free"].sem, S["dve_free"].at(t + 1))
                    lt = slice(t * P, (t + 1) * P)
                    for k in range(KH):
                        kk = kh * KH + k
                        last = mm3(nc, ps[:, t, :], lhs.hi[:, kk, lt], lhs.lo[:, kk, lt], ring[p % R].hi[:, k, :], ring[p % R].lo[:, k, :], kk == 0, kk == KT - 1)
                    last.then_inc(S["mm_done"].sem, 1)

        @block.scalar
        def _(act):
            for p in range(4):
                act.wait_ge(ld[p % R].sem, ld[p % R].at(16 * (p // R + 1)))
                nc.scalar.activation(ring[p % R].hi, ring[p % R].raw, ACT.Copy).then_inc(S["w_hi"].sem, 1)

        @block.vector
        def _(dve):
            for p in range(4):
                dve.wait_ge(S["w_hi"].sem, S["w_hi"].at(p + 1))
                nc.vector.tensor_tensor(ring[p % R].lo, ring[p % R].raw, ring[p % R].hi_raw, ALU.subtract).then_inc(S["w_lo"].sem, 1)
            if residual is not None:
                dve.wait_ge(S["x_ready"].sem, S["x_ready"].at(16))
            for u in range(2 * TT):
                c, t = u // TT, u % TT
                dve.wait_ge(S["mm_done"].sem, S["mm_done"].at(TT * (2 * c + 1) + t + 1))
                hv = h[:, t, c * BANK:(c + 1) * BANK]
                if gate is None:
                    nc.vector.tensor_tensor(hv, ps[:, t, :], hv, ALU.add).then_inc(S["dve_free"].sem, 1)
                else:
                    tmp = core.view3(tmp_kb, 2, BANK)[:, u % 2, :]
                    if u >= 2:
                        dve.wait_ge(S["pool_done"].sem, S["pool_done"].at(u - 1))
                    nc.vector.tensor_tensor(tmp, ps[:, t, :], gate[:, c * BANK:(c + 1) * BANK], ALU.mult).then_inc(S["dve_free"].sem, 1)

        @block.gpsimd
        def _(pool):
            if gate is not None:
                if residual is not None:
                    pool.wait_ge(S["x_ready"].sem, S["x_ready"].at(16))
                for u in range(2 * TT):
                    c, t = u // TT, u % TT
                    pool.wait_ge(S["dve_free"].sem, S["dve_free"].at(u + 1))
                    hv = h[:, t, c * BANK:(c + 1) * BANK]
                    nc.gpsimd.tensor_tensor(hv, core.view3(tmp_kb, 2, BANK)[:, u % 2, :], hv, ALU.add).then_inc(S["pool_done"].sem, 1)
    for s in range(R):
        ld[s].close(16 * len(range(s, 4, R)))
    if residual is not None:
        S["x_ready"].close(16)
    S["w_hi"].close(4)
    S["w_lo"].close(4)
    S["mm_done"].close(4 * TT)
    S["dve_free"].close(2 * TT)
    if gate is not None:
        S["pool_done"].close(2 * TT)


def phase_cols_gemm(core, tiles, ring_kb, beside=None, ahead=0):
    nc, S, ps = core.nc, core.sig, core.psum
    ring = [Split(core, kb, KT, P) for kb in ring_kb] if isinstance(ring_kb, tuple) else weight_tiles(core, ring_kb)
    n_tiles = len(tiles)
    ld = [S["loaded%d" % s] for s in range(4)]
    arrived, count = [], [0] * 4
    for n, (parts, _, _) in enumerate(tiles):
        count[n % 4] += 16 * len(parts)
        arrived.append(count[n % 4])
    with nc.Block() as block:
        @block.sync
        def _(sp):
            for n, (parts, xt, out) in enumerate(tiles):
                if n >= 4:
                    sp.wait_ge(S["mm_done"].sem, S["mm_done"].at(n - 3))
                at = 0
                if n < ahead:
                    continue
                for w in parts:
                    sp.dma_start(ring[n % 4].raw[:, :, at:at + w.shape[2]], w).then_inc(ld[n % 4].sem, 16)
                    at += w.shape[2]

        @block.tensor
        def _(pe):
            for n, (parts, xt, out) in enumerate(tiles):
                pe.wait_ge(S["w_lo"].sem, S["w_lo"].at(n + 1))
                if n >= 4:
                    pe.wait_ge(S["act_free"].sem, S["act_free"].at(n - 3))
                width = xt.hi.shape[2]
                for a in range(0, width, BANK):
                    b = min(a + BANK, width)
                    last = mm3_cols(nc, ps[:, 2 * (n % 4) + a // BANK, 0:b - a], ring[n % 4], slice(0, P), xt, a, b)
                last.then_inc(S["mm_done"].sem, 1)

        @block.scalar
        def _(act):
            def weights(n):
                act.wait_ge(ld[n % 4].sem, ld[n % 4].at(arrived[n]))
                nc.scalar.activation(ring[n % 4].hi, ring[n % 4].raw, ACT.Copy).then_inc(S["w_hi"].sem, 1)

            weights(0)
            weights(1)
            for n, (parts, xt, out) in enumerate(tiles):
                if n + 2 < n_tiles:
                    weights(n + 2)
                act.wait_ge(S["mm_done"].sem, S["mm_done"].at(n + 1))
                src = ps[:, 2 * (n % 4):2 * (n % 4) + 2, :].rearrange("p a b -> p (a b)")[:, 0:out.shape[1]]
                nc.scalar.activation(out, src, ACT.Copy).then_inc(S["act_free"].sem, 1)

        @block.vector
        def _(dve):
            for n in range(n_tiles):
                dve.wait_ge(S["w_hi"].sem, S["w_hi"].at(n + 1))
                nc.vector.tensor_tensor(ring[n % 4].lo, ring[n % 4].raw, ring[n % 4].hi_raw, ALU.subtract).then_inc(S["w_lo"].sem, 1)
                if beside is not None:
                    beside(dve)
    for n in ("mm_done", "act_free", "w_hi", "w_lo"):
        S[n].close(n_tiles)
    for s in range(4):
        ld[s].close(count[s])


def phase_cross_attention(core, qt, kt, v, ot, scratch, ahead):
    nc, S, ps = core.nc, core.sig, core.psum
    scale = float(NMEM) ** -0.5
    prob = [core.view3(scratch + 4 * s, 4, NMEM) for s in range(2)]
    probt = [core.view3(scratch + 8 + 4 * s, 2, BANK) for s in range(2)]
    mx, rs = core.tiny2[:, 0:64].rearrange("p (a b) -> p a b", b=8), core.tiny2[:, 64:128].rearrange("p (a b) -> p a b", b=8)
    groups = [(h, half) for h in range(4) for half in range(2)]
    G = len(groups)
    sbank = lambda g: ps[:, 2 * (g % 2):2 * (g % 2) + 2, :].rearrange("p a (b c) -> p (a b) c", c=NMEM)
    with nc.Block() as block:
        @block.sync
        def _(sp):
            load_ahead(sp, ahead)

        @block.tensor
        def _(pe):
            def scores(g):
                h, half = groups[g]
                if g >= 2:
                    pe.wait_ge(S["act_done"].sem, S["act_done"].at(g - 1))
                for i in range(4):
                    t = 4 * half + i
                    for c in range(2):
                        last = nc.tensor.matmul(sbank(g)[:, i, :], qt[:, 2 * h + c, t * P:(t + 1) * P], kt[:, 2 * h + c, :], start=c == 0, stop=c == 1)
                last.then_inc(S["mm_done"].sem, 1)

            def transposes(g):
                pe.wait_ge(S["dve_done"].sem, S["dve_done"].at(g + 1))
                if g >= 1:
                    pe.wait_ge(S["dve_free"].sem, S["dve_free"].at(g))
                for m in range(2):
                    for i in range(4):
                        last = nc.tensor.transpose(ps[:, 4 + m, i * P:(i + 1) * P], prob[g % 2][:, i, m * P:(m + 1) * P], core.ident)
                last.then_inc(S["tr_done"].sem, 1)

            def values(g):
                h, half = groups[g]
                pe.wait_ge(S["dve_free"].sem, S["dve_free"].at(g + 1))
                if g >= 1:
                    pe.wait_ge(S["act_free"].sem, S["act_free"].at(g))
                for e in range(2):
                    for m in range(2):
                        last = nc.tensor.matmul(ps[:, 6 + e, :], v[:, m, h * 256 + e * P:h * 256 + (e + 1) * P], probt[g % 2][:, m, :], start=m == 0, stop=m == 1)
                last.then_inc(S["aux_done"].sem, 1)

            scores(0)
            scores(1)
            for g in range(G + 1):
                if g < G:
                    transposes(g)
                if g + 2 < G:
                    scores(g + 2)
                if g >= 1:
                    values(g - 1)

        @block.vector
        def _(dve):
            chain = Chain(dve, S["dve_chain"])

            def maxima(g):
                dve.wait_ge(S["mm_done"].sem, S["mm_done"].at(g + 1))
                chain(nc.vector.reduce_max(mx[:, g, 0:4], sbank(g), AX.X))
                nc.vector.tensor_scalar(mx[:, g, 4:8], mx[:, g, 0:4], -scale, None, ALU.mult).then_inc(S["stat_ready"].sem, 1)

            maxima(0)
            for g in range(G):
                if g + 1 < G:
                    maxima(g + 1)
                dve.wait_ge(S["act_done"].sem, S["act_done"].at(g + 1))
                chain(nc.vector.reciprocal(rs[:, g, 4:8], rs[:, g, 0:4]))
                nc.vector.tensor_tensor(prob[g % 2], prob[g % 2], rs[:, g, 4:8].unsqueeze(2).to_broadcast([P, 4, NMEM]), ALU.mult).then_inc(S["dve_done"].sem, 1)
                dve.wait_ge(S["tr_done"].sem, S["tr_done"].at(g + 1))
                if g >= 2:
                    dve.wait_ge(S["aux_done"].sem, S["aux_done"].at(g - 1))
                nc.vector.tensor_copy(probt[g % 2], ps[:, 4:6, :]).then_inc(S["dve_free"].sem, 1)

        @block.scalar
        def _(act):
            def outputs(g):
                h, half = groups[g]
                act.wait_ge(S["aux_done"].sem, S["aux_done"].at(g + 1))
                nc.scalar.activation(ot[:, 2 * h:2 * h + 2, half * BANK:(half + 1) * BANK], ps[:, 6:8, :], ACT.Copy).then_inc(S["act_free"].sem, 1)

            for g, (h, half) in enumerate(groups):
                act.wait_ge(S["stat_ready"].sem, S["stat_ready"].at(g + 1))
                if g >= 2:
                    act.wait_ge(S["tr_done"].sem, S["tr_done"].at(g - 1))
                for i in range(4):
                    last = nc.scalar.activation(prob[g % 2][:, i, :], sbank(g)[:, i, :], ACT.Exp, scale=scale, bias=mx[:, g, 4 + i:5 + i], accum_out=rs[:, g, i:i + 1])
                last.then_inc(S["act_done"].sem, 1)
                if g >= 2:
                    outputs(g - 2)
            outputs(G - 2)
            outputs(G - 1)

    for n in ("mm_done", "tr_done", "aux_done", "stat_ready", "act_done", "act_free", "dve_done", "dve_free", "dve_chain"):
        S[n].close(G * (2 if n == "dve_chain" else 1))


def first_up(core, places, gated):
    ring = weight_tiles(core, places["ring"])
    w1 = core.ap["w_gu_2" if gated else "ff_w1"].rearrange("a (k p) n -> p (a k) n", p=P)
    starts = (0, FF2, P, FF2 + P) if gated else (0, P)
    return [(ring[s].raw, w1[:, :, at:at + P], core.sig["loaded%d" % s]) for s, at in enumerate(starts)]


def phase_ffn(core, xt, h, gated, places):
    nc, ap, S, ps = core.nc, core.ap, core.sig, core.psum
    ft = [Split(core, places["ft"] + 16 * s, 2, L) for s in range(2)]
    ring = weight_tiles(core, places["ring"])
    w2s = [Split(core, places["w2"] + 8 * s, 2, BANK) for s in range(2)]
    first = [core.view(places["act"] + 2 * s, BANK) for s in range(2)]
    full = [core.view(places["full"] + 2 * s, BANK) for s in range(2)]
    tmp = [core.view(places["tmp"] + 2 * s, BANK) for s in range(2)]
    G = (FF2 if gated is not None else FF) // (2 * P)
    per = 4 if gated is not None else 2
    w1 = ap["w_gu_2" if gated is not None else "ff_w1"].rearrange("a (k p) n -> p (a k) n", p=P)
    w2 = ap["w_down_2" if gated is not None else "ff_w2"].rearrange("a (k p) n -> p (a k) n", p=P)
    ld = [S["loaded%d" % s] for s in range(4)]
    ld2 = [S["loaded"], S["stored"]]
    unit = lambda g, f, half: 4 * g + 2 * f + half

    def slots(b, f):
        return (2 * f, 2 * f + 1) if gated is not None else (2 * b + f,)

    def over_groups(eng, body):
        body(0, 0, 0)
        body(1, 1, 0)
        with eng.Fori(1, (G - 1) // 2) as i:
            body(2 * i, 0, i)
            body(2 * i + 1, 1, i)
        for g in range((G - 1) // 2 * 2, G):
            body(g, g % 2, g // 2)

    known = lambda v: isinstance(v, int)
    last_group = lambda g: known(g) and g == G - 1

    with nc.Block() as block:
        @block.sync
        def _(sp):
            def up_weights(g, b):
                back = 1 if gated is not None else 2
                for f in range(2):
                    for part, slot in enumerate(slots(b, f)):
                        if not (known(g) and g < back):
                            sp.wait_ge(S["mm_done"].sem, S["mm_done"].at(unit(g - back, f, 1) + 1))
                        sp.dma_start(ring[slot].raw, w1[:, :, bass.ds(part * FF2 + (2 * g + f) * P, P)]).then_inc(ld[slot].sem, 16)

            def group(g, b, n):
                if not last_group(g):
                    up_weights(g + 1, 1 - b)
                for c in range(2):
                    if not (known(g) and g < 1):
                        sp.wait_ge(S["aux_done"].sem, S["aux_done"].at(2 * TT * (g - 1) + TT * (c + 1)))
                    sp.dma_start(w2s[c].raw, w2[:, bass.ds(2 * g, 2), c * BANK:(c + 1) * BANK]).then_inc(ld2[c].sem, 16)

            over_groups(sp, group)

        @block.tensor
        def _(pe):
            def up(g, b):
                for f in range(2):
                    pe.wait_ge(S["w_lo"].sem, S["w_lo"].at(per * g + per // 2 * (f + 1)))
                    for half in range(2):
                        banks = (2 * half, 2 * half + 1) if gated is not None else (2 * f + half,)
                        u = unit(g, f, half)
                        if gated is not None and not (known(u) and u < 2):
                            pe.wait_ge(S["square_done"].sem, S["square_done"].at(u - 1))
                        if gated is None and not (known(u) and u < 4):
                            pe.wait_ge(S["bank_free"].sem, S["bank_free"].at(u - 3))
                        for bank, slot in zip(banks, slots(b, f)):
                            last = mm3_cols(nc, ps[:, bank, :], ring[slot], slice(0, P), xt, half * BANK, (half + 1) * BANK)
                        last.then_inc(S["mm_done"].sem, 1)

            def down(g, b):
                pe.wait_ge(S["ft_lo"].sem, S["ft_lo"].at(4 * g + 4))
                for c in range(2):
                    pe.wait_ge(S["v_lo"].sem, S["v_lo"].at(2 * g + c + 1))
                    for t in range(TT):
                        u = 2 * TT * g + TT * c + t
                        if not (known(u) and u < 4):
                            pe.wait_ge(S["dve_free"].sem, S["dve_free"].at(u - 3))
                        lt = slice(t * P, (t + 1) * P)
                        for k in range(2):
                            last = mm3(nc, ps[:, 4 + t % 4, :], ft[b].hi[:, k, lt], ft[b].lo[:, k, lt], w2s[c].hi[:, k, :], w2s[c].lo[:, k, :], k == 0, k == 1)
                        last.then_inc(S["aux_done"].sem, 1)

            def group(g, b, n):
                up(g, b)
                if not (known(g) and g == 0):
                    down(g - 1, 1 - b)
            over_groups(pe, group)
            down(G - 1, (G - 1) % 2)

        @block.scalar
        def _(act):
            def weights(g, b, f, n):
                for part, slot in enumerate(slots(b, f)):
                    act.wait_ge(ld[slot].sem, ld[slot].at(16 * (g + 1 if gated is not None else n + 1)))
                    nc.scalar.activation(ring[slot].hi, ring[slot].raw, ACT.Copy).then_inc(S["w_hi"].sem, 1)

            def split(g, b, f, half):
                u = unit(g, f, half)
                act.wait_ge(S["square_done"].sem, S["square_done"].at(u + 1))
                nc.scalar.activation(ft[b].hi[:, f, half * BANK:(half + 1) * BANK], full[half], ACT.Copy).then_inc(S["ft_hi"].sem, 1)

            def group(g, b, n):
                for f in range(2):
                    for half in range(2):
                        u = unit(g, f, half)
                        act.wait_ge(S["mm_done"].sem, S["mm_done"].at(u + 1))
                        if not (known(u) and u < 2):
                            act.wait_ge(S["square_done"].sem, S["square_done"].at(u - 1))
                        if gated is not None:
                            nc.scalar.activation(first[half], ps[:, 2 * half, :], ACT.Silu).then_inc(S["act_done"].sem, 1)
                        else:
                            nc.scalar.activation(first[half], ps[:, 2 * f + half, :], ACT.Relu).then_inc(S["bank_free"].sem, 1)
                        if (f, half) != (0, 0):
                            if (f, half) == (0, 1) and not (known(g) and g < 2):
                                act.wait_ge(S["aux_done"].sem, S["aux_done"].at(2 * TT * (g - 1)))
                            split(g, b, *((0, 0) if (f, half) == (0, 1) else (0, 1) if (f, half) == (1, 0) else (1, 0)))
                        if (f, half) == (1, 0) and not (known(g) and g == 0):
                            down_weights(g - 1, 1)
                split(g, b, 1, 1)
                if not last_group(g):
                    for f in range(2):
                        weights(g + 1, 1 - b, f, n + b)
                down_weights(g, 0)

            def down_weights(g, c):
                act.wait_ge(ld2[c].sem, ld2[c].at(16 * (g + 1)))
                nc.scalar.activation(w2s[c].hi, w2s[c].raw, ACT.Copy).then_inc(S["v_hi"].sem, 1)

            for f in range(2):
                weights(0, 0, f, 0)
            over_groups(act, group)
            down_weights(G - 1, 1)

        if gated is None:
            @block.gpsimd
            def _(pool):
                def squares(g, b, n):
                    for f in range(2):
                        for half in range(2):
                            u = unit(g, f, half)
                            pool.wait_ge(S["bank_free"].sem, S["bank_free"].at(u + 1))
                            if not (known(u) and u < 2):
                                pool.wait_ge(S["ft_lo"].sem, S["ft_lo"].at(u - 1))
                            nc.gpsimd.tensor_tensor(full[half], first[half], first[half], ALU.mult).then_inc(S["square_done"].sem, 1)
                over_groups(pool, squares)
        else:
            @block.gpsimd
            def _(pool):
                def sums(g):
                    for c in range(2):
                        for t in range(TT):
                            u = 2 * TT * g + TT * c + t
                            pool.wait_ge(S["dve_free"].sem, S["dve_free"].at(u + 1))
                            hv = h[:, t, c * BANK:(c + 1) * BANK]
                            nc.gpsimd.tensor_tensor(hv, tmp[t % 2], hv, ALU.add).then_inc(S["pool_done"].sem, 1)

                def group(g, b, n):
                    if not (known(g) and g == 0):
                        sums(g - 1)
                over_groups(pool, group)
                sums(G - 1)

        @block.vector
        def _(dve):
            def weights(g, b, f):
                for part, slot in enumerate(slots(b, f)):
                    dve.wait_ge(S["w_hi"].sem, S["w_hi"].at(per * g + per // 2 * f + part + 1))
                    nc.vector.tensor_tensor(ring[slot].lo, ring[slot].raw, ring[slot].hi_raw, ALU.subtract).then_inc(S["w_lo"].sem, 1)

            def split(g, b, f, half):
                dve.wait_ge(S["ft_hi"].sem, S["ft_hi"].at(unit(g, f, half) + 1))
                cols = slice(half * BANK, (half + 1) * BANK)
                nc.vector.tensor_tensor(ft[b].lo[:, f, cols], full[half], ft[b].hi_raw[:, f, cols], ALU.subtract).then_inc(S["ft_lo"].sem, 1)

            def sums(g, which):
                for v in which:
                    c, t = v // TT, v % TT
                    u = 2 * TT * g + v
                    dve.wait_ge(S["aux_done"].sem, S["aux_done"].at(u + 1))
                    hv = h[:, t, c * BANK:(c + 1) * BANK]
                    if gated is None:
                        nc.vector.tensor_tensor(hv, ps[:, 4 + t % 4, :], hv, ALU.add).then_inc(S["dve_free"].sem, 1)
                    else:
                        if not (known(u) and u < 2):
                            dve.wait_ge(S["pool_done"].sem, S["pool_done"].at(u - 1))
                        nc.vector.tensor_tensor(tmp[t % 2], ps[:, 4 + t % 4, :], gated[:, c * BANK:(c + 1) * BANK], ALU.mult).then_inc(S["dve_free"].sem, 1)

            def group(g, b, n):
                order = [(0, 0), (0, 1), (1, 0), (1, 1)]
                for m, (f, half) in enumerate(order):
                    u = unit(g, f, half)
                    if gated is not None:
                        dve.wait_ge(S["act_done"].sem, S["act_done"].at(u + 1))
                        if not (known(u) and u < 2):
                            dve.wait_ge(S["ft_lo"].sem, S["ft_lo"].at(u - 1))
                        nc.vector.tensor_tensor(full[half], ps[:, 2 * half + 1, :], first[half], ALU.mult).then_inc(S["square_done"].sem, 1)
                    if m:
                        split(g, b, *order[m - 1])
                    if m == 3 and not (known(g) and g == 0):
                        down_weights(g - 1, 1)
                split(g, b, 1, 1)
                follow = not last_group(g)
                has_sums = not (known(g) and g == 0)
                for which, then in ((range(0, 3), lambda: follow and weights(g + 1, 1 - b, 0)), (range(3, 6), lambda: follow and weights(g + 1, 1 - b, 1)),
                                    (range(6, 13), lambda: down_weights(g, 0)), (range(13, 16), lambda: None)):
                    if has_sums:
                        sums(g - 1, which)
                    then()

            def down_weights(g, c):
                dve.wait_ge(S["v_hi"].sem, S["v_hi"].at(2 * g + c + 1))
                nc.vector.tensor_tensor(w2s[c].lo, w2s[c].raw, w2s[c].hi_raw, ALU.subtract).then_inc(S["v_lo"].sem, 1)

            for f in range(2):
                weights(0, 0, f)
            over_groups(dve, group)
            down_weights(G - 1, 1)
            sums(G - 1, range(2 * TT))
    for s in range(4):
        ld[s].close(16 * (G if gated is not None else G // 2))
    for s in ld2:
        s.close(16 * G)
    for n, k in (("mm_done", 4), ("ft_hi", 4), ("ft_lo", 4), ("square_done", 4), ("aux_done", 2 * TT), ("dve_free", 2 * TT),
                 ("w_hi", per), ("w_lo", per), ("v_hi", 2), ("v_lo", 2)):
        S[n].close(k * G)
    if gated is None:
        S["bank_free"].close(4 * G)
    else:
        S["act_done"].close(4 * G)
        S["pool_done"].close(2 * TT * G)


class FinalNorm:

    def __init__(self, core, h, gain, gain_kb):
        self.core, self.h, self.gain = core, h, gain
        self.g = core.view(gain_kb, D)
        self.junk = core.view3(gain_kb + 4, 2, D)
        self.ss, self.rstd = core.tiny[:, 0:TT], core.tiny[:, 8:8 + TT]

    def load(self, sp):
        sp.dma_start(self.g, self.gain.partition_broadcast(P)).then_inc(self.core.sig["loaded"].sem, 16)

    def scalar(self, act):
        nc, S = self.core.nc, self.core.sig
        chain = Chain(act, S["act_chain"])
        for i in range(0, TT, 2):
            chain(nc.scalar.activation(self.junk[:, 0, :], self.h[:, i, :], ACT.Square, accum_out=self.ss[:, i:i + 1]))
        act.wait_ge(S["square_done"].sem, S["square_done"].at(TT // 2))
        nc.scalar.activation(self.rstd, self.ss, ACT.Sqrt, scale=1.0 / D, bias=self.core.eps).then_inc(S["stat_ready"].sem, 1)

    def vector(self, dve):
        nc, S, rstd = self.core.nc, self.core.sig, self.rstd
        squares = Chain(dve, S["square_done"])
        for i in range(1, TT, 2):
            row = self.h[:, i, :]
            squares(nc.vector.tensor_tensor_reduce(out=self.junk[:, 1, :], in0=row, in1=row, scale=1.0, scalar=0.0,
                                                   op0=ALU.mult, op1=ALU.add, accum_out=self.ss[:, i:i + 1]))
        dve.wait_ge(S["loaded"].sem, S["loaded"].at(16))
        dve.wait_ge(S["stat_ready"].sem, S["stat_ready"].at(1))
        nc.vector.reciprocal(rstd, rstd).then_inc(S["dve_chain"].sem, 1)
        dve.wait_ge(S["dve_chain"].sem, S["dve_chain"].at(1))
        for t in range(TT):
            row = self.h[:, t, :]
            nc.vector.scalar_tensor_tensor(out=row, in0=row, scalar=rstd[:, t:t + 1], in1=self.g, op0=ALU.mult, op1=ALU.mult).then_inc(S["dve_done"].sem, 1)

    def close(self):
        for n, count in (("loaded", 16), ("act_chain", TT // 2), ("square_done", TT // 2), ("stat_ready", 1), ("dve_chain", 1), ("dve_done", TT)):
            self.core.sig[n].close(count)


def phase_final_norm(core, h, gain, gain_kb, out_dram):
    nc, S = core.nc, core.sig
    norm = FinalNorm(core, h, gain, gain_kb)
    rows = out_dram.rearrange("a (t p) d -> p (a t) d", p=P)
    with nc.Block() as block:
        @block.sync
        def _(sp):
            norm.load(sp)
            for t in range(TT):
                sp.wait_ge(S["dve_done"].sem, S["dve_done"].at(t + 1))
                sp.dma_start(rows[:, t, :], h[:, t, :]).then_inc(S["stored"].sem, 16)
            sp.wait_ge(S["stored"].sem, S["stored"].at(16 * TT))

        @block.scalar
        def _(act):
            norm.scalar(act)

        @block.vector
        def _(dve):
            norm.vector(dve)
    norm.close()
    S["stored"].close(16 * TT)


def first_block(core):
    ap = core.ap
    x, xt = core.view3(118, TT, D), Split(core, 6, KT, L)
    w_in = ap["w_in"]
    phase_load(core)
    w_rows = w_in.rearrange("a (k p) n -> p (a k) n", p=P)
    phase_norm(core, x, xt, core.colsA[:, G_MIX:G_MIX + 8], ahead=first_columns(core, weight_tiles(core, CONV_RING_KB), w_rows, 0))
    hy = core.view3(HY_KB, TT, HY_COLS)
    phase_conv_proj(core, xt, w_in, hy)
    phase_filter_hidden(core, hy)
    tables = Tables(core)
    for o in range(2):
        phase_filter_time(core, tables, o)
        phase_filter_spectrum(core, tables, hy)
        phase_signal_spectrum(core, tables)
        phase_inverse_gate(core, tables, hy, o)
    yht, ymt = core.view3(191.5, 4, L), core.view3(70, 4, L)
    phase_group_norm(core, hy[:, :, 0:DH], 8, yht, core.colsB[:, G_HY:G_HY + 4], 182, mirrored=True,
                     ahead=[(x, ap["x"].rearrange("a (t p) d -> p (a t) d", p=P), core.sig["x_ready"])])
    phase_norm(core, x, xt, core.colsA[:, G_MIX:G_MIX + 8], scratch=70, arrives=True,
               ahead=first_columns(core, weight_tiles(core, QK_RING_KB), w_rows, HY_COLS))
    base = HY_COLS + 1024
    phase_qk_proj(core, xt, w_in, first_pieces(core, VO_KB, w_rows[:, :, base:base + DH], count=1))
    phase_vo(core, xt, w_in)
    phase_gates(core, xt, w_in)
    phase_gate_scans(core)
    phase_mlstm(core)
    phase_group_norm(core, core.view3(O_KB, TT, DH), 4, ymt, core.colsB[:, G_ML:G_ML + 4], 182,
                     ahead=first_pieces(core, (102,), ap["w_out"].rearrange("a (k p) n -> p (a k) n", p=P)[:, :, 0:BANK], count=1))
    mixed = Split(core, 6, 8, L)
    phase_split(core, split_pairs(yht, mixed) + split_pairs(ymt, mixed, at=4))
    second_half(core, mixed)


def second_half(core, mixed):
    ap = core.ap
    h = core.view3(H_KB, TT, D)
    phase_rows_gemm(core, mixed, ap["w_out"], h, residual=ap["x"], ahead=1)
    xt = Split(core, 6, KT, L)
    mem, memt = core.view3(134, 2, D), Split(core, 142, KT, NMEM)
    phase_norm(core, h, xt, core.colsA[:, G_X:G_X + 8], ahead=[(mem, ap["mem"].rearrange("a (t p) d -> p (a t) d", p=P), core.sig["x_ready"])])
    wk = ap["xa_wk"].rearrange("a (k p) n -> p (a k) n", p=P)
    phase_norm(core, mem, memt, core.colsA[:, G_MEM:G_MEM + 8], scratch=162, arrives=True, ahead=first_columns(core, weight_tiles(core, 174), wk, 0))
    qt, kt, v = core.view3(102, 8, L), core.view3(158, 8, NMEM), core.view3(166, 2, D)
    wt = {n: ap[n].rearrange("a (k p) n -> p (a k) n", p=P) for n in ("xa_wq", "xa_wk", "xa_wv")}
    phase_cols_gemm(core, [([wt["xa_wk"][:, :, n * P:(n + 1) * P]], memt, kt[:, n, :]) for n in range(8)]
                    + [([wt["xa_wq"][:, :, n * P:(n + 1) * P]], xt, qt[:, n, :]) for n in range(8)], 174, ahead=4)
    phase_rows_proj(core, [(wt["xa_wv"][:, :, c * BANK:(c + 1) * BANK], memt, lambda t, c=c: v[:, t, c * BANK:(c + 1) * BANK], ACT.Copy) for c in range(2)], (6, 22, 38))
    ot = core.view3(6, 8, L)
    phase_cross_attention(core, qt, kt, v, ot, 182,
                          first_pieces(core, (38,), ap["xa_wo"].rearrange("a (k p) n -> p (a k) n", p=P)[:, :, 0:BANK], count=1))
    attended = Split(core, 102, 8, L)
    phase_split(core, split_pairs(ot, attended))
    phase_rows_gemm(core, attended, ap["xa_wo"], h, ring_kb=(38, 6, 22), ahead=1)
    places = {"ft": 102, "ring": 134, "w2": 166, "act": 182, "full": 186, "tmp": 190}
    phase_norm(core, h, xt, core.colsA[:, G_FF:G_FF + 8], scratch=182, ahead=first_up(core, places, False))
    phase_ffn(core, xt, h, None, places)
QAT_KB, KAT_KB, QBT_KB, QIT_KB, KIT_KB, VA_KB, CKV_KB, CKVT_KB = 70, 86, 102, 118, 134, 138, 154, 192
GA1_KB, GA2_KB, QLT_KB, SEL_KB, MIX_KB, H2_KB = 199.75, 203.75, 6, 160, 38, 38
IDX_SCALE = (8 * 64) ** -0.5
TAKEN = -3.0e38
FIRST_SEL = TOPK // P
SCALE = HD ** -0.5


ADA_KB = (6, 22, 38, 54, 102, 118)


def modulation_load(core, n):
    w = core.ap["w_ada_2"].rearrange("a (k p) n -> p (a k) n", p=P)
    return core.view3(ADA_KB[n % 6], KT, BANK), w[:, :, n * BANK:(n + 1) * BANK], core.sig["ada%d" % (n % 6)]


GATES = [4, 5, 10, 11]


def modulation_biases(core):
    return core.view(146, P, 48), core.view3(134, 4, BANK)


def first_modulation(core):
    b, S = core.ap["b_ada_2"], core.sig
    bias_rows, brow = modulation_biases(core)
    small = [(bias_rows, b.rearrange("a (r c) -> (a r) c", c=P), S["loaded0"])]
    small += [(brow[:, m, :], b[0, n * BANK:(n + 1) * BANK].partition_broadcast(P), S["loaded1"]) for m, n in enumerate(GATES)]
    return small + [modulation_load(core, n) for n in range(6)]


def phase_ada(core, h, saved):
    nc, ap, S, ps = core.nc, core.ap, core.sig, core.psum
    ring = [core.view3(kb, KT, BANK) for kb in ADA_KB]
    N = 12
    arrived = [S["ada%d" % s] for s in range(6)]
    crep = core.view3(142, KT, P)
    bias_rows, brow = modulation_biases(core)
    bias, picked = core.view(147, 48), core.view3(148, 4, P)
    ga1, ga2 = core.view3(GA1_KB, 2, BANK), core.view3(GA2_KB, 2, BANK)
    gate_rows = [ga1[:, 0, :], ga1[:, 1, :], ga2[:, 0, :], ga2[:, 1, :]]
    cact = core.tiny[:, 24:32]
    cols = core.tiny2[:, 200:248]
    core.mod_scale = [core.tiny2[:, 256:264], core.tiny2[:, 264:272]]
    core.mod_shift = [cols[:, 0:8], cols[:, 24:32]]
    norm = FinalNorm(core, h, ap["final_norm_g"], 182)
    with nc.Block() as block:
        @block.sync
        def _(sp):
            norm.load(sp)
            load_ahead(sp, first_modulation(core))
            sp.wait_ge(S["dve_done"].sem, S["dve_done"].at(TT))
            sp.dma_start(saved.rearrange("a (t p) d -> p (a t) d", p=P), h).then_inc(S["stored"].sem, 16)
            for n in range(6, N):
                sp.wait_ge(S["mm_done"].sem, S["mm_done"].at(n - 5))
                dst, src, signal = modulation_load(core, n)
                sp.dma_start(dst, src).then_inc(signal.sem, 16)
            sp.wait_ge(S["stored"].sem, S["stored"].at(16))

        @block.scalar
        def _(act):
            nc.scalar.activation(cact, core.colsB[:, C_ACT:C_ACT + 8], ACT.Silu).then_inc(S["act_done"].sem, 1)
            norm.scalar(act)

        @block.tensor
        def _(pe):
            pe.wait_ge(S["loaded0"].sem, S["loaded0"].at(16))
            nc.tensor.transpose(ps[:, 6, 0:48], bias_rows, core.ident[0:48, 0:48]).then_inc(S["tr_done"].sem, 1)
            pe.wait_ge(S["mod_ready"].sem, S["mod_ready"].at(1))
            for n in range(N):
                pe.wait_ge(arrived[n % 6].sem, arrived[n % 6].at(16 * (n // 6 + 1)))
                if n >= 4:
                    pe.wait_ge(S["dve_free"].sem, S["dve_free"].at(n - 3))
                for k in range(KT):
                    last = nc.tensor.matmul(ps[:, n % 4, :], crep[:, k, :], ring[n % 6][:, k, :], start=k == 0, stop=k == KT - 1)
                last.then_inc(S["mm_done"].sem, 1)

        @block.vector
        def _(dve):
            dve.wait_ge(S["act_done"].sem, S["act_done"].at(1))
            nc.vector.tensor_copy(crep, cact.unsqueeze(2).to_broadcast([P, KT, P])).then_inc(S["mod_ready"].sem, 1)
            chain = Chain(dve, S["mod_chain"])
            dve.wait_ge(S["tr_done"].sem, S["tr_done"].at(1))
            chain(nc.vector.tensor_copy(bias, ps[:, 6, 0:48]))
            norm.vector(dve)
            dve.wait_ge(S["loaded1"].sem, S["loaded1"].at(16 * 4))
            for n in range(N):
                dve.wait_ge(S["mm_done"].sem, S["mm_done"].at(n + 1))
                if n in GATES:
                    m = GATES.index(n)
                    nc.vector.tensor_tensor(gate_rows[m], ps[:, n % 4, :], brow[:, m, :], ALU.add).then_inc(S["dve_free"].sem, 1)
                else:
                    own = core.ident.unsqueeze(1).to_broadcast([P, 4, P])
                    nc.vector.tensor_tensor(picked, ps[:, n % 4, :].rearrange("p (a b) -> p a b", a=4), own, ALU.mult).then_inc(S["dve_free"].sem, 1)
                    dve.wait_ge(S["dve_free"].sem, S["dve_free"].at(n + 1))
                    chain(nc.vector.reduce_sum(cols[:, 4 * n:4 * n + 4], picked, AX.X))
            for a, b in ((0, 16), (24, 40)):
                chain(nc.vector.tensor_tensor(cols[:, a:b], cols[:, a:b], bias[:, a:b], ALU.add))
            for n, (scale, gain) in enumerate(((cols[:, 8:16], G_ATT2), (cols[:, 32:40], G_FFN2))):
                nc.vector.scalar_tensor_tensor(out=core.mod_scale[n], in0=scale, scalar=1.0, in1=core.colsA[:, gain:gain + 8], op0=ALU.add, op1=ALU.mult)
    S["stored"].close(16)
    S["loaded0"].close(16)
    S["loaded1"].close(16 * 4)
    for s in range(6):
        arrived[s].close(16 * 2)
    S["mm_done"].close(N)
    S["act_done"].close(1)
    S["mod_ready"].close(1)
    norm.close()
    S["tr_done"].close(1)
    S["mod_chain"].close(3 + N - len(GATES))
    S["dve_free"].close(N)


def phase_latent(core, beside):
    nc, ap, S, ps = core.nc, core.ap, core.sig, core.psum
    ckv, ckvt = core.view3(CKV_KB, TT, RANK), core.view(CKVT_KB, L)
    qbt = core.view3(QBT_KB, 4, L)
    qlt = core.view3(QLT_KB, 8, L)
    wuk, grow, junk = core.view3(118, 4, RANK), core.view(120, RANK), core.view3(122, TT, RANK)
    ss, rstd = core.tiny[:, 0:TT], core.tiny[:, 8:8 + TT]
    with nc.Block() as block:
        @block.sync
        def _(sp):
            sp.dma_start(wuk, ap["w_uk_2"][0].rearrange("(a b) d r -> (b d) a r", b=2)).then_inc(S["loaded0"].sem, 16)
            sp.dma_start(grow, ap["kv_norm_g_2"][0].partition_broadcast(P)).then_inc(S["loaded1"].sem, 16)

        @block.scalar
        def _(act):
            for t in range(TT):
                last = nc.scalar.activation(junk[:, t, :], ckv[:, t, :], ACT.Square, accum_out=ss[:, t:t + 1])
            last.then_inc(S["act_chain"].sem, 1)
            act.wait_ge(S["act_chain"].sem, S["act_chain"].at(1))
            nc.scalar.activation(rstd, ss, ACT.Sqrt, scale=1.0 / RANK, bias=core.eps).then_inc(S["stat_ready"].sem, 1)
            for n in range(16):
                act.wait_ge(S["mm_done"].sem, S["mm_done"].at(n + 1))
                nc.scalar.activation(qlt[:, n // 2, (n % 2) * BANK:(n % 2 + 1) * BANK], ps[:, n % 4, :], ACT.Copy).then_inc(S["act_free"].sem, 1)

        @block.vector
        def _(dve):
            dve.wait_ge(S["stat_ready"].sem, S["stat_ready"].at(1))
            nc.vector.reciprocal(rstd, rstd).then_inc(S["dve_chain"].sem, 1)
            dve.wait_ge(S["dve_chain"].sem, S["dve_chain"].at(1))
            dve.wait_ge(S["loaded1"].sem, S["loaded1"].at(16))
            for t in range(TT):
                last = nc.vector.scalar_tensor_tensor(out=ckv[:, t, :], in0=ckv[:, t, :], scalar=rstd[:, t:t + 1], in1=grow, op0=ALU.mult, op1=ALU.mult)
            last.then_inc(S["dve_done"].sem, 1)
            beside(dve)
            dve.wait_ge(S["tr_done"].sem, S["tr_done"].at(1))
            nc.vector.tensor_copy(ckvt, ps[:, 4:6, :].rearrange("p a b -> p (a b)"))

        @block.tensor
        def _(pe):
            pe.wait_ge(S["loaded0"].sem, S["loaded0"].at(16))
            for n in range(16):
                h, half = n // 2, n % 2
                if n >= 4:
                    pe.wait_ge(S["act_free"].sem, S["act_free"].at(n - 3))
                rows = slice(64 * (h % 2), 64 * (h % 2) + 64)
                nc.tensor.matmul(ps[:, n % 4, :], wuk[rows, h // 2, :], qbt[rows, h // 2, half * BANK:(half + 1) * BANK], start=True, stop=True).then_inc(S["mm_done"].sem, 1)
            pe.wait_ge(S["dve_done"].sem, S["dve_done"].at(1))
            for t in range(TT):
                last = nc.tensor.transpose(ps[:, 4 + t // 4, (t % 4) * P:(t % 4 + 1) * P], ckv[:, t, :], core.ident)
            last.then_inc(S["tr_done"].sem, 1)
    S["loaded0"].close(16)
    S["loaded1"].close(16)
    for n in ("act_chain", "stat_ready", "dve_chain", "dve_done", "tr_done"):
        S[n].close(1)
    S["mm_done"].close(16)
    S["act_free"].close(16)


def sel_tile(core, i):
    start = i * (i + 1) // 2 * P
    return core.view(SEL_KB, 36 * P)[:, start:start + (i + 1) * P]


def phase_index_scores(core):
    nc, ap, S, ps = core.nc, core.ap, core.sig, core.psum
    qit, kit = core.view3(QIT_KB, 4, L), core.view(KIT_KB, L)
    rel = [core.view(178 + 4 * s, L) for s in range(3)]
    steps = [(i, h) for i in range(FIRST_SEL, TT) for h in range(8)]
    pair = lambda n, w: ps[:, 2 * (n % 4):2 * (n % 4) + 2, :].rearrange("p a b -> p (a b)")[:, 0:w]
    with nc.Block() as block:
        @block.tensor
        def _(pe):
            keep_clock(core)
            for n, (i, h) in enumerate(steps):
                if n >= 4:
                    pe.wait_ge(S["act_done"].sem, S["act_done"].at(n - 3))
                rows = slice(64 * (h % 2), 64 * (h % 2) + 64)
                w = (i + 1) * P
                for a in range(0, w, BANK):
                    b = min(a + BANK, w)
                    last = nc.tensor.matmul(ps[:, 2 * (n % 4) + a // BANK, 0:b - a], qit[rows, h // 2, i * P:(i + 1) * P], kit[rows, a:b], start=True, stop=True)
                last.then_inc(S["mm_done"].sem, 1)

        @block.scalar
        def _(act):
            for n, (i, h) in enumerate(steps):
                act.wait_ge(S["mm_done"].sem, S["mm_done"].at(n + 1))
                if n >= 3:
                    act.wait_ge(S["dve_done"].sem, S["dve_done"].at(n - 2))
                w = (i + 1) * P
                nc.scalar.activation(rel[n % 3][:, 0:w], pair(n, w), ACT.Relu).then_inc(S["act_done"].sem, 1)

        @block.vector
        def _(dve):
            Chain(dve, S["dve_chain"])(nc.vector.tensor_scalar(core.wi, core.wi, IDX_SCALE, None, ALU.mult))
            for n, (i, h) in enumerate(steps):
                dve.wait_ge(S["act_done"].sem, S["act_done"].at(n + 1))
                w = (i + 1) * P
                sc, wc = sel_tile(core, i), core.wi[:, i, h:h + 1]
                if h == 0:
                    ins = nc.vector.tensor_scalar(sc, rel[n % 3][:, 0:w], wc, None, ALU.mult)
                else:
                    dve.wait_ge(S["dve_done"].sem, S["dve_done"].at(n))
                    ins = nc.vector.scalar_tensor_tensor(out=sc, in0=rel[n % 3][:, 0:w], scalar=wc, in1=sc, op0=ALU.mult, op1=ALU.add)
                ins.then_inc(S["dve_done"].sem, 1)
            dve.wait_ge(S["dve_done"].sem, S["dve_done"].at(len(steps)))
            for i in range(TT):
                sc = sel_tile(core, i)
                if i < FIRST_SEL:
                    if i:
                        nc.vector.memset(sc[:, 0:i * P], 0.0)
                    nc.vector.tensor_copy(sc[:, i * P:], core.small[:, 4, :])
                else:
                    nc.vector.tensor_tensor(sc[:, i * P:], sc[:, i * P:], core.small[:, 4, :], ALU.add)
    for n in ("mm_done", "act_done", "dve_done"):
        S[n].close(len(steps))
    S["dve_chain"].close(1)


class Selection:

    def __init__(self, core):
        self.core, self.tile, self.round, self.steps, self.credit = core, FIRST_SEL, 0, 0, 0.0
        self.done = core.sig["selected"].sem
        self.top = core.tiny[:, 32:48].rearrange("p (a b) -> p a b", a=2)

    def rounds(self, dve, us=None):
        nc = self.core.nc
        self.credit += us or 0
        while self.tile < TT and (us is None or self.credit > 0):
            sc, best = sel_tile(self.core, self.tile), self.top[:, self.round % 2, :]
            if self.steps:
                dve.wait_ge(self.done, self.steps)
            nc.vector.max(best, sc).then_inc(self.done, 1)
            dve.wait_ge(self.done, self.steps + 1)
            nc.vector.match_replace(out=sc, in_to_replace=best, in_values=sc, imm_value=TAKEN).then_inc(self.done, 1)
            self.steps += 2
            self.round += 1
            self.credit -= 2 * (0.12 + (self.tile + 1) * P / 960)
            if self.round == TOPK // 8:
                dve.wait_ge(self.done, self.steps)
                nc.vector.tensor_scalar(sc, sc, TAKEN, NEG, ALU.not_equal, ALU.mult)
                self.tile, self.round = self.tile + 1, 0


def phase_attention(core, sparse, selection=None):
    nc, ap, S, ps = core.nc, core.ap, core.sig, core.psum
    qat, kat = core.view3(QAT_KB, 4, L), core.view3(KAT_KB, 4, L)
    qlt, ckvt = core.view3(QLT_KB, 8, L), core.view(CKVT_KB, L)
    va, ckv = core.view3(VA_KB, TT, 512), core.view3(CKV_KB, TT, RANK)
    mix = core.view3(MIX_KB, TT, D)
    sc = [core.view(102 + 4 * s, L) for s in range(2)]
    pt = [core.view3(110 + 4 * s, TT, P) for s in range(2)]
    biases = [core.view(118 + 4 * s, L) for s in range(2)]
    tb = [core.view(126 + 4 * s, L) for s in range(2)]
    mdist = core.view(178, L)
    olt = core.view3(182, 2, P)
    wuv = core.view3(183, 8, HD)
    stat = core.tiny2[:, 0:64].rearrange("p (a b) -> p a b", b=4)
    steps = [(h, i) for h in range(8) for i in range(TT)]
    N = len(steps)
    pair = lambda n, w: ps[:, 2 * (n % 2):2 * (n % 2) + 2, :].rearrange("p a b -> p (a b)")[:, 0:w]

    def turned(n):
        w = (steps[n][1] + 1) * P
        return pt[n % 2].rearrange("p a b -> p (a b)")[:, 0:w], ps[:, 4:6, :].rearrange("p a b -> p (a b)")[:, 0:w]

    def turned_wait(eng, n):
        eng.wait_ge(S["tr_done"].sem, S["tr_done"].at(n + 1))
        if n >= 2:
            eng.wait_ge(S["aux_done"].sem, S["aux_done"].at(n - 1))

    with nc.Block() as block:
        @block.sync
        def _(sp):
            if sparse:
                sp.dma_start(mdist, ap["c_mdist"]).then_inc(S["loaded0"].sem, 16)
                sp.dma_start(wuv, ap["w_uv_2"][0].rearrange("h r d -> r h d")).then_inc(S["loaded1"].sem, 16)
            else:
                for h in range(8):
                    if h >= 2:
                        sp.wait_ge(S["dve_done"].sem, S["dve_done"].at(TT * (h - 1)))
                    sp.dma_start(biases[h % 2], ap["c_bias_a"][h]).then_inc(S["loaded%d" % (2 + h % 2)].sem, 16)

        @block.tensor
        def _(pe):
            def scores(n):
                h, i = steps[n]
                if n >= 2:
                    pe.wait_ge(S["dve_done"].sem, S["dve_done"].at(n - 1))
                w = (i + 1) * P
                if sparse:
                    q, k = qlt[:, h, i * P:(i + 1) * P], ckvt
                else:
                    rows = slice(64 * (h % 2), 64 * (h % 2) + 64)
                    q, k = qat[rows, h // 2, i * P:(i + 1) * P], kat[rows, h // 2, :]
                for a in range(0, w, BANK):
                    b = min(a + BANK, w)
                    last = nc.tensor.matmul(ps[:, 2 * (n % 2) + a // BANK, 0:b - a], q, k[:, a:b], start=True, stop=True)
                last.then_inc(S["mm_done"].sem, 1)

            def transposes(n):
                h, i = steps[n]
                pe.wait_ge(S["act_done"].sem, S["act_done"].at(n + 1))
                if n >= 1:
                    pe.wait_ge(S["probs_turned"].sem, S["probs_turned"].at(n))
                for j in range(i + 1):
                    last = nc.tensor.transpose(ps[:, 4 + j // 4, (j % 4) * P:(j % 4 + 1) * P], sc[n % 2][:, j * P:(j + 1) * P], core.ident)
                last.then_inc(S["tr_done"].sem, 1)

            def values(n):
                h, i = steps[n]
                pe.wait_ge(S["probs_turned"].sem, S["probs_turned"].at(n + 1))
                if sparse and n >= 1:
                    pe.wait_ge(S["row_ready"].sem, S["row_ready"].at(n))
                elif not sparse and n >= 2:
                    pe.wait_ge(S["act_free"].sem, S["act_free"].at(n - 1))
                if not sparse:
                    keep_clock(core, 1, bank=6 + n % 2)
                for j in range(i + 1):
                    if sparse:
                        last = nc.tensor.matmul(ps[:, 6, 0:P], ckv[:, j, :], pt[n % 2][:, j, :], start=j == 0, stop=j == i)
                    else:
                        last = nc.tensor.matmul(ps[:, 6 + n % 2, 0:HD], pt[n % 2][:, j, :], va[:, j, h * HD:(h + 1) * HD], start=j == 0, stop=j == i)
                last.then_inc(S["aux_done"].sem, 1)

            def expand(n):
                h, i = steps[n]
                if n == 0:
                    pe.wait_ge(S["loaded1"].sem, S["loaded1"].at(16))
                pe.wait_ge(S["row_ready"].sem, S["row_ready"].at(n + 1))
                if n >= 1:
                    pe.wait_ge(S["act_free"].sem, S["act_free"].at(n))
                nc.tensor.matmul(ps[:, 7, 0:HD], olt[:, n % 2, :], wuv[:, h, :], start=True, stop=True).then_inc(S["aux2_done"].sem, 1)

            keep_clock(core)
            scores(0)
            scores(1)
            for n in range(N + 3):
                if n < N:
                    transposes(n)
                if n + 2 < N:
                    scores(n + 2)
                if 1 <= n <= N:
                    values(n - 1)
                if sparse and n >= 3:
                    expand(n - 3)

        @block.gpsimd
        def _(pool):
            if sparse:
                for n, (h, i) in enumerate(steps):
                    pool.wait_ge(S["x_ready"].sem, S["x_ready"].at(h + 1))
                    if n >= 2:
                        pool.wait_ge(S["dve_done"].sem, S["dve_done"].at(n - 1))
                    w = (i + 1) * P
                    nc.gpsimd.tensor_tensor(tb[n % 2][:, 0:w], biases[h % 2][:, L - w:L], sel_tile(core, i), ALU.add).then_inc(S["pool_done"].sem, 1)

        @block.vector
        def _(dve):
            chain = Chain(dve, S["dve_chain"])

            def biased(n):
                h, i = steps[n]
                w = (i + 1) * P
                if sparse:
                    dve.wait_ge(S["pool_done"].sem, S["pool_done"].at(n + 1))
                elif i == 0:
                    dve.wait_ge(S["loaded%d" % (2 + h % 2)].sem, S["loaded%d" % (2 + h % 2)].at(16 * (h // 2 + 1)))
                dve.wait_ge(S["mm_done"].sem, S["mm_done"].at(n + 1))
                if n >= 2:
                    dve.wait_ge(S["tr_done"].sem, S["tr_done"].at(n - 1))
                b = tb[n % 2][:, 0:w] if sparse else biases[h % 2][:, L - w:L]
                st = stat[:, n % 16, :]
                nc.vector.tensor_tensor_reduce(out=sc[n % 2][:, 0:w], in0=pair(n, w), in1=b, scale=SCALE, scalar=-3.0e38,
                                               op0=ALU.add, op1=ALU.max, accum_out=st[:, 0:1]).then_inc(S["dve_done"].sem, 1)
                dve.wait_ge(S["dve_done"].sem, S["dve_done"].at(n + 1))
                nc.vector.tensor_scalar(st[:, 1:2], st[:, 0:1], -1.0, None, ALU.mult).then_inc(S["stat_ready"].sem, 1)

            def copied(n):
                dve.wait_ge(S["act_done"].sem, S["act_done"].at(n + 1))
                nc.vector.reciprocal(stat[:, n % 16, 3:4], stat[:, n % 16, 2:3]).then_inc(S["dve_free"].sem, 1)
                if sparse:
                    turned_wait(dve, n)
                    nc.vector.tensor_copy(*turned(n)).then_inc(S["probs_turned"].sem, 1)

            biased(0)
            for n in range(N):
                if n + 1 < N:
                    biased(n + 1)
                copied(n)
                if selection is not None:
                    selection.rounds(dve, 0.55 * (steps[n][1] + 1) if n + 1 < N else None)

        @block.scalar
        def _(act):
            if sparse:
                act.wait_ge(S["loaded0"].sem, S["loaded0"].at(16))

            def output(n):
                h, i = steps[n]
                if sparse:
                    act.wait_ge(S["aux2_done"].sem, S["aux2_done"].at(n + 1))
                    src, at = ps[:, 7, 0:HD], 512 + h * HD
                else:
                    act.wait_ge(S["aux_done"].sem, S["aux_done"].at(n + 1))
                    src, at = ps[:, 6 + n % 2, 0:HD], h * HD
                act.wait_ge(S["dve_free"].sem, S["dve_free"].at(n + 1))
                nc.scalar.activation(mix[:, i, at:at + HD], src, ACT.Copy, scale=stat[:, n % 16, 3:4]).then_inc(S["act_free"].sem, 1)

            def latent(n):
                act.wait_ge(S["aux_done"].sem, S["aux_done"].at(n + 1))
                if n >= 2:
                    act.wait_ge(S["aux2_done"].sem, S["aux2_done"].at(n - 1))
                nc.scalar.activation(olt[:, n % 2, :], ps[:, 6, 0:P], ACT.Copy).then_inc(S["row_ready"].sem, 1)

            for n in range(N + 4):
                if n < N:
                    h, i = steps[n]
                    w = (i + 1) * P
                    if sparse and i == 0:
                        if h >= 2:
                            act.wait_ge(S["pool_done"].sem, S["pool_done"].at(n - TT))
                        nc.scalar.activation(biases[h % 2], mdist, ACT.Copy, scale=SLOPES_B[h] / SCALE).then_inc(S["x_ready"].sem, 1)
                    act.wait_ge(S["stat_ready"].sem, S["stat_ready"].at(n + 1))
                    nc.scalar.activation(sc[n % 2][:, 0:w], sc[n % 2][:, 0:w], ACT.Exp, bias=stat[:, n % 16, 1:2],
                                         accum_out=stat[:, n % 16, 2:3]).then_inc(S["act_done"].sem, 1)
                if sparse:
                    if 2 <= n <= N + 1:
                        latent(n - 2)
                    if n >= 4:
                        output(n - 4)
                else:
                    if 1 <= n <= N:
                        turned_wait(act, n - 1)
                        nc.scalar.activation(*turned(n - 1), ACT.Copy).then_inc(S["probs_turned"].sem, 1)
                    if 2 <= n <= N + 1:
                        output(n - 2)
    for n in ("mm_done", "tr_done", "aux_done", "dve_done", "stat_ready", "dve_free", "act_done", "act_free", "probs_turned"):
        S[n].close(N)
    if sparse:
        for n in ("aux2_done", "row_ready", "pool_done"):
            S[n].close(N)
        S["x_ready"].close(8)
        S["loaded0"].close(16)
        S["loaded1"].close(16)
    else:
        S["loaded2"].close(16 * 4)
        S["loaded3"].close(16 * 4)


def phase_mix_transpose(core, mix, mixt, ahead):
    nc, S, ps = core.nc, core.sig, core.psum
    part = lambda x, u: x[:, 4 * (u % 2):4 * (u % 2) + 4, (u // 2) * P:(u // 2 + 1) * P]
    bank = lambda u: ps[:, u % 8, :].rearrange("p (a b) -> p a b", a=4)
    with nc.Block() as block:
        @block.sync
        def _(sp):
            load_ahead(sp, ahead)

        @block.tensor
        def _(pe):
            for u in range(2 * TT):
                i, q = u // 2, u % 2
                if u >= 8:
                    pe.wait_ge(S["dve_free"].sem, S["dve_free"].at(u - 7))
                for j in range(4):
                    last = nc.tensor.transpose(ps[:, u % 8, j * P:(j + 1) * P], mix[:, i, (4 * q + j) * P:(4 * q + j + 1) * P], core.ident)
                last.then_inc(S["tr_done"].sem, 1)

        @block.scalar
        def _(act):
            for u in range(2 * TT):
                act.wait_ge(S["tr_done"].sem, S["tr_done"].at(u + 1))
                nc.scalar.activation(part(mixt.hi, u), bank(u), ACT.Copy).then_inc(S["act_done"].sem, 1)

        @block.vector
        def _(dve):
            for u in range(2 * TT):
                dve.wait_ge(S["act_done"].sem, S["act_done"].at(u + 1))
                nc.vector.tensor_tensor(part(mixt.lo, u), bank(u), part(mixt.hi_raw, u), ALU.subtract).then_inc(S["dve_free"].sem, 1)
    for n in ("tr_done", "act_done", "dve_free"):
        S[n].close(2 * TT)


def second_block(core):
    ap = core.ap
    h, xt = core.view3(H_KB, TT, D), Split(core, 6, KT, L)
    saved = core.nc.dram_tensor("saved_x", (1, L, D), F32, kind="Internal").ap()
    phase_ada(core, h, saved)
    w = ap["w_in_2"].rearrange("a (k p) n -> p (a k) n", p=P)
    phase_norm(core, h, xt, core.mod_scale[0], shift=core.mod_shift[0], scratch=142,
               ahead=first_pieces(core, (102, 118), w[:, :, WI0 + 8 - P:WI0 + 8]))
    columns = lambda kb, start: [([w[:, :, start + n * P:start + (n + 1) * P]], xt, core.view3(kb, 4, L)[:, n, :]) for n in range(4)]
    core.wi = core.tiny2[:, 300:364].rearrange("p (t h) -> p t h", t=TT)
    phase_rows_proj(core, [(w[:, :, WI0 + 8 - P:WI0 + 8], xt, lambda t: core.wi[:, t, :], ACT.Copy)], (102, 118), ahead=2)
    phase_cols_gemm(core, columns(QIT_KB, QI0) + [([w[:, :, KI0:KI0 + 64]] * 2, xt, core.view(KIT_KB, L))], 70)
    phase_index_scores(core)
    selection = Selection(core)
    phase_cols_gemm(core, columns(QAT_KB, QA0) + columns(KAT_KB, KA0) + columns(QBT_KB, QB0), (118, 126, 178, 186),
                    beside=lambda dve: selection.rounds(dve, 7.2))
    va, ckv = core.view3(VA_KB, TT, 512), core.view3(CKV_KB, TT, RANK)
    phase_rows_proj(core, [(w[:, :, VA0:VA0 + 512], xt, lambda t: va[:, t, :], ACT.Copy),
                           (w[:, :, CK0:CK0 + RANK], xt, lambda t: ckv[:, t, :], ACT.Copy)], (118, 178),
                    beside=lambda dve: selection.rounds(dve, 14.0))
    phase_latent(core, beside=lambda dve: selection.rounds(dve, 14.0))
    phase_attention(core, sparse=False, selection=selection)
    phase_attention(core, sparse=True)
    mix, mixt = core.view3(MIX_KB, TT, D), Split(core, 70, 8, L)
    w_out = ap["w_out_2"].rearrange("a (k p) n -> p (a k) n", p=P)
    phase_mix_transpose(core, mix, mixt, first_pieces(core, (134, 150), w_out[:, :, 0:BANK]))
    h, xt = core.view3(H2_KB, TT, D), Split(core, 70, KT, L)
    phase_rows_gemm(core, mixt, ap["w_out_2"], h, gate=core.view(GA1_KB, D), residual=saved, ring_kb=(134, 150, 166), tmp_kb=182, ahead=2)
    places = {"ft": 6, "ring": 134, "w2": 166, "act": 182, "full": 186, "tmp": 190}
    phase_norm(core, h, xt, core.mod_scale[1], shift=core.mod_shift[1], scratch=182, ahead=first_up(core, places, True))
    phase_ffn(core, xt, h, core.view(GA2_KB, D), places)
    phase_final_norm(core, h, ap["g_final_2"][:], 134, ap["out"])


def build_program(nc, ap):
    core = Core(nc, ap)
    first_block(core)
    second_block(core)


def kernel(**inputs):
    import concourse.bacc as bacc
    from concourse.bass_utils import run_bass_kernel_spmd

    nc = bacc.Bacc("TRN2", target_bir_lowering=False, num_devices=1)
    arrays, ap = {}, {}
    for name, value in [*inputs.items(), *constants().items()]:
        a = np.ascontiguousarray(value)
        arrays[f"in_{name}_dram"] = a
        ap[name] = nc.dram_tensor(f"in_{name}_dram", a.shape, mybir.dt.from_np(a.dtype), kind="ExternalInput").ap()
    ap["out"] = nc.dram_tensor("out_0_dram", (1, L, D), F32, kind="ExternalOutput").ap()
    build_program(nc, ap)
    r = run_bass_kernel_spmd(nc, [arrays], core_ids=[0])
    return r.results[0]["out_0_dram"]
```
